# Optimizing a Trainium2 kernel written in Bass

```python
import math
import jax, jax.numpy as jnp
from jax import lax
import numpy as np

D_MODEL = 1024
BATCH = 1
SEQ = 256
DEPTH = 2
DEC_BATCH = 8
DEC_SEQ = 8
PAST_LEN = 1024
PAGE_SIZE = 128

HEAD_DIM = 64
SB_HEADS = D_MODEL // 128
SB_WIDTH = SB_HEADS * HEAD_DIM
GLA_HEADS = 4
GLA_DV = D_MODEL // (2 * GLA_HEADS)
GLA_DK = GLA_DV // 2
GLA_GATE_RANK = 16
GLA_TAU = 16.0
GLA_CHUNK = 64
EVEN_IN = 3 * SB_WIDTH + 2 * GLA_HEADS * GLA_DK + 2 * GLA_HEADS * GLA_DV + GLA_GATE_RANK
EVEN_MIX = SB_WIDTH + GLA_HEADS * GLA_DV
NSA_HEADS = D_MODEL // HEAD_DIM
NSA_KV_HEADS = 4
NSA_GROUP = NSA_HEADS // NSA_KV_HEADS
CMP_BLOCK = 32
CMP_STRIDE = 16
CMP_HIDDEN = 2 * HEAD_DIM
SLC_BLOCK = 64
SLC_TOPN = 16
WINDOW = 512
ODD_IN = NSA_HEADS * HEAD_DIM + 6 * NSA_KV_HEADS * HEAD_DIM + 3 * NSA_HEADS
ODD_MIX = NSA_HEADS * HEAD_DIM
REL_BUCKETS = 32
REL_MAX_DIST = 1024
D_FF = 256 * ((8 * D_MODEL // 3 + 255) // 256)
Q_BLOCK = 128
N_EVEN = (DEPTH + 1) // 2
N_ODD = DEPTH // 2
EPS = 1e-6
NEG = -1e30
FORCE = 1e6

kernel_name = "hybrid_stickbreak_gla_nsa_macaron_step"

def _offsets(sizes):
    out, acc = [], 0
    for s in sizes[:-1]:
        acc += s
        out.append(acc)
    return out

def rms(x, g):
    xf = x.astype(jnp.float32)
    y = xf * lax.rsqrt(jnp.mean(xf * xf, axis=-1, keepdims=True) + EPS)
    return (y * g.astype(jnp.float32)).astype(x.dtype)

def modulate(x, g, shift, scale):
    return rms(x, g) * (1 + scale) + shift

def swiglu(h, w_in, w_out):
    a, b = jnp.split(h @ w_in, 2, axis=-1)
    return (jax.nn.silu(a) * b) @ w_out

def masked_softmax(s, mask):
    s = jnp.where(mask, s, NEG)
    m = jnp.max(s, axis=-1, keepdims=True)
    p = jnp.where(mask, jnp.exp(s - m), 0.0)
    return p / jnp.maximum(jnp.sum(p, axis=-1, keepdims=True), 1e-30)

def rel_bucket(dist):
    exact = REL_BUCKETS // 2
    d = jnp.maximum(dist, 0)
    ratio = jnp.log(jnp.maximum(d, exact).astype(jnp.float32) / exact) / math.log(REL_MAX_DIST / exact)
    large = jnp.minimum(exact + (ratio * (REL_BUCKETS - exact)).astype(jnp.int32), REL_BUCKETS - 1)
    return jnp.where(d < exact, d, large)

def gather_pages(pool, page_table):
    g = pool[page_table]
    return g.reshape(g.shape[0], -1, pool.shape[2], pool.shape[3])

def sb_mixer(q, k, v, q_base):
    B, L, H, dh = q.shape
    blk = min(Q_BLOCK, L)
    nblk = L // blk
    k_pos = jnp.arange(k.shape[1])
    qb = q.reshape(B, nblk, blk, H, dh).swapaxes(0, 1)

    def one(args):
        qi, i = args
        q_pos = q_base + i * blk + jnp.arange(blk)
        z = jnp.einsum('bqhd,bkhd->bhqk', qi, k).astype(jnp.float32) * (dh ** -0.5)
        before = k_pos[None, :] < q_pos[:, None]
        log_keep = jnp.where(before, jax.nn.log_sigmoid(-z), 0.0)
        after = lax.cumsum(log_keep, axis=3, reverse=True) - log_keep
        w = jnp.where(before, jnp.exp(jax.nn.log_sigmoid(z) + after), 0.0)
        return jnp.einsum('bhqk,bkhd->bqhd', w.astype(v.dtype), v)

    o = lax.map(one, (qb, jnp.arange(nblk)))
    return o.swapaxes(0, 1).reshape(B, L, H, dh)

def gla_chunked(q, k, v, log_a, s0):
    B, L, H, dk = q.shape
    dv = v.shape[-1]
    C = min(GLA_CHUNK, L)
    n = L // C
    f32 = jnp.float32

    def to_chunks(t):
        return t.astype(f32).reshape(B, n, C, H, t.shape[-1]).transpose(1, 0, 3, 2, 4)

    qc, kc, vc, ac = to_chunks(q), to_chunks(k), to_chunks(v), to_chunks(log_a)
    causal = jnp.tril(jnp.ones((C, C), bool))

    def step(s, inp):
        qi, ki, vi, ai = inp
        b = jnp.cumsum(ai, axis=2)
        b_last = b[:, :, -1:, :]
        q_in = qi * jnp.exp(b)
        k_in = ki * jnp.exp(-b)
        att = jnp.where(causal, jnp.einsum('bhcd,bhed->bhce', q_in, k_in), 0.0)
        o = jnp.einsum('bhce,bhev->bhcv', att, vi) + jnp.einsum('bhcd,bhdv->bhcv', q_in, s)
        k_dec = ki * jnp.exp(b_last - b)
        s_new = jnp.exp(b_last[:, :, 0, :])[..., None] * s + jnp.einsum('bhcd,bhcv->bhdv', k_dec, vi)
        return s_new, o

    s_fin, o = lax.scan(step, s0.astype(f32), (qc, kc, vc, ac))
    return o.transpose(1, 0, 3, 2, 4).reshape(B, L, H, dv), s_fin

def even_mixer(h, w_in, w_a2, b_a2, onorm_g, w_out, past):
    B, L, _ = h.shape
    sizes = [SB_WIDTH] * 3 + [GLA_HEADS * GLA_DK] * 2 + [GLA_HEADS * GLA_DV] * 2 + [GLA_GATE_RANK]
    qa, ka, va, qb, kb, vb, rb, a1 = jnp.split(h @ w_in, _offsets(sizes), axis=-1)
    qa = qa.reshape(B, L, SB_HEADS, HEAD_DIM)
    ka = ka.reshape(B, L, SB_HEADS, HEAD_DIM)
    va = va.reshape(B, L, SB_HEADS, HEAD_DIM)
    qb = qb.reshape(B, L, GLA_HEADS, GLA_DK) * (GLA_DK ** -0.5)
    kb = kb.reshape(B, L, GLA_HEADS, GLA_DK)
    vb = vb.reshape(B, L, GLA_HEADS, GLA_DV)
    log_a = (jax.nn.log_sigmoid((a1 @ w_a2 + b_a2).astype(jnp.float32)) / GLA_TAU).reshape(B, L, GLA_HEADS, GLA_DK)
    if past is None:
        q_base = 0
        k_all, v_all = ka, va
        s0 = jnp.zeros((B, GLA_HEADS, GLA_DK, GLA_DV), jnp.float32)
    else:
        q_base = past['q_base']
        k_all = jnp.concatenate([past['sb_k'], ka], axis=1)
        v_all = jnp.concatenate([past['sb_v'], va], axis=1)
        s0 = past['gla']
    o_a = sb_mixer(qa, k_all, v_all, q_base)
    o_b, s_fin = gla_chunked(qb, kb, vb, log_a, s0)
    o_b = rms(o_b.astype(h.dtype), onorm_g) * jax.nn.silu(rb).reshape(B, L, GLA_HEADS, GLA_DV)
    out = jnp.concatenate([o_a.reshape(B, L, -1), o_b.reshape(B, L, -1)], axis=-1) @ w_out
    return out, (ka, va, s_fin.astype(h.dtype))

def compress(x, w1, b1, w2, b2):
    B, T, H, dh = x.shape
    nseg = T // CMP_STRIDE
    seg = x[:, :nseg * CMP_STRIDE].reshape(B, nseg, CMP_STRIDE, H, dh).transpose(0, 1, 3, 2, 4)
    seg = seg.reshape(B, nseg, H, CMP_STRIDE * dh)
    r = CMP_BLOCK // CMP_STRIDE
    w1s = w1.reshape(r, CMP_STRIDE * dh, w1.shape[-1])
    nb = nseg - r + 1
    hid = b1
    for m in range(r):
        hid = hid + jnp.einsum('bnhf,fe->bnhe', seg[:, m:m + nb], w1s[m])
    return jax.nn.gelu(hid) @ w2 + b2

def nsa_block(q, g, q_pos, kc, vc, c_end, ks_t, vs_t, cover, kw, vw, w_pos, rel_table):
    B, Lq, Hkv, G, dh = q.shape
    f32 = jnp.float32
    scale = dh ** -0.5

    def bias_2d(dist):
        b = rel_table[rel_bucket(dist)]
        return b.reshape(Lq, -1, Hkv, G).transpose(2, 3, 0, 1).astype(f32)

    dist_c = q_pos[:, None] - c_end[None, :]
    s_c = jnp.einsum('bqhgd,bnhd->bhgqn', q, kc).astype(f32) * scale + bias_2d(dist_c)
    p_c = masked_softmax(s_c, dist_c >= 0)
    o_c = jnp.einsum('bhgqn,bnhd->bqhgd', p_c.astype(vc.dtype), vc)
    n_sel = ks_t.shape[2]
    imp = jnp.einsum('bhgqn,nj->bhqj', p_c, cover)
    j = jnp.arange(n_sel)[None, :]
    cur = (q_pos // SLC_BLOCK)[:, None]
    valid = j * SLC_BLOCK <= q_pos[:, None]
    forced = valid & ((j == 0) | (j == cur) | (j == cur - 1))
    score = jnp.where(forced, FORCE, jnp.where(valid, imp, -FORCE))
    _, idx = lax.top_k(score, min(SLC_TOPN, n_sel))
    bi = jnp.arange(B)[:, None, None, None]
    hi = jnp.arange(Hkv)[None, :, None, None]
    kg = ks_t[bi, hi, idx].reshape(B, Hkv, Lq, -1, dh)
    vg = vs_t[bi, hi, idx].reshape(B, Hkv, Lq, -1, dh)
    s_pos = (idx[..., None] * SLC_BLOCK + jnp.arange(SLC_BLOCK)).reshape(B, Hkv, Lq, -1)
    tg = rel_table.reshape(REL_BUCKETS, Hkv, G)
    b_s = tg[rel_bucket(q_pos[:, None] - s_pos), hi].transpose(0, 1, 4, 2, 3).astype(f32)
    s_s = jnp.einsum('bqhgd,bhqkd->bhgqk', q, kg).astype(f32) * scale + b_s
    p_s = masked_softmax(s_s, (s_pos <= q_pos[:, None])[:, :, None])
    o_s = jnp.einsum('bhgqk,bhqkd->bqhgd', p_s.astype(vg.dtype), vg)
    dist_w = q_pos[:, None] - w_pos[None, :]
    s_w = jnp.einsum('bqhgd,bkhd->bhgqk', q, kw).astype(f32) * scale + bias_2d(dist_w)
    p_w = masked_softmax(s_w, (dist_w >= 0) & (dist_w < WINDOW) & (w_pos[None, :] >= 0))
    o_w = jnp.einsum('bhgqk,bkhd->bqhgd', p_w.astype(vw.dtype), vw)
    return g[..., 0:1] * o_c + g[..., 1:2] * o_s + g[..., 2:3] * o_w

def nsa_mixer(q, gates, kc, vc, ks_t, vs_t, kw_src, vw_src, q_base, rel_table):
    B, L, Hkv, G, dh = q.shape
    blk = min(Q_BLOCK, L)
    nblk = L // blk
    nb = kc.shape[1]
    c_end = jnp.arange(nb) * CMP_STRIDE + CMP_BLOCK - 1
    ci = jnp.arange(nb) * CMP_STRIDE
    sj = jnp.arange(ks_t.shape[2]) * SLC_BLOCK
    cover = ((ci[:, None] < sj[None, :] + SLC_BLOCK) & (ci[:, None] + CMP_BLOCK > sj[None, :])).astype(jnp.float32)
    qb = q.reshape(B, nblk, blk, Hkv, G, dh).swapaxes(0, 1)
    gb = gates.reshape(B, nblk, blk, Hkv, G, 3).swapaxes(0, 1)

    def one(args):
        qi, gi, i = args
        q_pos = q_base + i * blk + jnp.arange(blk)
        kw = lax.dynamic_slice_in_dim(kw_src, i * blk, blk + WINDOW, axis=1)
        vw = lax.dynamic_slice_in_dim(vw_src, i * blk, blk + WINDOW, axis=1)
        w_pos = q_base + i * blk - WINDOW + jnp.arange(blk + WINDOW)
        return nsa_block(qi, gi, q_pos, kc, vc, c_end, ks_t, vs_t, cover, kw, vw, w_pos, rel_table)

    o = lax.map(one, (qb, gb, jnp.arange(nblk)))
    return o.swapaxes(0, 1).reshape(B, L, Hkv, G, dh)

def odd_mixer(h, w_in, qk_g, cmp_w1, cmp_b1, cmp_w2, cmp_b2, rel_table, w_out, past):
    B, L, _ = h.shape
    kvw = NSA_KV_HEADS * HEAD_DIM
    sizes = [NSA_HEADS * HEAD_DIM] + [kvw] * 6 + [3 * NSA_HEADS]
    q, kc, vc, ks, vs, kw, vw, gt = jnp.split(h @ w_in, _offsets(sizes), axis=-1)

    def kv(t):
        return t.reshape(B, L, NSA_KV_HEADS, HEAD_DIM)

    q = rms(q.reshape(B, L, NSA_HEADS, HEAD_DIM), qk_g[0]).reshape(B, L, NSA_KV_HEADS, NSA_GROUP, HEAD_DIM)
    kc, vc, vs, vw = kv(kc), kv(vc), kv(vs), kv(vw)
    ks = rms(kv(ks), qk_g[2])
    kw = rms(kv(kw), qk_g[3])
    gates = jax.nn.sigmoid(gt.reshape(B, L, NSA_KV_HEADS, NSA_GROUP, 3))
    pad4 = lambda t, n: jnp.pad(t, ((0, 0), (n, 0), (0, 0), (0, 0)))
    if past is None:
        q_base = 0
        kc_all, vc_all, ks_all, vs_all = kc, vc, ks, vs
        kw_src, vw_src = pad4(kw, WINDOW), pad4(vw, WINDOW)
        w_keep = min(WINDOW, L)
        win_k_new, win_v_new = kw[:, L - w_keep:], vw[:, L - w_keep:]
    else:
        q_base = past['q_base']
        kc_all = jnp.concatenate([past['cmp_k'], kc], axis=1)
        vc_all = jnp.concatenate([past['cmp_v'], vc], axis=1)
        ks_all = jnp.concatenate([past['slc_k'], ks], axis=1)
        vs_all = jnp.concatenate([past['slc_v'], vs], axis=1)
        wk = jnp.concatenate([past['win_k'], kw], axis=1)
        wv = jnp.concatenate([past['win_v'], vw], axis=1)
        front = WINDOW - past['win_k'].shape[1]
        kw_src, vw_src = pad4(wk, front), pad4(wv, front)
        win_k_new, win_v_new = wk[:, L:], wv[:, L:]
    k_cmp = rms(compress(kc_all, cmp_w1[0], cmp_b1[0], cmp_w2[0], cmp_b2[0]), qk_g[1])
    v_cmp = compress(vc_all, cmp_w1[1], cmp_b1[1], cmp_w2[1], cmp_b2[1])
    T = ks_all.shape[1]
    n_sel = -(-T // SLC_BLOCK)
    tail = n_sel * SLC_BLOCK - T
    ks_p = jnp.pad(ks_all, ((0, 0), (0, tail), (0, 0), (0, 0)))
    vs_p = jnp.pad(vs_all, ((0, 0), (0, tail), (0, 0), (0, 0)))
    ks_t = ks_p.reshape(B, n_sel, SLC_BLOCK, NSA_KV_HEADS, HEAD_DIM).transpose(0, 3, 1, 2, 4)
    vs_t = vs_p.reshape(B, n_sel, SLC_BLOCK, NSA_KV_HEADS, HEAD_DIM).transpose(0, 3, 1, 2, 4)
    o = nsa_mixer(q, gates, k_cmp, v_cmp, ks_t, vs_t, kw_src, vw_src, q_base, rel_table)
    out = o.reshape(B, L, ODD_MIX) @ w_out
    return out, (kc, vc, ks, vs, win_k_new, win_v_new)

def trunk(x, c, past, norm_g, ada_w, ada_b, ffn_w_in, ffn_w_out, even_w_in, gla_w_a2, gla_b_a2,
          gla_onorm_g, even_w_out, odd_w_in, nsa_qk_g, cmp_w1, cmp_b1, cmp_w2, cmp_b2, rel_table, odd_w_out):
    B = x.shape[0]
    even_states, odd_states = [], []
    for li in range(DEPTH):
        mod = (jax.nn.silu(c) @ ada_w[li] + ada_b[li]).reshape(B, 9, 1, D_MODEL)
        h = modulate(x, norm_g[li, 0], mod[:, 0], mod[:, 1])
        x = x + 0.5 * mod[:, 2] * swiglu(h, ffn_w_in[li, 0], ffn_w_out[li, 0])
        h = modulate(x, norm_g[li, 1], mod[:, 3], mod[:, 4])
        if li % 2 == 0:
            e = li // 2
            lp = None
            if past is not None:
                pt = past['page_table']
                lp = {'q_base': past['q_base'], 'sb_k': gather_pages(past['sb_k'][e], pt),
                      'sb_v': gather_pages(past['sb_v'][e], pt), 'gla': past['gla'][e]}
            out, st = even_mixer(h, even_w_in[e], gla_w_a2[e], gla_b_a2[e], gla_onorm_g[e], even_w_out[e], lp)
            even_states.append(st)
        else:
            o_i = li // 2
            lp = None
            if past is not None:
                pt = past['page_table']
                lp = {'q_base': past['q_base'],
                      'cmp_k': gather_pages(past['cmp_k'][o_i], pt), 'cmp_v': gather_pages(past['cmp_v'][o_i], pt),
                      'slc_k': gather_pages(past['slc_k'][o_i], pt), 'slc_v': gather_pages(past['slc_v'][o_i], pt),
                      'win_k': past['win_k'][o_i], 'win_v': past['win_v'][o_i]}
            out, st = odd_mixer(h, odd_w_in[o_i], nsa_qk_g[o_i], cmp_w1[o_i], cmp_b1[o_i], cmp_w2[o_i], cmp_b2[o_i],
                                rel_table, odd_w_out[o_i], lp)
            odd_states.append(st)
        x = x + mod[:, 5] * out
        h = modulate(x, norm_g[li, 2], mod[:, 6], mod[:, 7])
        x = x + 0.5 * mod[:, 8] * swiglu(h, ffn_w_in[li, 1], ffn_w_out[li, 1])
    even_new = [jnp.stack([s[i] for s in even_states]) for i in range(3)]
    odd_new = [jnp.stack([s[i] for s in odd_states]) for i in range(6)]
    return x, even_new, odd_new

def setup_inputs(seed: int = 0) -> dict:
    key = jax.random.key(seed)
    ks = jax.random.split(key, 40)
    n_pages = PAST_LEN // PAGE_SIZE
    n_pool = (DEC_BATCH * n_pages * 5) // 4
    w_buf = min(WINDOW, PAST_LEN)
    f32 = jnp.float32

    def nrm(k, shape, s=1.0):
        return s * jax.random.normal(k, shape, f32)

    page_table = jax.random.permutation(ks[0], n_pool)[:DEC_BATCH * n_pages].reshape(DEC_BATCH, n_pages).astype(jnp.int32)
    return {
        'x_prompt': nrm(ks[1], (BATCH, SEQ, D_MODEL)),
        'x_sample': nrm(ks[2], (DEC_BATCH, DEC_SEQ, D_MODEL)),
        'cache_sb_k': nrm(ks[3], (N_EVEN, n_pool, PAGE_SIZE, SB_HEADS, HEAD_DIM)),
        'cache_sb_v': nrm(ks[4], (N_EVEN, n_pool, PAGE_SIZE, SB_HEADS, HEAD_DIM)),
        'state_gla': nrm(ks[5], (N_EVEN, DEC_BATCH, GLA_HEADS, GLA_DK, GLA_DV)),
        'cache_cmp_k': nrm(ks[6], (N_ODD, n_pool, PAGE_SIZE, NSA_KV_HEADS, HEAD_DIM)),
        'cache_cmp_v': nrm(ks[7], (N_ODD, n_pool, PAGE_SIZE, NSA_KV_HEADS, HEAD_DIM)),
        'cache_slc_k': nrm(ks[8], (N_ODD, n_pool, PAGE_SIZE, NSA_KV_HEADS, HEAD_DIM)),
        'cache_slc_v': nrm(ks[9], (N_ODD, n_pool, PAGE_SIZE, NSA_KV_HEADS, HEAD_DIM)),
        'cache_win_k': nrm(ks[10], (N_ODD, DEC_BATCH, w_buf, NSA_KV_HEADS, HEAD_DIM)),
        'cache_win_v': nrm(ks[11], (N_ODD, DEC_BATCH, w_buf, NSA_KV_HEADS, HEAD_DIM)),
        'page_table': page_table,
        'c_prompt': nrm(ks[12], (BATCH, D_MODEL)),
        'c_sample': nrm(ks[13], (DEC_BATCH, D_MODEL)),
        'norm_g': 1.0 + nrm(ks[14], (DEPTH, 3, D_MODEL), 0.02),
        'ada_w': nrm(ks[15], (DEPTH, D_MODEL, 9 * D_MODEL), 0.5 * D_MODEL ** -0.5),
        'ada_b': nrm(ks[16], (DEPTH, 9 * D_MODEL), 0.02),
        'ffn_w_in': nrm(ks[17], (DEPTH, 2, D_MODEL, 2 * D_FF), D_MODEL ** -0.5),
        'ffn_w_out': nrm(ks[18], (DEPTH, 2, D_FF, D_MODEL), D_FF ** -0.5),
        'even_w_in': nrm(ks[19], (N_EVEN, D_MODEL, EVEN_IN), D_MODEL ** -0.5),
        'gla_w_a2': nrm(ks[20], (N_EVEN, GLA_GATE_RANK, GLA_HEADS * GLA_DK), GLA_GATE_RANK ** -0.5),
        'gla_b_a2': nrm(ks[21], (N_EVEN, GLA_HEADS * GLA_DK), 0.1),
        'gla_onorm_g': 1.0 + nrm(ks[22], (N_EVEN, GLA_DV), 0.02),
        'even_w_out': nrm(ks[23], (N_EVEN, EVEN_MIX, D_MODEL), EVEN_MIX ** -0.5),
        'odd_w_in': nrm(ks[24], (N_ODD, D_MODEL, ODD_IN), D_MODEL ** -0.5),
        'nsa_qk_g': 1.0 + nrm(ks[25], (N_ODD, 4, HEAD_DIM), 0.02),
        'cmp_w1': nrm(ks[26], (N_ODD, 2, CMP_BLOCK * HEAD_DIM, CMP_HIDDEN), (CMP_BLOCK * HEAD_DIM) ** -0.5),
        'cmp_b1': nrm(ks[27], (N_ODD, 2, CMP_HIDDEN), 0.02),
        'cmp_w2': nrm(ks[28], (N_ODD, 2, CMP_HIDDEN, HEAD_DIM), CMP_HIDDEN ** -0.5),
        'cmp_b2': nrm(ks[29], (N_ODD, 2, HEAD_DIM), 0.02),
        'rel_table': nrm(ks[30], (REL_BUCKETS, NSA_HEADS), 0.5),
        'odd_w_out': nrm(ks[31], (N_ODD, ODD_MIX, D_MODEL), ODD_MIX ** -0.5),
    }

def reference(x_prompt, x_sample, cache_sb_k, cache_sb_v, state_gla, cache_cmp_k, cache_cmp_v,
              cache_slc_k, cache_slc_v, cache_win_k, cache_win_v, page_table, c_prompt, c_sample,
              norm_g, ada_w, ada_b, ffn_w_in, ffn_w_out, even_w_in, gla_w_a2, gla_b_a2, gla_onorm_g,
              even_w_out, odd_w_in, nsa_qk_g, cmp_w1, cmp_b1, cmp_w2, cmp_b2, rel_table, odd_w_out):
    y_prompt, p_even, p_odd = trunk(
        x_prompt, c_prompt, None, norm_g, ada_w, ada_b, ffn_w_in, ffn_w_out, even_w_in, gla_w_a2, gla_b_a2,
        gla_onorm_g, even_w_out, odd_w_in, nsa_qk_g, cmp_w1, cmp_b1, cmp_w2, cmp_b2, rel_table, odd_w_out)
    past = {'q_base': page_table.shape[1] * cache_sb_k.shape[2], 'page_table': page_table,
            'sb_k': cache_sb_k, 'sb_v': cache_sb_v, 'gla': state_gla,
            'cmp_k': cache_cmp_k, 'cmp_v': cache_cmp_v, 'slc_k': cache_slc_k, 'slc_v': cache_slc_v,
            'win_k': cache_win_k, 'win_v': cache_win_v}
    y_sample, s_even, s_odd = trunk(
        x_sample, c_sample, past, norm_g, ada_w, ada_b, ffn_w_in, ffn_w_out, even_w_in, gla_w_a2, gla_b_a2,
        gla_onorm_g, even_w_out, odd_w_in, nsa_qk_g, cmp_w1, cmp_b1, cmp_w2, cmp_b2, rel_table, odd_w_out)
    p_sb_k, p_sb_v, p_gla = p_even
    p_cmp_k, p_cmp_v, p_slc_k, p_slc_v, p_win_k, p_win_v = p_odd
    s_sb_k, s_sb_v, s_gla = s_even
    s_cmp_k, s_cmp_v, s_slc_k, s_slc_v, s_win_k, s_win_v = s_odd
    return (y_prompt, y_sample, p_sb_k, p_sb_v, p_gla, p_cmp_k, p_cmp_v, p_slc_k, p_slc_v, p_win_k, p_win_v,
            s_sb_k, s_sb_v, s_gla, s_cmp_k, s_cmp_v, s_slc_k, s_slc_v, s_win_k, s_win_v)


_drawn_inputs = setup_inputs


def setup_inputs(seed=0):
    import zlib

    import numpy as np

    out = dict(_drawn_inputs(seed))
    spreads = {}
    factors = {'cache_cmp_k': 4.326,
     'cache_cmp_v': 3.082,
     'cache_slc_k': 7.74,
     'cache_slc_v': 6.269,
     'gla_onorm_g': 8.0,
     'nsa_qk_g': 3.158,
     'cmp_b1': 8.0,
     'cmp_b2': 8.0}
    for name, (base, spread) in spreads.items():
        noise = np.random.default_rng([zlib.crc32(name.encode()), seed]).standard_normal(out[name].shape)
        drawn = base * np.exp(spread * noise) if base else spread * noise
        out[name] = __import__('jax').numpy.asarray(drawn.astype(out[name].dtype))
    for name, factor in factors.items():
        out[name] = (out[name] * factor).astype(out[name].dtype)
    return out
```

```python
import math
from contextlib import ExitStack

import numpy as np
import concourse.bass as bass
from concourse import mybir

F32 = mybir.dt.float32
I32 = mybir.dt.int32
ACT = mybir.ActivationFunctionType
ALU = mybir.AluOpType
AX = mybir.AxisListType

P = 128
D = 1024
KT = D // P
NPR = 256
NB = 8
LS = 8
NT = NPR + NB * LS
NSEQ = 1 + NB
DFF = 2816
FT = DFF // P
PAST = 1024
PAGE = 128
NPG = PAST // PAGE
NPOOL = NB * NPG * 5 // 4
WIN = 512
RING = 4
SLOT = KT * 512
ADA_SLOTS = 9 * D // 512
IN_SLOTS = 2 * DFF // 512
OUT_GROUPS = (FT + KT - 1) // KT
OUT_SLOTS = 2 * OUT_GROUPS
EVEN_SLOTS = 6
ODD_SLOTS = 5
EPS = 1e-6
NEG = -1e30
SCALE = 64 ** -0.5
DIST_LO = -127
DIST_HI = PAST + LS - 1
NDIST = DIST_HI - DIST_LO + 1
NDIST_P = 255 - DIST_LO + 1
TILE_ROWS = [128, 128, 64]


def rep(ap, axis, n):
    dims = [list(x) for x in ap.ap]
    return bass.AP(ap.tensor, ap.offset, dims[:axis] + [[0, n]] + dims[axis:])


class Signal:

    def __init__(self, ctx, nc, name):
        self.sem = ctx.enter_context(nc.semaphore(name))
        self.base = 0
        self.count = 0

    def at(self, n):
        return self.base + n

    def by(self, ins, n=1):
        ins.then_inc(self.sem, n)
        return ins

    def close(self, n):
        self.base = self.base + n


def build(nc, io):
    ctx = ExitStack()
    with ctx:
        def sb(name, shape, dt=F32, where=ctx):
            return where.enter_context(nc.sbuf_tensor("sb_" + name, shape, dt))

        def signal(name):
            return Signal(ctx, nc, name)

        PS = ctx.enter_context(nc.psum_tensor("PS", [P, 8, 512], F32))
        X = sb("X", [P, KT, NT])
        H = sb("H", [P, KT, NT])
        OT = sb("OT", [P, KT, NT])
        ring = sb("ring", [P, RING, KT, 512])
        silu_c = sb("silu_c", [P, KT, NSEQ])
        mod = sb("mod", [P, 9, KT, NSEQ])
        gain = sb("gain", [P, 3, KT, NSEQ])
        norm_g = sb("norm_g", [P, 2, 3, KT])
        ada_b = sb("ada_b", [P, 2, 9 * KT])
        rstd = sb("rstd", [P, NT])
        ones = sb("ones", [P, P])
        ident = sb("ident", [P, P])
        halves = sb("halves", [P, P])
        later = sb("later", [P, P])
        strict = sb("strict", [P, P])

        landed = [signal(f"landed{r}") for r in range(RING)]
        slot_done = signal("slot_done")
        slot_read = signal("slot_read")
        loads = signal("loads")
        pool_step = signal("pool_step")
        dve_step = signal("dve_step")
        act_step = signal("act_step")
        squared = signal("squared")
        summed = signal("summed")
        variance = signal("variance")
        deviation = signal("deviation")
        centred = signal("centred")
        h_ready = signal("h_ready")
        gate_ready = signal("gate_ready")
        stored = signal("stored")

        NSLOT = io["w_slots"].shape[0]

        def slot_at(n0, it, j):
            return (n0 + j) % RING, 16 * ((n0 + j) // RING + 1) + it * 16

        def refill(sp, n0, it, j):
            r, _ = slot_at(n0, 0, j)
            sp.wait_ge(slot_done.sem, n0 + j + 1 + it * RING)
            n = n0 + j + RING + it * RING
            src = io["w_slots"][n] if isinstance(n, int) else io["w_slots"][bass.ds(n, 1), :, :].rearrange("a p n -> p (a n)")
            sp.dma_start(ring[:, r, :, :].rearrange("p k n -> p (k n)"), src).then_inc(landed[r].sem, 16)

        def refill_all(sp, n0, count):
            whole = count // RING
            if n0 + count + RING > NSLOT:
                whole = 0
            if whole > 1:
                with sp.Fori(0, whole) as it:
                    for j in range(RING):
                        refill(sp, n0, it, j)
            else:
                whole = 0
            for j in range(whole * RING, count):
                if n0 + j + RING < NSLOT:
                    refill(sp, n0, 0, j)

        class Chain:

            def __init__(self, eng, sig):
                self.eng, self.sig, self.n, self.start = eng, sig, 0, 0

            def __call__(self, ins):
                ins.then_inc(self.sig.sem, 1)
                self.n += 1
                self.eng.wait_ge(self.sig.sem, self.sig.at(self.n + self.start))

            def loop(self, it, per):
                self.start = self.n + it * per
                self.n, self.before, self.per = 0, self.n, per

            def done(self, times):
                assert self.n == self.per, (self.n, self.per)
                self.n, self.start = self.before + times * self.per, 0

        with nc.Block(no_gpsimd_drain=True) as block:
            @block.sync
            def _(sp):
                for dst, src in ((silu_c, "cT"), (X, "xT"), (norm_g, "norm_gT"), (ada_b, "ada_bT")):
                    sp.dma_start(dst[:], io[src]).then_inc(loads.sem, 16)
                for n in range(RING):
                    sp.dma_start(ring[:, n, :, :].rearrange("p k n -> p (k n)"), io["w_slots"][n])\
                        .then_inc(landed[n].sem, 16)

            @block.scalar
            def _(act):
                act.wait_ge(loads.sem, 64)
                nc.scalar.activation(silu_c[:], silu_c[:], ACT.Silu).then_inc(act_step.sem, 1)

            @block.gpsimd
            def _(pool):
                step = Chain(pool, pool_step)
                pool.memset(ones[:], 1.0)
                pool.memset(ident[:], 0.0)
                pool.memset(later[:], 1.0)
                step(pool.memset(strict[:], 1.0))
                pool.memset(halves[:], 0.0)
                step(pool.affine_select(out=ident[:], in_=ident[:], compare_op=ALU.not_equal, fill=1.0,
                                        base=0, pattern=[[-1, P]], channel_multiplier=1))
                step(pool.affine_select(out=later[:], in_=later[:], compare_op=ALU.is_ge, fill=0.0,
                                        base=0, pattern=[[-1, P]], channel_multiplier=1))
                step(pool.affine_select(out=strict[:], in_=strict[:], compare_op=ALU.is_gt, fill=0.0,
                                        base=0, pattern=[[1, P]], channel_multiplier=-1))
                step(pool.memset(halves[0:64, 0:64], 1.0))
                step(pool.memset(halves[64:128, 64:128], 1.0))
                pool_step.count = step.n
        loads.close(64)
        act_step.close(1)
        pool_step.close(pool_step.count)

        def ada_stage(layer, n0):
            with nc.Block(no_gpsimd_drain=True) as block:
                whole, rest = ADA_SLOTS // RING, ADA_SLOTS % RING

                @block.sync
                def _(sp):
                    refill_all(sp, n0, ADA_SLOTS)

                @block.tensor
                def _(pe):
                    def one(it, j):
                        r, there = slot_at(n0, it, j)
                        pe.wait_ge(landed[r].sem, there)
                        if not (isinstance(it, int) and j < 2):
                            pe.wait_ge(slot_read.sem, slot_read.at(j - 1) + it * RING)
                        for m in range(4):
                            for k in range(KT):
                                mm = nc.tensor.matmul(PS[:, j % 2, m * NSEQ:(m + 1) * NSEQ],
                                                      ring[:, r, k, m * P:(m + 1) * P], silu_c[:, k, :],
                                                      start=(k == 0), stop=(k == KT - 1))
                        mm.then_inc(slot_done.sem, 1)
                    for j in range(RING):
                        one(0, j)
                    with pe.Fori(1, whole) as it:
                        for j in range(RING):
                            one(it, j)
                    for j in range(whole * RING, ADA_SLOTS):
                        one(0, j)

                @block.vector
                def _(dve):
                    flat = mod[:].rearrange("p i k s -> p (i k) s")

                    def one(it, j):
                        dve.wait_ge(slot_done.sem, n0 + j + 1 + it * RING)
                        src = PS[:, j % 2, 0:4 * NSEQ].rearrange("p (m s) -> p m s", s=NSEQ)
                        c = 4 * j + it * (4 * RING)
                        at = slice(c, c + 4) if isinstance(c, int) else bass.ds(c, 4)
                        bias = ada_b[:, layer, at]
                        bias = bass.AP(bias.tensor, bias.offset, [list(x) for x in bias.ap] + [[0, NSEQ]])
                        nc.vector.tensor_tensor(flat[:, at, :], src, bias, ALU.add).then_inc(slot_read.sem, 1)
                    for j in range(ADA_SLOTS):
                        one(0, j)
                    dve.wait_ge(slot_read.sem, slot_read.at(ADA_SLOTS))
                    for i in range(3):
                        g = norm_g[:, layer, i, :]
                        g = bass.AP(g.tensor, g.offset, [list(x) for x in g.ap] + [[0, NSEQ]])
                        nc.vector.scalar_tensor_tensor(out=gain[:, i, :, :], in0=mod[:, 3 * i + 1, :, :], scalar=1.0,
                                                       in1=g, op0=ALU.add, op1=ALU.mult).then_inc(dve_step.sem, 1)
                    for i in (2, 8):
                        nc.vector.tensor_scalar(mod[:, i, :, :], mod[:, i, :, :], 0.5, None, ALU.mult)\
                            .then_inc(dve_step.sem, 1)
            slot_read.close(ADA_SLOTS)
            dve_step.close(5)
            return n0 + ADA_SLOTS

        NORM_BANK = 7

        def norm_act(act, i):
            nc.scalar.activation(OT[:], X[:], ACT.Square).then_inc(squared.sem, 1)
            act.wait_ge(variance.sem, variance.at(1))
            nc.scalar.activation(rstd[:], rstd[:], ACT.Sqrt).then_inc(deviation.sem, 1)
            act.wait_ge(centred.sem, centred.at(1))
            for k in range(KT):
                nc.scalar.activation(H[:, k, 0:NPR], H[:, k, 0:NPR], ACT.Identity, bias=mod[:, 3 * i, k, 0:1],
                                     scale=gain[:, i, k, 0:1]).then_inc(h_ready.sem, 1)

        def norm_pe(pe):
            pe.wait_ge(squared.sem, squared.at(1))
            for k in range(KT):
                mm = nc.tensor.matmul(PS[:, NORM_BANK, 0:NT], ones[:], OT[:, k, :], start=(k == 0), stop=(k == KT - 1))
            mm.then_inc(summed.sem, 1)

        def norm_dve(dve, i, step):
            dve.wait_ge(summed.sem, summed.at(1))
            nc.vector.tensor_scalar(rstd[:], PS[:, NORM_BANK, 0:NT], 1.0 / D, EPS, ALU.mult, ALU.add)\
                .then_inc(variance.sem, 1)
            dve.wait_ge(deviation.sem, deviation.at(1))
            step(nc.vector.reciprocal(rstd[:], rstd[:]))
            nc.vector.tensor_tensor(H[:], X[:], rep(rstd[:], 1, KT), ALU.mult).then_inc(centred.sem, 1)
            dve.wait_ge(centred.sem, centred.at(1))
            part = H[:, :, NPR:NT].rearrange("p k (b l) -> p k b l", l=LS)

            def per_seq(t, n):
                a = t[:, n, :, 1:NSEQ]
                return bass.AP(a.tensor, a.offset, [list(x) for x in a.ap] + [[0, LS]])
            step(nc.vector.tensor_tensor(part, part, per_seq(gain, i), ALU.mult))
            nc.vector.tensor_tensor(part, part, per_seq(mod, 3 * i), ALU.add).then_inc(h_ready.sem, 1)

        H_READY = KT + 1

        def norm_close():
            for s in (squared, summed, variance, deviation, centred):
                s.close(1)
            h_ready.close(H_READY)

        def add_gated(dve, step, i, banks, m0):
            for m in range(4):
                nc.vector.scalar_tensor_tensor(out=X[:, m0 + m, 0:NPR], in0=PS[:, banks + m, 0:NPR],
                                               scalar=mod[:, i, m0 + m, 0:1], in1=X[:, m0 + m, 0:NPR],
                                               op0=ALU.mult, op1=ALU.add).then_inc(gate_ready.sem, 1)
            src = PS[:, banks:banks + 4, NPR:NT].rearrange("p m (b l) -> p m b l", l=LS)
            gate = mod[:, i, m0:m0 + 4, 1:NSEQ]
            gate = bass.AP(gate.tensor, gate.offset, [list(x) for x in gate.ap] + [[0, LS]])
            tmp = gated_rows[:].rearrange("p m (b l) -> p m b l", l=LS)
            step(nc.vector.tensor_tensor(tmp, src, gate, ALU.mult))
            part = X[:, m0:m0 + 4, NPR:NT]
            nc.vector.tensor_tensor(part, part, gated_rows[:], ALU.add).then_inc(slot_read.sem, 1)

        gated_rows = sb("gated_rows", [P, 4, NT - NPR])

        def ffn_stage(layer, which, n0):
            ni = 2 * which
            stage = ExitStack()
            with stage:
                G = sb(f"G{layer}{which}", [P, FT, NT], F32, stage)
                S = sb(f"S{layer}{which}", [P, 2, 2, NT], F32, stage)
                whole = IN_SLOTS // RING
                n1 = n0 + IN_SLOTS
                block = stage.enter_context(nc.Block(no_gpsimd_drain=True))

                @block.sync
                def _(sp):
                    refill_all(sp, n0, IN_SLOTS + OUT_SLOTS)

                @block.tensor
                def _(pe):
                    norm_pe(pe)
                    pe.wait_ge(h_ready.sem, h_ready.at(H_READY))

                    def into_hidden(it, j, first):
                        r, there = slot_at(n0, it, j)
                        pe.wait_ge(landed[r].sem, there)
                        if not first:
                            pe.wait_ge(slot_read.sem, slot_read.at(j - 1) + it * RING)
                        for m in range(4):
                            for k in range(KT):
                                mm = nc.tensor.matmul(PS[:, 4 * (j % 2) + m, 0:NT], ring[:, r, k, m * P:(m + 1) * P],
                                                      H[:, k, :], start=(k == 0), stop=(k == KT - 1))
                        mm.then_inc(slot_done.sem, 1)
                    for j in range(RING):
                        into_hidden(0, j, j < 2)
                    with pe.Fori(1, whole) as it:
                        for j in range(RING):
                            into_hidden(it, j, False)
                    for j in range(whole * RING, IN_SLOTS):
                        into_hidden(0, j, False)
                    for half in range(2):
                        for g in range(OUT_GROUPS):
                            j = half * OUT_GROUPS + g
                            r, there = slot_at(n1, 0, j)
                            pe.wait_ge(landed[r].sem, there)
                            tiles = range(KT * g, min(KT * (g + 1), FT))
                            if half == 0:
                                need = IN_SLOTS - 1 if g < OUT_GROUPS - 1 else IN_SLOTS
                                pe.wait_ge(slot_read.sem, slot_read.at(need))
                            for m in range(4):
                                for k in tiles:
                                    mm = nc.tensor.matmul(PS[:, 4 * ((IN_SLOTS + half) % 2) + m, 0:NT],
                                                          ring[:, r, k - KT * g, m * P:(m + 1) * P], G[:, k, :],
                                                          start=(k == 0), stop=(k == FT - 1))
                            mm.then_inc(slot_done.sem, 1)

                @block.scalar
                def _(act):
                    norm_act(act, ni)
                    for j in range(IN_SLOTS):
                        act.wait_ge(slot_done.sem, n0 + j + 1)
                        if j >= 2:
                            act.wait_ge(slot_read.sem, slot_read.at(j - 1))
                        b = 4 * (j % 2)
                        nc.scalar.activation(S[:, j % 2, :, :], PS[:, b:b + 2, 0:NT], ACT.Silu)\
                            .then_inc(act_step.sem, 1)

                @block.vector
                def _(dve):
                    step = Chain(dve, dve_step)
                    norm_dve(dve, ni, step)
                    for j in range(IN_SLOTS):
                        dve.wait_ge(act_step.sem, act_step.at(j + 1))
                        b = 4 * (j % 2)
                        nc.vector.tensor_tensor(G[:, 2 * j:2 * j + 2, :], S[:, j % 2, :, :], PS[:, b + 2:b + 4, 0:NT],
                                                ALU.mult).then_inc(slot_read.sem, 1)
                    for half in range(2):
                        dve.wait_ge(slot_done.sem, n1 + (half + 1) * OUT_GROUPS)
                        if half:
                            dve.wait_ge(slot_read.sem, slot_read.at(IN_SLOTS + 1))
                        add_gated(dve, step, 3 * ni + 2, 4 * ((IN_SLOTS + half) % 2), 4 * half)
                    dve_step.count = step.n
            norm_close()
            act_step.close(IN_SLOTS)
            slot_read.close(IN_SLOTS + 2)
            dve_step.close(dve_step.count)
            gate_ready.close(8)
            return n0 + IN_SLOTS + OUT_SLOTS

        def out_stage(n0):
            with nc.Block(no_gpsimd_drain=True) as block:
                @block.sync
                def _(sp):
                    refill_all(sp, n0, 2)

                @block.tensor
                def _(pe):
                    for half in range(2):
                        r, there = slot_at(n0, 0, half)
                        pe.wait_ge(landed[r].sem, there)
                        for m in range(4):
                            for k in range(KT):
                                mm = nc.tensor.matmul(PS[:, 4 * half + m, 0:NT], ring[:, r, k, m * P:(m + 1) * P],
                                                      OT[:, k, :], start=(k == 0), stop=(k == KT - 1))
                        mm.then_inc(slot_done.sem, 1)

                @block.vector
                def _(dve):
                    step = Chain(dve, dve_step)
                    for half in range(2):
                        dve.wait_ge(slot_done.sem, n0 + half + 1)
                        if half:
                            dve.wait_ge(slot_read.sem, slot_read.at(1))
                        add_gated(dve, step, 5, 4 * half, 4 * half)
                    dve_step.count = step.n
            slot_read.close(2)
            dve_step.close(dve_step.count)
            gate_ready.close(8)
            return n0 + 2

        def project_stage(n0, kinds, tail_w, tail_cols, tail_dst, tail_rows):
            n = len(kinds)
            with nc.Block(no_gpsimd_drain=True) as block:
                @block.sync
                def _(sp):
                    refill_all(sp, n0, n)

                @block.tensor
                def _(pe):
                    norm_pe(pe)
                    pe.wait_ge(h_ready.sem, h_ready.at(H_READY))
                    for j, (transposed, _) in enumerate(kinds):
                        r, there = slot_at(n0, 0, j)
                        pe.wait_ge(landed[r].sem, there)
                        if j >= 2:
                            pe.wait_ge(slot_read.sem, slot_read.at(j - 1))
                        b = 4 * (j % 2)
                        if transposed:
                            for m in range(4):
                                for k in range(KT):
                                    mm = nc.tensor.matmul(PS[:, b + m, 0:NT], ring[:, r, k, m * P:(m + 1) * P],
                                                          H[:, k, :], start=(k == 0), stop=(k == KT - 1))
                        else:
                            for t, rows in enumerate(TILE_ROWS):
                                for k in range(KT):
                                    mm = nc.tensor.matmul(PS[0:rows, b + t, :], H[:, k, t * P:t * P + rows],
                                                          ring[:, r, k, :], start=(k == 0), stop=(k == KT - 1))
                        mm.then_inc(slot_done.sem, 1)
                    pe.wait_ge(slot_read.sem, slot_read.at(n - 1))
                    b = 4 * (n % 2)
                    if tail_rows:
                        for t, rows in enumerate(TILE_ROWS):
                            for k in range(KT):
                                mm = nc.tensor.matmul(PS[0:rows, b + t, 0:tail_cols], H[:, k, t * P:t * P + rows],
                                                      tail_w[:, k, :], start=(k == 0), stop=(k == KT - 1))
                    else:
                        for k in range(KT):
                            mm = nc.tensor.matmul(PS[0:tail_cols, b, 0:NT], tail_w[:, k, :], H[:, k, :],
                                                  start=(k == 0), stop=(k == KT - 1))
                    mm.then_inc(summed.sem, 1)

                @block.scalar
                def _(act):
                    norm_act(act, 1)
                    for j, (transposed, dst) in enumerate(kinds):
                        act.wait_ge(slot_done.sem, n0 + j + 1)
                        b = 4 * (j % 2)
                        if transposed:
                            nc.scalar.activation(dst, PS[:, b:b + 4, 0:NT], ACT.Copy).then_inc(slot_read.sem, 1)
                        else:
                            nc.scalar.activation(dst[:, 0:2, :], PS[:, b:b + 2, :], ACT.Copy)
                            nc.scalar.activation(dst[0:64, 2, :], PS[0:64, b + 2, :], ACT.Copy)\
                                .then_inc(slot_read.sem, 1)
                    act.wait_ge(summed.sem, summed.at(2))
                    b = 4 * (n % 2)
                    if tail_rows:
                        nc.scalar.activation(tail_dst[:, 0:2, :], PS[:, b:b + 2, 0:tail_cols], ACT.Copy)\
                            .then_inc(act_step.sem, 1)
                        nc.scalar.activation(tail_dst[0:64, 2, :], PS[0:64, b + 2, 0:tail_cols], ACT.Copy)\
                            .then_inc(act_step.sem, 1)
                    else:
                        nc.scalar.activation(tail_dst[:, :], PS[0:tail_cols, b, 0:NT], ACT.Copy)\
                            .then_inc(act_step.sem, 2)

                @block.vector
                def _(dve):
                    step = Chain(dve, dve_step)
                    norm_dve(dve, 1, step)
                    dve_step.count = step.n
            norm_close()
            summed.close(1)
            act_step.close(2)
            slot_read.close(n)
            dve_step.close(dve_step.count)
            return n0 + n

        def store(sp, dst, src):
            sp.dma_start(dst, src).then_inc(stored.sem, 16)

        logit_ready = signal("logit_ready")
        keep_ready = signal("keep_ready")
        tail_ready = signal("tail_ready")
        weight_ready = signal("weight_ready")
        out_ready = signal("out_ready")
        out_read = signal("out_read")
        page_in = [signal("page_in0"), signal("page_in1")]
        seq_ready = signal("seq_ready")
        scaled = signal("scaled")
        logged = signal("logged")
        exponent = signal("exponent")

        def even_stage(n0):
            stage = ExitStack()
            with stage:
                def tile(name, shape):
                    return sb(name, shape, F32, stage)

                qkT = tile("qkT", [P, 4, NT])
                vb = tile("vb", [P, 3, 512])
                rT = tile("rT", [P, 4, NT])
                a1T = tile("a1T", [16, NT])
                with ExitStack() as heads:
                    QT = sb("QT", [P, 4, NT], F32, heads)
                    KTT = sb("KTT", [P, 4, NT], F32, heads)
                    V = sb("V", [P, 3, 512], F32, heads)
                    w_a1 = sb("w_a1", [P, KT, 16], F32, heads)
                    with nc.Block(no_gpsimd_drain=True) as block:
                        @block.sync
                        def _(sp):
                            sp.dma_start(w_a1[:], io["w_a1"]).then_inc(loads.sem, 16)
                            sp.wait_ge(loads.sem, loads.at(16))
                    loads.close(16)
                    n1 = project_stage(n0, [(True, QT[:]), (True, KTT[:]), (False, V), (True, qkT[:]), (False, vb),
                                            (True, rT[:])], w_a1, 16, a1T, False)
                    stick_prompt(QT, KTT, V)
                    stick_sample(QT, KTT, V)
                linear_attention(qkT, vb, rT, a1T)
            return out_stage(n1)

        def stick_prompt(QT, KTT, V):
            W = 384
            PAIRS = 4
            with ExitStack() as stage:
                def tile(name, shape):
                    return sb(name, shape, F32, stage)
                sp1 = tile("p_sp1", [P, 2, 2, W])
                sp2 = tile("p_sp2", [P, 2, 2, W])
                u = tile("p_u", [P, 2, 2, W])
                mask = tile("p_mask", [P, W])
                fill = tile("p_fill", [P, W])
                block = stage.enter_context(nc.Block(no_gpsimd_drain=True))

                @block.sync
                def _(sp):
                    store(sp, io["o_sbk"], KTT[:])
                    store(sp, io["o_sbv"][0:NPR, :].rearrange("(t p) n -> p t n", p=P), V[:, 0:2, :])
                    store(sp, io["o_sbv"][NPR:NT, :], V[0:64, 2, :])
                    sp.dma_start(io["new_rows"][0], V[0:64, 2, :]).then_inc(loads.sem, 16)
                    sp.wait_ge(loads.sem, loads.at(16))

                def region(kt):
                    return (0, 256, 0) if kt == 0 else (256, W, 128)

                @block.tensor
                def _(pe):
                    def logits(a):
                        if a >= 2:
                            pe.wait_ge(scaled.sem, scaled.at(a - 1))
                        for hh in range(2):
                            for kt in range(2):
                                c0, c1, q0 = region(kt)
                                mm = nc.tensor.matmul(PS[:, 2 * (a % 2) + hh, c0:c1],
                                                      KTT[64 * hh:64 * hh + 64, a, kt * P:(kt + 1) * P],
                                                      QT[64 * hh:64 * hh + 64, a, q0:NPR], start=True, stop=True)
                        mm.then_inc(logit_ready.sem, 1)

                    def tails(a):
                        pe.wait_ge(keep_ready.sem, keep_ready.at(a + 1))
                        if a >= 1:
                            pe.wait_ge(exponent.sem, exponent.at(a))
                        for hh in range(2):
                            nc.tensor.matmul(PS[:, 4 + hh, 0:W], later[:], sp2[:, a % 2, hh, :], start=True, stop=False)
                            mm = nc.tensor.matmul(PS[:, 4 + hh, 128:256], ones[:], sp2[:, a % 2, hh, 256:W],
                                                  start=False, stop=True)
                        mm.then_inc(tail_ready.sem, 1)

                    def values(a):
                        pe.wait_ge(weight_ready.sem, weight_ready.at(a + 1))
                        if a >= 2:
                            pe.wait_ge(out_read.sem, out_read.at(a - 1))
                        for hh in range(2):
                            for kt in range(2):
                                c0, c1, q0 = region(kt)
                                h = 2 * a + hh
                                mm = nc.tensor.matmul(PS[64 * hh:64 * hh + 64, 6 + a % 2, q0:NPR],
                                                      V[:, kt, 64 * h:64 * h + 64], u[:, a % 2, hh, c0:c1],
                                                      start=(kt == 0), stop=(kt == 1))
                        mm.then_inc(out_ready.sem, 1)
                    logits(0)
                    for a in range(PAIRS):
                        if a + 1 < PAIRS:
                            logits(a + 1)
                        tails(a)
                        values(a)

                @block.gpsimd
                def _(pool):
                    step = Chain(pool, pool_step)
                    step(pool.memset(mask[:], 1.0))
                    step(pool.memset(fill[:], 0.0))
                    for c0, c1, q0 in (region(0), region(1)):
                        for t, v in ((mask, 0.0), (fill, NEG)):
                            step(pool.affine_select(out=t[:, c0:c1], in_=t[:, c0:c1], compare_op=ALU.is_gt, fill=v,
                                                    base=0, pattern=[[1, c1 - c0]], channel_multiplier=-1))
                    pool_step.count = step.n

                @block.scalar
                def _(act):
                    step = Chain(act, act_step)

                    def softplus(a):
                        act.wait_ge(scaled.sem, scaled.at(a + 1))
                        if a >= 2:
                            act.wait_ge(keep_ready.sem, keep_ready.at(a - 1))
                        step(nc.scalar.activation(sp1[:, a % 2, :, :], u[:, a % 2, :, :], ACT.Abs))
                        step(nc.scalar.activation(sp1[:, a % 2, :, :], sp1[:, a % 2, :, :], ACT.Exp, scale=-1.0))
                        nc.scalar.activation(sp1[:, a % 2, :, :], sp1[:, a % 2, :, :], ACT.Ln, bias=1.0)\
                            .then_inc(logged.sem, 1)

                    def weights(a):
                        act.wait_ge(exponent.sem, exponent.at(a + 1))
                        nc.scalar.activation(u[:, a % 2, :, :], u[:, a % 2, :, :], ACT.Exp)\
                            .then_inc(weight_ready.sem, 1)
                    softplus(0)
                    for a in range(PAIRS):
                        if a + 1 < PAIRS:
                            softplus(a + 1)
                        weights(a)
                    act_step.count = step.n

                @block.vector
                def _(dve):
                    step = Chain(dve, dve_step)

                    def logits(a):
                        dve.wait_ge(logit_ready.sem, logit_ready.at(a + 1))
                        if a >= 2:
                            dve.wait_ge(out_ready.sem, out_ready.at(a - 1))
                            dve.wait_ge(tail_ready.sem, tail_ready.at(a - 1))
                        nc.vector.tensor_scalar(u[:, a % 2, :, :], PS[:, 2 * (a % 2):2 * (a % 2) + 2, 0:W], SCALE,
                                                None, ALU.mult).then_inc(scaled.sem, 1)
                        dve.wait_ge(scaled.sem, scaled.at(a + 1))
                        step(nc.vector.tensor_scalar(sp2[:, a % 2, :, :], u[:, a % 2, :, :], 0.0, None, ALU.max))
                        dve.wait_ge(logged.sem, logged.at(a + 1))
                        step(nc.vector.tensor_tensor(sp2[:, a % 2, :, :], sp2[:, a % 2, :, :], sp1[:, a % 2, :, :],
                                                     ALU.add))
                        nc.vector.tensor_tensor(sp2[:, a % 2, :, :], sp2[:, a % 2, :, :], rep(mask[:], 1, 2), ALU.mult)\
                            .then_inc(keep_ready.sem, 1)

                    def exponents(a):
                        dve.wait_ge(tail_ready.sem, tail_ready.at(a + 1))
                        step(nc.vector.tensor_tensor(u[:, a % 2, :, :], u[:, a % 2, :, :], PS[:, 4:6, 0:W],
                                                     ALU.subtract))
                        nc.vector.tensor_tensor(u[:, a % 2, :, :], u[:, a % 2, :, :], rep(fill[:], 1, 2), ALU.add)\
                            .then_inc(exponent.sem, 1)

                    def outs(a):
                        dve.wait_ge(out_ready.sem, out_ready.at(a + 1))
                        nc.vector.tensor_copy(OT[:, a, 0:NPR], PS[:, 6 + a % 2, 0:NPR]).then_inc(out_read.sem, 1)
                    dve.wait_ge(pool_step.sem, pool_step.at(6))
                    logits(0)
                    for a in range(PAIRS):
                        if a + 1 < PAIRS:
                            logits(a + 1)
                        exponents(a)
                        if a >= 1:
                            outs(a - 1)
                    outs(PAIRS - 1)
                    dve_step.count = step.n
            pool_step.close(pool_step.count)
            act_step.close(act_step.count)
            dve_step.close(dve_step.count)
            for s in (logit_ready, keep_ready, tail_ready, weight_ready, out_ready, out_read, scaled, logged,
                      exponent):
                s.close(PAIRS)
            stored.close(48)
            loads.close(16)

        def stick_sample(QT, KTT, V):
            NP1 = NPG + 1
            W = NP1 * 64
            LOADED = 16 * (2 * NPG + 1)
            with ExitStack() as stage:
                def tile(name, shape):
                    return sb(name, shape, F32, stage)
                K = [tile(f"s_K{i}", [P, NPG, 4, P]) for i in range(2)]
                VV = [tile(f"s_V{i}", [P, NPG, 512]) for i in range(2)]
                VN = [tile(f"s_VN{i}", [P, 512]) for i in range(2)]
                QB = tile("s_QB", [P, 4, 16])
                free = H[:].rearrange("p k n -> p (k n)")
                sp1, sp2, u = (free[:, n * W:(n + 1) * W] for n in range(3))
                KN = free[:, 3 * W:3 * W + 4 * P].rearrange("p (a k) -> p a k", a=4)
                mask = tile("s_mask", [P, 64])
                fill = tile("s_fill", [P, 64])
                pages = sb("s_pages", [1, NB * NPG], I32, stage)
                zl = PS[:, 0:2, :].rearrange("p a n -> p (a n)")[:, 0:W]
                rl = PS[:, 2:4, :].rearrange("p a n -> p (a n)")[:, 0:W]
                block = stage.enter_context(nc.Block(no_gpsimd_drain=True))

                @block.sync
                def _(sp):
                    sp.dma_start(pages[:], io["pages"]).then_inc(loads.sem, 16)
                    sp.wait_ge(loads.sem, loads.at(16))
                    sp.wait_ge(pool_step.sem, pool_step.at(8))

                    def load(b, i, used=None):
                        for p in range(NPG):
                            at = b * NPG + p
                            cell = pages[0:1, at:at + 1] if isinstance(at, int) else pages[0:1, bass.ds(at, 1)]
                            page = sp.value_load(cell, min_val=0, max_val=NPOOL - 1)
                            if p == 0 and used is not None:
                                sp.wait_ge(out_ready.sem, used)
                            sp.dma_start(K[i][:, p, :, :].rearrange("p a n -> p (a n)"),
                                         io["sb_kT"][bass.ds(page, 1), :, :].rearrange("a p n -> p (a n)"))\
                                .then_inc(page_in[i].sem, 16)
                            sp.dma_start(VV[i][:, p, :],
                                         io["sb_v"][bass.ds(page, 1), :, :].rearrange("a p n -> p (a n)"))\
                                .then_inc(page_in[i].sem, 16)
                        at = slice(LS * b, LS * b + LS) if isinstance(b, int) else bass.ds(b * LS, LS)
                        sp.dma_start(VN[i][0:LS, :], io["new_rows"][0, at, :]).then_inc(page_in[i].sem, 16)
                    load(0, 0)
                    load(1, 1)
                    with sp.Fori(1, NB // 2) as g:
                        for i in range(2):
                            load(2 * g + i, i, out_ready.at(i - 1) + 2 * g)

                @block.gpsimd
                def _(pool):
                    step = Chain(pool, pool_step)
                    for t in (KN, VN[0][:], VN[1][:], QB[:]):
                        step(pool.memset(t, 0.0))
                    step(pool.memset(mask[:], 1.0))
                    step(pool.memset(fill[:], 0.0))
                    for t, v in ((mask, 0.0), (fill, NEG)):
                        step(pool.affine_select(out=t[:], in_=t[:], compare_op=ALU.is_gt, fill=v, base=0,
                                                pattern=[[0, 8], [1, 8]], channel_multiplier=-1))
                    pool_step.count = step.n

                @block.tensor
                def _(pe):
                    def one(g, i):
                        b = 2 * g + i
                        pe.wait_ge(page_in[i].sem, page_in[i].at(LOADED) + g * LOADED)
                        pe.wait_ge(seq_ready.sem, seq_ready.at(1) + b)
                        for p in range(NP1):
                            for a in range(4):
                                k = K[i][:, p, a, :] if p < NPG else KN[:, a, :]
                                mm = nc.tensor.matmul(zl[:, p * 64 + a * 16:p * 64 + a * 16 + 16], k, QB[:, a, :],
                                                      start=True, stop=True)
                        mm.then_inc(logit_ready.sem, 1)
                        pe.wait_ge(keep_ready.sem, keep_ready.at(1) + b)
                        nc.tensor.matmul(rl[:, 0:512], later[:], sp2[:, 0:512], start=True, stop=False)
                        for p in range(1, NP1):
                            nc.tensor.matmul(rl[:, 0:64 * p], ones[:], rep(sp2[:, 64 * p:64 * p + 64], 1, p),
                                             start=False, stop=(p == NP1 - 1))
                        mm = nc.tensor.matmul(rl[:, 512:W], later[:], sp2[:, 512:W], start=True, stop=True)
                        mm.then_inc(tail_ready.sem, 1)
                        pe.wait_ge(weight_ready.sem, weight_ready.at(1) + b)
                        for a in range(4):
                            for p in range(NP1):
                                v = VV[i][:, p, a * P:(a + 1) * P] if p < NPG else VN[i][:, a * P:(a + 1) * P]
                                mm = nc.tensor.matmul(PS[:, 4, a * 16:a * 16 + 16], v,
                                                      u[:, p * 64 + a * 16:p * 64 + a * 16 + 16],
                                                      start=(p == 0), stop=(p == NPG))
                        mm.then_inc(out_ready.sem, 1)
                    pe.wait_ge(pool_step.sem, pool_step.at(8))
                    with pe.Fori(0, NB // 2) as g:
                        one(g, 0)
                        one(g, 1)

                @block.scalar
                def _(act):
                    step = Chain(act, act_step)

                    def one(g, i):
                        b = 2 * g + i
                        at = bass.ds(b * LS + NPR, LS)
                        act.wait_ge(out_ready.sem, out_ready.at(0) + b)
                        nc.scalar.activation(KN[:, :, 0:LS], KTT[:, :, at], ACT.Copy)
                        for hh in range(2):
                            rows = slice(64 * hh, 64 * hh + 64)
                            last = nc.scalar.activation(QB[rows, :, 8 * hh:8 * hh + 8], QT[rows, :, at], ACT.Copy)
                        last.then_inc(seq_ready.sem, 1)
                        act.wait_ge(scaled.sem, scaled.at(1) + b)
                        step(nc.scalar.activation(sp1, u, ACT.Abs))
                        step(nc.scalar.activation(sp1, sp1, ACT.Exp, scale=-1.0))
                        nc.scalar.activation(sp1, sp1, ACT.Ln, bias=1.0).then_inc(logged.sem, 1)
                        act.wait_ge(exponent.sem, exponent.at(1) + b)
                        nc.scalar.activation(u, u, ACT.Exp).then_inc(weight_ready.sem, 1)
                    act.wait_ge(pool_step.sem, pool_step.at(8))
                    with act.Fori(0, NB // 2) as g:
                        step.loop(g, 4)
                        one(g, 0)
                        one(g, 1)
                        step.done(NB // 2)
                    act_step.count = step.n

                @block.vector
                def _(dve):
                    step = Chain(dve, dve_step)

                    def one(g, i):
                        b = 2 * g + i
                        dve.wait_ge(logit_ready.sem, logit_ready.at(1) + b)
                        nc.vector.tensor_scalar(u, zl, SCALE, None, ALU.mult).then_inc(scaled.sem, 1)
                        dve.wait_ge(scaled.sem, scaled.at(1) + b)
                        step(nc.vector.tensor_scalar(sp2, u, 0.0, None, ALU.max))
                        dve.wait_ge(logged.sem, logged.at(1) + b)
                        step(nc.vector.tensor_tensor(u[:, 512:W], u[:, 512:W], fill[:], ALU.add))
                        step(nc.vector.tensor_tensor(sp2, sp2, sp1, ALU.add))
                        nc.vector.tensor_tensor(sp2[:, 512:W], sp2[:, 512:W], mask[:], ALU.mult)\
                            .then_inc(keep_ready.sem, 1)
                        dve.wait_ge(tail_ready.sem, tail_ready.at(1) + b)
                        nc.vector.tensor_tensor(u, u, rl, ALU.subtract).then_inc(exponent.sem, 1)
                        dve.wait_ge(out_ready.sem, out_ready.at(1) + b)
                        for hh in range(2):
                            rows = slice(64 * hh, 64 * hh + 64)
                            src = PS[rows, 4, 0:64].rearrange("p (a h q) -> p a h q", a=4, h=2)[:, :, hh, :]
                            nc.vector.tensor_copy(OT[rows, 0:4, bass.ds(b * LS + NPR, LS)], src)\
                                .then_inc(out_read.sem, 1)
                    dve.wait_ge(pool_step.sem, pool_step.at(8))
                    with dve.Fori(0, NB // 2) as g:
                        step.loop(g, 6)
                        one(g, 0)
                        one(g, 1)
                        step.done(NB // 2)
                    dve_step.count = step.n
            pool_step.close(pool_step.count)
            act_step.close(act_step.count)
            dve_step.close(dve_step.count)
            for s in (logit_ready, keep_ready, tail_ready, weight_ready, out_ready, scaled, logged, exponent,
                      seq_ready):
                s.close(NB)
            out_read.close(2 * NB)
            loads.close(16)
            for s in page_in:
                s.close(LOADED * (NB // 2))

        def linear_attention(qkT, vb, rT, a1T):
            CH = [(t, c) for t in range(2) for c in range(2)]
            with ExitStack() as stage:
                def tile(name, shape):
                    return sb(name, shape, F32, stage)
                wa2 = tile("g_wa2", [16, 256])
                ba2 = tile("g_ba2", [P, 256])
                og = tile("g_og", [P, 1])
                S0 = tile("g_S0", [P, NB, 2, P])
                same = tile("g_same", [P, 2, P])
                upto = tile("g_upto", [P, 2, P])
                neg_upto = tile("g_neg_upto", [P, 2, P])
                neg_after = tile("g_neg_after", [P, 2, P])
                neg_chunk = tile("g_neg_chunk", [P, 2, NB])
                in_seq = tile("g_in_seq", [64, NB])
                x = tile("g_x", [P, 3, 256])
                soft = tile("g_soft", [P, 3, 256])
                EB = tile("g_EB", [P, 2, NT])
                EN = tile("g_EN", [P, 2, NT])
                ED = tile("g_ED", [P, 3, 256])
                EL = tile("g_EL", [P, 2, 12])
                qin = tile("g_qin", [P, 2, NT])
                kin = tile("g_kin", [P, 2, NT])
                kdec = tile("g_kdec", [P, 3, 256])
                att = tile("g_att", [P, 3, 4, P])
                S = tile("g_S", [P, 5, 2, P])
                vx = tile("g_vx", [64, 4, NB, P])
                sq = tile("g_sq", [P, 4, NT])
                rs = tile("g_rs", [P, 4, NT])
                so = tile("g_so", [P, NB, 2, P])
                INV = -1.0 / 16.0

                with nc.Block(no_gpsimd_drain=True) as block:
                    @block.sync
                    def _(sp):
                        sp.dma_start(wa2[:], io["w_a2"]).then_inc(loads.sem, 16)
                        sp.dma_start(ba2[:], bass.AP(io["b_a2"].tensor, 0, [[0, P], [1, 256]])).then_inc(loads.sem, 16)
                        sp.dma_start(og[:], io["onorm_g"]).then_inc(loads.sem, 16)
                        sp.dma_start(S0[:], io["gla_s"]).then_inc(loads.sem, 16)
                        sp.wait_ge(loads.sem, loads.at(64))

                    @block.gpsimd
                    def _(pool):
                        step = Chain(pool, pool_step)

                        def pick(t, op, base, pattern, mult):
                            step(pool.affine_select(out=t, in_=t, compare_op=op, fill=0.0, base=base, pattern=pattern,
                                                    channel_multiplier=mult))
                        step(pool.memset(same[:], 1.0))
                        step(pool.memset(neg_chunk[:], INV))
                        step(pool.memset(in_seq[:], 1.0))
                        for kind, size in ((0, 64), (1, 8)):
                            v = same[:, kind, :].rearrange("p (c i) -> p c i", i=size)
                            pick(v, ALU.is_ge, 0, [[-size, P // size], [0, size]], 1)
                            pick(v, ALU.is_ge, size - 1, [[size, P // size], [0, size]], -1)
                            v = neg_chunk[:, kind, :]
                            pick(v, ALU.is_ge, 0, [[-size, NB]], 1)
                            pick(v, ALU.is_ge, size - 1, [[size, NB]], -1)
                        pick(in_seq[:], ALU.is_ge, 0, [[-8, NB]], 1)
                        pick(in_seq[:], ALU.is_ge, 7, [[8, NB]], -1)
                        step(pool.tensor_copy(upto[:], same[:]))
                        pick(upto[:], ALU.is_ge, 0, [[0, 2], [1, P]], -1)
                        pool_step.count = step.n

                    @block.vector
                    def _(dve):
                        step = Chain(dve, dve_step)
                        dve.wait_ge(pool_step.sem, pool_step.at(pool_step.count))
                        step(nc.vector.tensor_scalar(neg_upto[:], upto[:], INV, None, ALU.mult))
                        step(nc.vector.tensor_tensor(neg_after[:], same[:], upto[:], ALU.subtract))
                        step(nc.vector.tensor_scalar(neg_after[:], neg_after[:], INV, None, ALU.mult))
                        for h in range(4):
                            v = vb[0:64, 2, h * P:(h + 1) * P]
                            m = in_seq[:]
                            m = bass.AP(m.tensor, m.offset, [list(a) for a in m.ap] + [[0, P]])
                            step(nc.vector.tensor_tensor(vx[:, h, :, :], rep(v, 1, NB), m, ALU.mult))
                        dve_step.count = step.n
                loads.close(64)
                pool_step.close(pool_step.count)
                dve_step.close(dve_step.count)

                kinds = [0, 0, 1]
                block = stage.enter_context(nc.Block(no_gpsimd_drain=True))

                @block.tensor
                def _(pe):
                    for t, rows in enumerate(TILE_ROWS):
                        mm = nc.tensor.matmul(PS[0:rows, t, 0:256], a1T[:, t * P:t * P + rows], wa2[:],
                                              start=True, stop=True)
                    mm.then_inc(logit_ready.sem, 1)
                    for t, rows in enumerate(TILE_ROWS):
                        for a in range(2):
                            mm = nc.tensor.transpose(PS[0:rows, 5 + t, a * P:(a + 1) * P],
                                                     qkT[:, 2 + a, t * P:t * P + rows], ident[:])
                    mm.then_inc(out_ready.sem, 1)
                    pe.wait_ge(keep_ready.sem, keep_ready.at(1))
                    for a in range(2):
                        for t, rows in enumerate(TILE_ROWS):
                            nc.tensor.matmul(PS[:, a, t * P:t * P + rows], soft[0:rows, t, a * P:(a + 1) * P],
                                             neg_upto[0:rows, kinds[t], 0:rows], start=(t == 0), stop=(t == 2),
                                             skip_group_check=True)
                    for t, rows in enumerate(TILE_ROWS):
                        nc.tensor.matmul(PS[0:rows, 2 + t // 2, (t % 2) * 256:(t % 2) * 256 + 256],
                                         neg_after[0:rows, kinds[t], 0:rows], soft[0:rows, t, :],
                                         start=True, stop=True)
                    for a in range(2):
                        for t, rows in enumerate(TILE_ROWS):
                            n = NB if t == 2 else 2
                            mm = nc.tensor.matmul(PS[:, 4, a * 12 + 2 * t:a * 12 + 2 * t + n],
                                                  soft[0:rows, t, a * P:(a + 1) * P], neg_chunk[0:rows, kinds[t], 0:n],
                                                  start=True, stop=True)
                    mm.then_inc(tail_ready.sem, 1)
                    pe.wait_ge(weight_ready.sem, weight_ready.at(1))
                    for t, rows in enumerate(TILE_ROWS):
                        for h in range(4):
                            r = slice(64 * (h % 2), 64 * (h % 2) + 64)
                            mm = nc.tensor.matmul(PS[0:rows, 3 * (h % 2) + t, (h // 2) * P:(h // 2) * P + rows],
                                                  kin[r, h // 2, t * P:t * P + rows],
                                                  qin[r, h // 2, t * P:t * P + rows], start=True, stop=True)
                    mm.then_inc(logit_ready.sem, 1)
                    for n, (t, c) in enumerate(CH):
                        for h in range(4):
                            r = slice(64 * (h % 2), 64 * (h % 2) + 64)
                            e = slice(64 * c, 64 * c + 64)
                            mm = nc.tensor.matmul(PS[r, 6 + c, t * 256 + (h // 2) * P:t * 256 + (h // 2 + 1) * P],
                                                  kdec[e, t, 64 * h:64 * h + 64], vb[e, t, h * P:(h + 1) * P],
                                                  start=True, stop=True)
                    mm.then_inc(out_ready.sem, 1)
                    pe.wait_ge(seq_ready.sem, seq_ready.at(1))
                    for h in range(4):
                        bank = h
                        r = slice(64 * (h % 2), 64 * (h % 2) + 64)
                        for t, rows in enumerate(TILE_ROWS):
                            nc.tensor.matmul(PS[:, bank, t * P:t * P + rows], vb[:, t, h * P:(h + 1) * P],
                                             att[:, t, h, 0:rows], start=(t == 0), stop=False,
                                             skip_group_check=True)
                        for n in range(1, 4):
                            nc.tensor.matmul(PS[:, bank, 64 * n:64 * n + 64], S[r, n, h // 2, :],
                                             qin[r, h // 2, 64 * n:64 * n + 64], start=False, stop=False,
                                             skip_group_check=True)
                        for b in range(NB):
                            at = slice(NPR + LS * b, NPR + LS * b + LS)
                            mm = nc.tensor.matmul(PS[:, bank, at], S0[r, b, h // 2, :], qin[r, h // 2, at],
                                                  start=False, stop=(b == NB - 1), skip_group_check=True)
                        mm.then_inc(out_ready.sem, 1)
                    for a in range(2):
                        for hh in range(2):
                            for half in range(2):
                                h = 2 * a + hh
                                mm = nc.tensor.matmul(PS[64 * hh:64 * hh + 64, 4 + 2 * a + half, :],
                                                      kdec[0:64, 2, 64 * h:64 * h + 64],
                                                      vx[:, h, 4 * half:4 * half + 4, :], start=True, stop=True)
                    mm.then_inc(out_ready.sem, 1)
                    pe.wait_ge(squared.sem, squared.at(5))
                    for h in range(4):
                        mm = nc.tensor.matmul(PS[:, h, 0:NT], ones[:], sq[:, h, :], start=True, stop=True)
                    mm.then_inc(summed.sem, 1)

                @block.scalar
                def _(act):
                    step = Chain(act, act_step)
                    act.wait_ge(scaled.sem, scaled.at(1))
                    step(nc.scalar.activation(x[:], x[:], ACT.Exp, scale=-1.0))
                    nc.scalar.activation(x[:], x[:], ACT.Ln, bias=1.0).then_inc(logged.sem, 1)
                    act.wait_ge(tail_ready.sem, tail_ready.at(1))
                    nc.scalar.activation(EB[:], PS[:, 0:2, 0:NT], ACT.Exp)
                    nc.scalar.activation(EN[:], PS[:, 0:2, 0:NT], ACT.Exp, scale=-1.0)
                    nc.scalar.activation(ED[:, 0:2, :].rearrange("p t n -> p (t n)"), PS[:, 2, :], ACT.Exp)
                    nc.scalar.activation(ED[0:64, 2, :], PS[0:64, 3, 0:256], ACT.Exp)
                    nc.scalar.activation(EL[:].rearrange("p a n -> p (a n)"), PS[:, 4, 0:24], ACT.Exp)\
                        .then_inc(exponent.sem, 1)
                    nc.scalar.activation(rT[:], rT[:], ACT.Silu).then_inc(squared.sem, 1)
                    for h in range(4):
                        act.wait_ge(out_read.sem, out_read.at(h + 1))
                        nc.scalar.activation(sq[:, h, :], OT[:, 4 + h, :], ACT.Square).then_inc(squared.sem, 1)
                    act.wait_ge(variance.sem, variance.at(1))
                    nc.scalar.activation(rs[:], rs[:], ACT.Sqrt).then_inc(deviation.sem, 1)
                    act_step.count = step.n

                @block.vector
                def _(dve):
                    step = Chain(dve, dve_step)
                    dve.wait_ge(logit_ready.sem, logit_ready.at(1))
                    for t, rows in enumerate(TILE_ROWS):
                        last = nc.vector.tensor_tensor(x[0:rows, t, :], PS[0:rows, t, 0:256], ba2[0:rows, :], ALU.add)
                    step(nc.vector.memset(x[64:128, 2, :], 0.0))
                    step(nc.vector.tensor_scalar(soft[:], x[:], -1.0, 0.0, ALU.mult, ALU.max))
                    nc.vector.scalar_tensor_tensor(out=x[:], in0=x[:], scalar=-1.0, in1=x[:], op0=ALU.mult, op1=ALU.max).then_inc(scaled.sem, 1)
                    dve.wait_ge(logged.sem, logged.at(1))
                    nc.vector.tensor_tensor(soft[:], soft[:], x[:], ALU.add).then_inc(keep_ready.sem, 1)
                    dve.wait_ge(exponent.sem, exponent.at(1))
                    nc.vector.scalar_tensor_tensor(out=qin[:], in0=qkT[:, 0:2, :], scalar=SCALE, in1=EB[:],
                                                   op0=ALU.mult, op1=ALU.mult)
                    nc.vector.tensor_tensor(kin[:], qkT[:, 2:4, :], EN[:], ALU.mult)
                    dve.wait_ge(out_ready.sem, out_ready.at(1))
                    nc.vector.tensor_tensor(kdec[:, 0:2, :], PS[:, 5:7, 0:256], ED[:, 0:2, :], ALU.mult)
                    nc.vector.tensor_tensor(kdec[0:64, 2, :], PS[0:64, 7, 0:256], ED[0:64, 2, :], ALU.mult)\
                        .then_inc(weight_ready.sem, 1)
                    dve.wait_ge(logit_ready.sem, logit_ready.at(2))
                    for t, rows in enumerate(TILE_ROWS):
                        for hh in range(2):
                            a = PS[0:rows, 3 * hh + t, 0:256].rearrange("p (a c) -> p a c", a=2)[:, :, 0:rows]
                            m = rep(upto[0:rows, kinds[t], 0:rows], 1, 2)
                            to = att[0:rows, t, :, 0:rows].rearrange("p (a g) c -> p a g c", g=2)[:, :, hh, :]
                            nc.vector.tensor_tensor(to, a, m, ALU.mult)
                    nc.vector.memset(att[64:128, 2, :, :], 0.0)
                    nc.vector.memset(vb[64:128, 2, :], 0.0)
                    dve.wait_ge(out_ready.sem, out_ready.at(2))
                    for n in range(4):
                        t, c = CH[n]
                        new = PS[:, 6 + c, t * 256:t * 256 + 256].rearrange("p (a v) -> p a v", a=2)
                        if n == 0:
                            step(nc.vector.tensor_copy(S[:, 1, :, :], new))
                            continue
                        for a in range(2):
                            last = nc.vector.scalar_tensor_tensor(out=S[:, n + 1, a, :], in0=S[:, n, a, :],
                                                                  scalar=EL[:, a, n:n + 1], in1=new[:, a, :],
                                                                  op0=ALU.mult, op1=ALU.add)
                        if n < 3:
                            step(last)
                        else:
                            last.then_inc(seq_ready.sem, 1)
                    for h in range(4):
                        dve.wait_ge(out_ready.sem, out_ready.at(3 + h))
                        nc.vector.tensor_copy(OT[:, 4 + h, :], PS[:, h, 0:NT]).then_inc(out_read.sem, 1)
                    dve.wait_ge(out_ready.sem, out_ready.at(7))
                    for a in range(2):
                        e = EL[:, a, 4:12]
                        e = bass.AP(e.tensor, e.offset, [list(q) for q in e.ap] + [[0, P]])
                        step(nc.vector.tensor_tensor(so[:, :, a, :], S0[:, :, a, :], e, ALU.mult))
                        for half in range(2):
                            v = so[:, 4 * half:4 * half + 4, a, :]
                            src = PS[:, 4 + 2 * a + half, :].rearrange("p (b v) -> p b v", b=4)
                            step(nc.vector.tensor_tensor(v, v, src, ALU.add))
                    dve.wait_ge(summed.sem, summed.at(1))
                    for h in range(4):
                        last = nc.vector.tensor_scalar(rs[:, h, :], PS[:, h, 0:NT], 1.0 / P, EPS,
                                                       ALU.mult, ALU.add)
                    last.then_inc(variance.sem, 1)
                    dve.wait_ge(deviation.sem, deviation.at(1))
                    step(nc.vector.reciprocal(rs[:], rs[:]))
                    step(nc.vector.tensor_tensor(rs[:], rs[:], OT[:, 4:8, :], ALU.mult))
                    nc.vector.scalar_tensor_tensor(out=OT[:, 4:8, :], in0=rs[:], scalar=og[:, 0:1], in1=rT[:],
                                                   op0=ALU.mult, op1=ALU.mult).then_inc(centred.sem, 1)
                    dve_step.count = step.n

                @block.sync
                def _(sp):
                    sp.wait_ge(centred.sem, centred.at(1))
                    sp.dma_start(io["o_pgla"], S[:, 4, :, :]).then_inc(stored.sem, 16)
                    sp.dma_start(io["o_sgla"], so[:]).then_inc(stored.sem, 16)
                    sp.wait_ge(stored.sem, stored.at(32))
            act_step.close(act_step.count)
            dve_step.close(dve_step.count)
            logit_ready.close(2)
            keep_ready.close(1)
            tail_ready.close(1)
            weight_ready.close(1)
            out_ready.close(7)
            out_read.close(4)
            scaled.close(1)
            logged.close(1)
            exponent.close(1)
            seq_ready.close(1)
            squared.close(5)
            for s in (summed, variance, deviation, centred):
                s.close(1)
            stored.close(32)

        centre_ready = signal("centre_ready")
        turned = signal("turned")
        turned_read = signal("turned_read")
        table_in = signal("table_in")
        chosen = signal("chosen")

        def odd_stage(n0):
            stage = ExitStack()
            with stage:
                def tile(name, shape):
                    return sb(name, shape, F32, stage)

                Q2 = tile("Q2", [P, 8, NT])
                kskw = tile("kskw", [P, 4, NT])
                vsvw = tile("vsvw", [P, 3, 512])
                GT = tile("GT", [P, 3, 48])
                GS = tile("GS", [P, NB, 3])
                Bs = tile("Bs", [P, PAST + LS])
                Bw = tile("Bw", [P, WIN + LS])
                KC = tile("KC", [P, 2, NB * 64 + 16])
                VC = tile("VC", [64, NB + 1, 256])
                qkg = tile("qkg", [P, 4])
                w_gt = tile("w_gt", [P, KT, 48])
                bias_tables(Bs)
                with ExitStack() as early:
                    kcvc = sb("kcvc", [P, 4, NT], F32, early)
                    with nc.Block(no_gpsimd_drain=True) as block:
                        @block.sync
                        def _(sp):
                            sp.dma_start(w_gt[:], io["w_gt"]).then_inc(loads.sem, 16)
                            sp.dma_start(qkg[:], io["qk_g"]).then_inc(loads.sem, 16)
                            sp.wait_ge(loads.sem, loads.at(32))
                    loads.close(32)
                    n1 = project_stage(n0, [(True, Q2[:, 0:4, :]), (True, Q2[:, 4:8, :]), (True, kcvc[:]),
                                            (True, kskw[:]), (False, vsvw)], w_gt, 48, GT, True)
                    qk_norms(Q2, kskw, kcvc, vsvw, GT, GS, Bs, Bw, qkg)
                    compress(kcvc, KC, VC, qkg)
                sparse_prompt(Q2, kskw, vsvw, GT, KC, VC)
                sparse_sample(Q2, kskw, GS, Bs, Bw, KC, VC)
            return out_stage(n1)

        def bias_tables(Bs):
            BANKS = 5
            with ExitStack() as stage:
                rel = sb("rel", [33, 16], F32, stage)
                relb = sb("relb", [33, 16, P], F32, stage)
                rel8 = sb("rel8", [33, 16, 8], F32, stage)
                one_hot = sb("one_hot", [33, NDIST], F32, stage)
                F = sb("F", [P, NDIST], F32, stage)
                FP = sb("FP", [P, 16, NDIST_P], F32, stage)
                block = stage.enter_context(nc.Block(no_gpsimd_drain=True))

                @block.sync
                def _(sp):
                    sp.dma_start(rel[0:32, :], io["rel_table"]).then_inc(table_in.sem, 16)
                    sp.dma_start(one_hot[:], io["one_hot"]).then_inc(table_in.sem, 16)
                    sp.wait_ge(act_step.sem, act_step.at(1))
                    sp.dma_start(io["bias_rows"], F[:]).then_inc(loads.sem, 16)
                    sp.wait_ge(loads.sem, loads.at(16))
                    f = io["bias_rows"].tensor
                    for h in range(16):
                        sp.dma_start(Bs[8 * h:8 * h + 8, :],
                                     bass.AP(f, 8 * h * NDIST + DIST_HI - PAST, [[NDIST - 1, 8], [1, PAST + LS]]))\
                            .then_inc(loads.sem, 16)
                    sp.wait_ge(act_step.sem, act_step.at(17))
                    sp.dma_start(io["bias_prompt"], FP[:]).then_inc(loads.sem, 16)
                    sp.wait_ge(loads.sem, loads.at(18 * 16))

                @block.gpsimd
                def _(pool):
                    pool.memset(rel[32:33, :], NEG).then_inc(pool_step.sem, 1)

                @block.vector
                def _(dve):
                    dve.wait_ge(table_in.sem, table_in.at(32))
                    dve.wait_ge(pool_step.sem, pool_step.at(1))
                    r = rel[:]
                    r = bass.AP(r.tensor, r.offset, [list(x) for x in r.ap] + [[0, P]])
                    nc.vector.tensor_copy(relb[:], r).then_inc(dve_step.sem, 1)
                    r = bass.AP(r.tensor, r.offset, [list(x) for x in rel[:].ap] + [[0, 8]])
                    nc.vector.tensor_copy(rel8[:], r).then_inc(dve_step.sem, 1)

                @block.tensor
                def _(pe):
                    pe.wait_ge(dve_step.sem, dve_step.at(2))
                    for c in range(0, NDIST, 512):
                        n = min(512, NDIST - c)
                        mm = nc.tensor.matmul(PS[:, c // 512, 0:n], rel8[:].rearrange("p h q -> p (h q)"), one_hot[:, c:c + n],
                                              start=True, stop=True)
                    mm.then_inc(turned.sem, 1)
                    for h in range(16):
                        if h >= BANKS:
                            pe.wait_ge(act_step.sem, act_step.at(h - BANKS + 2))
                        nc.tensor.matmul(PS[:, 3 + h % BANKS, 0:NDIST_P], relb[:, h, :],
                                         one_hot[:, DIST_HI - 255:DIST_HI - 255 + NDIST_P], start=True, stop=True)\
                            .then_inc(turned.sem, 1)

                @block.scalar
                def _(act):
                    act.wait_ge(turned.sem, turned.at(1))
                    nc.scalar.activation(F[:], PS[:, 0:3, :].rearrange("p a n -> p (a n)")[:, 0:NDIST], ACT.Copy)\
                        .then_inc(act_step.sem, 1)
                    for h in range(16):
                        act.wait_ge(turned.sem, turned.at(h + 2))
                        nc.scalar.activation(FP[:, h, :], PS[:, 3 + h % BANKS, 0:NDIST_P], ACT.Copy)\
                            .then_inc(act_step.sem, 1)
            table_in.close(32)
            loads.close(18 * 16)
            pool_step.close(1)
            dve_step.close(2)
            turned.close(17)
            act_step.close(17)

        def qk_norms(Q2, kskw, kcvc, vsvw, GT, GS, Bs, Bw, qkg):
            with ExitStack() as stage:
                sel8 = sb("sel8", [8, P], F32, stage)
                low8 = sb("low8", [8, 8], F32, stage)
                sq = OT[:, 0:4, :]
                block = stage.enter_context(nc.Block(no_gpsimd_drain=True))

                @block.sync
                def _(sp):
                    store(sp, io["o_kcvc"], kcvc[:])
                    store(sp, io["o_vsvw"][0:NPR, :].rearrange("(t p) n -> p t n", p=P), vsvw[:, 0:2, :])
                    store(sp, io["o_vsvw"][NPR:NT, :], vsvw[0:64, 2, :])
                    sp.dma_start(io["new_rows"][1], vsvw[0:64, 2, :]).then_inc(loads.sem, 16)
                    store(sp, io["o_wink"], io["win_k"][:, LS:WIN, :])
                    store(sp, io["o_winv"], io["win_v"][:, LS:WIN, :])
                    sp.wait_ge(act_step.sem, act_step.at(1))
                    sp.dma_start(io["gate_rows"].rearrange("b l h c -> (b l) (h c)"), GT[0:64, 2, :])\
                        .then_inc(loads.sem, 16)
                    sp.wait_ge(loads.sem, loads.at(32))
                    g = io["gate_rows"].tensor
                    for h in range(16):
                        sp.dma_start(GS[8 * h:8 * h + 8, :, :], bass.AP(g, 3 * h, [[48, 8], [8 * 48, NB], [1, 3]]))\
                            .then_inc(loads.sem, 16)
                    sp.wait_ge(centred.sem, centred.at(1))
                    store(sp, io["o_kskw"], kskw[:])
                    sp.wait_ge(loads.sem, loads.at(32 + 256))

                @block.gpsimd
                def _(pool):
                    step = Chain(pool, pool_step)
                    step(pool.memset(sel8[:], 0.0))
                    step(pool.affine_select(out=sel8[:], in_=sel8[:], compare_op=ALU.not_equal, fill=1.0, base=0,
                                            pattern=[[0, 16], [1, 8]], channel_multiplier=-1))
                    pool_step.count = step.n

                @block.tensor
                def _(pe):
                    pe.wait_ge(squared.sem, squared.at(1))
                    for m in range(4):
                        mm = nc.tensor.matmul(PS[:, m, 0:NT], halves[:], sq[:, m, :], start=True, stop=True)
                    mm.then_inc(summed.sem, 1)
                    pe.wait_ge(squared.sem, squared.at(2))
                    for m in range(4):
                        mm = nc.tensor.matmul(PS[:, 4 + m, 0:NT], halves[:], H[:, m, :], start=True, stop=True)
                    mm.then_inc(summed.sem, 1)
                    pe.wait_ge(variance.sem, variance.at(1))
                    for m in range(4):
                        mm = nc.tensor.matmul(PS[:, m, 0:NT], halves[:], H[:, 4 + m, :], start=True, stop=True)
                    mm.then_inc(summed.sem, 1)
                    pe.wait_ge(pool_step.sem, pool_step.at(2))
                    pe.wait_ge(variance.sem, variance.at(3))
                    pe.wait_ge(dve_step.sem, dve_step.at(1))
                    mm = nc.tensor.matmul(PS[:, 7, 0:8], sel8[:], low8[:], start=True, stop=True)
                    mm.then_inc(out_ready.sem, 1)

                @block.scalar
                def _(act):
                    nc.scalar.activation(sq, kskw[:], ACT.Square).then_inc(squared.sem, 1)
                    nc.scalar.activation(H[:], Q2[:], ACT.Square).then_inc(squared.sem, 1)
                    nc.scalar.activation(GT[:, 0:2, :], GT[:, 0:2, :], ACT.Sigmoid)
                    nc.scalar.activation(GT[0:64, 2, :], GT[0:64, 2, :], ACT.Sigmoid).then_inc(act_step.sem, 1)
                    act.wait_ge(variance.sem, variance.at(1))
                    nc.scalar.activation(sq, sq, ACT.Sqrt).then_inc(deviation.sem, 1)
                    act.wait_ge(variance.sem, variance.at(3))
                    nc.scalar.activation(H[:], H[:], ACT.Sqrt).then_inc(deviation.sem, 1)

                @block.vector
                def _(dve):
                    step = Chain(dve, dve_step)
                    step(nc.vector.tensor_scalar(low8[:], strict[0:8, 0:8], -1.0, -NEG, ALU.add, ALU.mult))
                    dve.wait_ge(summed.sem, summed.at(1))
                    nc.vector.tensor_scalar(sq, PS[:, 0:4, 0:NT], 1.0 / 64, EPS, ALU.mult, ALU.add)\
                        .then_inc(variance.sem, 1)
                    dve.wait_ge(summed.sem, summed.at(3))
                    nc.vector.tensor_scalar(H[:, 0:4, :], PS[:, 4:8, 0:NT], 1.0 / 64, EPS, ALU.mult, ALU.add)\
                        .then_inc(variance.sem, 1)
                    nc.vector.tensor_scalar(H[:, 4:8, :], PS[:, 0:4, 0:NT], 1.0 / 64, EPS, ALU.mult, ALU.add)\
                        .then_inc(variance.sem, 1)
                    step(nc.vector.tensor_scalar(qkg[:, 0:1], qkg[:, 0:1], SCALE, None, ALU.mult))
                    dve.wait_ge(deviation.sem, deviation.at(1))
                    step(nc.vector.reciprocal(sq, sq))
                    for m in range(2):
                        last = nc.vector.scalar_tensor_tensor(out=kskw[:, 2 * m:2 * m + 2, :], in0=sq[:, 2 * m:2 * m + 2, :],
                                                              scalar=qkg[:, 2 + m:3 + m], in1=kskw[:, 2 * m:2 * m + 2, :],
                                                              op0=ALU.mult, op1=ALU.mult)
                    last.then_inc(centred.sem, 1)
                    dve.wait_ge(deviation.sem, deviation.at(2))
                    step(nc.vector.reciprocal(H[:], H[:]))
                    nc.vector.scalar_tensor_tensor(out=Q2[:], in0=H[:], scalar=qkg[:, 0:1], in1=Q2[:],
                                                   op0=ALU.mult, op1=ALU.mult)
                    step(nc.vector.tensor_copy(Bw[:], Bs[:, PAST - WIN:PAST + LS]))
                    dve.wait_ge(out_ready.sem, out_ready.at(1))
                    nc.vector.tensor_tensor(Bw[:, 0:8], Bw[:, 0:8], PS[:, 7, 0:8], ALU.add)
                    dve_step.count = step.n
            loads.close(32 + 256)
            stored.close(16 * 6)
            pool_step.close(pool_step.count)
            dve_step.close(dve_step.count)
            act_step.close(1)
            out_ready.close(1)
            squared.close(2)
            summed.close(3)
            variance.close(3)
            deviation.close(2)
            centred.close(1)

        def compress(kcvc, KC, VC, qkg):
            with ExitStack() as stage:
                def tile(name, shape):
                    return sb(name, shape, F32, stage)
                w1 = tile("w1", [P, 2, 2, 8, P])
                w2 = tile("w2", [P, 2, 64])
                b1 = tile("b1", [P, 2])
                b2k = tile("b2k", [P, 1])
                b2v = tile("b2v", [64, 64])
                C = [tile(f"C{i}", [P, 2 * NPG, 4, 8, 8]) for i in range(2)]
                pages = sb("c_pages", [1, NB * NPG], I32, stage)
                free = H[:].rearrange("p k n -> p (k n)")
                A1 = free[:, 0:2 * 4 * 65].rearrange("p (b v n) -> p b v n", b=2, v=4)
                hid = [free[:, 520 + 512 * i:1032 + 512 * i].rearrange("p (b v n) -> p b v n", b=2, v=4)
                       for i in range(2)]
                free2 = OT[:].rearrange("p k n -> p (k n)")
                PX = free2[:, 0:1024].rearrange("p (i v n) -> p i v n", i=2, v=4)
                rsc = free2[:, 1024:1024 + 2 * 528].rearrange("p (t n) -> p t n", t=2)
                A1p = free[:, 1544:1544 + 4 * 17].rearrange("p (v n) -> p v n", v=4)
                hidp = free[:, 1624:1624 + 64].rearrange("p (v n) -> p v n", v=4)
                LOADED = 16 * 2 * NPG
                PAIRS = NB // 2
                block = stage.enter_context(nc.Block(no_gpsimd_drain=True))

                @block.sync
                def _(sp):
                    sp.dma_start(w1[:], io["cmp_w1"]).then_inc(loads.sem, 16)
                    sp.dma_start(w2[:], io["cmp_w2"]).then_inc(loads.sem, 16)
                    sp.dma_start(b1[:], io["cmp_b1"]).then_inc(loads.sem, 16)
                    sp.dma_start(b2k[:], io["cmp_b2k"]).then_inc(loads.sem, 16)
                    sp.dma_start(b2v[:], bass.AP(io["cmp_b2v"].tensor, 0, [[0, 64], [1, 64]])).then_inc(loads.sem, 16)
                    sp.dma_start(pages[:], io["pages"]).then_inc(loads.sem, 16)
                    sp.wait_ge(loads.sem, loads.at(96))
                    with sp.Fori(0, PAIRS) as g:
                        for i in range(2):
                            for p in range(2 * NPG):
                                page = sp.value_load(pages[0:1, bass.ds(g * (2 * NPG) + p, 1)],
                                                     min_val=0, max_val=NPOOL - 1)
                                src = io["cmp_k"] if i == 0 else io["cmp_v"]
                                if p == 0:
                                    sp.wait_ge(logit_ready.sem, logit_ready.at(0) + 2 * g)
                                sp.dma_start(C[i][:, p, :, :, :].rearrange("p v a s -> p (v a s)"),
                                             src[bass.ds(page, 1), :, :].rearrange("a p n -> p (a n)"))\
                                    .then_inc(page_in[i].sem, 16)

                @block.tensor
                def _(pe):
                    pe.wait_ge(loads.sem, loads.at(96))
                    for kvh in range(2):
                        for i in range(2):
                            for t in range(2):
                                for s2 in range(2):
                                    src = kcvc[64 * kvh:64 * kvh + 64, 2 * i + t, 0:NPR]
                                    src = src.rearrange("p (n s) -> p s n", s=2)[:, s2, :]
                                    mm = nc.tensor.matmul(PS[64 * s2:64 * s2 + 64, 4 + 2 * kvh + i, t * P:(t + 1) * P],
                                                          ident[64 * kvh:64 * kvh + 64, 64 * kvh:64 * kvh + 64], src,
                                                          start=True, stop=True)
                    mm.then_inc(turned.sem, 1)
                    pe.wait_ge(turned_read.sem, turned_read.at(1))
                    for i in range(2):
                        for m in range(2):
                            for a in range(8):
                                rhs = PX[:, i, :, :].rearrange("p v (n a) -> p v n a", a=8)[:, :, :, a]
                                mm = nc.tensor.matmul(PS[:, 2 * i + m, 0:64], w1[:, i, m, a, :], rhs,
                                                      start=(a == 0), stop=(a == 7))
                        mm.then_inc(chosen.sem, 1)
                        pe.wait_ge(chosen.sem, chosen.at(4 * i + 4))
                        if i == 0:
                            for v in range(4):
                                mm = nc.tensor.matmul(PS[64 * (v % 2):64 * (v % 2) + 64, 4, (v // 2) * 16:(v // 2) * 16 + 16],
                                                      w2[:, 0, :], hidp[:, v, :], start=True, stop=True)
                        else:
                            for v in range(4):
                                mm = nc.tensor.matmul(PS[0:16, 5, 64 * v:64 * v + 64], hidp[:, v, :], w2[:, 1, :],
                                                      start=True, stop=True)
                        mm.then_inc(turned.sem, 1)
                    pe.wait_ge(turned_read.sem, turned_read.at(3))

                    def one(g, i):
                        pe.wait_ge(page_in[i].sem, page_in[i].at(LOADED) + g * LOADED)
                        pe.wait_ge(weight_ready.sem, weight_ready.at(0) + 2 * g)
                        for m in range(2):
                            for a in range(8):
                                mm = nc.tensor.matmul(PS[:, 2 * i + m, :], w1[:, i, m, a, :], C[i][:, :, :, a, :],
                                                      start=(a == 0), stop=(a == 7))
                        mm.then_inc(logit_ready.sem, 1)

                    def second(g, i):
                        pe.wait_ge(weight_ready.sem, weight_ready.at(i + 1) + 2 * g)
                        pe.wait_ge(out_read.sem, out_read.at(i) + 2 * g)
                        if i == 0:
                            for v in range(4):
                                mm = nc.tensor.matmul(PS[64 * (v % 2):64 * (v % 2) + 64, 4, (v // 2) * P:(v // 2 + 1) * P],
                                                      w2[:, 0, :], hid[0][:, :, v, :], start=True, stop=True)
                        else:
                            for b in range(2):
                                for v in range(4):
                                    mm = nc.tensor.matmul(PS[0:64, 5, 256 * b + 64 * v:256 * b + 64 * v + 64],
                                                          hid[1][:, b, v, :], w2[:, 1, :], start=True, stop=True)
                        mm.then_inc(out_ready.sem, 1)
                    with pe.Fori(0, PAIRS) as g:
                        one(g, 0)
                        one(g, 1)
                        second(g, 0)
                        second(g, 1)
                    pe.wait_ge(squared.sem, squared.at(1))
                    for t in range(2):
                        nc.tensor.matmul(PS[:, t, :], halves[:], rsc[:, t, 0:512], start=True, stop=True)
                        mm = nc.tensor.matmul(PS[:, 2 + t, 0:16], halves[:], rsc[:, t, 512:528], start=True, stop=True)
                    mm.then_inc(summed.sem, 1)

                @block.scalar
                def _(act):
                    act.wait_ge(loads.sem, loads.at(96))
                    act.wait_ge(turned.sem, turned.at(1))
                    for i in range(2):
                        for kvh in range(2):
                            to = PX[:, i, :, :].rearrange("p (t k) n -> p t k n", k=2)[:, :, kvh, :]
                            last = nc.scalar.activation(to, PS[:, 4 + 2 * kvh + i, 0:256].rearrange("p (t n) -> p t n", t=2),
                                                        ACT.Copy)
                    last.then_inc(turned_read.sem, 1)
                    for i in range(2):
                        act.wait_ge(chosen.sem, chosen.at(4 * i + 1))
                        nc.scalar.activation(A1p[:, :, 0:16], PS[:, 2 * i + 1, 0:64].rearrange("p (v n) -> p v n", v=4),
                                             ACT.Copy).then_inc(chosen.sem, 1)
                        act.wait_ge(chosen.sem, chosen.at(4 * i + 3))
                        nc.scalar.activation(hidp, hidp, ACT.Gelu_apprx_tanh, bias=b1[:, i:i + 1])\
                            .then_inc(chosen.sem, 1)

                    def one(g, i):
                        act.wait_ge(logit_ready.sem, logit_ready.at(i + 1) + 2 * g)
                        act.wait_ge(keep_ready.sem, keep_ready.at(i) + 2 * g)
                        for b in range(2):
                            to = A1[:, b, :, 0:64].rearrange("p v (g s) -> p g v s", s=8)
                            src = PS[:, 2 * i + 1, 256 * b:256 * b + 256].rearrange("p (g v s) -> p g v s", v=4, s=8)
                            last = nc.scalar.activation(to, src, ACT.Copy)
                        last.then_inc(logged.sem, 1)
                        act.wait_ge(keep_ready.sem, keep_ready.at(i + 1) + 2 * g)
                        nc.scalar.activation(hid[i], hid[i], ACT.Gelu_apprx_tanh, bias=b1[:, i:i + 1])\
                            .then_inc(weight_ready.sem, 1)
                    with act.Fori(0, PAIRS) as g:
                        one(g, 0)
                        one(g, 1)
                    act.wait_ge(out_read.sem, out_read.at(2 * PAIRS))
                    nc.scalar.activation(rsc, KC[:], ACT.Square).then_inc(squared.sem, 1)
                    act.wait_ge(variance.sem, variance.at(1))
                    nc.scalar.activation(rsc, rsc, ACT.Sqrt).then_inc(deviation.sem, 1)

                @block.vector
                def _(dve):
                    step = Chain(dve, dve_step)
                    step(nc.vector.memset(A1[:, :, :, 64:65], 0.0))
                    step(nc.vector.memset(A1p[:, :, 16:17], 0.0))
                    dve.wait_ge(loads.sem, loads.at(96))
                    for i in range(2):
                        dve.wait_ge(chosen.sem, chosen.at(4 * i + 2))
                        nc.vector.tensor_tensor(hidp, A1p[:, :, 1:17],
                                                PS[:, 2 * i, 0:64].rearrange("p (v n) -> p v n", v=4),
                                                ALU.add).then_inc(chosen.sem, 1)
                        dve.wait_ge(turned.sem, turned.at(2 + i))
                        if i == 0:
                            nc.vector.tensor_scalar(KC[:, :, 512:528], PS[:, 4, 0:32].rearrange("p (t n) -> p t n", t=2),
                                                    b2k[:, 0:1], None, ALU.add).then_inc(turned_read.sem, 1)
                        else:
                            nc.vector.tensor_tensor(VC[0:16, NB, :].rearrange("p (v d) -> p v d", v=4),
                                                    PS[0:16, 5, 0:256].rearrange("p (v d) -> p v d", v=4),
                                                    rep(b2v[0:16, :], 1, 4), ALU.add).then_inc(turned_read.sem, 1)

                    def one(g, i):
                        dve.wait_ge(logged.sem, logged.at(i + 1) + 2 * g)
                        dve.wait_ge(out_ready.sem, out_ready.at(0) + 2 * g)
                        for b in range(2):
                            to = hid[i][:, b, :, :].rearrange("p v (g s) -> p g v s", s=8)
                            a0 = PS[:, 2 * i, 256 * b:256 * b + 256].rearrange("p (g v s) -> p g v s", v=4, s=8)
                            a1 = A1[:, b, :, 1:65].rearrange("p v (g s) -> p g v s", s=8)
                            last = nc.vector.tensor_tensor(to, a0, a1, ALU.add)
                        last.then_inc(keep_ready.sem, 1)

                    def second(g, i):
                        dve.wait_ge(out_ready.sem, out_ready.at(i + 1) + 2 * g)
                        if i == 0:
                            nc.vector.tensor_scalar(KC[:, :, bass.ds(g * P, P)],
                                                    PS[:, 4, 0:256].rearrange("p (t n) -> p t n", t=2),
                                                    b2k[:, 0:1], None, ALU.add).then_inc(out_read.sem, 1)
                        else:
                            to = VC[:, bass.ds(2 * g, 2), :].rearrange("p b (v d) -> p b v d", v=4)
                            nc.vector.tensor_tensor(to, PS[0:64, 5, :].rearrange("p (b v d) -> p b v d", b=2, v=4),
                                                    rep(rep(b2v[:], 1, 4), 1, 2), ALU.add).then_inc(out_read.sem, 1)
                    with dve.Fori(0, PAIRS) as g:
                        one(g, 0)
                        one(g, 1)
                        second(g, 0)
                        second(g, 1)
                    dve.wait_ge(summed.sem, summed.at(1))
                    nc.vector.tensor_scalar(rsc[:, :, 0:512], PS[:, 0:2, :], 1.0 / 64, EPS, ALU.mult, ALU.add)
                    nc.vector.tensor_scalar(rsc[:, :, 512:528], PS[:, 2:4, 0:16], 1.0 / 64, EPS, ALU.mult, ALU.add)\
                        .then_inc(variance.sem, 1)
                    dve.wait_ge(deviation.sem, deviation.at(1))
                    step(nc.vector.reciprocal(rsc, rsc))
                    nc.vector.scalar_tensor_tensor(out=KC[:], in0=rsc, scalar=qkg[:, 1:2], in1=KC[:],
                                                   op0=ALU.mult, op1=ALU.mult)
                    dve_step.count = step.n
            loads.close(96)
            dve_step.close(dve_step.count)
            turned.close(3)
            turned_read.close(3)
            chosen.close(8)
            for s in (logit_ready, keep_ready, logged, weight_ready, out_ready, out_read):
                s.close(2 * PAIRS)
            for s in page_in:
                s.close(LOADED * PAIRS)
            for s in (squared, summed, variance, deviation):
                s.close(1)

        def sparse_prompt(Q2, kskw, vsvw, GT, KC, VC):
            BATCHES = [(t, v) for t in range(2) for v in range(4)]
            with ExitStack() as stage:
                def tile(name, shape):
                    return sb(name, shape, F32, stage)
                B1 = tile("B1", [P, 16, 256])
                zs = [tile(f"zs{i}", [P, 8, 256]) for i in range(2)]
                zc = [tile(f"zc{i}", [P, 4, 16]) for i in range(2)]
                mx = tile("mx", [P, 2, 12])
                sm = tile("sm", [P, 2, 12])
                pT = tile("pT", [P, 5, 4, P])
                block = stage.enter_context(nc.Block(no_gpsimd_drain=True))

                def shape(t):
                    return P * (t + 1), 7 if t == 0 else 15

                def rounds(t):
                    out = [(2 * br + kt, 4 * br, kt * P) for br in range(2) for kt in range(t + 1)]
                    return out + [(4, None, 0)]
                first_round = []
                for t, v in BATCHES:
                    first_round.append(sum(len(rounds(t2)) for t2, _ in BATCHES[:len(first_round)]))

                @block.sync
                def _(sp):
                    f = io["bias_prompt"].tensor
                    sp.dma_start(B1[:], bass.AP(f, 127, [[16 * NDIST_P - 1, P], [NDIST_P, 16], [1, 256]]))\
                        .then_inc(loads.sem, 16)

                @block.tensor
                def _(pe):
                    def scores(n):
                        t, v = BATCHES[n]
                        nk, ncmp = shape(t)
                        r = slice(64 * (v % 2), 64 * (v % 2) + 64)
                        if n:
                            pe.wait_ge(scaled.sem, scaled.at(n))
                        for g in range(4):
                            q = Q2[r, 4 * (v // 2) + g, t * P:(t + 1) * P]
                            for br in range(2):
                                nc.tensor.matmul(PS[:, 2 * br + g // 2, (g % 2) * 256:(g % 2) * 256 + nk], q,
                                                 kskw[r, 2 * br + v // 2, 0:nk], start=True, stop=True)
                            mm = nc.tensor.matmul(PS[:, 4, 16 * g:16 * g + ncmp], q, KC[r, v // 2, 512:512 + ncmp],
                                                  start=True, stop=True)
                        mm.then_inc(logit_ready.sem, 1)

                    def turn(n):
                        t, v = BATCHES[n]
                        _, ncmp = shape(t)
                        pe.wait_ge(weight_ready.sem, weight_ready.at(n + 1))
                        for k, (slot, row, k0) in enumerate(rounds(t)):
                            at = first_round[n] + k
                            if at >= 2:
                                pe.wait_ge(turned_read.sem, turned_read.at(at - 1))
                            for g in range(4):
                                if row is None:
                                    mm = nc.tensor.transpose(PS[0:ncmp, 5 + at % 2, g * P:(g + 1) * P],
                                                             zc[n % 2][:, g, 0:ncmp], ident[:])
                                else:
                                    mm = nc.tensor.transpose(PS[:, 5 + at % 2, g * P:(g + 1) * P],
                                                             zs[n % 2][:, row + g, k0:k0 + P], ident[:])
                            mm.then_inc(turned.sem, 1)

                    def values(n):
                        t, v = BATCHES[n]
                        _, ncmp = shape(t)
                        last = first_round[n] + len(rounds(t))
                        pe.wait_ge(turned_read.sem, turned_read.at(last))
                        if n:
                            pe.wait_ge(out_read.sem, out_read.at(n))
                        r = slice(64 * (v % 2), 64 * (v % 2) + 64)
                        for g in range(4):
                            to = PS[r, 7, g * P:(g + 1) * P]
                            for br in range(2):
                                for kt in range(t + 1):
                                    nc.tensor.matmul(to, vsvw[:, kt, 256 * br + 64 * v:256 * br + 64 * v + 64],
                                                     pT[:, 2 * br + kt, g, :], start=(br == 0 and kt == 0), stop=False,
                                                     skip_group_check=True)
                            mm = nc.tensor.matmul(to, VC[0:ncmp, NB, 64 * v:64 * v + 64], pT[0:ncmp, 4, g, :],
                                                  start=False, stop=True, skip_group_check=True)
                        mm.then_inc(out_ready.sem, 1)
                    scores(0)
                    for n in range(len(BATCHES)):
                        if n + 1 < len(BATCHES):
                            scores(n + 1)
                        turn(n)
                        values(n)

                @block.scalar
                def _(act):
                    def exps(n):
                        nk, ncmp = shape(BATCHES[n][0])
                        act.wait_ge(centre_ready.sem, centre_ready.at(n + 1))
                        nc.scalar.activation(zs[n % 2][:, :, 0:nk], zs[n % 2][:, :, 0:nk], ACT.Exp)
                        nc.scalar.activation(zc[n % 2][:, :, 0:ncmp], zc[n % 2][:, :, 0:ncmp], ACT.Exp)\
                            .then_inc(exponent.sem, 1)

                    def copies(n):
                        t, _ = BATCHES[n]
                        _, ncmp = shape(t)
                        if n:
                            act.wait_ge(out_ready.sem, out_ready.at(n))
                        for k, (slot, row, k0) in enumerate(rounds(t)):
                            at = first_round[n] + k
                            act.wait_ge(turned.sem, turned.at(at + 1))
                            rows = P if row is not None else ncmp
                            nc.scalar.activation(pT[0:rows, slot, :, :].rearrange("p g q -> p (g q)"),
                                                 PS[0:rows, 5 + at % 2, :], ACT.Copy).then_inc(turned_read.sem, 1)
                    exps(0)
                    for n in range(len(BATCHES)):
                        if n + 1 < len(BATCHES):
                            exps(n + 1)
                        copies(n)

                @block.vector
                def _(dve):
                    step = Chain(dve, dve_step)
                    dve.wait_ge(loads.sem, loads.at(16))

                    def last_dim(ap, n):
                        return bass.AP(ap.tensor, ap.offset, [list(x) for x in ap.ap] + [[0, n]])

                    def centre(n):
                        t, v = BATCHES[n]
                        nk, ncmp = shape(t)
                        z, c, m = zs[n % 2], zc[n % 2], mx[:, n % 2, :]
                        bias = B1[:, 4 * v:4 * v + 4, 0:nk] if t else B1[:, 4 * v:4 * v + 4, P:2 * P]
                        k0 = 31 if t else P + 31
                        bias_c = B1[:, 4 * v:4 * v + 4, k0:k0 + 16 * (ncmp - 1) + 1:16]
                        dve.wait_ge(logit_ready.sem, logit_ready.at(n + 1))
                        if n >= 2:
                            dve.wait_ge(turned.sem, turned.at(first_round[n - 1]))
                        zp = PS[:, 0:4, :].rearrange("p a (h k) -> p (a h) k", h=2)[:, :, 0:nk]
                        nc.vector.tensor_tensor(z[:, :, 0:nk].rearrange("p (b g) k -> p b g k", b=2),
                                                zp.rearrange("p (b g) k -> p b g k", b=2), rep(bias, 1, 2), ALU.add)
                        nc.vector.tensor_tensor(c[:, :, 0:ncmp],
                                                PS[:, 4, 0:64].rearrange("p (g k) -> p g k", g=4)[:, :, 0:ncmp],
                                                bias_c, ALU.add).then_inc(scaled.sem, 1)
                        dve.wait_ge(scaled.sem, scaled.at(n + 1))
                        nc.vector.tensor_reduce(m[:, 0:8], z[:, :, 0:nk], AX.X, ALU.max)
                        step(nc.vector.tensor_reduce(m[:, 8:12], c[:, :, 0:ncmp], AX.X, ALU.max))
                        step(nc.vector.tensor_scalar(m, m, NEG / 10, None, ALU.max))
                        nc.vector.tensor_tensor(z[:, :, 0:nk], z[:, :, 0:nk], last_dim(m[:, 0:8], nk), ALU.subtract)
                        nc.vector.tensor_tensor(c[:, :, 0:ncmp], c[:, :, 0:ncmp], last_dim(m[:, 8:12], ncmp),
                                                ALU.subtract).then_inc(centre_ready.sem, 1)

                    def weights(n):
                        t, v = BATCHES[n]
                        nk, ncmp = shape(t)
                        z, c, s = zs[n % 2], zc[n % 2], sm[:, n % 2, :]
                        dve.wait_ge(exponent.sem, exponent.at(n + 1))
                        nc.vector.tensor_reduce(s[:, 0:8], z[:, :, 0:nk], AX.X, ALU.add)
                        step(nc.vector.tensor_reduce(s[:, 8:12], c[:, :, 0:ncmp], AX.X, ALU.add))
                        step(nc.vector.tensor_scalar(s, s, 1e-30, None, ALU.max))
                        step(nc.vector.reciprocal(s, s))
                        gate = GT[:, t, 12 * v:12 * v + 12].rearrange("p (g b) -> p b g", b=3)
                        nc.vector.tensor_tensor(s[:, 0:8].rearrange("p (b g) -> p b g", b=2),
                                                s[:, 0:8].rearrange("p (b g) -> p b g", b=2), gate[:, 1:3, :], ALU.mult)
                        step(nc.vector.tensor_tensor(s[:, 8:12], s[:, 8:12], gate[:, 0, :], ALU.mult))
                        nc.vector.tensor_tensor(z[:, :, 0:nk], z[:, :, 0:nk], last_dim(s[:, 0:8], nk), ALU.mult)
                        nc.vector.tensor_tensor(c[:, :, 0:ncmp], c[:, :, 0:ncmp], last_dim(s[:, 8:12], ncmp),
                                                ALU.mult).then_inc(weight_ready.sem, 1)

                    def outs(n):
                        t, v = BATCHES[n]
                        r = slice(64 * (v % 2), 64 * (v % 2) + 64)
                        dve.wait_ge(out_ready.sem, out_ready.at(n + 1))
                        nc.vector.tensor_copy(OT[r, 4 * (v // 2):4 * (v // 2) + 4, t * P:(t + 1) * P],
                                              PS[r, 7, :].rearrange("p (g q) -> p g q", g=4)).then_inc(out_read.sem, 1)
                    centre(0)
                    for n in range(len(BATCHES)):
                        if n + 1 < len(BATCHES):
                            centre(n + 1)
                        weights(n)
                        if n:
                            outs(n - 1)
                    outs(len(BATCHES) - 1)
                    dve_step.count = step.n
            loads.close(16)
            dve_step.close(dve_step.count)
            for s in (logit_ready, scaled, centre_ready, exponent, weight_ready, out_ready, out_read):
                s.close(len(BATCHES))
            n = sum(len(rounds(t)) for t, _ in BATCHES)
            turned.close(n)
            turned_read.close(n)

        def sparse_sample(Q2, kskw, GS, Bs, Bw, KC, VC):
            NC = PAST // 16 - 1
            NS, NW = PAST + LS, WIN + LS
            LOADED = 16 * (2 * NPG + 3)
            with ExitStack() as stage:
                def tile(name, shape):
                    return sb(name, shape, F32, stage)
                KS = [tile(f"KS{i}", [P, NPG, 2, P]) for i in range(2)]
                VS = [tile(f"VS{i}", [P, NPG, 256]) for i in range(2)]
                KW = [tile(f"KW{i}", [P, 2, WIN]) for i in range(2)]
                VW = [tile(f"VW{i}", [P, 4, 256]) for i in range(2)]
                VN = [tile(f"VN{i}", [LS, 512]) for i in range(2)]
                QB = tile("QB2", [P, 2, P])
                pages = sb("o_pages", [1, NB * NPG], I32, stage)
                pT = tile("pT2", [P, 15, P])
                free = H[:].rearrange("p k n -> p (k n)")
                zs = free[:, 0:NS]
                zw = free[:, NS:NS + NW]
                zc = free[:, NS + NW:NS + NW + NC]
                pc = free[:, 1664:1664 + P]
                cover = free[0:64, 1800:1817]
                cov = free[:, 1820:1837]
                hit = free[:, 1840:1854]
                drop = free[:, 1860:1876]
                block_no = free[:, 1880:1896]
                st = free[:, 1900:1916]
                same_q = free[:, 1920:1920 + P]
                VCs = free[0:64, 2048:2304]
                zsp = PS[:, 0:3, :].rearrange("p a n -> p (a n)")[:, 0:NS]
                zwp = PS[:, 3:5, :].rearrange("p a n -> p (a n)")[:, 0:NW]
                zcp = PS[:, 2, 256:256 + NC]
                block = stage.enter_context(nc.Block(no_gpsimd_drain=True))
                BUILT = 16

                @block.sync
                def _(sp):
                    sp.dma_start(pages[:], io["pages"]).then_inc(loads.sem, 16)
                    sp.wait_ge(loads.sem, loads.at(16))

                    def load(b, i, used=None):
                        for p in range(NPG):
                            at = b * NPG + p
                            cell = pages[0:1, at:at + 1] if isinstance(at, int) else pages[0:1, bass.ds(at, 1)]
                            page = sp.value_load(cell, min_val=0, max_val=NPOOL - 1)
                            if p == 0 and used is not None:
                                sp.wait_ge(out_ready.sem, used)
                            sp.dma_start(KS[i][:, p, :, :].rearrange("p a n -> p (a n)"),
                                         io["slc_kT"][bass.ds(page, 1), :, :].rearrange("a p n -> p (a n)"))\
                                .then_inc(page_in[i].sem, 16)
                            sp.dma_start(VS[i][:, p, :],
                                         io["slc_v"][bass.ds(page, 1), :, :].rearrange("a p n -> p (a n)"))\
                                .then_inc(page_in[i].sem, 16)
                        one = slice(b, b + 1) if isinstance(b, int) else bass.ds(b, 1)
                        new = slice(LS * b, LS * b + LS) if isinstance(b, int) else bass.ds(b * LS, LS)
                        sp.dma_start(KW[i][:].rearrange("p t n -> p (t n)"),
                                     io["win_kT"][one, :, :].rearrange("a p n -> p (a n)")).then_inc(page_in[i].sem, 16)
                        sp.dma_start(VW[i][:], io["win_v"][one, :, :].rearrange("a (c p) n -> p (a c) n", p=P))\
                            .then_inc(page_in[i].sem, 16)
                        sp.dma_start(VN[i][:], io["new_rows"][1, new, :]).then_inc(page_in[i].sem, 16)
                    load(0, 0)
                    load(1, 1)
                    with sp.Fori(1, NB // 2) as g:
                        for i in range(2):
                            load(2 * g + i, i, out_ready.at(i - 1) + 2 * g)

                @block.gpsimd
                def _(pool):
                    step = Chain(pool, pool_step)

                    def pick(t, op, base, pattern, mult, fill=0.0):
                        step(pool.affine_select(out=t, in_=t, compare_op=op, fill=fill, base=base, pattern=pattern,
                                                channel_multiplier=mult))
                    step(pool.memset(QB[:], 0.0))
                    step(pool.memset(same_q, 0.0))
                    step(pool.memset(cover, 1.0))
                    step(pool.memset(pc, 0.0))
                    for d in range(-3, 4):
                        pick(same_q, ALU.not_equal, -8 * d, [[-1, P]], 1, 1.0)
                    v = same_q.rearrange("p (c i) -> p c i", i=32)
                    pick(v, ALU.is_ge, 0, [[-32, 4], [0, 32]], 1)
                    pick(v, ALU.is_ge, 31, [[32, 4], [0, 32]], -1)
                    pick(cover, ALU.is_ge, 63, [[64, 17]], -16)
                    pick(cover, ALU.is_gt, 32, [[-64, 17]], 16)
                    step(pool.iota(block_no, pattern=[[1, 16]], base=0, channel_multiplier=0,
                                   allow_small_or_imprecise_dtypes=True))
                    assert step.n == BUILT
                    pool_step.count = step.n

                @block.tensor
                def _(pe):
                    def turn(round_no, b, items):
                        bank = 6 + round_no % 2
                        for rows, c, src in items:
                            mm = nc.tensor.transpose(PS[0:rows, bank, c:c + P], src, ident[:])
                        mm.then_inc(turned.sem, 1)

                    def one(g, i):
                        b = 2 * g + i
                        pe.wait_ge(page_in[i].sem, page_in[i].at(LOADED) + g * LOADED)
                        pe.wait_ge(seq_ready.sem, seq_ready.at(1) + b)
                        new = bass.ds(b * LS + NPR, LS)
                        for t in range(2):
                            mm = nc.tensor.matmul(zcp, QB[:, t, :], KC[:, t, bass.ds(b * 64, NC)],
                                                  start=(t == 0), stop=(t == 1))
                        mm.then_inc(chosen.sem, 1)
                        for c in range(2):
                            for t in range(2):
                                nc.tensor.matmul(PS[:, c, :], QB[:, t, :], KS[i][:, 4 * c:4 * c + 4, t, :],
                                                 start=(t == 0), stop=(t == 1))
                        for t in range(2):
                            nc.tensor.matmul(PS[:, 3, :], QB[:, t, :], KW[i][:, t, :], start=(t == 0), stop=(t == 1))
                        for t in range(2):
                            nc.tensor.matmul(PS[:, 4, 0:LS], QB[:, t, :], kskw[:, 2 + t, new],
                                             start=(t == 0), stop=(t == 1))
                        pe.wait_ge(scaled.sem, scaled.at(1) + 2 * b)
                        for t in range(2):
                            mm = nc.tensor.matmul(PS[:, 2, 0:LS], QB[:, t, :], kskw[:, t, new],
                                                  start=(t == 0), stop=(t == 1))
                        mm.then_inc(logit_ready.sem, 1)
                        pe.wait_ge(keep_ready.sem, keep_ready.at(1) + 3 * b)
                        nc.tensor.transpose(PS[:, 6, 0:P], pc, ident[:]).then_inc(chosen.sem, 1)
                        pe.wait_ge(logged.sem, logged.at(1) + b)
                        nc.tensor.matmul(PS[:, 5, 0:17], pT[0:NC, 14, :], cover[0:NC, :], start=True, stop=True)\
                            .then_inc(chosen.sem, 1)
                        pe.wait_ge(keep_ready.sem, keep_ready.at(2) + 3 * b)
                        nc.tensor.matmul(PS[:, 5, 32:49], same_q, cov, start=True, stop=True)\
                            .then_inc(chosen.sem, 1)
                        pe.wait_ge(weight_ready.sem, weight_ready.at(1) + b)
                        turn(0, b, [(P, P * k, zs[:, k * P:(k + 1) * P]) for k in range(4)])
                        turn(1, b, [(P, P * k, zs[:, (k + 4) * P:(k + 5) * P]) for k in range(4)])
                        pe.wait_ge(turned_read.sem, turned_read.at(1) + 4 * b)
                        turn(2, b, [(P, P * k, zw[:, k * P:(k + 1) * P]) for k in range(4)])
                        pe.wait_ge(turned_read.sem, turned_read.at(2) + 4 * b)
                        turn(3, b, [(LS, 0, zs[:, PAST:NS]), (LS, P, zw[:, WIN:NW]), (NC, 2 * P, zc)])
                        pe.wait_ge(turned_read.sem, turned_read.at(4) + 4 * b)
                        for t in range(2):
                            cols = slice(t * P, t * P + P)
                            parts = [(VS[i][:, k, cols], k, P) for k in range(NPG)]
                            parts += [(VW[i][:, k, cols], 8 + k, P) for k in range(4)]
                            parts += [(VN[i][:, cols], 12, LS), (VN[i][:, 256 + t * P:256 + t * P + P], 13, LS),
                                      (VCs[0:NC, cols], 14, NC)]
                            for n, (v, k, rows) in enumerate(parts):
                                mm = nc.tensor.matmul(PS[:, 5, 64 + 64 * t:128 + 64 * t], v,
                                                      pT[0:rows, k, 64 * t:64 * t + 64],
                                                      start=(n == 0), stop=(n == len(parts) - 1))
                        mm.then_inc(out_ready.sem, 1)

                    pe.wait_ge(pool_step.sem, pool_step.at(BUILT))
                    with pe.Fori(0, NB // 2) as g:
                        one(g, 0)
                        one(g, 1)

                @block.scalar
                def _(act):
                    def one(g, i):
                        b = 2 * g + i
                        at = bass.ds(b * LS + NPR, LS)
                        act.wait_ge(out_ready.sem, out_ready.at(0) + b)
                        for kvh in range(2):
                            r = slice(64 * kvh, 64 * kvh + 64)
                            for t in range(2):
                                c = 32 * (2 * t + kvh)
                                nc.scalar.activation(QB[r, t, c:c + 32].rearrange("p (g q) -> p g q", g=4),
                                                     Q2[r, 4 * t:4 * t + 4, at], ACT.Copy)
                        nc.scalar.activation(VCs, VC[:, bass.ds(b, 1), :].rearrange("p a n -> p (a n)"),
                                             ACT.Copy).then_inc(seq_ready.sem, 1)
                        act.wait_ge(centre_ready.sem, centre_ready.at(1) + 2 * b)
                        nc.scalar.activation(zc, zc, ACT.Exp, bias=st[:, 0:1], accum_out=st[:, 1:2])\
                            .then_inc(exponent.sem, 1)
                        act.wait_ge(chosen.sem, chosen.at(2) + 4 * b)
                        nc.scalar.activation(pT[0:NC, 14, :], PS[0:NC, 6, 0:P], ACT.Copy).then_inc(logged.sem, 1)
                        act.wait_ge(centre_ready.sem, centre_ready.at(2) + 2 * b)
                        nc.scalar.activation(zw, zw, ACT.Exp, bias=st[:, 4:5], accum_out=st[:, 7:8])
                        nc.scalar.activation(zs, zs, ACT.Exp, bias=st[:, 3:4], accum_out=st[:, 6:7])\
                            .then_inc(exponent.sem, 1)
                        for n in range(3):
                            act.wait_ge(turned.sem, turned.at(n + 1) + 4 * b)
                            nc.scalar.activation(pT[:, 4 * n:4 * n + 4, :].rearrange("p k r -> p (k r)"),
                                                 PS[:, 6 + n % 2, :], ACT.Copy).then_inc(turned_read.sem, 1)
                        act.wait_ge(turned.sem, turned.at(4) + 4 * b)
                        nc.scalar.activation(pT[0:LS, 12:14, :].rearrange("p k r -> p (k r)"), PS[0:LS, 7, 0:2 * P],
                                             ACT.Copy)
                        nc.scalar.activation(pT[0:NC, 14, :], PS[0:NC, 7, 2 * P:3 * P], ACT.Copy)\
                            .then_inc(turned_read.sem, 1)
                    act.wait_ge(pool_step.sem, pool_step.at(BUILT))
                    with act.Fori(0, NB // 2) as g:
                        one(g, 0)
                        one(g, 1)

                @block.vector
                def _(dve):
                    step = Chain(dve, dve_step)

                    def one(g, i):
                        b = 2 * g + i
                        gate = GS[:, bass.ds(b, 1), :].rearrange("p a c -> p (a c)")
                        dve.wait_ge(chosen.sem, chosen.at(1) + 4 * b)
                        nc.vector.tensor_tensor(zc, zcp, Bs[:, 31:31 + 16 * (NC - 1) + 1:16], ALU.add)\
                            .then_inc(scaled.sem, 1)
                        dve.wait_ge(scaled.sem, scaled.at(1) + 2 * b)
                        nc.vector.tensor_reduce(st[:, 0:1], zc, AX.X, ALU.max, negate=True).then_inc(centre_ready.sem, 1)
                        dve.wait_ge(exponent.sem, exponent.at(1) + 2 * b)
                        step(nc.vector.reciprocal(st[:, 2:3], st[:, 1:2]))
                        nc.vector.tensor_scalar(pc[:, 0:NC], zc, st[:, 2:3], None, ALU.mult).then_inc(keep_ready.sem, 1)
                        dve.wait_ge(keep_ready.sem, keep_ready.at(1) + 3 * b)
                        step(nc.vector.tensor_scalar(zc, pc[:, 0:NC], gate[:, 0:1], None, ALU.mult))
                        dve.wait_ge(logit_ready.sem, logit_ready.at(1) + b)
                        nc.vector.tensor_tensor(zw, zwp, Bw[:], ALU.add)
                        nc.vector.tensor_tensor(zs, zsp, Bs[:], ALU.add).then_inc(scaled.sem, 1)
                        dve.wait_ge(chosen.sem, chosen.at(3) + 4 * b)
                        nc.vector.tensor_copy(cov, PS[:, 5, 0:17]).then_inc(keep_ready.sem, 1)
                        dve.wait_ge(chosen.sem, chosen.at(4) + 4 * b)
                        step(nc.vector.tensor_copy(drop[:, 0:14], PS[:, 5, 33:47]))
                        step(nc.vector.tensor_reduce(st[:, 8:9], drop[:, 0:14], AX.X, ALU.min))
                        step(nc.vector.scalar_tensor_tensor(out=hit, in0=drop[:, 0:14], scalar=st[:, 8:9],
                                                            in1=block_no[:, 1:15], op0=ALU.is_le, op1=ALU.mult))
                        step(nc.vector.tensor_reduce(st[:, 9:10], hit, AX.X, ALU.max))
                        step(nc.vector.tensor_scalar(drop, block_no, st[:, 9:10], NEG, ALU.is_equal, ALU.mult))
                        dve.wait_ge(scaled.sem, scaled.at(2) + 2 * b)
                        d = bass.AP(drop.tensor, drop.offset, [list(x) for x in drop.ap] + [[0, 64]])
                        v = zs[:, 0:PAST].rearrange("p (j k) -> p j k", j=16)
                        step(nc.vector.tensor_tensor(v, v, d, ALU.add))
                        nc.vector.tensor_reduce(st[:, 4:5], zw, AX.X, ALU.max, negate=True)
                        nc.vector.tensor_reduce(st[:, 3:4], zs, AX.X, ALU.max, negate=True)\
                            .then_inc(centre_ready.sem, 1)
                        dve.wait_ge(exponent.sem, exponent.at(2) + 2 * b)
                        step(nc.vector.reciprocal(st[:, 6:8], st[:, 6:8]))
                        step(nc.vector.tensor_tensor(st[:, 6:8], st[:, 6:8], gate[:, 1:3], ALU.mult))
                        nc.vector.tensor_scalar(zw, zw, st[:, 7:8], None, ALU.mult).then_inc(keep_ready.sem, 1)
                        nc.vector.tensor_scalar(zs, zs, st[:, 6:7], None, ALU.mult).then_inc(weight_ready.sem, 1)
                        dve.wait_ge(out_ready.sem, out_ready.at(1) + b)
                        for kvh in range(2):
                            r = slice(64 * kvh, 64 * kvh + 64)
                            src = PS[r, 5, 64:192].rearrange("p (t k g q) -> p t k g q", t=2, k=2, g=4)[:, :, kvh, :, :]
                            to = OT[r, :, bass.ds(b * LS + NPR, LS)].rearrange("p (t g) q -> p t g q", t=2)
                            nc.vector.tensor_copy(to, src).then_inc(out_read.sem, 1)
                    dve.wait_ge(pool_step.sem, pool_step.at(BUILT))
                    with dve.Fori(0, NB // 2) as g:
                        step.loop(g, 20)
                        one(g, 0)
                        one(g, 1)
                        step.done(NB // 2)
                    dve_step.count = step.n
            loads.close(16)
            pool_step.close(pool_step.count)
            dve_step.close(dve_step.count)
            for s in (logit_ready, logged, weight_ready, out_ready, seq_ready):
                s.close(NB)
            for s in (scaled, centre_ready, exponent, out_read):
                s.close(2 * NB)
            keep_ready.close(3 * NB)
            chosen.close(4 * NB)
            turned.close(4 * NB)
            turned_read.close(4 * NB)
            for s in page_in:
                s.close(LOADED * (NB // 2))

        n = 0
        n = ada_stage(0, n)
        n = ffn_stage(0, 0, n)
        n = even_stage(n)
        n = ffn_stage(0, 1, n)
        n = ada_stage(1, n)
        n = ffn_stage(1, 0, n)
        n = odd_stage(n)
        n = ffn_stage(1, 1, n)
        assert n == NSLOT

        with nc.Block() as block:
            @block.sync
            def _(sp):
                sp.dma_start(io["yT"], X[:]).then_inc(stored.sem, 16)
                sp.wait_ge(stored.sem, stored.at(16))


def bucket_one_hot():
    dist = DIST_HI - np.arange(NDIST)
    d = np.maximum(dist, 0)
    ratio = np.log(np.maximum(d, 16).astype(np.float32) / np.float32(16)) / np.float32(math.log(1024 / 16))
    bucket = np.where(d < 16, d, np.minimum(16 + (ratio * np.float32(16)).astype(np.int32), 31))
    bucket = np.where(dist < 0, 32, bucket)
    return (np.arange(33)[:, None] == bucket[None, :]).astype(np.float32)


def slots_of(w):
    n = w.shape[1] // 512
    return w.reshape(KT, P, n, 512).transpose(2, 1, 0, 3).reshape(n, P, SLOT)


def weight_slots(i):
    out = []

    def ffn(l, f):
        w = i["ffn_w_in"][l, f].reshape(D, 2, DFF // 256, 256).transpose(0, 2, 1, 3).reshape(D, 2 * DFF)
        out.append(slots_of(w))
        w = np.zeros((OUT_GROUPS * D, D), np.float32)
        w[:DFF] = i["ffn_w_out"][l, f]
        w = w.reshape(OUT_GROUPS, D, D)
        w = np.stack([slots_of(w[g]) for g in range(OUT_GROUPS)], axis=1)
        out.append(w.reshape(OUT_SLOTS, P, SLOT))

    out.append(slots_of(i["ada_w"][0]))
    ffn(0, 0)
    w = i["even_w_in"][0]
    out.append(slots_of(w[:, :3072]))
    out.append(slots_of(i["even_w_out"][0]))
    ffn(0, 1)
    out.append(slots_of(i["ada_w"][1]))
    ffn(1, 0)
    w = i["odd_w_in"][0]
    q = w[:, :1024].reshape(D, 2, 2, 4, 64).transpose(0, 1, 3, 2, 4).reshape(D, 1024)
    kc, vc, ks, vs, kw, vw = [w[:, 1024 + 256 * n:1280 + 256 * n] for n in range(6)]
    out.append(slots_of(np.concatenate([q, kc, vc, ks, kw, vs, vw], axis=1)))
    wo = i["odd_w_out"][0].reshape(2, 2, 4, 64, D).transpose(0, 2, 1, 3, 4).reshape(D, D)
    out.append(slots_of(wo))
    ffn(1, 1)
    return np.concatenate(out, axis=0)


def lay_out(i):
    def feat(a):
        a = a.reshape(a.shape[:-1] + (KT, P))
        return np.moveaxis(a, -1, 0)

    x = np.concatenate([i["x_prompt"].reshape(NPR, D), i["x_sample"].reshape(NB * LS, D)])
    c = np.concatenate([i["c_prompt"], i["c_sample"]])
    a = {}
    a["xT"] = feat(x).transpose(0, 2, 1)
    a["cT"] = feat(c).transpose(0, 2, 1)
    a["norm_gT"] = feat(i["norm_g"])
    a["ada_bT"] = feat(i["ada_b"].reshape(2, 9, D)).reshape(P, 2, 9 * KT)
    a["w_slots"] = weight_slots(i)
    a["w_a1"] = i["even_w_in"][0][:, 3072:].reshape(KT, P, 16).transpose(1, 0, 2)
    a["w_a2"] = i["gla_w_a2"][0]
    a["b_a2"] = i["gla_b_a2"]
    a["onorm_g"] = i["gla_onorm_g"].reshape(P, 1)
    a["w_gt"] = i["odd_w_in"][0][:, 2560:].reshape(KT, P, 48).transpose(1, 0, 2)
    a["pages"] = i["page_table"].reshape(1, NB * NPG)
    a["sb_kT"] = i["cache_sb_k"][0].reshape(NPOOL, PAGE, 4, P).transpose(0, 3, 2, 1).reshape(NPOOL, P, 4 * PAGE)
    a["sb_v"] = i["cache_sb_v"][0].reshape(NPOOL, PAGE, 512)
    a["gla_s"] = i["state_gla"][0].reshape(NB, 2, P, P).transpose(2, 0, 1, 3)
    a["slc_kT"] = i["cache_slc_k"][0].reshape(NPOOL, PAGE, 2, P).transpose(0, 3, 2, 1).reshape(NPOOL, P, 2 * PAGE)
    a["slc_v"] = i["cache_slc_v"][0].reshape(NPOOL, PAGE, 256)
    for n in "kv":
        t = i["cache_cmp_" + n][0].reshape(NPOOL, 8, 8, 2, 4, 64)
        a["cmp_" + n] = t.transpose(0, 3, 5, 4, 2, 1).reshape(NPOOL, P, 256)
    a["win_kT"] = i["cache_win_k"][0].reshape(NB, WIN, 2, P).transpose(0, 3, 2, 1).reshape(NB, P, 2 * WIN)
    a["win_k"] = i["cache_win_k"][0].reshape(NB, WIN, 256)
    a["win_v"] = i["cache_win_v"][0].reshape(NB, WIN, 256)
    g = i["nsa_qk_g"][0].T
    a["qk_g"] = np.concatenate([g, g])
    w1 = i["cmp_w1"][0].reshape(2, 2, 8, P, P)
    a["cmp_w1"] = w1.transpose(3, 0, 1, 2, 4)
    a["cmp_b1"] = i["cmp_b1"][0].T
    a["cmp_w2"] = i["cmp_w2"][0].transpose(1, 0, 2)
    b2 = i["cmp_b2"][0]
    a["cmp_b2k"] = np.concatenate([b2[0], b2[0]]).reshape(P, 1)
    a["cmp_b2v"] = b2[1:2]
    a["rel_table"] = i["rel_table"]
    a["one_hot"] = bucket_one_hot()
    return {k: np.ascontiguousarray(v) for k, v in a.items()}


OUTS = {
    "yT": (P, KT, NT), "o_sbk": (P, 4, NT), "o_sbv": (NT, 512), "o_pgla": (P, 2, P), "o_sgla": (P, NB, 2, P),
    "o_kcvc": (P, 4, NT), "o_kskw": (P, 4, NT), "o_vsvw": (NT, 512),
    "o_wink": (NB, WIN - LS, 256), "o_winv": (NB, WIN - LS, 256),
}


def kernel(**inputs):
    import concourse.bacc as _bacc
    from concourse.bass_utils import run_bass_kernel_spmd as _run

    arrays = lay_out({k: np.asarray(v) for k, v in inputs.items()})
    nc = _bacc.Bacc("TRN2", target_bir_lowering=False, num_devices=1)
    io = {}
    for name, a in arrays.items():
        io[name] = nc.dram_tensor(name, a.shape, mybir.dt.from_np(a.dtype), kind="ExternalInput").ap()
    for name, shape in OUTS.items():
        io[name] = nc.dram_tensor(name, shape, F32, kind="ExternalOutput").ap()
    io["bias_rows"] = nc.dram_tensor("bias_rows", (P, NDIST), F32, kind="Internal").ap()
    io["bias_prompt"] = nc.dram_tensor("bias_prompt", (P, 16, NDIST_P), F32, kind="Internal").ap()
    io["gate_rows"] = nc.dram_tensor("gate_rows", (NB, LS, 16, 3), F32, kind="Internal").ap()
    io["new_rows"] = nc.dram_tensor("new_rows", (2, NB * LS, 512), F32, kind="Internal").ap()
    build(nc, io)
    o = _run(nc, [arrays], core_ids=[0]).results[0]

    def rows(t, heads):
        t = t.transpose(2, 1, 0).reshape(NT, heads, 64)
        return t[:NPR].reshape(1, 1, NPR, heads, 64), t[NPR:].reshape(1, NB, LS, heads, 64)

    def natural(t, heads):
        t = t.reshape(NT, heads, 64)
        return t[:NPR].reshape(1, 1, NPR, heads, 64), t[NPR:].reshape(1, NB, LS, heads, 64)

    y = o["yT"].transpose(2, 1, 0).reshape(NT, D)
    p_sbk, s_sbk = rows(o["o_sbk"], 8)
    p_sbv, s_sbv = natural(o["o_sbv"], 8)
    p_gla = o["o_pgla"].transpose(1, 0, 2).reshape(1, 1, 4, 64, P)
    s_gla = o["o_sgla"].transpose(1, 2, 0, 3).reshape(1, NB, 4, 64, P)
    p_kc, s_kc = rows(o["o_kcvc"][:, 0:2], 4)
    p_vc, s_vc = rows(o["o_kcvc"][:, 2:4], 4)
    p_ks, s_ks = rows(o["o_kskw"][:, 0:2], 4)
    p_kw, s_kw = rows(o["o_kskw"][:, 2:4], 4)
    p_vs, s_vs = natural(o["o_vsvw"][:, 0:256], 4)
    p_vw, s_vw = natural(o["o_vsvw"][:, 256:512], 4)

    def window(old, new):
        return np.concatenate([old.reshape(1, NB, WIN - LS, 4, 64), new], axis=2)

    return (y[:NPR].reshape(1, NPR, D), y[NPR:].reshape(NB, LS, D), p_sbk, p_sbv, p_gla, p_kc, p_vc, p_ks, p_vs,
            p_kw, p_vw, s_sbk, s_sbv, s_gla, s_kc, s_vc, s_ks, s_vs, window(o["o_wink"], s_kw),
            window(o["o_winv"], s_vw))
```

```python
import math
from contextlib import ExitStack

import numpy as np
import concourse.bass as bass
from concourse import mybir

F32 = mybir.dt.float32
I32 = mybir.dt.int32
ACT = mybir.ActivationFunctionType
ALU = mybir.AluOpType
AX = mybir.AxisListType

P = 128
D = 1024
KT = D // P
NPR = 256
NB = 8
LS = 8
NT = NPR + NB * LS
NSEQ = 1 + NB
DFF = 2816
FT = DFF // P
PAST = 1024
PAGE = 128
NPG = PAST // PAGE
NPOOL = NB * NPG * 5 // 4
WIN = 512
RING = 4


def ffn_plan(n_ada):
    if n_ada:
        pairs = IN_SLOTS // 2 * 2
        before = [("a", a) for a in range(min(4, n_ada - pairs))]
        b = len(before)
        body = [("h", 0), ("a", b), ("h", 1), ("a", b + 1)]
        rounds, left = pairs // 2, n_ada - pairs - b
        after = [("h", IN_SLOTS - 1)]
        for i in range(OUT_SLOTS):
            after.append(("o", i))
            if i < left:
                after.append(("a", b + pairs + i))
    else:
        before, rounds = [], IN_SLOTS // RING
        body = [("h", j) for j in range(RING)]
        after = [("h", j) for j in range(rounds * RING, IN_SLOTS)] + [("o", i) for i in range(OUT_SLOTS)]
    return before, body, rounds, after


SLOT = KT * 512
ADA_SLOTS = 9 * D // 512
ADA_FIRST = 3 * D // 512
IN_SLOTS = 2 * DFF // 512
OUT_GROUPS = (FT + KT - 1) // KT
OUT_SLOTS = 2 * OUT_GROUPS
EVEN_SLOTS = 6
ODD_SLOTS = 5
EPS = 1e-6
NEG = -1e30
SCALE = 64 ** -0.5
DIST_LO = -127
DIST_HI = PAST + LS - 1
NDIST = DIST_HI - DIST_LO + 1
NDIST_P = 255 - DIST_LO + 1
TILE_ROWS = [128, 128, 64]


def rep(ap, axis, n):
    dims = [list(x) for x in ap.ap]
    return bass.AP(ap.tensor, ap.offset, dims[:axis] + [[0, n]] + dims[axis:])


class Signal:

    def __init__(self, ctx, nc, name):
        self.sem = ctx.enter_context(nc.semaphore(name))
        self.base = 0
        self.count = 0

    def at(self, n):
        return self.base + n

    def by(self, ins, n=1):
        ins.then_inc(self.sem, n)
        return ins

    def close(self, n):
        self.base = self.base + n


def build(nc, io):
    ctx = ExitStack()
    with ctx:
        def sb(name, shape, dt=F32, where=ctx):
            return where.enter_context(nc.sbuf_tensor("sb_" + name, shape, dt))

        def signal(name):
            return Signal(ctx, nc, name)

        PS = ctx.enter_context(nc.psum_tensor("PS", [P, 8, 512], F32))
        X = sb("X", [P, KT, NT])
        H = sb("H", [P, KT, NT])
        OT = sb("OT", [P, KT, NT])
        ring = sb("ring", [P, RING, KT, 512])
        silu_c = sb("silu_c", [P, KT, NSEQ])
        mods = [sb(f"mod{i}", [P, 9, KT, NSEQ]) for i in range(2)]
        gains = [sb(f"gain{i}", [P, 3, KT, NSEQ]) for i in range(2)]
        silu_c32 = sb("silu_c32", [P, KT, 32])
        ada_rows = sb("ada_rows", [P, P])
        norm_g = sb("norm_g", [P, 2, 3, KT])
        ada_b = sb("ada_b", [P, 2, 9 * KT])
        rstd = sb("rstd", [P, NT])
        ones = sb("ones", [P, P])
        ident = sb("ident", [P, P])
        halves = sb("halves", [P, P])
        later = sb("later", [P, P])
        strict = sb("strict", [P, P])

        ada_done = signal("ada_done")
        ada_out = signal("ada_out")
        ada_turned = signal("ada_turned")
        ada_read = signal("ada_read")
        unit_done = signal("unit_done")
        gated = signal("gated")
        out_done = signal("out_done")
        pair_read = signal("pair_read")
        landed = [signal(f"landed{r}") for r in range(RING)]
        slot_done = signal("slot_done")
        slot_read = signal("slot_read")
        loads = signal("loads")
        pool_step = signal("pool_step")
        dve_step = signal("dve_step")
        act_step = signal("act_step")
        squared = signal("squared")
        summed = signal("summed")
        variance = signal("variance")
        deviation = signal("deviation")
        centred = signal("centred")
        h_ready = signal("h_ready")
        gate_ready = signal("gate_ready")
        stored = signal("stored")

        NSLOT = io["w_slots"].shape[0]

        def slot_at(n0, it, j):
            return (n0 + j) % RING, 16 * ((n0 + j) // RING + 1) + it * 16

        def refill(sp, n0, it, j):
            sp.wait_ge(slot_done.sem, slot_done.at(j + 1) + it * RING)
            fetch(sp, n0, it, j)

        def fetch(sp, n0, it, j):
            r, _ = slot_at(n0, 0, j)
            n = n0 + j + RING + it * RING
            src = io["w_slots"][n] if isinstance(n, int) else io["w_slots"][bass.ds(n, 1), :, :].rearrange("a p n -> p (a n)")
            sp.dma_start(ring[:, r, :, :].rearrange("p k n -> p (k n)"), src).then_inc(landed[r].sem, 16)

        def refill_all(sp, n0, count):
            for j in range(count):
                if n0 + j + RING < NSLOT:
                    refill(sp, n0, 0, j)

        class Chain:

            def __init__(self, eng, sig):
                self.eng, self.sig, self.n, self.start = eng, sig, 0, 0

            def __call__(self, ins):
                ins.then_inc(self.sig.sem, 1)
                self.n += 1
                self.eng.wait_ge(self.sig.sem, self.sig.at(self.n + self.start))

            def loop(self, it, per):
                self.start = self.n + it * per
                self.n, self.before, self.per = 0, self.n, per

            def done(self, times):
                assert self.n == self.per, (self.n, self.per)
                self.n, self.start = self.before + times * self.per, 0

        with nc.Block(no_gpsimd_drain=True) as block:
            @block.sync
            def _(sp):
                for dst, src in ((silu_c, "cT"), (X, "xT"), (norm_g, "norm_gT"), (ada_b, "ada_bT")):
                    sp.dma_start(dst[:], io[src]).then_inc(loads.sem, 16)
                for n in range(RING):
                    sp.dma_start(ring[:, n, :, :].rearrange("p k n -> p (k n)"), io["w_slots"][n])\
                        .then_inc(landed[n].sem, 16)

            @block.scalar
            def _(act):
                act.wait_ge(loads.sem, 64)
                act.wait_ge(pool_step.sem, 1)
                nc.scalar.activation(silu_c32[:, :, 0:NSEQ], silu_c[:], ACT.Silu).then_inc(act_step.sem, 1)

            @block.gpsimd
            def _(pool):
                step = Chain(pool, pool_step)
                step(pool.memset(silu_c32[:], 0.0))
                pool.memset(ones[:], 1.0)
                pool.memset(ident[:], 0.0)
                pool.memset(later[:], 1.0)
                step(pool.memset(strict[:], 1.0))
                pool.memset(halves[:], 0.0)
                step(pool.affine_select(out=ident[:], in_=ident[:], compare_op=ALU.not_equal, fill=1.0,
                                        base=0, pattern=[[-1, P]], channel_multiplier=1))
                step(pool.affine_select(out=later[:], in_=later[:], compare_op=ALU.is_ge, fill=0.0,
                                        base=0, pattern=[[-1, P]], channel_multiplier=1))
                step(pool.affine_select(out=strict[:], in_=strict[:], compare_op=ALU.is_gt, fill=0.0,
                                        base=0, pattern=[[1, P]], channel_multiplier=-1))
                step(pool.memset(halves[0:64, 0:64], 1.0))
                step(pool.memset(halves[64:128, 64:128], 1.0))
                pool_step.count = step.n
        loads.close(64)
        act_step.close(1)
        pool_step.close(pool_step.count)

        def ada_turn(pe, a):
            pe.wait_ge(ada_out.sem, ada_out.at(a + 1))
            if a:
                pe.wait_ge(ada_read.sem, ada_read.at(a))
            nc.tensor.transpose(PS[:, 5, 0:P], ada_rows[:], ident[:]).then_inc(ada_turned.sem, 1)

        def ada_products(pe, n0, it, j, a):
            r, there = slot_at(n0, it, j)
            if not isinstance(it, int) or a > 0:
                step = 0 if isinstance(it, int) else 2 * it
                pe.wait_ge(ada_out.sem, ada_out.at(a) + step)
                if not isinstance(it, int) or a > 1:
                    pe.wait_ge(ada_read.sem, ada_read.at(a - 1) + step)
                nc.tensor.transpose(PS[:, 5, 0:P], ada_rows[:], ident[:]).then_inc(ada_turned.sem, 1)
            pe.wait_ge(landed[r].sem, there)
            for k in range(KT):
                for m in range(4):
                    mm = nc.tensor.matmul(PS[32 * m:32 * m + 32, 4, 0:P], silu_c32[:, k, :],
                                          ring[:, r, k, m * P:(m + 1) * P], start=(k == 0), stop=(k == KT - 1))
            mm.then_inc(ada_done.sem, 1)

        def ada_copy(act, a):
            act.wait_ge(ada_done.sem, ada_done.at(a + 1))
            nc.scalar.activation(ada_rows[:], PS[:, 4, 0:P], ACT.Copy).then_inc(ada_out.sem, 1)

        def ada_store(dve, layer, a, c):
            dve.wait_ge(ada_turned.sem, ada_turned.at(a + 1))
            flat = mods[layer][:].rearrange("p i k s -> p (i k) s")
            src = PS[:, 5, 0:P].rearrange("p (m s) -> p m s", s=32)[:, :, 0:NSEQ]
            bias = ada_b[:, layer, 4 * c:4 * c + 4]
            bias = bass.AP(bias.tensor, bias.offset, [list(x) for x in bias.ap] + [[0, NSEQ]])
            nc.vector.tensor_tensor(flat[:, 4 * c:4 * c + 4, :], src, bias, ALU.add).then_inc(ada_read.sem, 1)

        def ada_finish(dve, layer, norms, step):
            mod, gain = mods[layer], gains[layer]
            for i in norms:
                g = norm_g[:, layer, i, :]
                g = bass.AP(g.tensor, g.offset, [list(x) for x in g.ap] + [[0, NSEQ]])
                step(nc.vector.scalar_tensor_tensor(out=gain[:, i, :, :], in0=mod[:, 3 * i + 1, :, :], scalar=1.0,
                                                    in1=g, op0=ALU.add, op1=ALU.mult))
                if i != 1:
                    step(nc.vector.tensor_scalar(mod[:, 3 * i + 2, :, :], mod[:, 3 * i + 2, :, :], 0.5, None, ALU.mult))

        def ada_close(n):
            for s in (ada_done, ada_out, ada_turned, ada_read):
                s.close(n)

        def first_ada_stage(n0):
            with nc.Block(no_gpsimd_drain=True) as block:
                @block.sync
                def _(sp):
                    for a in range(ADA_FIRST):
                        sp.wait_ge(ada_done.sem, ada_done.at(a + 1))
                        fetch(sp, n0, 0, a)

                @block.tensor
                def _(pe):
                    for a in range(ADA_FIRST):
                        ada_products(pe, n0, 0, a, a)
                    ada_turn(pe, ADA_FIRST - 1)

                @block.scalar
                def _(act):
                    for a in range(ADA_FIRST):
                        ada_copy(act, a)

                @block.vector
                def _(dve):
                    step = Chain(dve, dve_step)
                    for a in range(ADA_FIRST):
                        ada_store(dve, 0, a, a)
                    dve.wait_ge(ada_read.sem, ada_read.at(ADA_FIRST))
                    ada_finish(dve, 0, [0], step)
                    dve_step.count = step.n
            ada_close(ADA_FIRST)
            dve_step.close(dve_step.count)
            return n0 + ADA_FIRST

        NORM_BANK = 7

        def squares(act):
            nc.scalar.activation(OT[:], X[:], ACT.Square).then_inc(squared.sem, 1)

        def norm_act(act, layer, i):
            act.wait_ge(variance.sem, variance.at(1))
            nc.scalar.activation(rstd[:], rstd[:], ACT.Sqrt).then_inc(deviation.sem, 1)
            act.wait_ge(centred.sem, centred.at(1))
            for k in range(KT):
                nc.scalar.activation(H[:, k, 0:NPR], H[:, k, 0:NPR], ACT.Identity, bias=mods[layer][:, 3 * i, k, 0:1],
                                     scale=gains[layer][:, i, k, 0:1]).then_inc(h_ready.sem, 1)

        def norm_pe(pe):
            pe.wait_ge(squared.sem, squared.at(1))
            for k in range(KT):
                mm = nc.tensor.matmul(PS[:, NORM_BANK, 0:NT], ones[:], OT[:, k, :], start=(k == 0), stop=(k == KT - 1))
            mm.then_inc(summed.sem, 1)

        def norm_dve(dve, layer, i, step, between=None):
            dve.wait_ge(summed.sem, summed.at(1))
            nc.vector.tensor_scalar(rstd[:], PS[:, NORM_BANK, 0:NT], 1.0 / D, EPS, ALU.mult, ALU.add)\
                .then_inc(variance.sem, 1)
            if between is not None:
                between()
            dve.wait_ge(deviation.sem, deviation.at(1))
            step(nc.vector.reciprocal(rstd[:], rstd[:]))
            nc.vector.tensor_tensor(H[:], X[:], rep(rstd[:], 1, KT), ALU.mult).then_inc(centred.sem, 1)
            dve.wait_ge(centred.sem, centred.at(1))
            part = H[:, :, NPR:NT].rearrange("p k (b l) -> p k b l", l=LS)

            def per_seq(t, n):
                a = t[:, n, :, 1:NSEQ]
                return bass.AP(a.tensor, a.offset, [list(x) for x in a.ap] + [[0, LS]])
            step(nc.vector.tensor_tensor(part, part, per_seq(gains[layer], i), ALU.mult))
            nc.vector.tensor_tensor(part, part, per_seq(mods[layer], 3 * i), ALU.add).then_inc(h_ready.sem, 1)

        H_READY = KT + 1

        def norm_close():
            for s in (squared, summed, variance, deviation, centred):
                s.close(1)
            h_ready.close(H_READY)

        gated_rows = sb("gated_rows", [P, 2, 2, NT - NPR])

        def add_gated(dve, step, layer, i, pair, banks):
            mod, m0 = mods[layer], 2 * pair
            for m in range(2):
                nc.vector.scalar_tensor_tensor(out=X[:, m0 + m, 0:NPR], in0=PS[:, banks + m, 0:NPR],
                                               scalar=mod[:, i, m0 + m, 0:1], in1=X[:, m0 + m, 0:NPR],
                                               op0=ALU.mult, op1=ALU.add).then_inc(gate_ready.sem, 1)
            src = PS[:, banks:banks + 2, NPR:NT].rearrange("p m (b l) -> p m b l", l=LS)
            gate = mod[:, i, m0:m0 + 2, 1:NSEQ]
            gate = bass.AP(gate.tensor, gate.offset, [list(x) for x in gate.ap] + [[0, LS]])
            rows = gated_rows[:, pair % 2, :, :]
            if pair >= 2:
                dve.wait_ge(gate_ready.sem, gate_ready.at(3 * pair - 3))
            nc.vector.tensor_tensor(rows.rearrange("p m (b l) -> p m b l", l=LS), src, gate, ALU.mult)\
                .then_inc(pair_read.sem, 1)
            dve.wait_ge(pair_read.sem, pair_read.at(pair + 1))
            part = X[:, m0:m0 + 2, NPR:NT]
            nc.vector.tensor_tensor(part, part, rows, ALU.add).then_inc(gate_ready.sem, 1)

        def ffn_stage(layer, which, n0, ada_layer=0, ada_from=0, n_ada=0):
            ni = 2 * which
            before, body, rounds, after = ffn_plan(n_ada)
            n1 = n0 + len(before)
            n2 = n1 + rounds * RING
            per_h = sum(kind == "h" for kind, _ in body)
            UNITS = 2 * IN_SLOTS
            OUT_BANKS = [0, 2, 6, 0]
            with ExitStack() as stage:
                G = sb(f"G{layer}{which}", [P, FT, NT], F32, stage)
                S = sb(f"S{layer}{which}", [P, 2, NT], F32, stage)
                block = stage.enter_context(nc.Block(no_gpsimd_drain=True))

                @block.sync
                def _(sp):
                    def one(n, it, j, kind, k):
                        per = {"h": 2 * per_h, "a": 2, "o": 0}[kind]
                        sig, at = {"h": (unit_done, 2 * k + 2), "a": (ada_done, k + 1), "o": (out_done, k + 1)}[kind]
                        sp.wait_ge(sig.sem, sig.at(at) + it * per)
                        fetch(sp, n, it, j)
                    for j, (kind, k) in enumerate(before):
                        one(n0, 0, j, kind, k)
                    with sp.Fori(0, rounds) as it:
                        for j, (kind, k) in enumerate(body):
                            one(n1, it, j, kind, k)
                    for j, (kind, k) in enumerate(after):
                        if n2 + j + RING < NSLOT:
                            one(n2, 0, j, kind, k)

                @block.tensor
                def _(pe):
                    def hidden(n, it, j, k, first):
                        r, there = slot_at(n, it, j)
                        pe.wait_ge(landed[r].sem, there)
                        for m in range(2):
                            if not first:
                                pe.wait_ge(gated.sem, gated.at(2 * k + m - 1) + it * (2 * per_h))
                            for part in range(2):
                                for q in range(KT):
                                    c = 256 * part + m * P
                                    mm = nc.tensor.matmul(PS[:, 2 * m + part, 0:NT], ring[:, r, q, c:c + P],
                                                          H[:, q, :], start=(q == 0), stop=(q == KT - 1))
                            mm.then_inc(unit_done.sem, 1)

                    def output(n, j, i):
                        half, g = i // OUT_GROUPS, i % OUT_GROUPS
                        r, there = slot_at(n, 0, j)
                        pe.wait_ge(landed[r].sem, there)
                        if i == 0:
                            pe.wait_ge(gated.sem, gated.at(UNITS))
                        for m in range(4):
                            if half and g == 0 and m == 2:
                                pe.wait_ge(pair_read.sem, pair_read.at(1))
                            for q in range(KT * g, min(KT * (g + 1), FT)):
                                mm = nc.tensor.matmul(PS[:, OUT_BANKS[2 * half + m // 2] + m % 2, 0:NT],
                                                      ring[:, r, q - KT * g, m * P:(m + 1) * P], G[:, q, :],
                                                      start=(q == 0), stop=(q == FT - 1))
                        mm.then_inc(out_done.sem, 1)

                    norm_pe(pe)
                    for j, (_, a) in enumerate(before):
                        ada_products(pe, n0, 0, j, a)
                    pe.wait_ge(h_ready.sem, h_ready.at(H_READY))

                    def round_of(it, first):
                        for j, (kind, k) in enumerate(body):
                            if kind == "h":
                                hidden(n1, it, j, k, first and k == 0)
                            else:
                                ada_products(pe, n1, it, j, k)
                    round_of(0, True)
                    with pe.Fori(1, rounds) as it:
                        round_of(it, False)
                    for j, (kind, k) in enumerate(after):
                        if kind == "h":
                            hidden(n2, 0, j, k, False)
                        elif kind == "a":
                            ada_products(pe, n2, 0, j, k)
                        else:
                            output(n2, j, k)
                    if n_ada:
                        ada_turn(pe, n_ada - 1)

                order = before + [(kind, k + it * (per_h if kind == "h" else 2)) for it in range(rounds)
                                  for kind, k in body] + after

                @block.scalar
                def _(act):
                    def hidden(k):
                        for u in (2 * k, 2 * k + 1):
                            act.wait_ge(unit_done.sem, unit_done.at(u + 1))
                            if u >= 2:
                                act.wait_ge(gated.sem, gated.at(u - 1))
                            nc.scalar.activation(S[:, u % 2, :], PS[:, 2 * (u % 2), 0:NT], ACT.Silu)\
                                .then_inc(act_step.sem, 1)
                    squares(act)
                    for kind, k in before:
                        ada_copy(act, k)
                    norm_act(act, layer, ni)
                    for kind, k in order[len(before):]:
                        if kind == "h":
                            hidden(k)
                        elif kind == "a":
                            ada_copy(act, k)

                @block.vector
                def _(dve):
                    step = Chain(dve, dve_step)
                    done = 0

                    def stores(upto):
                        for a in range(done, upto):
                            ada_store(dve, ada_layer, a, ada_from + a)
                        return max(done, upto)
                    norm_dve(dve, layer, ni, step, lambda: stores(len(before) - 1))
                    done = max(0, len(before) - 1)
                    for kind, k in order[len(before):]:
                        if kind == "h":
                            for u in (2 * k, 2 * k + 1):
                                dve.wait_ge(act_step.sem, act_step.at(u + 1))
                                nc.vector.tensor_tensor(G[:, u, :], S[:, u % 2, :], PS[:, 2 * (u % 2) + 1, 0:NT],
                                                        ALU.mult).then_inc(gated.sem, 1)
                        elif kind == "a":
                            done = stores(k)
                        elif k % OUT_GROUPS == OUT_GROUPS - 1:
                            half = k // OUT_GROUPS
                            dve.wait_ge(out_done.sem, out_done.at(k + 1))
                            for pair in (2 * half, 2 * half + 1):
                                add_gated(dve, step, layer, 3 * ni + 2, pair, OUT_BANKS[pair])
                    done = stores(n_ada)
                    if n_ada:
                        dve.wait_ge(ada_read.sem, ada_read.at(n_ada))
                        ada_finish(dve, ada_layer, [1, 2] if ada_from else [0, 1, 2], step)
                    dve_step.count = step.n
            norm_close()
            ada_close(n_ada)
            act_step.close(UNITS)
            unit_done.close(UNITS)
            gated.close(UNITS)
            out_done.close(OUT_SLOTS)
            pair_read.close(4)
            gate_ready.close(12)
            dve_step.close(dve_step.count)
            return n2 + len(after)

        def out_stage(layer, n0):
            with nc.Block(no_gpsimd_drain=True) as block:
                @block.sync
                def _(sp):
                    refill_all(sp, n0, 2)

                @block.tensor
                def _(pe):
                    for half in range(2):
                        r, there = slot_at(n0, 0, half)
                        pe.wait_ge(landed[r].sem, there)
                        for m in range(4):
                            for k in range(KT):
                                mm = nc.tensor.matmul(PS[:, 4 * half + m, 0:NT], ring[:, r, k, m * P:(m + 1) * P],
                                                      OT[:, k, :], start=(k == 0), stop=(k == KT - 1))
                        mm.then_inc(slot_done.sem, 1)

                @block.vector
                def _(dve):
                    step = Chain(dve, dve_step)
                    for half in range(2):
                        dve.wait_ge(slot_done.sem, slot_done.at(half + 1))
                        for pair in (2 * half, 2 * half + 1):
                            add_gated(dve, step, layer, 5, pair, 2 * pair)
                    dve_step.count = step.n
            slot_done.close(2)
            pair_read.close(4)
            dve_step.close(dve_step.count)
            gate_ready.close(12)
            return n0 + 2

        def project_stage(layer, n0, kinds, tail_w, tail_cols, tail_dst, tail_rows):
            n = len(kinds)
            with nc.Block(no_gpsimd_drain=True) as block:
                @block.sync
                def _(sp):
                    refill_all(sp, n0, n)

                @block.tensor
                def _(pe):
                    norm_pe(pe)
                    pe.wait_ge(h_ready.sem, h_ready.at(H_READY))
                    for j, (transposed, _) in enumerate(kinds):
                        r, there = slot_at(n0, 0, j)
                        pe.wait_ge(landed[r].sem, there)
                        if j >= 2:
                            pe.wait_ge(slot_read.sem, slot_read.at(j - 1))
                        b = 4 * (j % 2)
                        if transposed:
                            for m in range(4):
                                for k in range(KT):
                                    mm = nc.tensor.matmul(PS[:, b + m, 0:NT], ring[:, r, k, m * P:(m + 1) * P],
                                                          H[:, k, :], start=(k == 0), stop=(k == KT - 1))
                        else:
                            for t, rows in enumerate(TILE_ROWS):
                                for k in range(KT):
                                    mm = nc.tensor.matmul(PS[0:rows, b + t, :], H[:, k, t * P:t * P + rows],
                                                          ring[:, r, k, :], start=(k == 0), stop=(k == KT - 1))
                        mm.then_inc(slot_done.sem, 1)
                    pe.wait_ge(slot_read.sem, slot_read.at(n - 1))
                    b = 4 * (n % 2)
                    if tail_rows:
                        for t, rows in enumerate(TILE_ROWS):
                            for k in range(KT):
                                mm = nc.tensor.matmul(PS[0:rows, b + t, 0:tail_cols], H[:, k, t * P:t * P + rows],
                                                      tail_w[:, k, :], start=(k == 0), stop=(k == KT - 1))
                    else:
                        for k in range(KT):
                            mm = nc.tensor.matmul(PS[0:tail_cols, b, 0:NT], tail_w[:, k, :], H[:, k, :],
                                                  start=(k == 0), stop=(k == KT - 1))
                    mm.then_inc(summed.sem, 1)

                @block.scalar
                def _(act):
                    squares(act)
                    norm_act(act, layer, 1)
                    for j, (transposed, dst) in enumerate(kinds):
                        act.wait_ge(slot_done.sem, slot_done.at(j + 1))
                        b = 4 * (j % 2)
                        if transposed:
                            nc.scalar.activation(dst, PS[:, b:b + 4, 0:NT], ACT.Copy).then_inc(slot_read.sem, 1)
                        else:
                            nc.scalar.activation(dst[:, 0:2, :], PS[:, b:b + 2, :], ACT.Copy)
                            nc.scalar.activation(dst[0:64, 2, :], PS[0:64, b + 2, :], ACT.Copy)\
                                .then_inc(slot_read.sem, 1)
                    act.wait_ge(summed.sem, summed.at(2))
                    b = 4 * (n % 2)
                    if tail_rows:
                        nc.scalar.activation(tail_dst[:, 0:2, :], PS[:, b:b + 2, 0:tail_cols], ACT.Copy)\
                            .then_inc(act_step.sem, 1)
                        nc.scalar.activation(tail_dst[0:64, 2, :], PS[0:64, b + 2, 0:tail_cols], ACT.Copy)\
                            .then_inc(act_step.sem, 1)
                    else:
                        nc.scalar.activation(tail_dst[:, :], PS[0:tail_cols, b, 0:NT], ACT.Copy)\
                            .then_inc(act_step.sem, 2)

                @block.vector
                def _(dve):
                    step = Chain(dve, dve_step)
                    norm_dve(dve, layer, 1, step)
                    dve_step.count = step.n
            norm_close()
            summed.close(1)
            act_step.close(2)
            slot_read.close(n)
            slot_done.close(n)
            dve_step.close(dve_step.count)
            return n0 + n

        def store(sp, dst, src):
            sp.dma_start(dst, src).then_inc(stored.sem, 16)

        logit_ready = signal("logit_ready")
        keep_ready = signal("keep_ready")
        tail_ready = signal("tail_ready")
        weight_ready = signal("weight_ready")
        out_ready = signal("out_ready")
        out_read = signal("out_read")
        page_in = [signal("page_in0"), signal("page_in1")]
        seq_ready = signal("seq_ready")
        scaled = signal("scaled")
        logged = signal("logged")
        exponent = signal("exponent")

        def even_stage(n0):
            stage = ExitStack()
            with stage:
                def tile(name, shape):
                    return sb(name, shape, F32, stage)

                qkT = tile("qkT", [P, 4, NT])
                vb = tile("vb", [P, 3, 512])
                rT = tile("rT", [P, 4, NT])
                a1T = tile("a1T", [16, NT])
                with ExitStack() as heads:
                    QT = sb("QT", [P, 4, NT], F32, heads)
                    KTT = sb("KTT", [P, 4, NT], F32, heads)
                    V = sb("V", [P, 3, 512], F32, heads)
                    w_a1 = sb("w_a1", [P, KT, 16], F32, heads)
                    with nc.Block(no_gpsimd_drain=True) as block:
                        @block.sync
                        def _(sp):
                            sp.dma_start(w_a1[:], io["w_a1"]).then_inc(loads.sem, 16)
                            sp.wait_ge(loads.sem, loads.at(16))
                    loads.close(16)
                    n1 = project_stage(0, n0, [(True, QT[:]), (True, KTT[:]), (False, V), (True, qkT[:]), (False, vb),
                                            (True, rT[:])], w_a1, 16, a1T, False)
                    stick_prompt(QT, KTT, V)
                    stick_sample(QT, KTT, V)
                linear_attention(qkT, vb, rT, a1T)
            return out_stage(0, n1)

        def stick_prompt(QT, KTT, V):
            W = 384
            PAIRS = 4
            with ExitStack() as stage:
                def tile(name, shape):
                    return sb(name, shape, F32, stage)
                sp1 = tile("p_sp1", [P, 2, 2, W])
                sp2 = tile("p_sp2", [P, 2, 2, W])
                u = tile("p_u", [P, 2, 2, W])
                mask = tile("p_mask", [P, W])
                fill = tile("p_fill", [P, W])
                block = stage.enter_context(nc.Block(no_gpsimd_drain=True))

                @block.sync
                def _(sp):
                    store(sp, io["o_sbk"], KTT[:])
                    store(sp, io["o_sbv"][0:NPR, :].rearrange("(t p) n -> p t n", p=P), V[:, 0:2, :])
                    store(sp, io["o_sbv"][NPR:NT, :], V[0:64, 2, :])
                    sp.dma_start(io["new_rows"][0], V[0:64, 2, :]).then_inc(loads.sem, 16)
                    sp.wait_ge(loads.sem, loads.at(16))

                def region(kt):
                    return (0, 256, 0) if kt == 0 else (256, W, 128)

                @block.tensor
                def _(pe):
                    def logits(a):
                        if a >= 2:
                            pe.wait_ge(scaled.sem, scaled.at(a - 1))
                        for hh in range(2):
                            for kt in range(2):
                                c0, c1, q0 = region(kt)
                                mm = nc.tensor.matmul(PS[:, 2 * (a % 2) + hh, c0:c1],
                                                      KTT[64 * hh:64 * hh + 64, a, kt * P:(kt + 1) * P],
                                                      QT[64 * hh:64 * hh + 64, a, q0:NPR], start=True, stop=True)
                        mm.then_inc(logit_ready.sem, 1)

                    def tails(a):
                        pe.wait_ge(keep_ready.sem, keep_ready.at(a + 1))
                        if a >= 1:
                            pe.wait_ge(exponent.sem, exponent.at(a))
                        for hh in range(2):
                            nc.tensor.matmul(PS[:, 4 + hh, 0:W], later[:], sp2[:, a % 2, hh, :], start=True, stop=False)
                            mm = nc.tensor.matmul(PS[:, 4 + hh, 128:256], ones[:], sp2[:, a % 2, hh, 256:W],
                                                  start=False, stop=True)
                        mm.then_inc(tail_ready.sem, 1)

                    def values(a):
                        pe.wait_ge(weight_ready.sem, weight_ready.at(a + 1))
                        if a >= 2:
                            pe.wait_ge(out_read.sem, out_read.at(a - 1))
                        for hh in range(2):
                            for kt in range(2):
                                c0, c1, q0 = region(kt)
                                h = 2 * a + hh
                                mm = nc.tensor.matmul(PS[64 * hh:64 * hh + 64, 6 + a % 2, q0:NPR],
                                                      V[:, kt, 64 * h:64 * h + 64], u[:, a % 2, hh, c0:c1],
                                                      start=(kt == 0), stop=(kt == 1))
                        mm.then_inc(out_ready.sem, 1)
                    logits(0)
                    for a in range(PAIRS):
                        if a + 1 < PAIRS:
                            logits(a + 1)
                        tails(a)
                        values(a)

                @block.gpsimd
                def _(pool):
                    step = Chain(pool, pool_step)
                    step(pool.memset(mask[:], 1.0))
                    step(pool.memset(fill[:], 0.0))
                    for c0, c1, q0 in (region(0), region(1)):
                        for t, v in ((mask, 0.0), (fill, NEG)):
                            step(pool.affine_select(out=t[:, c0:c1], in_=t[:, c0:c1], compare_op=ALU.is_gt, fill=v,
                                                    base=0, pattern=[[1, c1 - c0]], channel_multiplier=-1))
                    pool_step.count = step.n

                @block.scalar
                def _(act):
                    step = Chain(act, act_step)

                    def softplus(a):
                        act.wait_ge(scaled.sem, scaled.at(a + 1))
                        if a >= 2:
                            act.wait_ge(keep_ready.sem, keep_ready.at(a - 1))
                        step(nc.scalar.activation(sp1[:, a % 2, :, :], u[:, a % 2, :, :], ACT.Abs))
                        step(nc.scalar.activation(sp1[:, a % 2, :, :], sp1[:, a % 2, :, :], ACT.Exp, scale=-1.0))
                        nc.scalar.activation(sp1[:, a % 2, :, :], sp1[:, a % 2, :, :], ACT.Ln, bias=1.0)\
                            .then_inc(logged.sem, 1)

                    def weights(a):
                        act.wait_ge(exponent.sem, exponent.at(a + 1))
                        nc.scalar.activation(u[:, a % 2, :, :], u[:, a % 2, :, :], ACT.Exp)\
                            .then_inc(weight_ready.sem, 1)
                    softplus(0)
                    for a in range(PAIRS):
                        if a + 1 < PAIRS:
                            softplus(a + 1)
                        weights(a)
                    act_step.count = step.n

                @block.vector
                def _(dve):
                    step = Chain(dve, dve_step)

                    def logits(a):
                        dve.wait_ge(logit_ready.sem, logit_ready.at(a + 1))
                        if a >= 2:
                            dve.wait_ge(out_ready.sem, out_ready.at(a - 1))
                            dve.wait_ge(tail_ready.sem, tail_ready.at(a - 1))
                        nc.vector.tensor_scalar(u[:, a % 2, :, :], PS[:, 2 * (a % 2):2 * (a % 2) + 2, 0:W], SCALE,
                                                None, ALU.mult).then_inc(scaled.sem, 1)
                        dve.wait_ge(scaled.sem, scaled.at(a + 1))
                        step(nc.vector.tensor_scalar(sp2[:, a % 2, :, :], u[:, a % 2, :, :], 0.0, None, ALU.max))
                        dve.wait_ge(logged.sem, logged.at(a + 1))
                        step(nc.vector.tensor_tensor(sp2[:, a % 2, :, :], sp2[:, a % 2, :, :], sp1[:, a % 2, :, :],
                                                     ALU.add))
                        nc.vector.tensor_tensor(sp2[:, a % 2, :, :], sp2[:, a % 2, :, :], rep(mask[:], 1, 2), ALU.mult)\
                            .then_inc(keep_ready.sem, 1)

                    def exponents(a):
                        dve.wait_ge(tail_ready.sem, tail_ready.at(a + 1))
                        step(nc.vector.tensor_tensor(u[:, a % 2, :, :], u[:, a % 2, :, :], PS[:, 4:6, 0:W],
                                                     ALU.subtract))
                        nc.vector.tensor_tensor(u[:, a % 2, :, :], u[:, a % 2, :, :], rep(fill[:], 1, 2), ALU.add)\
                            .then_inc(exponent.sem, 1)

                    def outs(a):
                        dve.wait_ge(out_ready.sem, out_ready.at(a + 1))
                        nc.vector.tensor_copy(OT[:, a, 0:NPR], PS[:, 6 + a % 2, 0:NPR]).then_inc(out_read.sem, 1)
                    dve.wait_ge(pool_step.sem, pool_step.at(6))
                    logits(0)
                    for a in range(PAIRS):
                        if a + 1 < PAIRS:
                            logits(a + 1)
                        exponents(a)
                        if a >= 1:
                            outs(a - 1)
                    outs(PAIRS - 1)
                    dve_step.count = step.n
            pool_step.close(pool_step.count)
            act_step.close(act_step.count)
            dve_step.close(dve_step.count)
            for s in (logit_ready, keep_ready, tail_ready, weight_ready, out_ready, out_read, scaled, logged,
                      exponent):
                s.close(PAIRS)
            stored.close(48)
            loads.close(16)

        def stick_sample(QT, KTT, V):
            STEPS = NB // 2
            W = PAST + LS
            LOADED = 16 * 2 * NPG
            LOADED_V = LOADED + 2 * 16
            with ExitStack() as stage:
                def tile(name, shape):
                    return sb(name, shape, F32, stage)
                K = [tile(f"s_K{s}", [P, NPG, 4, P]) for s in range(2)]
                VV = [tile(f"s_V{s}", [P, NPG, 512]) for s in range(2)]
                VN = [V[0:LS, s, :] for s in range(2)]
                out_rows = tile("s_out", [P, 2, P])
                mask = tile("s_mask", [P, LS])
                fill = tile("s_fill", [P, LS])
                pages = sb("s_pages", [1, NB * NPG], I32, stage)
                free = H[:].rearrange("p k n -> p (k n)")
                soft = free[:, 0:2 * W].rearrange("p (i n) -> p i n", i=2)
                QB = free[:, 2 * W:2 * W + 256].rearrange("p (s a r) -> p s a r", s=2, a=4)
                pT = OT[:, 4:8, :].rearrange("p k n -> p (k n)")[:, 0:(NPG + 1) * P]\
                    .rearrange("p (k r) -> p k r", r=P)
                KN = OT[:, 4:8, :].rearrange("p k n -> p (k n)")[:, (NPG + 1) * P:(NPG + 1) * P + 8 * LS]\
                    .rearrange("p (a k) -> p a k", a=4)
                of_query = pT[0:LS, 0, :]
                earlier = pT[0:LS, 1, 0:LS]
                BUILT = 4
                z = PS[:, 0:3, :].rearrange("p a n -> p (a n)")[:, 0:W]
                block = stage.enter_context(nc.Block(no_gpsimd_drain=True))

                def backwards(ap):
                    (step0, rows), (step1, n) = [list(x) for x in ap.ap]
                    return bass.AP(ap.tensor, ap.offset + step1 * (n - 1), [[step0, rows], [-step1, n]])

                @block.sync
                def _(sp):
                    sp.dma_start(pages[:], io["pages"]).then_inc(loads.sem, 16)
                    sp.wait_ge(loads.sem, loads.at(16))

                    def load(g, s, to, src, sig, used=None):
                        for p in range(NPG):
                            at = (2 * g + s) * NPG + p
                            cell = pages[0:1, at:at + 1] if isinstance(at, int) else pages[0:1, bass.ds(at, 1)]
                            page = sp.value_load(cell, min_val=0, max_val=NPOOL - 1)
                            if p == 0 and used is not None:
                                sp.wait_ge(used[0], used[1])
                            dst = to[s][:, p]
                            if len(dst.shape) == 3:
                                dst = dst.rearrange("p a n -> p (a n)")
                            sp.dma_start(dst, src[bass.ds(page, 1), :, :].rearrange("a p n -> p (a n)"))\
                                .then_inc(sig.sem, 16)

                    def step(g, keys_used=None, values_used=None):
                        load(g, 0, K, io["sb_kT"], page_in[0], keys_used)
                        load(g, 1, K, io["sb_kT"], page_in[0])
                        load(g, 0, VV, io["sb_v"], page_in[1], values_used)
                        load(g, 1, VV, io["sb_v"], page_in[1])
                        for s in range(2):
                            b = 2 * g + s
                            at = slice(LS * b, LS * b + LS) if isinstance(b, int) else bass.ds(b * LS, LS)
                            sp.dma_start(VN[s], io["new_rows"][0, at, :]).then_inc(page_in[1].sem, 16)
                    sp.wait_ge(stored.sem, stored.at(0))
                    step(0)
                    with sp.Fori(1, STEPS) as g:
                        step(g, (logit_ready.sem, logit_ready.at(0) + g), (out_ready.sem, out_ready.at(0) + g))

                @block.gpsimd
                def _(pool):
                    step = Chain(pool, pool_step)
                    step(pool.memset(QB, 0.0))
                    step(pool.memset(of_query, 0.0))
                    step(pool.affine_select(out=of_query, in_=of_query, compare_op=ALU.not_equal, fill=1.0, base=0,
                                            pattern=[[0, P // LS], [1, LS]], channel_multiplier=-1))
                    step(pool.tensor_tensor(earlier, later[0:LS, 0:LS], ident[0:LS, 0:LS], ALU.subtract))
                    assert step.n == BUILT
                    pool_step.count = step.n

                @block.tensor
                def _(pe):
                    pe.wait_ge(pool_step.sem, pool_step.at(BUILT))
                    nc.tensor.matmul(PS[:, 7, 0:LS], of_query, earlier, start=True, stop=True).then_inc(summed.sem, 1)
                    with pe.Fori(0, STEPS) as g:
                        pe.wait_ge(page_in[0].sem, page_in[0].at(LOADED) + g * LOADED)
                        pe.wait_ge(seq_ready.sem, seq_ready.at(1) + g)
                        for c in range(2):
                            for s in range(2):
                                for a in range(4):
                                    nc.tensor.matmul(PS[32 * a:32 * a + 32, c, :], QB[:, s, a, :],
                                                     K[s][:, 4 * c:4 * c + 4, a, :], start=(s == 0), stop=(s == 1))
                        for s in range(2):
                            for a in range(4):
                                mm = nc.tensor.matmul(PS[32 * a:32 * a + 32, 2, 0:LS], QB[:, s, a, :],
                                                      KN[:, a, LS * s:LS * s + LS],
                                                      start=(s == 0), stop=(s == 1))
                        mm.then_inc(logit_ready.sem, 1)
                        pe.wait_ge(weight_ready.sem, weight_ready.at(1) + g)
                        for n in range(2):
                            for p in range(4 * n, 4 * n + 4):
                                mm = nc.tensor.transpose(PS[:, 3 + n, (p % 4) * P:(p % 4 + 1) * P],
                                                         soft[:, 1, p * P:(p + 1) * P], ident[:])
                            mm.then_inc(turned.sem, 1)
                        nc.tensor.transpose(PS[0:LS, 5, 0:P], soft[:, 1, PAST:W], ident[:]).then_inc(turned.sem, 1)
                        pe.wait_ge(page_in[1].sem, page_in[1].at(LOADED_V) + g * LOADED_V)
                        pe.wait_ge(turned_read.sem, turned_read.at(2) + 2 * g)
                        pe.wait_ge(scaled.sem, scaled.at(2) + 2 * g)
                        for s in range(2):
                            for p in range(NPG + 1):
                                for a in range(4):
                                    w = pT[:, p, 32 * a:32 * a + 32] if p < NPG else pT[0:LS, p, 32 * a:32 * a + 32]
                                    v = VV[s][:, p, a * P:(a + 1) * P] if p < NPG else VN[s][:, a * P:(a + 1) * P]
                                    mm = nc.tensor.matmul(PS[32 * a:32 * a + 32, 6, s * P:(s + 1) * P], w, v,
                                                          start=(p == 0), stop=(p == NPG))
                        mm.then_inc(out_ready.sem, 1)
                        pe.wait_ge(keep_ready.sem, keep_ready.at(1) + g)
                        for s in range(2):
                            mm = nc.tensor.transpose(PS[:, 7, s * P:(s + 1) * P], out_rows[:, s, :], ident[:])
                        mm.then_inc(tail_ready.sem, 1)

                @block.scalar
                def _(act):
                    step = Chain(act, act_step)
                    act.wait_ge(pool_step.sem, pool_step.at(BUILT))
                    with act.Fori(0, STEPS) as g:
                        step.loop(g, 2)
                        act.wait_ge(logit_ready.sem, logit_ready.at(0) + g)
                        nc.scalar.activation(KN, KTT[:, :, bass.ds(g * 2 * LS + NPR, 2 * LS)], ACT.Copy)
                        for s in range(2):
                            for hh in range(2):
                                rows = slice(64 * hh, 64 * hh + 64)
                                c = 16 * s + 8 * hh
                                last = nc.scalar.activation(QB[rows, s, :, c:c + LS],
                                                            QT[rows, :, bass.ds(g * 2 * LS + (NPR + LS * s), LS)],
                                                            ACT.Copy)
                        last.then_inc(seq_ready.sem, 1)
                        act.wait_ge(scaled.sem, scaled.at(1) + 2 * g)
                        step(nc.scalar.activation(soft[:, 0, :], z, ACT.Abs, scale=SCALE))
                        step(nc.scalar.activation(soft[:, 0, :], soft[:, 0, :], ACT.Exp, scale=-1.0))
                        nc.scalar.activation(soft[:, 0, :], soft[:, 0, :], ACT.Ln, bias=1.0).then_inc(logged.sem, 1)
                        act.wait_ge(exponent.sem, exponent.at(1) + g)
                        nc.scalar.activation(soft[:, 1, :], soft[:, 1, :], ACT.Exp).then_inc(weight_ready.sem, 1)
                        act.wait_ge(turned.sem, turned.at(1) + 3 * g)
                        nc.scalar.activation(pT[:, 0:4, :].rearrange("p k r -> p (k r)"), PS[:, 3, :], ACT.Copy)\
                            .then_inc(turned_read.sem, 1)
                        act.wait_ge(turned.sem, turned.at(3) + 3 * g)
                        nc.scalar.activation(pT[0:LS, NPG, :], PS[0:LS, 5, 0:P], ACT.Copy)\
                            .then_inc(turned_read.sem, 1)
                        step.done(STEPS)
                    act_step.count = step.n

                @block.vector
                def _(dve):
                    step = Chain(dve, dve_step)
                    dve.wait_ge(summed.sem, summed.at(1))
                    step(nc.vector.tensor_copy(mask[:], PS[:, 7, 0:LS]))
                    step(nc.vector.tensor_scalar(fill[:], mask[:], -1.0, -NEG, ALU.add, ALU.mult))
                    with dve.Fori(0, STEPS) as g:
                        step.loop(g, 3)
                        dve.wait_ge(logit_ready.sem, logit_ready.at(1) + g)
                        nc.vector.tensor_scalar(soft[:, 1, :], z, SCALE, 0.0, ALU.mult, ALU.max)\
                            .then_inc(scaled.sem, 1)
                        dve.wait_ge(logged.sem, logged.at(1) + g)
                        step(nc.vector.tensor_tensor(soft[:, :, PAST:W], soft[:, :, PAST:W], rep(mask[:], 1, 2),
                                                     ALU.mult))
                        step(nc.vector.tensor_tensor_scan(backwards(soft[:, 0, :]), backwards(soft[:, 0, :]),
                                                          backwards(soft[:, 1, :]), 0.0, ALU.add, ALU.add))
                        step(nc.vector.scalar_tensor_tensor(out=soft[:, 1, :], in0=z, scalar=SCALE,
                                                            in1=soft[:, 0, :], op0=ALU.mult, op1=ALU.subtract))
                        nc.vector.tensor_tensor(soft[:, 1, PAST:W], soft[:, 1, PAST:W], fill[:], ALU.add)\
                            .then_inc(exponent.sem, 1)
                        dve.wait_ge(turned.sem, turned.at(2) + 3 * g)
                        nc.vector.tensor_copy(pT[:, 4:8, :].rearrange("p k r -> p (k r)"), PS[:, 4, :])\
                            .then_inc(scaled.sem, 1)
                        dve.wait_ge(out_ready.sem, out_ready.at(1) + g)
                        nc.vector.tensor_copy(out_rows[:].rearrange("p s n -> p (s n)"), PS[:, 6, 0:2 * P])\
                            .then_inc(keep_ready.sem, 1)
                        dve.wait_ge(tail_ready.sem, tail_ready.at(1) + g)
                        for hh in range(2):
                            rows = slice(64 * hh, 64 * hh + 64)
                            src = PS[rows, 7, 8 * hh:8 * hh + 1]
                            src = bass.AP(src.tensor, src.offset,
                                          [list(src.ap[0]), [32, 4], [P + 16, 2], [1, LS]])
                            to = OT[rows, 0:4, bass.ds(g * 2 * LS + NPR, 2 * LS)].rearrange("p a (s q) -> p a s q", s=2)
                            nc.vector.tensor_copy(to, src).then_inc(out_read.sem, 1)
                        step.done(STEPS)
                    dve_step.count = step.n
            pool_step.close(pool_step.count)
            act_step.close(act_step.count)
            dve_step.close(dve_step.count)
            for s in (logit_ready, keep_ready, tail_ready, weight_ready, out_ready, logged, exponent, seq_ready):
                s.close(STEPS)
            for s in (out_read, scaled, turned_read):
                s.close(2 * STEPS)
            turned.close(3 * STEPS)
            loads.close(16)
            summed.close(1)
            page_in[0].close(LOADED * STEPS)
            page_in[1].close(LOADED_V * STEPS)

        def linear_attention(qkT, vb, rT, a1T):
            CH = [(t, c) for t in range(2) for c in range(2)]
            with ExitStack() as stage:
                def tile(name, shape):
                    return sb(name, shape, F32, stage)
                wa2 = tile("g_wa2", [16, 256])
                ba2 = tile("g_ba2", [P, 256])
                og = tile("g_og", [P, 1])
                S0 = tile("g_S0", [P, NB, 2, P])
                same = tile("g_same", [P, 2, P])
                upto = tile("g_upto", [P, 2, P])
                neg_upto = tile("g_neg_upto", [P, 2, P])
                neg_after = tile("g_neg_after", [P, 2, P])
                neg_chunk = tile("g_neg_chunk", [P, 2, NB])
                in_seq = tile("g_in_seq", [64, NB])
                x = tile("g_x", [P, 3, 256])
                soft = tile("g_soft", [P, 3, 256])
                EB = tile("g_EB", [P, 2, NT])
                EN = tile("g_EN", [P, 2, NT])
                ED = tile("g_ED", [P, 3, 256])
                EL = tile("g_EL", [P, 2, 12])
                qin = tile("g_qin", [P, 2, NT])
                kin = tile("g_kin", [P, 2, NT])
                kdec = tile("g_kdec", [P, 3, 256])
                att = tile("g_att", [P, 3, 4, P])
                S = tile("g_S", [P, 5, 2, P])
                vx = tile("g_vx", [64, 4, NB, P])
                sq = tile("g_sq", [P, 4, NT])
                rs = tile("g_rs", [P, 4, NT])
                so = tile("g_so", [P, NB, 2, P])
                INV = -1.0 / 16.0

                with nc.Block(no_gpsimd_drain=True) as block:
                    @block.sync
                    def _(sp):
                        sp.dma_start(wa2[:], io["w_a2"]).then_inc(loads.sem, 16)
                        sp.dma_start(ba2[:], bass.AP(io["b_a2"].tensor, 0, [[0, P], [1, 256]])).then_inc(loads.sem, 16)
                        sp.dma_start(og[:], io["onorm_g"]).then_inc(loads.sem, 16)
                        sp.dma_start(S0[:], io["gla_s"]).then_inc(loads.sem, 16)
                        sp.wait_ge(loads.sem, loads.at(64))

                    @block.gpsimd
                    def _(pool):
                        step = Chain(pool, pool_step)

                        def pick(t, op, base, pattern, mult):
                            step(pool.affine_select(out=t, in_=t, compare_op=op, fill=0.0, base=base, pattern=pattern,
                                                    channel_multiplier=mult))
                        step(pool.memset(same[:], 1.0))
                        step(pool.memset(neg_chunk[:], INV))
                        step(pool.memset(in_seq[:], 1.0))
                        for kind, size in ((0, 64), (1, 8)):
                            v = same[:, kind, :].rearrange("p (c i) -> p c i", i=size)
                            pick(v, ALU.is_ge, 0, [[-size, P // size], [0, size]], 1)
                            pick(v, ALU.is_ge, size - 1, [[size, P // size], [0, size]], -1)
                            v = neg_chunk[:, kind, :]
                            pick(v, ALU.is_ge, 0, [[-size, NB]], 1)
                            pick(v, ALU.is_ge, size - 1, [[size, NB]], -1)
                        pick(in_seq[:], ALU.is_ge, 0, [[-8, NB]], 1)
                        pick(in_seq[:], ALU.is_ge, 7, [[8, NB]], -1)
                        step(pool.tensor_copy(upto[:], same[:]))
                        pick(upto[:], ALU.is_ge, 0, [[0, 2], [1, P]], -1)
                        pool_step.count = step.n

                    @block.vector
                    def _(dve):
                        step = Chain(dve, dve_step)
                        dve.wait_ge(pool_step.sem, pool_step.at(pool_step.count))
                        step(nc.vector.tensor_scalar(neg_upto[:], upto[:], INV, None, ALU.mult))
                        step(nc.vector.tensor_tensor(neg_after[:], same[:], upto[:], ALU.subtract))
                        step(nc.vector.tensor_scalar(neg_after[:], neg_after[:], INV, None, ALU.mult))
                        for h in range(4):
                            v = vb[0:64, 2, h * P:(h + 1) * P]
                            m = in_seq[:]
                            m = bass.AP(m.tensor, m.offset, [list(a) for a in m.ap] + [[0, P]])
                            step(nc.vector.tensor_tensor(vx[:, h, :, :], rep(v, 1, NB), m, ALU.mult))
                        dve_step.count = step.n
                loads.close(64)
                pool_step.close(pool_step.count)
                dve_step.close(dve_step.count)

                kinds = [0, 0, 1]
                block = stage.enter_context(nc.Block(no_gpsimd_drain=True))

                @block.tensor
                def _(pe):
                    for t, rows in enumerate(TILE_ROWS):
                        mm = nc.tensor.matmul(PS[0:rows, t, 0:256], a1T[:, t * P:t * P + rows], wa2[:],
                                              start=True, stop=True)
                    mm.then_inc(logit_ready.sem, 1)
                    for t, rows in enumerate(TILE_ROWS):
                        for a in range(2):
                            mm = nc.tensor.transpose(PS[0:rows, 5 + t, a * P:(a + 1) * P],
                                                     qkT[:, 2 + a, t * P:t * P + rows], ident[:])
                    mm.then_inc(out_ready.sem, 1)
                    pe.wait_ge(keep_ready.sem, keep_ready.at(1))
                    for a in range(2):
                        for t, rows in enumerate(TILE_ROWS):
                            nc.tensor.matmul(PS[:, a, t * P:t * P + rows], soft[0:rows, t, a * P:(a + 1) * P],
                                             neg_upto[0:rows, kinds[t], 0:rows], start=(t == 0), stop=(t == 2),
                                             skip_group_check=True)
                    for t, rows in enumerate(TILE_ROWS):
                        nc.tensor.matmul(PS[0:rows, 2 + t // 2, (t % 2) * 256:(t % 2) * 256 + 256],
                                         neg_after[0:rows, kinds[t], 0:rows], soft[0:rows, t, :],
                                         start=True, stop=True)
                    for a in range(2):
                        for t, rows in enumerate(TILE_ROWS):
                            n = NB if t == 2 else 2
                            mm = nc.tensor.matmul(PS[:, 4, a * 12 + 2 * t:a * 12 + 2 * t + n],
                                                  soft[0:rows, t, a * P:(a + 1) * P], neg_chunk[0:rows, kinds[t], 0:n],
                                                  start=True, stop=True)
                    mm.then_inc(tail_ready.sem, 1)
                    pe.wait_ge(weight_ready.sem, weight_ready.at(1))
                    for t, rows in enumerate(TILE_ROWS):
                        for h in range(4):
                            r = slice(64 * (h % 2), 64 * (h % 2) + 64)
                            mm = nc.tensor.matmul(PS[0:rows, 3 * (h % 2) + t, (h // 2) * P:(h // 2) * P + rows],
                                                  kin[r, h // 2, t * P:t * P + rows],
                                                  qin[r, h // 2, t * P:t * P + rows], start=True, stop=True)
                    mm.then_inc(logit_ready.sem, 1)
                    for n, (t, c) in enumerate(CH):
                        for h in range(4):
                            r = slice(64 * (h % 2), 64 * (h % 2) + 64)
                            e = slice(64 * c, 64 * c + 64)
                            mm = nc.tensor.matmul(PS[r, 6 + c, t * 256 + (h // 2) * P:t * 256 + (h // 2 + 1) * P],
                                                  kdec[e, t, 64 * h:64 * h + 64], vb[e, t, h * P:(h + 1) * P],
                                                  start=True, stop=True)
                    mm.then_inc(out_ready.sem, 1)
                    pe.wait_ge(seq_ready.sem, seq_ready.at(1))
                    for h in range(4):
                        bank = h
                        r = slice(64 * (h % 2), 64 * (h % 2) + 64)
                        for t, rows in enumerate(TILE_ROWS):
                            nc.tensor.matmul(PS[:, bank, t * P:t * P + rows], vb[:, t, h * P:(h + 1) * P],
                                             att[:, t, h, 0:rows], start=(t == 0), stop=False,
                                             skip_group_check=True)
                        for n in range(1, 4):
                            nc.tensor.matmul(PS[:, bank, 64 * n:64 * n + 64], S[r, n, h // 2, :],
                                             qin[r, h // 2, 64 * n:64 * n + 64], start=False, stop=False,
                                             skip_group_check=True)
                        for b in range(NB):
                            at = slice(NPR + LS * b, NPR + LS * b + LS)
                            mm = nc.tensor.matmul(PS[:, bank, at], S0[r, b, h // 2, :], qin[r, h // 2, at],
                                                  start=False, stop=(b == NB - 1), skip_group_check=True)
                        mm.then_inc(out_ready.sem, 1)
                    for a in range(2):
                        for hh in range(2):
                            for half in range(2):
                                h = 2 * a + hh
                                mm = nc.tensor.matmul(PS[64 * hh:64 * hh + 64, 4 + 2 * a + half, :],
                                                      kdec[0:64, 2, 64 * h:64 * h + 64],
                                                      vx[:, h, 4 * half:4 * half + 4, :], start=True, stop=True)
                    mm.then_inc(out_ready.sem, 1)
                    pe.wait_ge(squared.sem, squared.at(5))
                    for h in range(4):
                        mm = nc.tensor.matmul(PS[:, h, 0:NT], ones[:], sq[:, h, :], start=True, stop=True)
                    mm.then_inc(summed.sem, 1)

                @block.scalar
                def _(act):
                    step = Chain(act, act_step)
                    act.wait_ge(scaled.sem, scaled.at(1))
                    step(nc.scalar.activation(x[:], x[:], ACT.Exp, scale=-1.0))
                    nc.scalar.activation(x[:], x[:], ACT.Ln, bias=1.0).then_inc(logged.sem, 1)
                    act.wait_ge(tail_ready.sem, tail_ready.at(1))
                    nc.scalar.activation(EB[:], PS[:, 0:2, 0:NT], ACT.Exp)
                    nc.scalar.activation(EN[:], PS[:, 0:2, 0:NT], ACT.Exp, scale=-1.0)
                    nc.scalar.activation(ED[:, 0:2, :].rearrange("p t n -> p (t n)"), PS[:, 2, :], ACT.Exp)
                    nc.scalar.activation(ED[0:64, 2, :], PS[0:64, 3, 0:256], ACT.Exp)
                    nc.scalar.activation(EL[:].rearrange("p a n -> p (a n)"), PS[:, 4, 0:24], ACT.Exp)\
                        .then_inc(exponent.sem, 1)
                    nc.scalar.activation(rT[:], rT[:], ACT.Silu).then_inc(squared.sem, 1)
                    for h in range(4):
                        act.wait_ge(out_read.sem, out_read.at(h + 1))
                        nc.scalar.activation(sq[:, h, :], OT[:, 4 + h, :], ACT.Square).then_inc(squared.sem, 1)
                    act.wait_ge(variance.sem, variance.at(1))
                    nc.scalar.activation(rs[:], rs[:], ACT.Sqrt).then_inc(deviation.sem, 1)
                    act_step.count = step.n

                @block.vector
                def _(dve):
                    step = Chain(dve, dve_step)
                    dve.wait_ge(logit_ready.sem, logit_ready.at(1))
                    for t, rows in enumerate(TILE_ROWS):
                        last = nc.vector.tensor_tensor(x[0:rows, t, :], PS[0:rows, t, 0:256], ba2[0:rows, :], ALU.add)
                    step(nc.vector.memset(x[64:128, 2, :], 0.0))
                    step(nc.vector.tensor_scalar(soft[:], x[:], -1.0, 0.0, ALU.mult, ALU.max))
                    nc.vector.scalar_tensor_tensor(out=x[:], in0=x[:], scalar=-1.0, in1=x[:], op0=ALU.mult, op1=ALU.max).then_inc(scaled.sem, 1)
                    dve.wait_ge(logged.sem, logged.at(1))
                    nc.vector.tensor_tensor(soft[:], soft[:], x[:], ALU.add).then_inc(keep_ready.sem, 1)
                    dve.wait_ge(exponent.sem, exponent.at(1))
                    nc.vector.scalar_tensor_tensor(out=qin[:], in0=qkT[:, 0:2, :], scalar=SCALE, in1=EB[:],
                                                   op0=ALU.mult, op1=ALU.mult)
                    nc.vector.tensor_tensor(kin[:], qkT[:, 2:4, :], EN[:], ALU.mult)
                    dve.wait_ge(out_ready.sem, out_ready.at(1))
                    nc.vector.tensor_tensor(kdec[:, 0:2, :], PS[:, 5:7, 0:256], ED[:, 0:2, :], ALU.mult)
                    nc.vector.tensor_tensor(kdec[0:64, 2, :], PS[0:64, 7, 0:256], ED[0:64, 2, :], ALU.mult)\
                        .then_inc(weight_ready.sem, 1)
                    dve.wait_ge(logit_ready.sem, logit_ready.at(2))
                    for t, rows in enumerate(TILE_ROWS):
                        for hh in range(2):
                            a = PS[0:rows, 3 * hh + t, 0:256].rearrange("p (a c) -> p a c", a=2)[:, :, 0:rows]
                            m = rep(upto[0:rows, kinds[t], 0:rows], 1, 2)
                            to = att[0:rows, t, :, 0:rows].rearrange("p (a g) c -> p a g c", g=2)[:, :, hh, :]
                            nc.vector.tensor_tensor(to, a, m, ALU.mult)
                    nc.vector.memset(att[64:128, 2, :, :], 0.0)
                    nc.vector.memset(vb[64:128, 2, :], 0.0)
                    dve.wait_ge(out_ready.sem, out_ready.at(2))
                    for n in range(4):
                        t, c = CH[n]
                        new = PS[:, 6 + c, t * 256:t * 256 + 256].rearrange("p (a v) -> p a v", a=2)
                        if n == 0:
                            step(nc.vector.tensor_copy(S[:, 1, :, :], new))
                            continue
                        for a in range(2):
                            last = nc.vector.scalar_tensor_tensor(out=S[:, n + 1, a, :], in0=S[:, n, a, :],
                                                                  scalar=EL[:, a, n:n + 1], in1=new[:, a, :],
                                                                  op0=ALU.mult, op1=ALU.add)
                        if n < 3:
                            step(last)
                        else:
                            last.then_inc(seq_ready.sem, 1)
                    for h in range(4):
                        dve.wait_ge(out_ready.sem, out_ready.at(3 + h))
                        nc.vector.tensor_copy(OT[:, 4 + h, :], PS[:, h, 0:NT]).then_inc(out_read.sem, 1)
                    dve.wait_ge(out_ready.sem, out_ready.at(7))
                    for a in range(2):
                        e = EL[:, a, 4:12]
                        e = bass.AP(e.tensor, e.offset, [list(q) for q in e.ap] + [[0, P]])
                        step(nc.vector.tensor_tensor(so[:, :, a, :], S0[:, :, a, :], e, ALU.mult))
                        for half in range(2):
                            v = so[:, 4 * half:4 * half + 4, a, :]
                            src = PS[:, 4 + 2 * a + half, :].rearrange("p (b v) -> p b v", b=4)
                            step(nc.vector.tensor_tensor(v, v, src, ALU.add))
                    dve.wait_ge(summed.sem, summed.at(1))
                    for h in range(4):
                        last = nc.vector.tensor_scalar(rs[:, h, :], PS[:, h, 0:NT], 1.0 / P, EPS,
                                                       ALU.mult, ALU.add)
                    last.then_inc(variance.sem, 1)
                    dve.wait_ge(deviation.sem, deviation.at(1))
                    step(nc.vector.reciprocal(rs[:], rs[:]))
                    step(nc.vector.tensor_tensor(rs[:], rs[:], OT[:, 4:8, :], ALU.mult))
                    nc.vector.scalar_tensor_tensor(out=OT[:, 4:8, :], in0=rs[:], scalar=og[:, 0:1], in1=rT[:],
                                                   op0=ALU.mult, op1=ALU.mult).then_inc(centred.sem, 1)
                    dve_step.count = step.n

                @block.sync
                def _(sp):
                    sp.wait_ge(centred.sem, centred.at(1))
                    sp.dma_start(io["o_pgla"], S[:, 4, :, :]).then_inc(stored.sem, 16)
                    sp.dma_start(io["o_sgla"], so[:]).then_inc(stored.sem, 16)
                    sp.wait_ge(stored.sem, stored.at(32))
            act_step.close(act_step.count)
            dve_step.close(dve_step.count)
            logit_ready.close(2)
            keep_ready.close(1)
            tail_ready.close(1)
            weight_ready.close(1)
            out_ready.close(7)
            out_read.close(4)
            scaled.close(1)
            logged.close(1)
            exponent.close(1)
            seq_ready.close(1)
            squared.close(5)
            for s in (summed, variance, deviation, centred):
                s.close(1)
            stored.close(32)

        centre_ready = signal("centre_ready")
        turned = signal("turned")
        turned_read = signal("turned_read")
        table_in = signal("table_in")
        chosen = signal("chosen")

        def odd_stage(n0):
            stage = ExitStack()
            with stage:
                def tile(name, shape):
                    return sb(name, shape, F32, stage)

                Q2 = tile("Q2", [P, 8, NT])
                kskw = tile("kskw", [P, 4, NT])
                vsvw = tile("vsvw", [P, 3, 512])
                GT = tile("GT", [P, 3, 48])
                GS = tile("GS", [P, NB, 3])
                Bs = tile("Bs", [P, PAST + LS])
                Bw = tile("Bw", [P, WIN + LS])
                KC = tile("KC", [P, 2, NB * 64 + 16])
                VC = tile("VC", [64, NB + 1, 256])
                qkg = tile("qkg", [P, 4])
                w_gt = tile("w_gt", [P, KT, 48])
                bias_tables(Bs)
                with ExitStack() as early:
                    kcvc = sb("kcvc", [P, 4, NT], F32, early)
                    with nc.Block(no_gpsimd_drain=True) as block:
                        @block.sync
                        def _(sp):
                            sp.dma_start(w_gt[:], io["w_gt"]).then_inc(loads.sem, 16)
                            sp.dma_start(qkg[:], io["qk_g"]).then_inc(loads.sem, 16)
                            sp.wait_ge(loads.sem, loads.at(32))
                    loads.close(32)
                    n1 = project_stage(1, n0, [(True, Q2[:, 0:4, :]), (True, Q2[:, 4:8, :]), (True, kcvc[:]),
                                            (True, kskw[:]), (False, vsvw)], w_gt, 48, GT, True)
                    qk_norms(Q2, kskw, kcvc, vsvw, GT, GS, Bs, Bw, qkg)
                    compress(kcvc, KC, VC, qkg)
                sparse_prompt(Q2, kskw, vsvw, GT, KC, VC)
                sparse_sample(Q2, kskw, vsvw, GS, Bs, Bw, KC, VC)
            return out_stage(1, n1)

        def bias_tables(Bs):
            BANKS = 5
            with ExitStack() as stage:
                rel = sb("rel", [33, 16], F32, stage)
                relb = sb("relb", [33, 16, P], F32, stage)
                rel8 = sb("rel8", [33, 16, 8], F32, stage)
                one_hot = sb("one_hot", [33, NDIST], F32, stage)
                F = sb("F", [P, NDIST], F32, stage)
                FP = sb("FP", [P, 16, NDIST_P], F32, stage)
                block = stage.enter_context(nc.Block(no_gpsimd_drain=True))

                @block.sync
                def _(sp):
                    sp.dma_start(rel[0:32, :], io["rel_table"]).then_inc(table_in.sem, 16)
                    sp.dma_start(one_hot[:], io["one_hot"]).then_inc(table_in.sem, 16)
                    sp.wait_ge(act_step.sem, act_step.at(1))
                    sp.dma_start(io["bias_rows"], F[:]).then_inc(loads.sem, 16)
                    sp.wait_ge(loads.sem, loads.at(16))
                    f = io["bias_rows"].tensor
                    for h in range(16):
                        sp.dma_start(Bs[8 * h:8 * h + 8, :],
                                     bass.AP(f, 8 * h * NDIST + DIST_HI - PAST, [[NDIST - 1, 8], [1, PAST + LS]]))\
                            .then_inc(loads.sem, 16)
                    sp.wait_ge(act_step.sem, act_step.at(17))
                    sp.dma_start(io["bias_prompt"], FP[:]).then_inc(loads.sem, 16)
                    sp.wait_ge(loads.sem, loads.at(18 * 16))

                @block.gpsimd
                def _(pool):
                    pool.memset(rel[32:33, :], NEG).then_inc(pool_step.sem, 1)

                @block.vector
                def _(dve):
                    dve.wait_ge(table_in.sem, table_in.at(32))
                    dve.wait_ge(pool_step.sem, pool_step.at(1))
                    r = rel[:]
                    r = bass.AP(r.tensor, r.offset, [list(x) for x in r.ap] + [[0, P]])
                    nc.vector.tensor_copy(relb[:], r).then_inc(dve_step.sem, 1)
                    r = bass.AP(r.tensor, r.offset, [list(x) for x in rel[:].ap] + [[0, 8]])
                    nc.vector.tensor_copy(rel8[:], r).then_inc(dve_step.sem, 1)

                @block.tensor
                def _(pe):
                    pe.wait_ge(dve_step.sem, dve_step.at(2))
                    for c in range(0, NDIST, 512):
                        n = min(512, NDIST - c)
                        mm = nc.tensor.matmul(PS[:, c // 512, 0:n], rel8[:].rearrange("p h q -> p (h q)"), one_hot[:, c:c + n],
                                              start=True, stop=True)
                    mm.then_inc(turned.sem, 1)
                    for h in range(16):
                        if h >= BANKS:
                            pe.wait_ge(act_step.sem, act_step.at(h - BANKS + 2))
                        nc.tensor.matmul(PS[:, 3 + h % BANKS, 0:NDIST_P], relb[:, h, :],
                                         one_hot[:, DIST_HI - 255:DIST_HI - 255 + NDIST_P], start=True, stop=True)\
                            .then_inc(turned.sem, 1)

                @block.scalar
                def _(act):
                    act.wait_ge(turned.sem, turned.at(1))
                    nc.scalar.activation(F[:], PS[:, 0:3, :].rearrange("p a n -> p (a n)")[:, 0:NDIST], ACT.Copy)\
                        .then_inc(act_step.sem, 1)
                    for h in range(16):
                        act.wait_ge(turned.sem, turned.at(h + 2))
                        nc.scalar.activation(FP[:, h, :], PS[:, 3 + h % BANKS, 0:NDIST_P], ACT.Copy)\
                            .then_inc(act_step.sem, 1)
            table_in.close(32)
            loads.close(18 * 16)
            pool_step.close(1)
            dve_step.close(2)
            turned.close(17)
            act_step.close(17)

        def qk_norms(Q2, kskw, kcvc, vsvw, GT, GS, Bs, Bw, qkg):
            with ExitStack() as stage:
                sel8 = sb("sel8", [8, P], F32, stage)
                low8 = sb("low8", [8, 8], F32, stage)
                sq = OT[:, 0:4, :]
                block = stage.enter_context(nc.Block(no_gpsimd_drain=True))

                @block.sync
                def _(sp):
                    store(sp, io["o_kcvc"], kcvc[:])
                    store(sp, io["o_vsvw"][0:NPR, :].rearrange("(t p) n -> p t n", p=P), vsvw[:, 0:2, :])
                    store(sp, io["o_vsvw"][NPR:NT, :], vsvw[0:64, 2, :])
                    sp.dma_start(io["new_rows"][1], vsvw[0:64, 2, :]).then_inc(loads.sem, 16)
                    store(sp, io["o_wink"], io["win_k"][:, LS:WIN, :])
                    store(sp, io["o_winv"], io["win_v"][:, LS:WIN, :])
                    sp.wait_ge(act_step.sem, act_step.at(1))
                    sp.dma_start(io["gate_rows"].rearrange("b l h c -> (b l) (h c)"), GT[0:64, 2, :])\
                        .then_inc(loads.sem, 16)
                    sp.wait_ge(loads.sem, loads.at(32))
                    g = io["gate_rows"].tensor
                    for h in range(16):
                        sp.dma_start(GS[8 * h:8 * h + 8, :, :], bass.AP(g, 3 * h, [[48, 8], [8 * 48, NB], [1, 3]]))\
                            .then_inc(loads.sem, 16)
                    sp.wait_ge(centred.sem, centred.at(1))
                    store(sp, io["o_kskw"], kskw[:])
                    sp.wait_ge(loads.sem, loads.at(32 + 256))

                @block.gpsimd
                def _(pool):
                    step = Chain(pool, pool_step)
                    step(pool.memset(sel8[:], 0.0))
                    step(pool.affine_select(out=sel8[:], in_=sel8[:], compare_op=ALU.not_equal, fill=1.0, base=0,
                                            pattern=[[0, 16], [1, 8]], channel_multiplier=-1))
                    pool_step.count = step.n

                @block.tensor
                def _(pe):
                    pe.wait_ge(squared.sem, squared.at(1))
                    for m in range(4):
                        mm = nc.tensor.matmul(PS[:, m, 0:NT], halves[:], sq[:, m, :], start=True, stop=True)
                    mm.then_inc(summed.sem, 1)
                    pe.wait_ge(squared.sem, squared.at(2))
                    for m in range(4):
                        mm = nc.tensor.matmul(PS[:, 4 + m, 0:NT], halves[:], H[:, m, :], start=True, stop=True)
                    mm.then_inc(summed.sem, 1)
                    pe.wait_ge(variance.sem, variance.at(1))
                    for m in range(4):
                        mm = nc.tensor.matmul(PS[:, m, 0:NT], halves[:], H[:, 4 + m, :], start=True, stop=True)
                    mm.then_inc(summed.sem, 1)
                    pe.wait_ge(pool_step.sem, pool_step.at(2))
                    pe.wait_ge(variance.sem, variance.at(3))
                    pe.wait_ge(dve_step.sem, dve_step.at(1))
                    mm = nc.tensor.matmul(PS[:, 7, 0:8], sel8[:], low8[:], start=True, stop=True)
                    mm.then_inc(out_ready.sem, 1)

                @block.scalar
                def _(act):
                    nc.scalar.activation(sq, kskw[:], ACT.Square).then_inc(squared.sem, 1)
                    nc.scalar.activation(H[:], Q2[:], ACT.Square).then_inc(squared.sem, 1)
                    nc.scalar.activation(GT[:, 0:2, :], GT[:, 0:2, :], ACT.Sigmoid)
                    nc.scalar.activation(GT[0:64, 2, :], GT[0:64, 2, :], ACT.Sigmoid).then_inc(act_step.sem, 1)
                    act.wait_ge(variance.sem, variance.at(1))
                    nc.scalar.activation(sq, sq, ACT.Sqrt).then_inc(deviation.sem, 1)
                    act.wait_ge(variance.sem, variance.at(3))
                    nc.scalar.activation(H[:], H[:], ACT.Sqrt).then_inc(deviation.sem, 1)

                @block.vector
                def _(dve):
                    step = Chain(dve, dve_step)
                    step(nc.vector.tensor_scalar(low8[:], strict[0:8, 0:8], -1.0, -NEG, ALU.add, ALU.mult))
                    dve.wait_ge(summed.sem, summed.at(1))
                    nc.vector.tensor_scalar(sq, PS[:, 0:4, 0:NT], 1.0 / 64, EPS, ALU.mult, ALU.add)\
                        .then_inc(variance.sem, 1)
                    dve.wait_ge(summed.sem, summed.at(3))
                    nc.vector.tensor_scalar(H[:, 0:4, :], PS[:, 4:8, 0:NT], 1.0 / 64, EPS, ALU.mult, ALU.add)\
                        .then_inc(variance.sem, 1)
                    nc.vector.tensor_scalar(H[:, 4:8, :], PS[:, 0:4, 0:NT], 1.0 / 64, EPS, ALU.mult, ALU.add)\
                        .then_inc(variance.sem, 1)
                    step(nc.vector.tensor_scalar(qkg[:, 0:1], qkg[:, 0:1], SCALE, None, ALU.mult))
                    dve.wait_ge(deviation.sem, deviation.at(1))
                    step(nc.vector.reciprocal(sq, sq))
                    for m in range(2):
                        last = nc.vector.scalar_tensor_tensor(out=kskw[:, 2 * m:2 * m + 2, :], in0=sq[:, 2 * m:2 * m + 2, :],
                                                              scalar=qkg[:, 2 + m:3 + m], in1=kskw[:, 2 * m:2 * m + 2, :],
                                                              op0=ALU.mult, op1=ALU.mult)
                    last.then_inc(centred.sem, 1)
                    dve.wait_ge(deviation.sem, deviation.at(2))
                    step(nc.vector.reciprocal(H[:], H[:]))
                    nc.vector.scalar_tensor_tensor(out=Q2[:], in0=H[:], scalar=qkg[:, 0:1], in1=Q2[:],
                                                   op0=ALU.mult, op1=ALU.mult)
                    step(nc.vector.tensor_copy(Bw[:], Bs[:, PAST - WIN:PAST + LS]))
                    dve.wait_ge(out_ready.sem, out_ready.at(1))
                    nc.vector.tensor_tensor(Bw[:, 0:8], Bw[:, 0:8], PS[:, 7, 0:8], ALU.add)
                    dve_step.count = step.n
            loads.close(32 + 256)
            stored.close(16 * 6)
            pool_step.close(pool_step.count)
            dve_step.close(dve_step.count)
            act_step.close(1)
            out_ready.close(1)
            squared.close(2)
            summed.close(3)
            variance.close(3)
            deviation.close(2)
            centred.close(1)

        def compress(kcvc, KC, VC, qkg):
            with ExitStack() as stage:
                def tile(name, shape):
                    return sb(name, shape, F32, stage)
                w1 = tile("w1", [P, 2, 2, 8, P])
                w2 = tile("w2", [P, 2, 64])
                b1 = tile("b1", [P, 2])
                b2k = tile("b2k", [P, 1])
                b2v = tile("b2v", [64, 64])
                C = [tile(f"C{i}", [P, 2 * NPG, 4, 8, 8]) for i in range(2)]
                pages = sb("c_pages", [1, NB * NPG], I32, stage)
                free = H[:].rearrange("p k n -> p (k n)")
                A1 = free[:, 0:2 * 4 * 65].rearrange("p (b v n) -> p b v n", b=2, v=4)
                hid = [free[:, 520 + 512 * i:1032 + 512 * i].rearrange("p (b v n) -> p b v n", b=2, v=4)
                       for i in range(2)]
                free2 = OT[:].rearrange("p k n -> p (k n)")
                PX = free2[:, 0:1024].rearrange("p (i v n) -> p i v n", i=2, v=4)
                rsc = free2[:, 1024:1024 + 2 * 528].rearrange("p (t n) -> p t n", t=2)
                A1p = free[:, 1544:1544 + 4 * 17].rearrange("p (v n) -> p v n", v=4)
                hidp = free[:, 1624:1624 + 64].rearrange("p (v n) -> p v n", v=4)
                LOADED = 16 * 2 * NPG
                PAIRS = NB // 2
                block = stage.enter_context(nc.Block(no_gpsimd_drain=True))

                @block.sync
                def _(sp):
                    sp.dma_start(w1[:], io["cmp_w1"]).then_inc(loads.sem, 16)
                    sp.dma_start(w2[:], io["cmp_w2"]).then_inc(loads.sem, 16)
                    sp.dma_start(b1[:], io["cmp_b1"]).then_inc(loads.sem, 16)
                    sp.dma_start(b2k[:], io["cmp_b2k"]).then_inc(loads.sem, 16)
                    sp.dma_start(b2v[:], bass.AP(io["cmp_b2v"].tensor, 0, [[0, 64], [1, 64]])).then_inc(loads.sem, 16)
                    sp.dma_start(pages[:], io["pages"]).then_inc(loads.sem, 16)
                    sp.wait_ge(loads.sem, loads.at(96))
                    with sp.Fori(0, PAIRS) as g:
                        for i in range(2):
                            for p in range(2 * NPG):
                                page = sp.value_load(pages[0:1, bass.ds(g * (2 * NPG) + p, 1)],
                                                     min_val=0, max_val=NPOOL - 1)
                                src = io["cmp_k"] if i == 0 else io["cmp_v"]
                                if p == 0:
                                    sp.wait_ge(logit_ready.sem, logit_ready.at(0) + 2 * g)
                                sp.dma_start(C[i][:, p, :, :, :].rearrange("p v a s -> p (v a s)"),
                                             src[bass.ds(page, 1), :, :].rearrange("a p n -> p (a n)"))\
                                    .then_inc(page_in[i].sem, 16)

                @block.tensor
                def _(pe):
                    pe.wait_ge(loads.sem, loads.at(96))
                    for kvh in range(2):
                        for i in range(2):
                            for t in range(2):
                                for s2 in range(2):
                                    src = kcvc[64 * kvh:64 * kvh + 64, 2 * i + t, 0:NPR]
                                    src = src.rearrange("p (n s) -> p s n", s=2)[:, s2, :]
                                    mm = nc.tensor.matmul(PS[64 * s2:64 * s2 + 64, 4 + 2 * kvh + i, t * P:(t + 1) * P],
                                                          ident[64 * kvh:64 * kvh + 64, 64 * kvh:64 * kvh + 64], src,
                                                          start=True, stop=True)
                    mm.then_inc(turned.sem, 1)
                    pe.wait_ge(turned_read.sem, turned_read.at(1))
                    for i in range(2):
                        for m in range(2):
                            for a in range(8):
                                rhs = PX[:, i, :, :].rearrange("p v (n a) -> p v n a", a=8)[:, :, :, a]
                                mm = nc.tensor.matmul(PS[:, 2 * i + m, 0:64], w1[:, i, m, a, :], rhs,
                                                      start=(a == 0), stop=(a == 7))
                        mm.then_inc(chosen.sem, 1)
                        pe.wait_ge(chosen.sem, chosen.at(4 * i + 4))
                        if i == 0:
                            for v in range(4):
                                mm = nc.tensor.matmul(PS[64 * (v % 2):64 * (v % 2) + 64, 4, (v // 2) * 16:(v // 2) * 16 + 16],
                                                      w2[:, 0, :], hidp[:, v, :], start=True, stop=True)
                        else:
                            for v in range(4):
                                mm = nc.tensor.matmul(PS[0:16, 5, 64 * v:64 * v + 64], hidp[:, v, :], w2[:, 1, :],
                                                      start=True, stop=True)
                        mm.then_inc(turned.sem, 1)
                    pe.wait_ge(turned_read.sem, turned_read.at(3))

                    def one(g, i):
                        pe.wait_ge(page_in[i].sem, page_in[i].at(LOADED) + g * LOADED)
                        pe.wait_ge(weight_ready.sem, weight_ready.at(0) + 2 * g)
                        for m in range(2):
                            for a in range(8):
                                mm = nc.tensor.matmul(PS[:, 2 * i + m, :], w1[:, i, m, a, :], C[i][:, :, :, a, :],
                                                      start=(a == 0), stop=(a == 7))
                        mm.then_inc(logit_ready.sem, 1)

                    def second(g, i):
                        pe.wait_ge(weight_ready.sem, weight_ready.at(i + 1) + 2 * g)
                        pe.wait_ge(out_read.sem, out_read.at(i) + 2 * g)
                        if i == 0:
                            for v in range(4):
                                mm = nc.tensor.matmul(PS[64 * (v % 2):64 * (v % 2) + 64, 4, (v // 2) * P:(v // 2 + 1) * P],
                                                      w2[:, 0, :], hid[0][:, :, v, :], start=True, stop=True)
                        else:
                            for b in range(2):
                                for v in range(4):
                                    mm = nc.tensor.matmul(PS[0:64, 5, 256 * b + 64 * v:256 * b + 64 * v + 64],
                                                          hid[1][:, b, v, :], w2[:, 1, :], start=True, stop=True)
                        mm.then_inc(out_ready.sem, 1)
                    with pe.Fori(0, PAIRS) as g:
                        one(g, 0)
                        one(g, 1)
                        second(g, 0)
                        second(g, 1)
                    pe.wait_ge(squared.sem, squared.at(1))
                    for t in range(2):
                        nc.tensor.matmul(PS[:, t, :], halves[:], rsc[:, t, 0:512], start=True, stop=True)
                        mm = nc.tensor.matmul(PS[:, 2 + t, 0:16], halves[:], rsc[:, t, 512:528], start=True, stop=True)
                    mm.then_inc(summed.sem, 1)

                @block.scalar
                def _(act):
                    act.wait_ge(loads.sem, loads.at(96))
                    act.wait_ge(turned.sem, turned.at(1))
                    for i in range(2):
                        for kvh in range(2):
                            to = PX[:, i, :, :].rearrange("p (t k) n -> p t k n", k=2)[:, :, kvh, :]
                            last = nc.scalar.activation(to, PS[:, 4 + 2 * kvh + i, 0:256].rearrange("p (t n) -> p t n", t=2),
                                                        ACT.Copy)
                    last.then_inc(turned_read.sem, 1)
                    for i in range(2):
                        act.wait_ge(chosen.sem, chosen.at(4 * i + 1))
                        nc.scalar.activation(A1p[:, :, 0:16], PS[:, 2 * i + 1, 0:64].rearrange("p (v n) -> p v n", v=4),
                                             ACT.Copy).then_inc(chosen.sem, 1)
                        act.wait_ge(chosen.sem, chosen.at(4 * i + 3))
                        nc.scalar.activation(hidp, hidp, ACT.Gelu_apprx_tanh, bias=b1[:, i:i + 1])\
                            .then_inc(chosen.sem, 1)

                    def one(g, i):
                        act.wait_ge(logit_ready.sem, logit_ready.at(i + 1) + 2 * g)
                        act.wait_ge(keep_ready.sem, keep_ready.at(i) + 2 * g)
                        for b in range(2):
                            to = A1[:, b, :, 0:64].rearrange("p v (g s) -> p g v s", s=8)
                            src = PS[:, 2 * i + 1, 256 * b:256 * b + 256].rearrange("p (g v s) -> p g v s", v=4, s=8)
                            last = nc.scalar.activation(to, src, ACT.Copy)
                        last.then_inc(logged.sem, 1)
                        act.wait_ge(keep_ready.sem, keep_ready.at(i + 1) + 2 * g)
                        nc.scalar.activation(hid[i], hid[i], ACT.Gelu_apprx_tanh, bias=b1[:, i:i + 1])\
                            .then_inc(weight_ready.sem, 1)
                    with act.Fori(0, PAIRS) as g:
                        one(g, 0)
                        one(g, 1)
                    act.wait_ge(out_read.sem, out_read.at(2 * PAIRS))
                    nc.scalar.activation(rsc, KC[:], ACT.Square).then_inc(squared.sem, 1)
                    act.wait_ge(variance.sem, variance.at(1))
                    nc.scalar.activation(rsc, rsc, ACT.Sqrt).then_inc(deviation.sem, 1)

                @block.vector
                def _(dve):
                    step = Chain(dve, dve_step)
                    step(nc.vector.memset(A1[:, :, :, 64:65], 0.0))
                    step(nc.vector.memset(A1p[:, :, 16:17], 0.0))
                    dve.wait_ge(loads.sem, loads.at(96))
                    for i in range(2):
                        dve.wait_ge(chosen.sem, chosen.at(4 * i + 2))
                        nc.vector.tensor_tensor(hidp, A1p[:, :, 1:17],
                                                PS[:, 2 * i, 0:64].rearrange("p (v n) -> p v n", v=4),
                                                ALU.add).then_inc(chosen.sem, 1)
                        dve.wait_ge(turned.sem, turned.at(2 + i))
                        if i == 0:
                            nc.vector.tensor_scalar(KC[:, :, 512:528], PS[:, 4, 0:32].rearrange("p (t n) -> p t n", t=2),
                                                    b2k[:, 0:1], None, ALU.add).then_inc(turned_read.sem, 1)
                        else:
                            nc.vector.tensor_tensor(VC[0:16, NB, :].rearrange("p (v d) -> p v d", v=4),
                                                    PS[0:16, 5, 0:256].rearrange("p (v d) -> p v d", v=4),
                                                    rep(b2v[0:16, :], 1, 4), ALU.add).then_inc(turned_read.sem, 1)

                    def one(g, i):
                        dve.wait_ge(logged.sem, logged.at(i + 1) + 2 * g)
                        dve.wait_ge(out_ready.sem, out_ready.at(0) + 2 * g)
                        for b in range(2):
                            to = hid[i][:, b, :, :].rearrange("p v (g s) -> p g v s", s=8)
                            a0 = PS[:, 2 * i, 256 * b:256 * b + 256].rearrange("p (g v s) -> p g v s", v=4, s=8)
                            a1 = A1[:, b, :, 1:65].rearrange("p v (g s) -> p g v s", s=8)
                            last = nc.vector.tensor_tensor(to, a0, a1, ALU.add)
                        last.then_inc(keep_ready.sem, 1)

                    def second(g, i):
                        dve.wait_ge(out_ready.sem, out_ready.at(i + 1) + 2 * g)
                        if i == 0:
                            nc.vector.tensor_scalar(KC[:, :, bass.ds(g * P, P)],
                                                    PS[:, 4, 0:256].rearrange("p (t n) -> p t n", t=2),
                                                    b2k[:, 0:1], None, ALU.add).then_inc(out_read.sem, 1)
                        else:
                            to = VC[:, bass.ds(2 * g, 2), :].rearrange("p b (v d) -> p b v d", v=4)
                            nc.vector.tensor_tensor(to, PS[0:64, 5, :].rearrange("p (b v d) -> p b v d", b=2, v=4),
                                                    rep(rep(b2v[:], 1, 4), 1, 2), ALU.add).then_inc(out_read.sem, 1)
                    with dve.Fori(0, PAIRS) as g:
                        one(g, 0)
                        one(g, 1)
                        second(g, 0)
                        second(g, 1)
                    dve.wait_ge(summed.sem, summed.at(1))
                    nc.vector.tensor_scalar(rsc[:, :, 0:512], PS[:, 0:2, :], 1.0 / 64, EPS, ALU.mult, ALU.add)
                    nc.vector.tensor_scalar(rsc[:, :, 512:528], PS[:, 2:4, 0:16], 1.0 / 64, EPS, ALU.mult, ALU.add)\
                        .then_inc(variance.sem, 1)
                    dve.wait_ge(deviation.sem, deviation.at(1))
                    step(nc.vector.reciprocal(rsc, rsc))
                    nc.vector.scalar_tensor_tensor(out=KC[:], in0=rsc, scalar=qkg[:, 1:2], in1=KC[:],
                                                   op0=ALU.mult, op1=ALU.mult)
                    dve_step.count = step.n
            loads.close(96)
            dve_step.close(dve_step.count)
            turned.close(3)
            turned_read.close(3)
            chosen.close(8)
            for s in (logit_ready, keep_ready, logged, weight_ready, out_ready, out_read):
                s.close(2 * PAIRS)
            for s in page_in:
                s.close(LOADED * PAIRS)
            for s in (squared, summed, variance, deviation):
                s.close(1)

        def sparse_prompt(Q2, kskw, vsvw, GT, KC, VC):
            BATCHES = [(t, v) for t in range(2) for v in range(4)]
            with ExitStack() as stage:
                def tile(name, shape):
                    return sb(name, shape, F32, stage)
                B1 = tile("B1", [P, 16, 256])
                zs = [tile(f"zs{i}", [P, 8, 256]) for i in range(2)]
                zc = [tile(f"zc{i}", [P, 4, 16]) for i in range(2)]
                mx = tile("mx", [P, 2, 12])
                sm = tile("sm", [P, 2, 12])
                pT = tile("pT", [P, 5, 4, P])
                block = stage.enter_context(nc.Block(no_gpsimd_drain=True))

                def shape(t):
                    return P * (t + 1), 7 if t == 0 else 15

                def rounds(t):
                    out = [(2 * br + kt, 4 * br, kt * P) for br in range(2) for kt in range(t + 1)]
                    return out + [(4, None, 0)]
                first_round = []
                for t, v in BATCHES:
                    first_round.append(sum(len(rounds(t2)) for t2, _ in BATCHES[:len(first_round)]))

                @block.sync
                def _(sp):
                    f = io["bias_prompt"].tensor
                    sp.dma_start(B1[:], bass.AP(f, 127, [[16 * NDIST_P - 1, P], [NDIST_P, 16], [1, 256]]))\
                        .then_inc(loads.sem, 16)

                @block.tensor
                def _(pe):
                    def scores(n):
                        t, v = BATCHES[n]
                        nk, ncmp = shape(t)
                        r = slice(64 * (v % 2), 64 * (v % 2) + 64)
                        if n:
                            pe.wait_ge(scaled.sem, scaled.at(n))
                        for g in range(4):
                            q = Q2[r, 4 * (v // 2) + g, t * P:(t + 1) * P]
                            for br in range(2):
                                nc.tensor.matmul(PS[:, 2 * br + g // 2, (g % 2) * 256:(g % 2) * 256 + nk], q,
                                                 kskw[r, 2 * br + v // 2, 0:nk], start=True, stop=True)
                            mm = nc.tensor.matmul(PS[:, 4, 16 * g:16 * g + ncmp], q, KC[r, v // 2, 512:512 + ncmp],
                                                  start=True, stop=True)
                        mm.then_inc(logit_ready.sem, 1)

                    def turn(n):
                        t, v = BATCHES[n]
                        _, ncmp = shape(t)
                        pe.wait_ge(weight_ready.sem, weight_ready.at(n + 1))
                        for k, (slot, row, k0) in enumerate(rounds(t)):
                            at = first_round[n] + k
                            if at >= 2:
                                pe.wait_ge(turned_read.sem, turned_read.at(at - 1))
                            for g in range(4):
                                if row is None:
                                    mm = nc.tensor.transpose(PS[0:ncmp, 5 + at % 2, g * P:(g + 1) * P],
                                                             zc[n % 2][:, g, 0:ncmp], ident[:])
                                else:
                                    mm = nc.tensor.transpose(PS[:, 5 + at % 2, g * P:(g + 1) * P],
                                                             zs[n % 2][:, row + g, k0:k0 + P], ident[:])
                            mm.then_inc(turned.sem, 1)

                    def values(n):
                        t, v = BATCHES[n]
                        _, ncmp = shape(t)
                        last = first_round[n] + len(rounds(t))
                        pe.wait_ge(turned_read.sem, turned_read.at(last))
                        if n:
                            pe.wait_ge(out_read.sem, out_read.at(n))
                        r = slice(64 * (v % 2), 64 * (v % 2) + 64)
                        for g in range(4):
                            to = PS[r, 7, g * P:(g + 1) * P]
                            for br in range(2):
                                for kt in range(t + 1):
                                    nc.tensor.matmul(to, vsvw[:, kt, 256 * br + 64 * v:256 * br + 64 * v + 64],
                                                     pT[:, 2 * br + kt, g, :], start=(br == 0 and kt == 0), stop=False,
                                                     skip_group_check=True)
                            mm = nc.tensor.matmul(to, VC[0:ncmp, NB, 64 * v:64 * v + 64], pT[0:ncmp, 4, g, :],
                                                  start=False, stop=True, skip_group_check=True)
                        mm.then_inc(out_ready.sem, 1)
                    scores(0)
                    for n in range(len(BATCHES)):
                        if n + 1 < len(BATCHES):
                            scores(n + 1)
                        turn(n)
                        values(n)

                @block.scalar
                def _(act):
                    def exps(n):
                        nk, ncmp = shape(BATCHES[n][0])
                        act.wait_ge(centre_ready.sem, centre_ready.at(n + 1))
                        nc.scalar.activation(zs[n % 2][:, :, 0:nk], zs[n % 2][:, :, 0:nk], ACT.Exp)
                        nc.scalar.activation(zc[n % 2][:, :, 0:ncmp], zc[n % 2][:, :, 0:ncmp], ACT.Exp)\
                            .then_inc(exponent.sem, 1)

                    def copies(n):
                        t, _ = BATCHES[n]
                        _, ncmp = shape(t)
                        if n:
                            act.wait_ge(out_ready.sem, out_ready.at(n))
                        for k, (slot, row, k0) in enumerate(rounds(t)):
                            at = first_round[n] + k
                            act.wait_ge(turned.sem, turned.at(at + 1))
                            rows = P if row is not None else ncmp
                            nc.scalar.activation(pT[0:rows, slot, :, :].rearrange("p g q -> p (g q)"),
                                                 PS[0:rows, 5 + at % 2, :], ACT.Copy).then_inc(turned_read.sem, 1)
                    exps(0)
                    for n in range(len(BATCHES)):
                        if n + 1 < len(BATCHES):
                            exps(n + 1)
                        copies(n)

                @block.vector
                def _(dve):
                    step = Chain(dve, dve_step)
                    dve.wait_ge(loads.sem, loads.at(16))

                    def last_dim(ap, n):
                        return bass.AP(ap.tensor, ap.offset, [list(x) for x in ap.ap] + [[0, n]])

                    def centre(n):
                        t, v = BATCHES[n]
                        nk, ncmp = shape(t)
                        z, c, m = zs[n % 2], zc[n % 2], mx[:, n % 2, :]
                        bias = B1[:, 4 * v:4 * v + 4, 0:nk] if t else B1[:, 4 * v:4 * v + 4, P:2 * P]
                        k0 = 31 if t else P + 31
                        bias_c = B1[:, 4 * v:4 * v + 4, k0:k0 + 16 * (ncmp - 1) + 1:16]
                        dve.wait_ge(logit_ready.sem, logit_ready.at(n + 1))
                        if n >= 2:
                            dve.wait_ge(turned.sem, turned.at(first_round[n - 1]))
                        zp = PS[:, 0:4, :].rearrange("p a (h k) -> p (a h) k", h=2)[:, :, 0:nk]
                        nc.vector.tensor_tensor(z[:, :, 0:nk].rearrange("p (b g) k -> p b g k", b=2),
                                                zp.rearrange("p (b g) k -> p b g k", b=2), rep(bias, 1, 2), ALU.add)
                        nc.vector.tensor_tensor(c[:, :, 0:ncmp],
                                                PS[:, 4, 0:64].rearrange("p (g k) -> p g k", g=4)[:, :, 0:ncmp],
                                                bias_c, ALU.add).then_inc(scaled.sem, 1)
                        dve.wait_ge(scaled.sem, scaled.at(n + 1))
                        nc.vector.tensor_reduce(m[:, 0:8], z[:, :, 0:nk], AX.X, ALU.max)
                        step(nc.vector.tensor_reduce(m[:, 8:12], c[:, :, 0:ncmp], AX.X, ALU.max))
                        step(nc.vector.tensor_scalar(m, m, NEG / 10, None, ALU.max))
                        nc.vector.tensor_tensor(z[:, :, 0:nk], z[:, :, 0:nk], last_dim(m[:, 0:8], nk), ALU.subtract)
                        nc.vector.tensor_tensor(c[:, :, 0:ncmp], c[:, :, 0:ncmp], last_dim(m[:, 8:12], ncmp),
                                                ALU.subtract).then_inc(centre_ready.sem, 1)

                    def weights(n):
                        t, v = BATCHES[n]
                        nk, ncmp = shape(t)
                        z, c, s = zs[n % 2], zc[n % 2], sm[:, n % 2, :]
                        dve.wait_ge(exponent.sem, exponent.at(n + 1))
                        nc.vector.tensor_reduce(s[:, 0:8], z[:, :, 0:nk], AX.X, ALU.add)
                        step(nc.vector.tensor_reduce(s[:, 8:12], c[:, :, 0:ncmp], AX.X, ALU.add))
                        step(nc.vector.tensor_scalar(s, s, 1e-30, None, ALU.max))
                        step(nc.vector.reciprocal(s, s))
                        gate = GT[:, t, 12 * v:12 * v + 12].rearrange("p (g b) -> p b g", b=3)
                        nc.vector.tensor_tensor(s[:, 0:8].rearrange("p (b g) -> p b g", b=2),
                                                s[:, 0:8].rearrange("p (b g) -> p b g", b=2), gate[:, 1:3, :], ALU.mult)
                        step(nc.vector.tensor_tensor(s[:, 8:12], s[:, 8:12], gate[:, 0, :], ALU.mult))
                        nc.vector.tensor_tensor(z[:, :, 0:nk], z[:, :, 0:nk], last_dim(s[:, 0:8], nk), ALU.mult)
                        nc.vector.tensor_tensor(c[:, :, 0:ncmp], c[:, :, 0:ncmp], last_dim(s[:, 8:12], ncmp),
                                                ALU.mult).then_inc(weight_ready.sem, 1)

                    def outs(n):
                        t, v = BATCHES[n]
                        r = slice(64 * (v % 2), 64 * (v % 2) + 64)
                        dve.wait_ge(out_ready.sem, out_ready.at(n + 1))
                        nc.vector.tensor_copy(OT[r, 4 * (v // 2):4 * (v // 2) + 4, t * P:(t + 1) * P],
                                              PS[r, 7, :].rearrange("p (g q) -> p g q", g=4)).then_inc(out_read.sem, 1)
                    centre(0)
                    for n in range(len(BATCHES)):
                        if n + 1 < len(BATCHES):
                            centre(n + 1)
                        weights(n)
                        if n:
                            outs(n - 1)
                    outs(len(BATCHES) - 1)
                    dve_step.count = step.n
            loads.close(16)
            dve_step.close(dve_step.count)
            for s in (logit_ready, scaled, centre_ready, exponent, weight_ready, out_ready, out_read):
                s.close(len(BATCHES))
            n = sum(len(rounds(t)) for t, _ in BATCHES)
            turned.close(n)
            turned_read.close(n)

        def sparse_sample(Q2, kskw, vsvw, GS, Bs, Bw, KC, VC):
            NC = PAST // 16 - 1
            NS, NW = PAST + LS, WIN + LS
            LOADED = 16 * (2 * NPG + 3)
            with ExitStack() as stage:
                def tile(name, shape):
                    return sb(name, shape, F32, stage)
                KS = [tile(f"KS{i}", [P, NPG, 2, P]) for i in range(2)]
                VS = [tile(f"VS{i}", [P, NPG, 256]) for i in range(2)]
                KW = [tile(f"KW{i}", [P, 2, WIN]) for i in range(2)]
                VW = [tile(f"VW{i}", [P, 4, 256]) for i in range(2)]
                VN = [vsvw[0:LS, i, :] for i in range(2)]
                QB = tile("QB2", [P, 2, P])
                pages = sb("o_pages", [1, NB * NPG], I32, stage)
                pT = tile("pT2", [P, 15, P])
                free = H[:].rearrange("p k n -> p (k n)")
                zs = free[:, 0:NS]
                zw = free[:, NS:NS + NW]
                zc = free[:, NS + NW:NS + NW + NC]
                pc = free[:, 1664:1664 + P]
                cover = free[0:64, 1800:1817]
                cov = free[:, 1820:1837]
                hit = free[:, 1840:1854]
                drop = free[:, 1860:1876]
                block_no = free[:, 1880:1896]
                st = free[:, 1900:1916]
                same_q = free[:, 1920:1920 + P]
                VCs = free[0:64, 2048:2304]
                zsp = PS[:, 0:3, :].rearrange("p a n -> p (a n)")[:, 0:NS]
                zwp = PS[:, 3:5, :].rearrange("p a n -> p (a n)")[:, 0:NW]
                zcp = PS[:, 2, 256:256 + NC]
                block = stage.enter_context(nc.Block(no_gpsimd_drain=True))
                BUILT = 16

                @block.sync
                def _(sp):
                    sp.dma_start(pages[:], io["pages"]).then_inc(loads.sem, 16)
                    sp.wait_ge(loads.sem, loads.at(16))

                    def load(b, i, used=None):
                        for p in range(NPG):
                            at = b * NPG + p
                            cell = pages[0:1, at:at + 1] if isinstance(at, int) else pages[0:1, bass.ds(at, 1)]
                            page = sp.value_load(cell, min_val=0, max_val=NPOOL - 1)
                            if p == 0 and used is not None:
                                sp.wait_ge(out_ready.sem, used)
                            sp.dma_start(KS[i][:, p, :, :].rearrange("p a n -> p (a n)"),
                                         io["slc_kT"][bass.ds(page, 1), :, :].rearrange("a p n -> p (a n)"))\
                                .then_inc(page_in[i].sem, 16)
                            sp.dma_start(VS[i][:, p, :],
                                         io["slc_v"][bass.ds(page, 1), :, :].rearrange("a p n -> p (a n)"))\
                                .then_inc(page_in[i].sem, 16)
                        one = slice(b, b + 1) if isinstance(b, int) else bass.ds(b, 1)
                        new = slice(LS * b, LS * b + LS) if isinstance(b, int) else bass.ds(b * LS, LS)
                        sp.dma_start(KW[i][:].rearrange("p t n -> p (t n)"),
                                     io["win_kT"][one, :, :].rearrange("a p n -> p (a n)")).then_inc(page_in[i].sem, 16)
                        sp.dma_start(VW[i][:], io["win_v"][one, :, :].rearrange("a (c p) n -> p (a c) n", p=P))\
                            .then_inc(page_in[i].sem, 16)
                        sp.dma_start(VN[i], io["new_rows"][1, new, :]).then_inc(page_in[i].sem, 16)
                    sp.wait_ge(stored.sem, stored.at(0))
                    load(0, 0)
                    load(1, 1)
                    with sp.Fori(1, NB // 2) as g:
                        for i in range(2):
                            load(2 * g + i, i, out_ready.at(i - 1) + 2 * g)

                @block.gpsimd
                def _(pool):
                    step = Chain(pool, pool_step)

                    def pick(t, op, base, pattern, mult, fill=0.0):
                        step(pool.affine_select(out=t, in_=t, compare_op=op, fill=fill, base=base, pattern=pattern,
                                                channel_multiplier=mult))
                    step(pool.memset(QB[:], 0.0))
                    step(pool.memset(same_q, 0.0))
                    step(pool.memset(cover, 1.0))
                    step(pool.memset(pc, 0.0))
                    for d in range(-3, 4):
                        pick(same_q, ALU.not_equal, -8 * d, [[-1, P]], 1, 1.0)
                    v = same_q.rearrange("p (c i) -> p c i", i=32)
                    pick(v, ALU.is_ge, 0, [[-32, 4], [0, 32]], 1)
                    pick(v, ALU.is_ge, 31, [[32, 4], [0, 32]], -1)
                    pick(cover, ALU.is_ge, 63, [[64, 17]], -16)
                    pick(cover, ALU.is_gt, 32, [[-64, 17]], 16)
                    step(pool.iota(block_no, pattern=[[1, 16]], base=0, channel_multiplier=0,
                                   allow_small_or_imprecise_dtypes=True))
                    assert step.n == BUILT
                    pool_step.count = step.n

                @block.tensor
                def _(pe):
                    def turn(round_no, b, items):
                        bank = 6 + round_no % 2
                        for rows, c, src in items:
                            mm = nc.tensor.transpose(PS[0:rows, bank, c:c + P], src, ident[:])
                        mm.then_inc(turned.sem, 1)

                    def one(g, i):
                        b = 2 * g + i
                        pe.wait_ge(page_in[i].sem, page_in[i].at(LOADED) + g * LOADED)
                        pe.wait_ge(seq_ready.sem, seq_ready.at(1) + b)
                        new = bass.ds(b * LS + NPR, LS)
                        for t in range(2):
                            mm = nc.tensor.matmul(zcp, QB[:, t, :], KC[:, t, bass.ds(b * 64, NC)],
                                                  start=(t == 0), stop=(t == 1))
                        mm.then_inc(chosen.sem, 1)
                        for c in range(2):
                            for t in range(2):
                                nc.tensor.matmul(PS[:, c, :], QB[:, t, :], KS[i][:, 4 * c:4 * c + 4, t, :],
                                                 start=(t == 0), stop=(t == 1))
                        for t in range(2):
                            nc.tensor.matmul(PS[:, 3, :], QB[:, t, :], KW[i][:, t, :], start=(t == 0), stop=(t == 1))
                        for t in range(2):
                            nc.tensor.matmul(PS[:, 4, 0:LS], QB[:, t, :], kskw[:, 2 + t, new],
                                             start=(t == 0), stop=(t == 1))
                        pe.wait_ge(scaled.sem, scaled.at(1) + 2 * b)
                        for t in range(2):
                            mm = nc.tensor.matmul(PS[:, 2, 0:LS], QB[:, t, :], kskw[:, t, new],
                                                  start=(t == 0), stop=(t == 1))
                        mm.then_inc(logit_ready.sem, 1)
                        pe.wait_ge(keep_ready.sem, keep_ready.at(1) + 3 * b)
                        nc.tensor.transpose(PS[:, 6, 0:P], pc, ident[:]).then_inc(chosen.sem, 1)
                        pe.wait_ge(logged.sem, logged.at(1) + b)
                        nc.tensor.matmul(PS[:, 5, 0:17], pT[0:NC, 14, :], cover[0:NC, :], start=True, stop=True)\
                            .then_inc(chosen.sem, 1)
                        pe.wait_ge(keep_ready.sem, keep_ready.at(2) + 3 * b)
                        nc.tensor.matmul(PS[:, 5, 32:49], same_q, cov, start=True, stop=True)\
                            .then_inc(chosen.sem, 1)
                        pe.wait_ge(weight_ready.sem, weight_ready.at(1) + b)
                        turn(0, b, [(P, P * k, zs[:, k * P:(k + 1) * P]) for k in range(4)])
                        turn(1, b, [(P, P * k, zs[:, (k + 4) * P:(k + 5) * P]) for k in range(4)])
                        pe.wait_ge(turned_read.sem, turned_read.at(1) + 4 * b)
                        turn(2, b, [(P, P * k, zw[:, k * P:(k + 1) * P]) for k in range(4)])
                        pe.wait_ge(turned_read.sem, turned_read.at(2) + 4 * b)
                        turn(3, b, [(LS, 0, zs[:, PAST:NS]), (LS, P, zw[:, WIN:NW]), (NC, 2 * P, zc)])
                        pe.wait_ge(turned_read.sem, turned_read.at(4) + 4 * b)
                        for t in range(2):
                            cols = slice(t * P, t * P + P)
                            parts = [(VS[i][:, k, cols], k, P) for k in range(NPG)]
                            parts += [(VW[i][:, k, cols], 8 + k, P) for k in range(4)]
                            parts += [(VN[i][:, cols], 12, LS), (VN[i][:, 256 + t * P:256 + t * P + P], 13, LS),
                                      (VCs[0:NC, cols], 14, NC)]
                            for n, (v, k, rows) in enumerate(parts):
                                mm = nc.tensor.matmul(PS[:, 5, 64 + 64 * t:128 + 64 * t], v,
                                                      pT[0:rows, k, 64 * t:64 * t + 64],
                                                      start=(n == 0), stop=(n == len(parts) - 1))
                        mm.then_inc(out_ready.sem, 1)

                    pe.wait_ge(pool_step.sem, pool_step.at(BUILT))
                    with pe.Fori(0, NB // 2) as g:
                        one(g, 0)
                        one(g, 1)

                @block.scalar
                def _(act):
                    def one(g, i):
                        b = 2 * g + i
                        at = bass.ds(b * LS + NPR, LS)
                        act.wait_ge(out_ready.sem, out_ready.at(0) + b)
                        for kvh in range(2):
                            r = slice(64 * kvh, 64 * kvh + 64)
                            for t in range(2):
                                c = 32 * (2 * t + kvh)
                                nc.scalar.activation(QB[r, t, c:c + 32].rearrange("p (g q) -> p g q", g=4),
                                                     Q2[r, 4 * t:4 * t + 4, at], ACT.Copy)
                        nc.scalar.activation(VCs, VC[:, bass.ds(b, 1), :].rearrange("p a n -> p (a n)"),
                                             ACT.Copy).then_inc(seq_ready.sem, 1)
                        act.wait_ge(centre_ready.sem, centre_ready.at(1) + 2 * b)
                        nc.scalar.activation(zc, zc, ACT.Exp, bias=st[:, 0:1], accum_out=st[:, 1:2])\
                            .then_inc(exponent.sem, 1)
                        act.wait_ge(chosen.sem, chosen.at(2) + 4 * b)
                        nc.scalar.activation(pT[0:NC, 14, :], PS[0:NC, 6, 0:P], ACT.Copy).then_inc(logged.sem, 1)
                        act.wait_ge(centre_ready.sem, centre_ready.at(2) + 2 * b)
                        nc.scalar.activation(zw, zw, ACT.Exp, bias=st[:, 4:5], accum_out=st[:, 7:8])
                        nc.scalar.activation(zs, zs, ACT.Exp, bias=st[:, 3:4], accum_out=st[:, 6:7])\
                            .then_inc(exponent.sem, 1)
                        for n in range(3):
                            act.wait_ge(turned.sem, turned.at(n + 1) + 4 * b)
                            nc.scalar.activation(pT[:, 4 * n:4 * n + 4, :].rearrange("p k r -> p (k r)"),
                                                 PS[:, 6 + n % 2, :], ACT.Copy).then_inc(turned_read.sem, 1)
                        act.wait_ge(turned.sem, turned.at(4) + 4 * b)
                        nc.scalar.activation(pT[0:LS, 12:14, :].rearrange("p k r -> p (k r)"), PS[0:LS, 7, 0:2 * P],
                                             ACT.Copy)
                        nc.scalar.activation(pT[0:NC, 14, :], PS[0:NC, 7, 2 * P:3 * P], ACT.Copy)\
                            .then_inc(turned_read.sem, 1)
                    act.wait_ge(pool_step.sem, pool_step.at(BUILT))
                    with act.Fori(0, NB // 2) as g:
                        one(g, 0)
                        one(g, 1)

                @block.vector
                def _(dve):
                    step = Chain(dve, dve_step)

                    def one(g, i):
                        b = 2 * g + i
                        gate = GS[:, bass.ds(b, 1), :].rearrange("p a c -> p (a c)")
                        dve.wait_ge(chosen.sem, chosen.at(1) + 4 * b)
                        nc.vector.tensor_tensor(zc, zcp, Bs[:, 31:31 + 16 * (NC - 1) + 1:16], ALU.add)\
                            .then_inc(scaled.sem, 1)
                        dve.wait_ge(scaled.sem, scaled.at(1) + 2 * b)
                        nc.vector.tensor_reduce(st[:, 0:1], zc, AX.X, ALU.max, negate=True).then_inc(centre_ready.sem, 1)
                        dve.wait_ge(exponent.sem, exponent.at(1) + 2 * b)
                        step(nc.vector.reciprocal(st[:, 2:3], st[:, 1:2]))
                        nc.vector.tensor_scalar(pc[:, 0:NC], zc, st[:, 2:3], None, ALU.mult).then_inc(keep_ready.sem, 1)
                        dve.wait_ge(keep_ready.sem, keep_ready.at(1) + 3 * b)
                        step(nc.vector.tensor_scalar(zc, pc[:, 0:NC], gate[:, 0:1], None, ALU.mult))
                        dve.wait_ge(logit_ready.sem, logit_ready.at(1) + b)
                        nc.vector.tensor_tensor(zw, zwp, Bw[:], ALU.add)
                        nc.vector.tensor_tensor(zs, zsp, Bs[:], ALU.add).then_inc(scaled.sem, 1)
                        dve.wait_ge(chosen.sem, chosen.at(3) + 4 * b)
                        nc.vector.tensor_copy(cov, PS[:, 5, 0:17]).then_inc(keep_ready.sem, 1)
                        dve.wait_ge(chosen.sem, chosen.at(4) + 4 * b)
                        step(nc.vector.tensor_copy(drop[:, 0:14], PS[:, 5, 33:47]))
                        step(nc.vector.tensor_reduce(st[:, 8:9], drop[:, 0:14], AX.X, ALU.min))
                        step(nc.vector.scalar_tensor_tensor(out=hit, in0=drop[:, 0:14], scalar=st[:, 8:9],
                                                            in1=block_no[:, 1:15], op0=ALU.is_le, op1=ALU.mult))
                        step(nc.vector.tensor_reduce(st[:, 9:10], hit, AX.X, ALU.max))
                        step(nc.vector.tensor_scalar(drop, block_no, st[:, 9:10], NEG, ALU.is_equal, ALU.mult))
                        dve.wait_ge(scaled.sem, scaled.at(2) + 2 * b)
                        d = bass.AP(drop.tensor, drop.offset, [list(x) for x in drop.ap] + [[0, 64]])
                        v = zs[:, 0:PAST].rearrange("p (j k) -> p j k", j=16)
                        step(nc.vector.tensor_tensor(v, v, d, ALU.add))
                        nc.vector.tensor_reduce(st[:, 4:5], zw, AX.X, ALU.max, negate=True)
                        nc.vector.tensor_reduce(st[:, 3:4], zs, AX.X, ALU.max, negate=True)\
                            .then_inc(centre_ready.sem, 1)
                        dve.wait_ge(exponent.sem, exponent.at(2) + 2 * b)
                        step(nc.vector.reciprocal(st[:, 6:8], st[:, 6:8]))
                        step(nc.vector.tensor_tensor(st[:, 6:8], st[:, 6:8], gate[:, 1:3], ALU.mult))
                        nc.vector.tensor_scalar(zw, zw, st[:, 7:8], None, ALU.mult).then_inc(keep_ready.sem, 1)
                        nc.vector.tensor_scalar(zs, zs, st[:, 6:7], None, ALU.mult).then_inc(weight_ready.sem, 1)
                        dve.wait_ge(out_ready.sem, out_ready.at(1) + b)
                        for kvh in range(2):
                            r = slice(64 * kvh, 64 * kvh + 64)
                            src = PS[r, 5, 64:192].rearrange("p (t k g q) -> p t k g q", t=2, k=2, g=4)[:, :, kvh, :, :]
                            to = OT[r, :, bass.ds(b * LS + NPR, LS)].rearrange("p (t g) q -> p t g q", t=2)
                            nc.vector.tensor_copy(to, src).then_inc(out_read.sem, 1)
                    dve.wait_ge(pool_step.sem, pool_step.at(BUILT))
                    with dve.Fori(0, NB // 2) as g:
                        step.loop(g, 20)
                        one(g, 0)
                        one(g, 1)
                        step.done(NB // 2)
                    dve_step.count = step.n
            loads.close(16)
            pool_step.close(pool_step.count)
            dve_step.close(dve_step.count)
            for s in (logit_ready, logged, weight_ready, out_ready, seq_ready):
                s.close(NB)
            for s in (scaled, centre_ready, exponent, out_read):
                s.close(2 * NB)
            keep_ready.close(3 * NB)
            chosen.close(4 * NB)
            turned.close(4 * NB)
            turned_read.close(4 * NB)
            for s in page_in:
                s.close(LOADED * (NB // 2))

        n = 0
        n = first_ada_stage(n)
        n = ffn_stage(0, 0, n, 0, ADA_FIRST, ADA_SLOTS - ADA_FIRST)
        n = even_stage(n)
        n = ffn_stage(0, 1, n, 1, 0, ADA_SLOTS)
        n = ffn_stage(1, 0, n)
        n = odd_stage(n)
        n = ffn_stage(1, 1, n)
        assert n == NSLOT

        with nc.Block() as block:
            @block.sync
            def _(sp):
                sp.dma_start(io["yT"], X[:]).then_inc(stored.sem, 16)
                sp.wait_ge(stored.sem, stored.at(16))


def bucket_one_hot():
    dist = DIST_HI - np.arange(NDIST)
    d = np.maximum(dist, 0)
    ratio = np.log(np.maximum(d, 16).astype(np.float32) / np.float32(16)) / np.float32(math.log(1024 / 16))
    bucket = np.where(d < 16, d, np.minimum(16 + (ratio * np.float32(16)).astype(np.int32), 31))
    bucket = np.where(dist < 0, 32, bucket)
    return (np.arange(33)[:, None] == bucket[None, :]).astype(np.float32)


def slots_of(w):
    n = w.shape[1] // 512
    return w.reshape(KT, P, n, 512).transpose(2, 1, 0, 3).reshape(n, P, SLOT)


def weight_slots(i):
    out = []

    def ffn(l, f, ada=None):
        w = i["ffn_w_in"][l, f].reshape(D, 2, DFF // 256, 256).transpose(0, 2, 1, 3).reshape(D, 2 * DFF)
        w_in = slots_of(w)
        w = np.zeros((OUT_GROUPS * D, D), np.float32)
        w[:DFF] = i["ffn_w_out"][l, f]
        w = w.reshape(OUT_GROUPS, D, D)
        w = np.stack([slots_of(w[g]) for g in range(OUT_GROUPS)], axis=1)
        w_out = w.reshape(OUT_SLOTS, P, SLOT)
        before, body, rounds, after = ffn_plan(0 if ada is None else len(ada))
        per_h = sum(kind == "h" for kind, _ in body)
        order = before + [(kind, k + r * (per_h if kind == "h" else 2)) for r in range(rounds)
                          for kind, k in body] + after
        at = {"h": w_in, "o": w_out, "a": ada}
        out.append(np.stack([at[kind][k] for kind, k in order]))

    ada = [slots_of(i["ada_w"][l]) for l in range(2)]
    out.append(ada[0][:ADA_FIRST])
    ffn(0, 0, ada[0][ADA_FIRST:])
    w = i["even_w_in"][0]
    out.append(slots_of(w[:, :3072]))
    out.append(slots_of(i["even_w_out"][0]))
    ffn(0, 1, ada[1])
    ffn(1, 0)
    w = i["odd_w_in"][0]
    q = w[:, :1024].reshape(D, 2, 2, 4, 64).transpose(0, 1, 3, 2, 4).reshape(D, 1024)
    kc, vc, ks, vs, kw, vw = [w[:, 1024 + 256 * n:1280 + 256 * n] for n in range(6)]
    out.append(slots_of(np.concatenate([q, kc, vc, ks, kw, vs, vw], axis=1)))
    wo = i["odd_w_out"][0].reshape(2, 2, 4, 64, D).transpose(0, 2, 1, 3, 4).reshape(D, D)
    out.append(slots_of(wo))
    ffn(1, 1)
    return np.concatenate(out, axis=0)


def lay_out(i):
    def feat(a):
        a = a.reshape(a.shape[:-1] + (KT, P))
        return np.moveaxis(a, -1, 0)

    x = np.concatenate([i["x_prompt"].reshape(NPR, D), i["x_sample"].reshape(NB * LS, D)])
    c = np.concatenate([i["c_prompt"], i["c_sample"]])
    a = {}
    a["xT"] = feat(x).transpose(0, 2, 1)
    a["cT"] = feat(c).transpose(0, 2, 1)
    a["norm_gT"] = feat(i["norm_g"])
    a["ada_bT"] = feat(i["ada_b"].reshape(2, 9, D)).reshape(P, 2, 9 * KT)
    a["w_slots"] = weight_slots(i)
    a["w_a1"] = i["even_w_in"][0][:, 3072:].reshape(KT, P, 16).transpose(1, 0, 2)
    a["w_a2"] = i["gla_w_a2"][0]
    a["b_a2"] = i["gla_b_a2"]
    a["onorm_g"] = i["gla_onorm_g"].reshape(P, 1)
    a["w_gt"] = i["odd_w_in"][0][:, 2560:].reshape(KT, P, 48).transpose(1, 0, 2)
    a["pages"] = i["page_table"].reshape(1, NB * NPG)
    a["sb_kT"] = i["cache_sb_k"][0].reshape(NPOOL, PAGE, 4, P).transpose(0, 3, 2, 1).reshape(NPOOL, P, 4 * PAGE)
    a["sb_v"] = i["cache_sb_v"][0].reshape(NPOOL, PAGE, 512)
    a["gla_s"] = i["state_gla"][0].reshape(NB, 2, P, P).transpose(2, 0, 1, 3)
    a["slc_kT"] = i["cache_slc_k"][0].reshape(NPOOL, PAGE, 2, P).transpose(0, 3, 2, 1).reshape(NPOOL, P, 2 * PAGE)
    a["slc_v"] = i["cache_slc_v"][0].reshape(NPOOL, PAGE, 256)
    for n in "kv":
        t = i["cache_cmp_" + n][0].reshape(NPOOL, 8, 8, 2, 4, 64)
        a["cmp_" + n] = t.transpose(0, 3, 5, 4, 2, 1).reshape(NPOOL, P, 256)
    a["win_kT"] = i["cache_win_k"][0].reshape(NB, WIN, 2, P).transpose(0, 3, 2, 1).reshape(NB, P, 2 * WIN)
    a["win_k"] = i["cache_win_k"][0].reshape(NB, WIN, 256)
    a["win_v"] = i["cache_win_v"][0].reshape(NB, WIN, 256)
    g = i["nsa_qk_g"][0].T
    a["qk_g"] = np.concatenate([g, g])
    w1 = i["cmp_w1"][0].reshape(2, 2, 8, P, P)
    a["cmp_w1"] = w1.transpose(3, 0, 1, 2, 4)
    a["cmp_b1"] = i["cmp_b1"][0].T
    a["cmp_w2"] = i["cmp_w2"][0].transpose(1, 0, 2)
    b2 = i["cmp_b2"][0]
    a["cmp_b2k"] = np.concatenate([b2[0], b2[0]]).reshape(P, 1)
    a["cmp_b2v"] = b2[1:2]
    a["rel_table"] = i["rel_table"]
    a["one_hot"] = bucket_one_hot()
    return {k: np.ascontiguousarray(v) for k, v in a.items()}


OUTS = {
    "yT": (P, KT, NT), "o_sbk": (P, 4, NT), "o_sbv": (NT, 512), "o_pgla": (P, 2, P), "o_sgla": (P, NB, 2, P),
    "o_kcvc": (P, 4, NT), "o_kskw": (P, 4, NT), "o_vsvw": (NT, 512),
    "o_wink": (NB, WIN - LS, 256), "o_winv": (NB, WIN - LS, 256),
}


def kernel(**inputs):
    import concourse.bacc as _bacc
    from concourse.bass_utils import run_bass_kernel_spmd as _run

    arrays = lay_out({k: np.asarray(v) for k, v in inputs.items()})
    nc = _bacc.Bacc("TRN2", target_bir_lowering=False, num_devices=1)
    io = {}
    for name, a in arrays.items():
        io[name] = nc.dram_tensor(name, a.shape, mybir.dt.from_np(a.dtype), kind="ExternalInput").ap()
    for name, shape in OUTS.items():
        io[name] = nc.dram_tensor(name, shape, F32, kind="ExternalOutput").ap()
    io["bias_rows"] = nc.dram_tensor("bias_rows", (P, NDIST), F32, kind="Internal").ap()
    io["bias_prompt"] = nc.dram_tensor("bias_prompt", (P, 16, NDIST_P), F32, kind="Internal").ap()
    io["gate_rows"] = nc.dram_tensor("gate_rows", (NB, LS, 16, 3), F32, kind="Internal").ap()
    io["new_rows"] = nc.dram_tensor("new_rows", (2, NB * LS, 512), F32, kind="Internal").ap()
    build(nc, io)
    o = _run(nc, [arrays], core_ids=[0]).results[0]

    def rows(t, heads):
        t = t.transpose(2, 1, 0).reshape(NT, heads, 64)
        return t[:NPR].reshape(1, 1, NPR, heads, 64), t[NPR:].reshape(1, NB, LS, heads, 64)

    def natural(t, heads):
        t = t.reshape(NT, heads, 64)
        return t[:NPR].reshape(1, 1, NPR, heads, 64), t[NPR:].reshape(1, NB, LS, heads, 64)

    y = o["yT"].transpose(2, 1, 0).reshape(NT, D)
    p_sbk, s_sbk = rows(o["o_sbk"], 8)
    p_sbv, s_sbv = natural(o["o_sbv"], 8)
    p_gla = o["o_pgla"].transpose(1, 0, 2).reshape(1, 1, 4, 64, P)
    s_gla = o["o_sgla"].transpose(1, 2, 0, 3).reshape(1, NB, 4, 64, P)
    p_kc, s_kc = rows(o["o_kcvc"][:, 0:2], 4)
    p_vc, s_vc = rows(o["o_kcvc"][:, 2:4], 4)
    p_ks, s_ks = rows(o["o_kskw"][:, 0:2], 4)
    p_kw, s_kw = rows(o["o_kskw"][:, 2:4], 4)
    p_vs, s_vs = natural(o["o_vsvw"][:, 0:256], 4)
    p_vw, s_vw = natural(o["o_vsvw"][:, 256:512], 4)

    def window(old, new):
        return np.concatenate([old.reshape(1, NB, WIN - LS, 4, 64), new], axis=2)

    return (y[:NPR].reshape(1, NPR, D), y[NPR:].reshape(NB, LS, D), p_sbk, p_sbv, p_gla, p_kc, p_vc, p_ks, p_vs,
            p_kw, p_vw, s_sbk, s_sbv, s_gla, s_kc, s_vc, s_ks, s_vs, window(o["o_wink"], s_kw),
            window(o["o_winv"], s_vw))
```

```python
import math
from contextlib import ExitStack

import numpy as np
import concourse.bass as bass
from concourse import mybir

F32 = mybir.dt.float32
F32R = mybir.dt.float32r
I32 = mybir.dt.int32
ACT = mybir.ActivationFunctionType
ALU = mybir.AluOpType
AX = mybir.AxisListType

P = 128
D = 1024
KT = D // P
NPR = 256
NB = 8
LS = 8
NT = NPR + NB * LS
NSEQ = 1 + NB
DFF = 2816
FT = DFF // P
PAST = 1024
PAGE = 128
NPG = PAST // PAGE
NPOOL = NB * NPG * 5 // 4
WIN = 512
RING = 4


def ffn_plan(n_ada):
    if n_ada:
        pairs = IN_SLOTS // 2 * 2
        before = [("a", a) for a in range(min(4, n_ada - pairs))]
        b = len(before)
        body = [("h", 0), ("a", b), ("h", 1), ("a", b + 1)]
        rounds, left = pairs // 2, n_ada - pairs - b
        after = [("h", IN_SLOTS - 1)]
        for i in range(OUT_SLOTS):
            after.append(("o", i))
            if i < left:
                after.append(("a", b + pairs + i))
    else:
        before, rounds = [], IN_SLOTS // RING
        body = [("h", j) for j in range(RING)]
        after = [("h", j) for j in range(rounds * RING, IN_SLOTS)] + [("o", i) for i in range(OUT_SLOTS)]
    return before, body, rounds, after


SLOT = KT * 512
ADA_SLOTS = 9 * D // 512
ADA_FIRST = 3 * D // 512
IN_SLOTS = 2 * DFF // 512
OUT_GROUPS = (FT + KT - 1) // KT
OUT_SLOTS = 2 * OUT_GROUPS
EVEN_SLOTS = 6
ODD_SLOTS = 5
EPS = 1e-6
NEG = -1e30
SCALE = 64 ** -0.5
DIST_LO = -127
DIST_HI = PAST + LS - 1
NDIST = DIST_HI - DIST_LO + 1
NDIST_P = 255 - DIST_LO + 1
TILE_ROWS = [128, 128, 64]


def rep(ap, axis, n):
    dims = [list(x) for x in ap.ap]
    return bass.AP(ap.tensor, ap.offset, dims[:axis] + [[0, n]] + dims[axis:])


class Signal:

    def __init__(self, ctx, nc, name):
        self.sem = ctx.enter_context(nc.semaphore(name))
        self.base = 0
        self.count = 0

    def at(self, n):
        return self.base + n

    def by(self, ins, n=1):
        ins.then_inc(self.sem, n)
        return ins

    def close(self, n):
        self.base = self.base + n


def build(nc, io):
    ctx = ExitStack()
    with ctx:
        def sb(name, shape, dt=F32, where=ctx):
            return where.enter_context(nc.sbuf_tensor("sb_" + name, shape, dt))

        def signal(name):
            return Signal(ctx, nc, name)

        PS = ctx.enter_context(nc.psum_tensor("PS", [P, 8, 512], F32))
        X = sb("X", [P, KT, NT])
        H = sb("H", [P, KT, NT])
        ring = sb("ring", [P, RING, KT, 512])
        silu_c = sb("silu_c", [P, KT, NSEQ])
        mods = [sb(f"mod{i}", [P, 9, KT, NSEQ]) for i in range(2)]
        gains = [sb(f"gain{i}", [P, 3, KT, NSEQ]) for i in range(2)]
        silu_c32 = sb("silu_c32", [P, KT, 32])
        ada_rows = sb("ada_rows", [P, P])
        norm_g = sb("norm_g", [P, 2, 3, KT])
        ada_b = sb("ada_b", [P, 2, 9 * KT])
        rstd = sb("rstd", [P, NT])
        ones = sb("ones", [P, P])
        ident = sb("ident", [P, P])
        eps = sb("eps", [P, 1])
        halves = sb("halves", [P, P])
        later = sb("later", [P, P])
        strict = sb("strict", [P, P])

        ada_done = signal("ada_done")
        ada_out = signal("ada_out")
        ada_turned = signal("ada_turned")
        ada_read = signal("ada_read")
        unit_done = signal("unit_done")
        gated = signal("gated")
        high_done = signal("high_done")
        low_done = signal("low_done")
        g_high = signal("g_high")
        g_low = signal("g_low")
        pair_read = signal("pair_read")
        landed = [signal(f"landed{r}") for r in range(RING)]
        slot_done = signal("slot_done")
        slot_read = signal("slot_read")
        loads = signal("loads")
        pool_step = signal("pool_step")
        dve_step = signal("dve_step")
        act_step = signal("act_step")
        squared = signal("squared")
        summed = signal("summed")
        tiles_summed = signal("tiles_summed")
        h_whole = signal("h_whole")
        variance = signal("variance")
        deviation = signal("deviation")
        centred = signal("centred")
        samples_ready = signal("samples_ready")
        h_ready = signal("h_ready")
        h_low = signal("h_low")
        gate_ready = signal("gate_ready")
        stored = signal("stored")

        NSLOT = io["w_slots"].shape[0]

        def slot_at(n0, it, j):
            return (n0 + j) % RING, 16 * ((n0 + j) // RING + 1) + it * 16

        def refill(sp, n0, it, j):
            sp.wait_ge(slot_done.sem, slot_done.at(j + 1) + it * RING)
            fetch(sp, n0, it, j)

        def fetch(sp, n0, it, j):
            r, _ = slot_at(n0, 0, j)
            n = n0 + j + RING + it * RING
            src = io["w_slots"][n] if isinstance(n, int) else io["w_slots"][bass.ds(n, 1), :, :].rearrange("a p n -> p (a n)")
            sp.dma_start(ring[:, r, :, :].rearrange("p k n -> p (k n)"), src).then_inc(landed[r].sem, 16)

        def refill_all(sp, n0, count):
            for j in range(count):
                if n0 + j + RING < NSLOT:
                    refill(sp, n0, 0, j)

        class Chain:

            def __init__(self, eng, sig):
                self.eng, self.sig, self.n, self.start = eng, sig, 0, 0

            def __call__(self, ins):
                ins.then_inc(self.sig.sem, 1)
                self.n += 1
                self.eng.wait_ge(self.sig.sem, self.sig.at(self.n + self.start))

            def loop(self, it, per):
                self.start = self.n + it * per
                self.n, self.before, self.per = 0, self.n, per

            def done(self, times):
                assert self.n == self.per, (self.n, self.per)
                self.n, self.start = self.before + times * self.per, 0

        with nc.Block(no_gpsimd_drain=True) as block:
            @block.sync
            def _(sp):
                for dst, src in ((silu_c, "cT"), (X, "xT"), (norm_g, "norm_gT"), (ada_b, "ada_bT")):
                    sp.dma_start(dst[:], io[src]).then_inc(loads.sem, 16)
                for n in range(RING):
                    sp.dma_start(ring[:, n, :, :].rearrange("p k n -> p (k n)"), io["w_slots"][n])\
                        .then_inc(landed[n].sem, 16)

            @block.scalar
            def _(act):
                act.wait_ge(loads.sem, 64)
                act.wait_ge(pool_step.sem, 1)
                nc.scalar.activation(silu_c32[:, :, 0:NSEQ], silu_c[:], ACT.Silu).then_inc(act_step.sem, 1)

            @block.gpsimd
            def _(pool):
                step = Chain(pool, pool_step)
                step(pool.memset(silu_c32[:], 0.0))
                pool.memset(ones[:], 1.0)
                pool.memset(eps[:], EPS)
                pool.memset(ident[:], 0.0)
                pool.memset(later[:], 1.0)
                step(pool.memset(strict[:], 1.0))
                pool.memset(halves[:], 0.0)
                step(pool.affine_select(out=ident[:], in_=ident[:], compare_op=ALU.not_equal, fill=1.0,
                                        base=0, pattern=[[-1, P]], channel_multiplier=1))
                step(pool.affine_select(out=later[:], in_=later[:], compare_op=ALU.is_ge, fill=0.0,
                                        base=0, pattern=[[-1, P]], channel_multiplier=1))
                step(pool.affine_select(out=strict[:], in_=strict[:], compare_op=ALU.is_gt, fill=0.0,
                                        base=0, pattern=[[1, P]], channel_multiplier=-1))
                step(pool.memset(halves[0:64, 0:64], 1.0))
                step(pool.memset(halves[64:128, 64:128], 1.0))
                pool_step.count = step.n
        loads.close(64)
        act_step.close(1)
        pool_step.close(pool_step.count)

        def ada_turn(pe, a):
            pe.wait_ge(ada_out.sem, ada_out.at(a + 1))
            if a:
                pe.wait_ge(ada_read.sem, ada_read.at(a))
            nc.tensor.transpose(PS[:, 5, 0:P], ada_rows[:], ident[:]).then_inc(ada_turned.sem, 1)

        def ada_products(pe, n0, it, j, a):
            r, there = slot_at(n0, it, j)
            if not isinstance(it, int) or a > 0:
                step = 0 if isinstance(it, int) else 2 * it
                pe.wait_ge(ada_out.sem, ada_out.at(a) + step)
                if not isinstance(it, int) or a > 1:
                    pe.wait_ge(ada_read.sem, ada_read.at(a - 1) + step)
                nc.tensor.transpose(PS[:, 5, 0:P], ada_rows[:], ident[:]).then_inc(ada_turned.sem, 1)
            pe.wait_ge(landed[r].sem, there)
            for k in range(KT):
                for m in range(4):
                    mm = nc.tensor.matmul(PS[32 * m:32 * m + 32, 4, 0:P], silu_c32[:, k, :],
                                          ring[:, r, k, m * P:(m + 1) * P], start=(k == 0), stop=(k == KT - 1))
            mm.then_inc(ada_done.sem, 1)

        def ada_copy(act, a):
            act.wait_ge(ada_done.sem, ada_done.at(a + 1))
            nc.scalar.activation(ada_rows[:], PS[:, 4, 0:P], ACT.Copy).then_inc(ada_out.sem, 1)

        def ada_store(dve, layer, a, c):
            dve.wait_ge(ada_turned.sem, ada_turned.at(a + 1))
            flat = mods[layer][:].rearrange("p i k s -> p (i k) s")
            src = PS[:, 5, 0:P].rearrange("p (m s) -> p m s", s=32)[:, :, 0:NSEQ]
            bias = ada_b[:, layer, 4 * c:4 * c + 4]
            bias = bass.AP(bias.tensor, bias.offset, [list(x) for x in bias.ap] + [[0, NSEQ]])
            nc.vector.tensor_tensor(flat[:, 4 * c:4 * c + 4, :], src, bias, ALU.add).then_inc(ada_read.sem, 1)

        def ada_finish(dve, layer, norms, step):
            mod, gain = mods[layer], gains[layer]
            for i in norms:
                g = norm_g[:, layer, i, :]
                g = bass.AP(g.tensor, g.offset, [list(x) for x in g.ap] + [[0, NSEQ]])
                step(nc.vector.scalar_tensor_tensor(out=gain[:, i, :, :], in0=mod[:, 3 * i + 1, :, :], scalar=1.0,
                                                    in1=g, op0=ALU.add, op1=ALU.mult))
                if i != 1:
                    step(nc.vector.tensor_scalar(mod[:, 3 * i + 2, :, :], mod[:, 3 * i + 2, :, :], 0.5, None, ALU.mult))

        def ada_close(n):
            for s in (ada_done, ada_out, ada_turned, ada_read):
                s.close(n)

        def first_ada_stage(n0):
            with nc.Block(no_gpsimd_drain=True) as block:
                @block.sync
                def _(sp):
                    for a in range(ADA_FIRST):
                        sp.wait_ge(ada_done.sem, ada_done.at(a + 1))
                        fetch(sp, n0, 0, a)

                @block.tensor
                def _(pe):
                    for a in range(ADA_FIRST):
                        ada_products(pe, n0, 0, a, a)
                    ada_turn(pe, ADA_FIRST - 1)

                @block.scalar
                def _(act):
                    for a in range(ADA_FIRST):
                        ada_copy(act, a)

                @block.vector
                def _(dve):
                    step = Chain(dve, dve_step)
                    for a in range(ADA_FIRST):
                        ada_store(dve, 0, a, a)
                    dve.wait_ge(ada_read.sem, ada_read.at(ADA_FIRST))
                    ada_finish(dve, 0, [0], step)
                    dve_step.count = step.n
            ada_close(ADA_FIRST)
            dve_step.close(dve_step.count)
            return n0 + ADA_FIRST

        NORM_BANK = 7
        SQUARES = 4

        def squares(act):
            for c in range(SQUARES):
                nc.scalar.activation(H[:, 2 * c:2 * c + 2, :], X[:, 2 * c:2 * c + 2, :], ACT.Square)\
                    .then_inc(squared.sem, 1)

        def sum_squares(dve):
            dve.wait_ge(squared.sem, squared.at(1))
            for c in range(1, SQUARES):
                dve.wait_ge(squared.sem, squared.at(c + 1))
                nc.vector.tensor_tensor(H[:, 0:2, :], H[:, 0:2, :], H[:, 2 * c:2 * c + 2, :], ALU.add)\
                    .then_inc(tiles_summed.sem, 1)
                dve.wait_ge(tiles_summed.sem, tiles_summed.at(c))

        def norm_pe(pe):
            pe.wait_ge(tiles_summed.sem, tiles_summed.at(SQUARES - 1))
            for k in range(2):
                mm = nc.tensor.matmul(PS[:, NORM_BANK, 0:NT], ones[:], H[:, k, :], start=(k == 0), stop=(k == 1))
            mm.then_inc(summed.sem, 1)

        def norm_deviation(act):
            act.wait_ge(summed.sem, summed.at(1))
            nc.scalar.activation(rstd[:], PS[:, NORM_BANK, 0:NT], ACT.Ln, scale=1.0 / D, bias=eps[:, 0:1])\
                .then_inc(variance.sem, 1)
            act.wait_ge(variance.sem, variance.at(1))
            nc.scalar.activation(rstd[:], rstd[:], ACT.Exp, scale=-0.5).then_inc(deviation.sem, 1)

        def norm_dve(dve, layer, i, step):
            dve.wait_ge(deviation.sem, deviation.at(1))
            part = H[:, :, NPR:NT]
            step(nc.vector.tensor_tensor(part, X[:, :, NPR:NT], rep(rstd[:, NPR:NT], 1, KT), ALU.mult))
            part = part.rearrange("p k (b l) -> p k b l", l=LS)

            def per_seq(t, n):
                a = t[:, n, :, 1:NSEQ]
                return bass.AP(a.tensor, a.offset, [list(x) for x in a.ap] + [[0, LS]])
            step(nc.vector.tensor_tensor(part, part, per_seq(gains[layer], i), ALU.mult))
            nc.vector.tensor_tensor(part, part, per_seq(mods[layer], 3 * i), ALU.add).then_inc(samples_ready.sem, 1)
            for k in range(KT):
                nc.vector.scalar_tensor_tensor(out=H[:, k, 0:NPR], in0=X[:, k, 0:NPR],
                                               scalar=gains[layer][:, i, k, 0:1], in1=rstd[:, 0:NPR],
                                               op0=ALU.mult, op1=ALU.mult).then_inc(centred.sem, 1)

        def high_act(act, layer, i, Hs):
            act.wait_ge(samples_ready.sem, samples_ready.at(1))
            nc.scalar.activation(Hs[0][:, :, NPR:NT], H[:, :, NPR:NT], ACT.Copy)
            for k in range(KT):
                act.wait_ge(centred.sem, centred.at(k + 1))
                nc.scalar.activation(Hs[0][:, k, 0:NPR], H[:, k, 0:NPR], ACT.Identity,
                                     bias=mods[layer][:, 3 * i, k, 0:1]).then_inc(h_ready.sem, 1)

        def low_dve(dve, layer, i, Hs):
            dve.wait_ge(h_ready.sem, h_ready.at(1))
            nc.vector.tensor_tensor(Hs[1][:, :, NPR:NT], H[:, :, NPR:NT], Hs[0][:, :, NPR:NT], ALU.subtract)
            for k in range(KT):
                dve.wait_ge(h_ready.sem, h_ready.at(k + 1))
                nc.vector.scalar_tensor_tensor(out=Hs[1][:, k, 0:NPR], in0=H[:, k, 0:NPR],
                                               scalar=mods[layer][:, 3 * i, k, 0:1], in1=Hs[0][:, k, 0:NPR],
                                               op0=ALU.add, op1=ALU.subtract).then_inc(h_low.sem, 1)

        def norm_close():
            squared.close(SQUARES)
            tiles_summed.close(SQUARES - 1)
            for s in (summed, variance, deviation, samples_ready):
                s.close(1)
            for s in (centred, h_ready, h_low):
                s.close(KT)

        def piece_high(act, Ws, b, columns):
            nc.scalar.activation(Ws[0][:, b], columns, ACT.Copy).then_inc(high_done.sem, 1)

        def piece_low(dve, Ws, b, columns):
            nc.vector.tensor_tensor(Ws[1][:, b], columns, Ws[0][:, b], ALU.subtract).then_inc(low_done.sem, 1)

        gated_rows = sb("gated_rows", [P, 2, 2, NT - NPR])

        def add_gated(dve, step, layer, i, pair, banks):
            mod, m0 = mods[layer], 2 * pair
            for m in range(2):
                nc.vector.scalar_tensor_tensor(out=X[:, m0 + m, 0:NPR], in0=PS[:, banks + m, 0:NPR],
                                               scalar=mod[:, i, m0 + m, 0:1], in1=X[:, m0 + m, 0:NPR],
                                               op0=ALU.mult, op1=ALU.add).then_inc(gate_ready.sem, 1)
            src = PS[:, banks:banks + 2, NPR:NT].rearrange("p m (b l) -> p m b l", l=LS)
            gate = mod[:, i, m0:m0 + 2, 1:NSEQ]
            gate = bass.AP(gate.tensor, gate.offset, [list(x) for x in gate.ap] + [[0, LS]])
            rows = gated_rows[:, pair % 2, :, :]
            if pair >= 2:
                dve.wait_ge(gate_ready.sem, gate_ready.at(3 * pair - 3))
            nc.vector.tensor_tensor(rows.rearrange("p m (b l) -> p m b l", l=LS), src, gate, ALU.mult)\
                .then_inc(pair_read.sem, 1)
            dve.wait_ge(pair_read.sem, pair_read.at(pair + 1))
            part = X[:, m0:m0 + 2, NPR:NT]
            nc.vector.tensor_tensor(part, part, rows, ALU.add).then_inc(gate_ready.sem, 1)

        def ffn_stage(layer, which, n0, ada_layer=0, ada_from=0, n_ada=0):
            ni = 2 * which
            before, body, rounds, after = ffn_plan(n_ada)
            n1 = n0 + len(before)
            n2 = n1 + rounds * RING
            per_h = sum(kind == "h" for kind, _ in body)
            UNITS = 2 * IN_SLOTS
            PIECES = UNITS + 2 * OUT_SLOTS
            OUT_BANKS = [0, 2, 6, 0]

            slots = before + [(kind, k + it * (per_h if kind == "h" else 2)) for it in range(rounds)
                              for kind, k in body] + after
            pieces = [(at, kind, k, m) for at, (kind, k) in enumerate(slots) if kind != "a" for m in range(2)]

            def columns(piece):
                at, kind, _, m = piece
                w = ring[:, (n0 + at) % RING, :, :]
                if kind == "h":
                    return w.rearrange("p k (i c) -> p k i c", i=2)[:, :, :, m * P:(m + 1) * P]
                return w[:, :, 2 * P * m:2 * P * m + 2 * P].rearrange("p k (i c) -> p k i c", i=2)

            with ExitStack() as stage:
                Gs = [sb(f"G{part}{layer}{which}", [P, FT, NT], F32R, stage) for part in ("high", "low")]
                Hs = [sb(f"H{part}{layer}{which}", [P, KT, NT], F32R, stage) for part in ("high", "low")]
                Ws = [sb(f"W{part}{layer}{which}", [P, 2, KT, 2, P], F32R, stage) for part in ("high", "low")]
                S = sb(f"S{layer}{which}", [P, 2, NT], F32, stage)
                block = stage.enter_context(nc.Block(no_gpsimd_drain=True))

                @block.sync
                def _(sp):
                    def one(n, it, j, kind, k):
                        sig, at, per = {"h": (low_done, 2 * k + 2, 2 * per_h), "a": (ada_done, k + 1, 2),
                                        "o": (low_done, UNITS + 2 * k + 2, 0)}[kind]
                        sp.wait_ge(sig.sem, sig.at(at) + it * per)
                        fetch(sp, n, it, j)
                    for j, (kind, k) in enumerate(before):
                        one(n0, 0, j, kind, k)
                    with sp.Fori(0, rounds) as it:
                        for j, (kind, k) in enumerate(body):
                            one(n1, it, j, kind, k)
                    for j, (kind, k) in enumerate(after):
                        if n2 + j + RING < NSLOT:
                            one(n2, 0, j, kind, k)

                @block.tensor
                def _(pe):
                    def product(to, b, i, ins, tiles, first, last, wait=None):
                        for a, (w, x) in enumerate(((0, 0), (0, 1), (1, 0))):
                            for q in tiles:
                                if wait is not None:
                                    wait(a, q)
                                mm = nc.tensor.matmul(to, Ws[w][:, b, q % KT, i, :], ins[x][:, q, :],
                                                      start=(first and a == 0 and q == tiles[0]),
                                                      stop=(last and a == 2 and q == tiles[-1]))
                        return mm

                    def input_wait(a, q):
                        if a == 0:
                            pe.wait_ge(h_ready.sem, h_ready.at(q + 1))
                        elif a == 1:
                            pe.wait_ge(h_low.sem, h_low.at(q + 1))

                    def hidden(it, k, first):
                        for m in range(2):
                            pe.wait_ge(low_done.sem, low_done.at(2 * k + m + 1) + it * (2 * per_h))
                            if not first:
                                pe.wait_ge(gated.sem, gated.at(2 * k + m - 1) + it * (2 * per_h))
                            for part in range(2):
                                mm = product(PS[:, 2 * m + part, 0:NT], m, part, Hs, range(KT), True, True,
                                             input_wait if first and m == part == 0 else None)
                            mm.then_inc(unit_done.sem, 1)

                    def output(i):
                        half, g = i // OUT_GROUPS, i % OUT_GROUPS
                        for j in range(2):
                            pe.wait_ge(low_done.sem, low_done.at(UNITS + 2 * i + j + 1))
                            if half == g == 0:
                                pe.wait_ge(gated.sem, gated.at(UNITS - 1 + j))
                            if half == j == 0:
                                pe.wait_ge(g_low.sem, g_low.at(min(KT * (g + 1), FT)))
                            if half and g == 0 and j == 1:
                                pe.wait_ge(pair_read.sem, pair_read.at(1))
                            for m in range(2):
                                mm = product(PS[:, OUT_BANKS[2 * half + j] + m, 0:NT], j, m, Gs,
                                             range(KT * g, min(KT * (g + 1), FT)), g == 0, g == OUT_GROUPS - 1)
                            mm.then_inc(unit_done.sem, 1)

                    norm_pe(pe)
                    for j, (_, a) in enumerate(before):
                        ada_products(pe, n0, 0, j, a)

                    def round_of(it, first):
                        for j, (kind, k) in enumerate(body):
                            if kind == "h":
                                hidden(it, k, first and k == 0)
                            else:
                                ada_products(pe, n1, it, j, k)
                    round_of(0, True)
                    with pe.Fori(1, rounds) as it:
                        round_of(it, False)
                    for j, (kind, k) in enumerate(after):
                        if kind == "h":
                            hidden(0, k, False)
                        elif kind == "a":
                            ada_products(pe, n2, 0, j, k)
                        else:
                            output(k)
                    if n_ada:
                        ada_turn(pe, n_ada - 1)

                @block.scalar
                def _(act):
                    def high(p):
                        if p >= len(pieces):
                            return
                        at = n0 + pieces[p][0]
                        act.wait_ge(landed[at % RING].sem, 16 * (at // RING + 1))
                        if p >= 2:
                            act.wait_ge(unit_done.sem, unit_done.at(p - 1))
                        piece_high(act, Ws, p % 2, columns(pieces[p]))
                    squares(act)
                    if not before:
                        high(0)
                    norm_deviation(act)
                    for _, a in before[:2]:
                        ada_copy(act, a)
                    high_act(act, layer, ni, Hs)
                    for _, a in before[2:]:
                        ada_copy(act, a)
                    if before:
                        high(0)
                    high(1)
                    p = 0
                    for kind, k in slots[len(before):]:
                        if kind == "a":
                            ada_copy(act, k)
                            continue
                        for m in range(2):
                            if kind == "h":
                                act.wait_ge(unit_done.sem, unit_done.at(p + 1))
                                if p >= 2:
                                    act.wait_ge(g_low.sem, g_low.at(p - 1))
                                nc.scalar.activation(S[:, p % 2, :], PS[:, 2 * (p % 2), 0:NT], ACT.Silu)\
                                    .then_inc(act_step.sem, 1)
                            high(p + 2)
                            if kind == "h":
                                act.wait_ge(gated.sem, gated.at(p + 1))
                                nc.scalar.activation(Gs[0][:, p, :], S[:, p % 2, :], ACT.Copy)\
                                    .then_inc(g_high.sem, 1)
                            p += 1

                @block.vector
                def _(dve):
                    step = Chain(dve, dve_step)
                    done = 0

                    def low(p):
                        if p >= len(pieces):
                            return
                        dve.wait_ge(high_done.sem, high_done.at(p + 1))
                        piece_low(dve, Ws, p % 2, columns(pieces[p]))

                    def stores(upto):
                        for a in range(done, upto):
                            ada_store(dve, ada_layer, a, ada_from + a)
                        return max(done, upto)
                    sum_squares(dve)
                    if not before:
                        low(0)
                    norm_dve(dve, layer, ni, step)
                    done = stores(min(1, len(before) - 1))
                    low_dve(dve, layer, ni, Hs)
                    done = stores(len(before) - 1)
                    if before:
                        low(0)
                    low(1)
                    p = 0
                    for kind, k in slots[len(before):]:
                        if kind == "a":
                            done = stores(k)
                            continue
                        for m in range(2):
                            if kind == "h":
                                dve.wait_ge(act_step.sem, act_step.at(p + 1))
                                nc.vector.tensor_tensor(S[:, p % 2, :], S[:, p % 2, :],
                                                        PS[:, 2 * (p % 2) + 1, 0:NT], ALU.mult)\
                                    .then_inc(gated.sem, 1)
                            low(p + 2)
                            if kind == "h":
                                dve.wait_ge(g_high.sem, g_high.at(p + 1))
                                nc.vector.tensor_tensor(Gs[1][:, p, :], S[:, p % 2, :], Gs[0][:, p, :],
                                                        ALU.subtract).then_inc(g_low.sem, 1)
                            elif k % OUT_GROUPS == OUT_GROUPS - 1:
                                pair = 2 * (k // OUT_GROUPS) + m
                                dve.wait_ge(unit_done.sem, unit_done.at(p + 1))
                                add_gated(dve, step, layer, 3 * ni + 2, pair, OUT_BANKS[pair])
                            p += 1
                    done = stores(n_ada)
                    if n_ada:
                        dve.wait_ge(ada_read.sem, ada_read.at(n_ada))
                        ada_finish(dve, ada_layer, [1, 2] if ada_from else [0, 1, 2], step)
                    dve_step.count = step.n
            norm_close()
            ada_close(n_ada)
            for s in (act_step, gated, g_high, g_low):
                s.close(UNITS)
            for s in (unit_done, high_done, low_done):
                s.close(PIECES)
            pair_read.close(4)
            gate_ready.close(12)
            dve_step.close(dve_step.count)
            return n2 + len(after)

        def out_stage(layer, n0, OT):
            with nc.Block(no_gpsimd_drain=True) as block:
                @block.sync
                def _(sp):
                    refill_all(sp, n0, 2)
                    sp.wait_ge(stored.sem, stored.at(0))

                @block.tensor
                def _(pe):
                    for half in range(2):
                        r, there = slot_at(n0, 0, half)
                        pe.wait_ge(landed[r].sem, there)
                        for m in range(4):
                            for k in range(KT):
                                mm = nc.tensor.matmul(PS[:, 4 * half + m, 0:NT], ring[:, r, k, m * P:(m + 1) * P],
                                                      OT[:, k, :], start=(k == 0), stop=(k == KT - 1))
                        mm.then_inc(slot_done.sem, 1)

                @block.vector
                def _(dve):
                    step = Chain(dve, dve_step)
                    for half in range(2):
                        dve.wait_ge(slot_done.sem, slot_done.at(half + 1))
                        for pair in (2 * half, 2 * half + 1):
                            add_gated(dve, step, layer, 5, pair, 2 * pair)
                    dve_step.count = step.n
            slot_done.close(2)
            pair_read.close(4)
            dve_step.close(dve_step.count)
            gate_ready.close(12)
            return n0 + 2

        def project_stage(layer, n0, kinds, tail_w, tail_cols, tail_dst, tail_rows):
            n = len(kinds)
            PIECES = 2 * n
            with ExitStack() as stage:
                Hs = [sb(f"PH{part}{layer}", [P, KT, 3 * P], F32R, stage) for part in ("high", "low")]
                Ws = [sb(f"PW{part}{layer}", [P, 2, KT, 2, P], F32R, stage) for part in ("high", "low")]
                block = stage.enter_context(nc.Block(no_gpsimd_drain=True))

                def columns(p):
                    w = ring[:, (n0 + p // 2) % RING, :, :]
                    return w[:, :, 2 * P * (p % 2):2 * P * (p % 2 + 1)].rearrange("p k (i c) -> p k i c", i=2)

                @block.sync
                def _(sp):
                    for j in range(n):
                        if n0 + j + RING < NSLOT:
                            sp.wait_ge(low_done.sem, low_done.at(2 * j + 2))
                            fetch(sp, n0, 0, j)

                @block.gpsimd
                def _(pool):
                    for part in range(2):
                        pool.memset(Hs[part][:, :, NT:3 * P].bitcast(F32), 0.0).then_inc(pool_step.sem, 1)

                @block.tensor
                def _(pe):
                    def passes(to, stationary, moving, wait=None):
                        for a, (w, x) in enumerate(((0, 0), (0, 1), (1, 0))):
                            for k in range(KT):
                                if wait is not None:
                                    wait(a, k)
                                mm = nc.tensor.matmul(to, stationary(w, x, k), moving(w, x, k),
                                                      start=(a == k == 0), stop=(a == 2 and k == KT - 1))
                        return mm

                    def input_wait(a, k):
                        if a == 0:
                            pe.wait_ge(h_ready.sem, h_ready.at(k + 1))
                        elif a == 1:
                            pe.wait_ge(h_low.sem, h_low.at(k + 1))
                    norm_pe(pe)
                    pe.wait_ge(pool_step.sem, pool_step.at(2))
                    for p in range(PIECES):
                        j, half = p // 2, p % 2
                        pe.wait_ge(low_done.sem, low_done.at(p + 1))
                        if j >= 2 and half == 0:
                            pe.wait_ge(slot_read.sem, slot_read.at(j - 1))
                        b = 4 * (j % 2)
                        if kinds[j][0]:
                            for m in range(2):
                                mm = passes(PS[:, b + 2 * half + m, 0:NT],
                                            lambda w, x, k: Ws[w][:, half, k, m, :],
                                            lambda w, x, k: Hs[x][:, k, 0:NT], input_wait if p == m == 0 else None)
                        else:
                            for t in range(3):
                                mm = passes(PS[:, b + t, 256 * half:256 * half + 256],
                                            lambda w, x, k: Hs[x][:, k, t * P:(t + 1) * P],
                                            lambda w, x, k: Ws[w][:, half, k, :, :])
                        mm.then_inc(unit_done.sem, 1)
                    pe.wait_ge(slot_read.sem, slot_read.at(n - 1))
                    pe.wait_ge(h_whole.sem, h_whole.at(1))
                    b = 4 * (n % 2)
                    if tail_rows:
                        for t, rows in enumerate(TILE_ROWS):
                            for k in range(KT):
                                mm = nc.tensor.matmul(PS[0:rows, b + t, 0:tail_cols], H[:, k, t * P:t * P + rows],
                                                      tail_w[:, k, :], start=(k == 0), stop=(k == KT - 1))
                    else:
                        for k in range(KT):
                            mm = nc.tensor.matmul(PS[0:tail_cols, b, 0:NT], tail_w[:, k, :], H[:, k, :],
                                                  start=(k == 0), stop=(k == KT - 1))
                    mm.then_inc(summed.sem, 1)

                @block.scalar
                def _(act):
                    def high(p):
                        if p >= PIECES:
                            return
                        at = n0 + p // 2
                        act.wait_ge(landed[at % RING].sem, 16 * (at // RING + 1))
                        if p >= 2:
                            act.wait_ge(unit_done.sem, unit_done.at(p - 1))
                        piece_high(act, Ws, p % 2, columns(p))
                    squares(act)
                    high(0)
                    norm_deviation(act)
                    high_act(act, layer, 1, Hs)
                    high(1)
                    act.wait_ge(h_low.sem, h_low.at(KT))
                    for k in range(KT):
                        last = nc.scalar.activation(H[:, k, 0:NPR], H[:, k, 0:NPR], ACT.Identity,
                                                    bias=mods[layer][:, 3, k, 0:1])
                    last.then_inc(h_whole.sem, 1)
                    for j, (transposed, dst) in enumerate(kinds):
                        high(2 * j + 2)
                        high(2 * j + 3)
                        act.wait_ge(unit_done.sem, unit_done.at(2 * j + 2))
                        b = 4 * (j % 2)
                        if transposed:
                            nc.scalar.activation(dst, PS[:, b:b + 4, 0:NT], ACT.Copy).then_inc(slot_read.sem, 1)
                        else:
                            nc.scalar.activation(dst[:, 0:2, :], PS[:, b:b + 2, :], ACT.Copy)
                            nc.scalar.activation(dst[0:64, 2, :], PS[0:64, b + 2, :], ACT.Copy)\
                                .then_inc(slot_read.sem, 1)
                    act.wait_ge(summed.sem, summed.at(2))
                    b = 4 * (n % 2)
                    if tail_rows:
                        nc.scalar.activation(tail_dst[:, 0:2, :], PS[:, b:b + 2, 0:tail_cols], ACT.Copy)\
                            .then_inc(act_step.sem, 1)
                        nc.scalar.activation(tail_dst[0:64, 2, :], PS[0:64, b + 2, 0:tail_cols], ACT.Copy)\
                            .then_inc(act_step.sem, 1)
                    else:
                        nc.scalar.activation(tail_dst[:, :], PS[0:tail_cols, b, 0:NT], ACT.Copy)\
                            .then_inc(act_step.sem, 2)

                @block.vector
                def _(dve):
                    step = Chain(dve, dve_step)

                    def low(p):
                        dve.wait_ge(high_done.sem, high_done.at(p + 1))
                        piece_low(dve, Ws, p % 2, columns(p))
                    sum_squares(dve)
                    low(0)
                    norm_dve(dve, layer, 1, step)
                    low_dve(dve, layer, 1, Hs)
                    for p in range(1, PIECES):
                        low(p)
                    dve_step.count = step.n
            norm_close()
            summed.close(1)
            h_whole.close(1)
            act_step.close(2)
            pool_step.close(2)
            slot_read.close(n)
            for s in (unit_done, high_done, low_done):
                s.close(PIECES)
            dve_step.close(dve_step.count)
            return n0 + n

        def store(sp, dst, src):
            sp.dma_start(dst, src).then_inc(stored.sem, 16)

        logit_ready = signal("logit_ready")
        keep_ready = signal("keep_ready")
        tail_ready = signal("tail_ready")
        weight_ready = signal("weight_ready")
        out_ready = signal("out_ready")
        out_read = signal("out_read")
        page_in = [signal("page_in0"), signal("page_in1")]
        value_in = [signal("value_in0"), signal("value_in1")]
        seq_ready = signal("seq_ready")
        scaled = signal("scaled")
        logged = signal("logged")
        exponent = signal("exponent")
        state_in = signal("state_in")
        expanded = signal("expanded")

        def even_stage(n0):
            stage = ExitStack()
            with stage:
                def tile(name, shape):
                    return sb(name, shape, F32, stage)

                OT = tile("OT0", [P, KT, NT])
                qkT = tile("qkT", [P, 4, NT])
                vb = tile("vb", [P, 3, 512])
                rT = tile("rT", [P, 4, NT])
                a1T = tile("a1T", [16, NT])
                with ExitStack() as heads:
                    QT = sb("QT", [P, 4, NT], F32, heads)
                    KTT = sb("KTT", [P, 4, NT], F32, heads)
                    V = sb("V", [P, 3, 512], F32, heads)
                    w_a1 = sb("w_a1", [P, KT, 16], F32, heads)
                    with nc.Block(no_gpsimd_drain=True) as block:
                        @block.sync
                        def _(sp):
                            sp.dma_start(w_a1[:], io["w_a1"]).then_inc(loads.sem, 16)
                            sp.wait_ge(loads.sem, loads.at(16))
                    loads.close(16)
                    n1 = project_stage(0, n0, [(True, QT[:]), (True, KTT[:]), (False, V), (True, qkT[:]), (False, vb),
                                            (True, rT[:])], w_a1, 16, a1T, False)
                    K = [sb(f"s_K{s}", [P, NPG, 4, P], F32, heads) for s in range(2)]
                    pages = sb("s_pages", [1, NB * NPG], I32, heads)
                    stick_prompt(QT, KTT, V, OT, K, pages)
                    stick_sample(QT, KTT, V, OT, K, pages)
                linear_attention(qkT, vb, rT, a1T, OT)
                return out_stage(0, n1, OT)

        def load_pages(eng, pages, g, s, to, src, sig, used=None):
            for p in range(NPG):
                at = (2 * g + s) * NPG + p
                cell = pages[0:1, at:at + 1] if isinstance(at, int) else pages[0:1, bass.ds(at, 1)]
                page = eng.value_load(cell, min_val=0, max_val=NPOOL - 1)
                if p == 0 and used is not None:
                    eng.wait_ge(*used)
                dst = to[s][:, p]
                if len(dst.shape) == 3:
                    dst = dst.rearrange("p a n -> p (a n)")
                eng.dma_start(dst, src[bass.ds(page, 1), :, :].rearrange("a p n -> p (a n)"))\
                    .then_inc(sig.sem, 16)

        def stick_prompt(QT, KTT, V, OT, K, pages):
            W = 384
            PAIRS = 4
            with ExitStack() as stage:
                def tile(name, shape):
                    return sb(name, shape, F32, stage)
                sp1 = tile("p_sp1", [P, 2, 2, W])
                sp2 = tile("p_sp2", [P, 2, 2, W])
                u = tile("p_u", [P, 3, 2, W])
                mask = tile("p_mask", [P, W])
                fill = tile("p_fill", [P, W])
                block = stage.enter_context(nc.Block(no_gpsimd_drain=True))

                @block.sync
                def _(sp):
                    store(sp, io["o_sbk"], KTT[:])
                    store(sp, io["o_sbv"][0:NPR, :].rearrange("(t p) n -> p t n", p=P), V[:, 0:2, :])
                    store(sp, io["o_sbv"][NPR:NT, :], V[0:64, 2, :])
                    sp.dma_start(io["new_rows"][0], V[0:64, 2, :]).then_inc(loads.sem, 16)
                    sp.dma_start(pages[:], io["pages"]).then_inc(loads.sem, 16)
                    sp.wait_ge(loads.sem, loads.at(32))
                    load_pages(sp, pages, 0, 0, K, io["sb_kT"], page_in[0])

                def region(kt):
                    return (0, 256, 0) if kt == 0 else (256, W, 128)

                @block.tensor
                def _(pe):
                    def logits(a):
                        if a >= 2:
                            pe.wait_ge(scaled.sem, scaled.at(a - 1))
                        for hh in range(2):
                            for kt in range(2):
                                c0, c1, q0 = region(kt)
                                mm = nc.tensor.matmul(PS[:, 2 * (a % 2) + hh, c0:c1],
                                                      KTT[64 * hh:64 * hh + 64, a, kt * P:(kt + 1) * P],
                                                      QT[64 * hh:64 * hh + 64, a, q0:NPR], start=True, stop=True)
                        mm.then_inc(logit_ready.sem, 1)

                    def tails(a):
                        pe.wait_ge(keep_ready.sem, keep_ready.at(a + 1))
                        if a >= 1:
                            pe.wait_ge(exponent.sem, exponent.at(a))
                        for hh in range(2):
                            nc.tensor.matmul(PS[:, 4 + hh, 0:W], later[:], sp2[:, a % 2, hh, :], start=True, stop=False)
                            mm = nc.tensor.matmul(PS[:, 4 + hh, 128:256], ones[:], sp2[:, a % 2, hh, 256:W],
                                                  start=False, stop=True)
                        mm.then_inc(tail_ready.sem, 1)

                    def values(a):
                        pe.wait_ge(weight_ready.sem, weight_ready.at(a + 1))
                        if a >= 2:
                            pe.wait_ge(out_read.sem, out_read.at(a - 1))
                        for hh in range(2):
                            for kt in range(2):
                                c0, c1, q0 = region(kt)
                                h = 2 * a + hh
                                mm = nc.tensor.matmul(PS[64 * hh:64 * hh + 64, 6 + a % 2, q0:NPR],
                                                      V[:, kt, 64 * h:64 * h + 64], u[:, a % 3, hh, c0:c1],
                                                      start=(kt == 0), stop=(kt == 1))
                        mm.then_inc(out_ready.sem, 1)
                    logits(0)
                    for a in range(PAIRS):
                        if a + 1 < PAIRS:
                            logits(a + 1)
                        tails(a)
                        values(a)

                @block.gpsimd
                def _(pool):
                    step = Chain(pool, pool_step)
                    step(pool.memset(mask[:], 1.0))
                    step(pool.memset(fill[:], 0.0))
                    for c0, c1, q0 in (region(0), region(1)):
                        for t, v in ((mask, 0.0), (fill, NEG)):
                            step(pool.affine_select(out=t[:, c0:c1], in_=t[:, c0:c1], compare_op=ALU.is_gt, fill=v,
                                                    base=0, pattern=[[1, c1 - c0]], channel_multiplier=-1))
                    pool_step.count = step.n
                    pool.wait_ge(loads.sem, loads.at(32))
                    load_pages(pool, pages, 0, 1, K, io["sb_kT"], value_in[0])

                @block.scalar
                def _(act):
                    step = Chain(act, act_step)

                    def softplus(a):
                        act.wait_ge(scaled.sem, scaled.at(a + 1))
                        if a >= 2:
                            act.wait_ge(keep_ready.sem, keep_ready.at(a - 1))
                        step(nc.scalar.activation(sp1[:, a % 2, :, :], u[:, a % 3, :, :], ACT.Abs))
                        step(nc.scalar.activation(sp1[:, a % 2, :, :], sp1[:, a % 2, :, :], ACT.Exp, scale=-1.0))
                        nc.scalar.activation(sp1[:, a % 2, :, :], sp1[:, a % 2, :, :], ACT.Ln, bias=1.0)\
                            .then_inc(logged.sem, 1)

                    def weights(a):
                        act.wait_ge(exponent.sem, exponent.at(a + 1))
                        nc.scalar.activation(u[:, a % 3, :, :], u[:, a % 3, :, :], ACT.Exp)\
                            .then_inc(weight_ready.sem, 1)
                    softplus(0)
                    for a in range(PAIRS):
                        if a + 1 < PAIRS:
                            softplus(a + 1)
                        weights(a)
                    act_step.count = step.n

                @block.vector
                def _(dve):
                    step = Chain(dve, dve_step)

                    def logits(a):
                        dve.wait_ge(logit_ready.sem, logit_ready.at(a + 1))
                        if a >= 3:
                            dve.wait_ge(out_ready.sem, out_ready.at(a - 2))
                        if a >= 2:
                            dve.wait_ge(tail_ready.sem, tail_ready.at(a - 1))
                        nc.vector.tensor_scalar(u[:, a % 3, :, :], PS[:, 2 * (a % 2):2 * (a % 2) + 2, 0:W], SCALE,
                                                None, ALU.mult).then_inc(scaled.sem, 1)
                        dve.wait_ge(scaled.sem, scaled.at(a + 1))
                        step(nc.vector.tensor_scalar(sp2[:, a % 2, :, :], u[:, a % 3, :, :], 0.0, None, ALU.max))

                    def keeps(a):
                        dve.wait_ge(logged.sem, logged.at(a + 1))
                        step(nc.vector.tensor_tensor(sp2[:, a % 2, :, :], sp2[:, a % 2, :, :], sp1[:, a % 2, :, :],
                                                     ALU.add))
                        nc.vector.tensor_tensor(sp2[:, a % 2, :, :], sp2[:, a % 2, :, :], rep(mask[:], 1, 2), ALU.mult)\
                            .then_inc(keep_ready.sem, 1)

                    def exponents(a):
                        dve.wait_ge(tail_ready.sem, tail_ready.at(a + 1))
                        step(nc.vector.tensor_tensor(u[:, a % 3, :, :], u[:, a % 3, :, :], PS[:, 4:6, 0:W],
                                                     ALU.subtract))
                        nc.vector.tensor_tensor(u[:, a % 3, :, :], u[:, a % 3, :, :], rep(fill[:], 1, 2), ALU.add)\
                            .then_inc(exponent.sem, 1)

                    def outs(a):
                        dve.wait_ge(out_ready.sem, out_ready.at(a + 1))
                        nc.vector.tensor_copy(OT[:, a, 0:NPR], PS[:, 6 + a % 2, 0:NPR]).then_inc(out_read.sem, 1)
                    dve.wait_ge(pool_step.sem, pool_step.at(6))
                    logits(0)
                    keeps(0)
                    for a in range(PAIRS):
                        if a + 1 < PAIRS:
                            logits(a + 1)
                        exponents(a)
                        if a + 1 < PAIRS:
                            keeps(a + 1)
                        if a >= 1:
                            outs(a - 1)
                    outs(PAIRS - 1)
                    dve_step.count = step.n
            pool_step.close(pool_step.count)
            act_step.close(act_step.count)
            dve_step.close(dve_step.count)
            for s in (logit_ready, keep_ready, tail_ready, weight_ready, out_ready, out_read, scaled, logged,
                      exponent):
                s.close(PAIRS)
            stored.close(48)
            loads.close(32)

        def stick_sample(QT, KTT, V, OT, K, pages):
            STEPS = NB // 2
            W = PAST + LS
            LOADED = 16 * NPG
            LOADED_V = LOADED + 16
            with ExitStack() as stage:
                def tile(name, shape):
                    return sb(name, shape, F32, stage)
                VV = [tile(f"s_V{s}", [P, NPG, 512]) for s in range(2)]
                VN = [V[0:LS, s, :] for s in range(2)]
                out_rows = tile("s_out", [P, 2, P])
                mask = tile("s_mask", [P, LS])
                fill = tile("s_fill", [P, LS])
                free = H[:].rearrange("p k n -> p (k n)")
                soft = free[:, 0:2 * W].rearrange("p (i n) -> p i n", i=2)
                QB = free[:, 2 * W:2 * W + 256].rearrange("p (s a r) -> p s a r", s=2, a=4)
                pT = OT[:, 4:8, :].rearrange("p k n -> p (k n)")[:, 0:(NPG + 1) * P]\
                    .rearrange("p (k r) -> p k r", r=P)
                KN = OT[:, 4:8, :].rearrange("p k n -> p (k n)")[:, (NPG + 1) * P:(NPG + 1) * P + 8 * LS]\
                    .rearrange("p (a k) -> p a k", a=4)
                of_query = pT[0:LS, 0, :]
                earlier = pT[0:LS, 1, 0:LS]
                BUILT = 4
                z = PS[:, 0:3, :].rearrange("p a n -> p (a n)")[:, 0:W]
                block = stage.enter_context(nc.Block(no_gpsimd_drain=True))

                def backwards(ap):
                    (step0, rows), (step1, n) = [list(x) for x in ap.ap]
                    return bass.AP(ap.tensor, ap.offset + step1 * (n - 1), [[step0, rows], [-step1, n]])

                def loads_of(eng, s, keys_in, values_in):
                    def new_values(g):
                        b = 2 * g + s
                        at = slice(LS * b, LS * b + LS) if isinstance(b, int) else bass.ds(b * LS, LS)
                        eng.dma_start(VN[s], io["new_rows"][0, at, :]).then_inc(values_in.sem, 16)
                    eng.wait_ge(stored.sem, stored.at(0))
                    load_pages(eng, pages, 0, s, VV, io["sb_v"], values_in)
                    new_values(0)
                    with eng.Fori(1, STEPS) as g:
                        load_pages(eng, pages, g, s, K, io["sb_kT"], keys_in, (logit_ready.sem, logit_ready.at(0) + g))
                        load_pages(eng, pages, g, s, VV, io["sb_v"], values_in, (out_ready.sem, out_ready.at(0) + g))
                        new_values(g)

                @block.sync
                def _(sp):
                    loads_of(sp, 0, page_in[0], page_in[1])

                @block.gpsimd
                def _(pool):
                    step = Chain(pool, pool_step)
                    step(pool.memset(QB, 0.0))
                    step(pool.memset(of_query, 0.0))
                    step(pool.affine_select(out=of_query, in_=of_query, compare_op=ALU.not_equal, fill=1.0, base=0,
                                            pattern=[[0, P // LS], [1, LS]], channel_multiplier=-1))
                    step(pool.tensor_tensor(earlier, later[0:LS, 0:LS], ident[0:LS, 0:LS], ALU.subtract))
                    assert step.n == BUILT
                    pool_step.count = step.n

                    loads_of(pool, 1, value_in[0], value_in[1])

                @block.tensor
                def _(pe):
                    pe.wait_ge(pool_step.sem, pool_step.at(BUILT))
                    nc.tensor.matmul(PS[:, 7, 0:LS], of_query, earlier, start=True, stop=True).then_inc(summed.sem, 1)
                    with pe.Fori(0, STEPS) as g:
                        for s in (page_in[0], value_in[0]):
                            pe.wait_ge(s.sem, s.at(LOADED) + g * LOADED)
                        pe.wait_ge(seq_ready.sem, seq_ready.at(1) + g)
                        for c in range(2):
                            for s in range(2):
                                for a in range(4):
                                    nc.tensor.matmul(PS[32 * a:32 * a + 32, c, :], QB[:, s, a, :],
                                                     K[s][:, 4 * c:4 * c + 4, a, :], start=(s == 0), stop=(s == 1))
                        for s in range(2):
                            for a in range(4):
                                mm = nc.tensor.matmul(PS[32 * a:32 * a + 32, 2, 0:LS], QB[:, s, a, :],
                                                      KN[:, a, LS * s:LS * s + LS],
                                                      start=(s == 0), stop=(s == 1))
                        mm.then_inc(logit_ready.sem, 1)
                        pe.wait_ge(weight_ready.sem, weight_ready.at(1) + g)
                        for n in range(2):
                            for p in range(4 * n, 4 * n + 4):
                                mm = nc.tensor.transpose(PS[:, 3 + n, (p % 4) * P:(p % 4 + 1) * P],
                                                         soft[:, 1, p * P:(p + 1) * P], ident[:])
                            mm.then_inc(turned.sem, 1)
                        nc.tensor.transpose(PS[0:LS, 5, 0:P], soft[:, 1, PAST:W], ident[:]).then_inc(turned.sem, 1)
                        for s in (page_in[1], value_in[1]):
                            pe.wait_ge(s.sem, s.at(LOADED_V) + g * LOADED_V)
                        pe.wait_ge(turned_read.sem, turned_read.at(2) + 2 * g)
                        pe.wait_ge(scaled.sem, scaled.at(2) + 2 * g)
                        for s in range(2):
                            for p in range(NPG + 1):
                                for a in range(4):
                                    w = pT[:, p, 32 * a:32 * a + 32] if p < NPG else pT[0:LS, p, 32 * a:32 * a + 32]
                                    v = VV[s][:, p, a * P:(a + 1) * P] if p < NPG else VN[s][:, a * P:(a + 1) * P]
                                    mm = nc.tensor.matmul(PS[32 * a:32 * a + 32, 6, s * P:(s + 1) * P], w, v,
                                                          start=(p == 0), stop=(p == NPG))
                        mm.then_inc(out_ready.sem, 1)
                        pe.wait_ge(keep_ready.sem, keep_ready.at(1) + g)
                        for s in range(2):
                            mm = nc.tensor.transpose(PS[:, 7, s * P:(s + 1) * P], out_rows[:, s, :], ident[:])
                        mm.then_inc(tail_ready.sem, 1)

                @block.scalar
                def _(act):
                    step = Chain(act, act_step)
                    act.wait_ge(pool_step.sem, pool_step.at(BUILT))
                    with act.Fori(0, STEPS) as g:
                        step.loop(g, 2)
                        act.wait_ge(logit_ready.sem, logit_ready.at(0) + g)
                        nc.scalar.activation(KN, KTT[:, :, bass.ds(g * 2 * LS + NPR, 2 * LS)], ACT.Copy)
                        for s in range(2):
                            for hh in range(2):
                                rows = slice(64 * hh, 64 * hh + 64)
                                c = 16 * s + 8 * hh
                                last = nc.scalar.activation(QB[rows, s, :, c:c + LS],
                                                            QT[rows, :, bass.ds(g * 2 * LS + (NPR + LS * s), LS)],
                                                            ACT.Copy)
                        last.then_inc(seq_ready.sem, 1)
                        act.wait_ge(scaled.sem, scaled.at(1) + 2 * g)
                        step(nc.scalar.activation(soft[:, 0, :], z, ACT.Abs, scale=SCALE))
                        step(nc.scalar.activation(soft[:, 0, :], soft[:, 0, :], ACT.Exp, scale=-1.0))
                        nc.scalar.activation(soft[:, 0, :], soft[:, 0, :], ACT.Ln, bias=1.0).then_inc(logged.sem, 1)
                        act.wait_ge(exponent.sem, exponent.at(1) + g)
                        nc.scalar.activation(soft[:, 1, :], soft[:, 1, :], ACT.Exp).then_inc(weight_ready.sem, 1)
                        act.wait_ge(turned.sem, turned.at(1) + 3 * g)
                        nc.scalar.activation(pT[:, 0:4, :].rearrange("p k r -> p (k r)"), PS[:, 3, :], ACT.Copy)\
                            .then_inc(turned_read.sem, 1)
                        act.wait_ge(turned.sem, turned.at(3) + 3 * g)
                        nc.scalar.activation(pT[0:LS, NPG, :], PS[0:LS, 5, 0:P], ACT.Copy)\
                            .then_inc(turned_read.sem, 1)
                        step.done(STEPS)
                    act_step.count = step.n

                @block.vector
                def _(dve):
                    step = Chain(dve, dve_step)
                    dve.wait_ge(summed.sem, summed.at(1))
                    step(nc.vector.tensor_copy(mask[:], PS[:, 7, 0:LS]))
                    step(nc.vector.tensor_scalar(fill[:], mask[:], -1.0, -NEG, ALU.add, ALU.mult))
                    with dve.Fori(0, STEPS) as g:
                        step.loop(g, 3)
                        dve.wait_ge(logit_ready.sem, logit_ready.at(1) + g)
                        nc.vector.tensor_scalar(soft[:, 1, :], z, SCALE, 0.0, ALU.mult, ALU.max)\
                            .then_inc(scaled.sem, 1)
                        dve.wait_ge(logged.sem, logged.at(1) + g)
                        step(nc.vector.tensor_tensor(soft[:, :, PAST:W], soft[:, :, PAST:W], rep(mask[:], 1, 2),
                                                     ALU.mult))
                        step(nc.vector.tensor_tensor_scan(backwards(soft[:, 0, :]), backwards(soft[:, 0, :]),
                                                          backwards(soft[:, 1, :]), 0.0, ALU.add, ALU.add))
                        step(nc.vector.scalar_tensor_tensor(out=soft[:, 1, :], in0=z, scalar=SCALE,
                                                            in1=soft[:, 0, :], op0=ALU.mult, op1=ALU.subtract))
                        nc.vector.tensor_tensor(soft[:, 1, PAST:W], soft[:, 1, PAST:W], fill[:], ALU.add)\
                            .then_inc(exponent.sem, 1)
                        dve.wait_ge(turned.sem, turned.at(2) + 3 * g)
                        nc.vector.tensor_copy(pT[:, 4:8, :].rearrange("p k r -> p (k r)"), PS[:, 4, :])\
                            .then_inc(scaled.sem, 1)
                        dve.wait_ge(out_ready.sem, out_ready.at(1) + g)
                        nc.vector.tensor_copy(out_rows[:].rearrange("p s n -> p (s n)"), PS[:, 6, 0:2 * P])\
                            .then_inc(keep_ready.sem, 1)
                        dve.wait_ge(tail_ready.sem, tail_ready.at(1) + g)
                        for hh in range(2):
                            rows = slice(64 * hh, 64 * hh + 64)
                            src = PS[rows, 7, 8 * hh:8 * hh + 1]
                            src = bass.AP(src.tensor, src.offset,
                                          [list(src.ap[0]), [32, 4], [P + 16, 2], [1, LS]])
                            to = OT[rows, 0:4, bass.ds(g * 2 * LS + NPR, 2 * LS)].rearrange("p a (s q) -> p a s q", s=2)
                            nc.vector.tensor_copy(to, src).then_inc(out_read.sem, 1)
                        step.done(STEPS)
                    dve_step.count = step.n
            pool_step.close(pool_step.count)
            act_step.close(act_step.count)
            dve_step.close(dve_step.count)
            for s in (logit_ready, keep_ready, tail_ready, weight_ready, out_ready, logged, exponent, seq_ready):
                s.close(STEPS)
            for s in (out_read, scaled, turned_read):
                s.close(2 * STEPS)
            turned.close(3 * STEPS)
            summed.close(1)
            for keys_in, values_in in (page_in, value_in):
                keys_in.close(LOADED * STEPS)
                values_in.close(LOADED_V * STEPS)

        def linear_attention(qkT, vb, rT, a1T, OT):
            CH = [(t, c) for t in range(2) for c in range(2)]
            with ExitStack() as stage:
                def tile(name, shape):
                    return sb(name, shape, F32, stage)
                wa2 = tile("g_wa2", [16, 256])
                ba2 = tile("g_ba2", [P, 256])
                og = tile("g_og", [P, 1])
                S0 = tile("g_S0", [P, NB, 2, P])
                same = tile("g_same", [P, 2, P])
                upto = tile("g_upto", [P, 2, P])
                neg_upto = tile("g_neg_upto", [P, 2, P])
                neg_after = tile("g_neg_after", [P, 2, P])
                neg_chunk = tile("g_neg_chunk", [P, 2, NB])
                in_seq = tile("g_in_seq", [64, NB])
                x = tile("g_x", [P, 3, 256])
                soft = tile("g_soft", [P, 3, 256])
                EB = tile("g_EB", [P, 2, NT])
                EN = tile("g_EN", [P, 2, NT])
                ED = tile("g_ED", [P, 3, 256])
                EL = tile("g_EL", [P, 2, 12])
                qin = tile("g_qin", [P, 2, NT])
                kin = tile("g_kin", [P, 2, NT])
                kdec = tile("g_kdec", [P, 3, 256])
                att = tile("g_att", [P, 3, 4, P])
                S = tile("g_S", [P, 5, 2, P])
                vx = tile("g_vx", [64, 4, NB, P])
                sq = tile("g_sq", [P, 4, NT])
                rs = tile("g_rs", [P, 4, NT])
                so = tile("g_so", [P, NB, 2, P])
                INV = -1.0 / 16.0

                kinds = [0, 0, 1]
                QB = x[:].rearrange("p t n -> p (t n)")[:, 0:512].rearrange("p (a b r) -> p a b r", a=2, b=NB)
                old_rows = soft[:].rearrange("p t n -> p (t n)")[:, 0:512]
                old = ED[:].rearrange("p t n -> p (t n)")[:, 0:512]
                BUILT = 15
                block = stage.enter_context(nc.Block(no_gpsimd_drain=True))

                @block.gpsimd
                def _(pool):
                    step = Chain(pool, pool_step)

                    def pick(t, op, base, pattern, mult):
                        step(pool.affine_select(out=t, in_=t, compare_op=op, fill=0.0, base=base, pattern=pattern,
                                                channel_multiplier=mult))
                    step(pool.memset(same[:], 1.0))
                    step(pool.memset(neg_chunk[:], INV))
                    step(pool.memset(in_seq[:], 1.0))
                    for kind, size in ((0, 64), (1, 8)):
                        v = same[:, kind, :].rearrange("p (c i) -> p c i", i=size)
                        pick(v, ALU.is_ge, 0, [[-size, P // size], [0, size]], 1)
                        pick(v, ALU.is_ge, size - 1, [[size, P // size], [0, size]], -1)
                        v = neg_chunk[:, kind, :]
                        pick(v, ALU.is_ge, 0, [[-size, NB]], 1)
                        pick(v, ALU.is_ge, size - 1, [[size, NB]], -1)
                    pick(in_seq[:], ALU.is_ge, 0, [[-8, NB]], 1)
                    pick(in_seq[:], ALU.is_ge, 7, [[8, NB]], -1)
                    step(pool.tensor_copy(upto[:], same[:]))
                    pick(upto[:], ALU.is_ge, 0, [[0, 2], [1, P]], -1)
                    assert step.n == BUILT
                    pool_step.count = step.n

                @block.tensor
                def _(pe):
                    pe.wait_ge(loads.sem, loads.at(32))
                    for t, rows in enumerate(TILE_ROWS):
                        mm = nc.tensor.matmul(PS[0:rows, t, 0:256], a1T[:, t * P:t * P + rows], wa2[:],
                                              start=True, stop=True)
                    mm.then_inc(logit_ready.sem, 1)
                    for t, rows in enumerate(TILE_ROWS):
                        for a in range(2):
                            mm = nc.tensor.transpose(PS[0:rows, 5 + t, a * P:(a + 1) * P],
                                                     qkT[:, 2 + a, t * P:t * P + rows], ident[:])
                    mm.then_inc(out_ready.sem, 1)
                    pe.wait_ge(keep_ready.sem, keep_ready.at(1))
                    pe.wait_ge(pool_step.sem, pool_step.at(BUILT))
                    for a in range(2):
                        for t, rows in enumerate(TILE_ROWS):
                            nc.tensor.matmul(PS[:, a, t * P:t * P + rows], soft[0:rows, t, a * P:(a + 1) * P],
                                             neg_upto[0:rows, kinds[t], 0:rows], start=(t == 0), stop=(t == 2),
                                             skip_group_check=True)
                    for t, rows in enumerate(TILE_ROWS):
                        nc.tensor.matmul(PS[0:rows, 2 + t // 2, (t % 2) * 256:(t % 2) * 256 + 256],
                                         neg_after[0:rows, kinds[t], 0:rows], soft[0:rows, t, :],
                                         start=True, stop=True)
                    for a in range(2):
                        for t, rows in enumerate(TILE_ROWS):
                            n = NB if t == 2 else 2
                            mm = nc.tensor.matmul(PS[:, 4, a * 12 + 2 * t:a * 12 + 2 * t + n],
                                                  soft[0:rows, t, a * P:(a + 1) * P], neg_chunk[0:rows, kinds[t], 0:n],
                                                  start=True, stop=True)
                    mm.then_inc(tail_ready.sem, 1)
                    pe.wait_ge(weight_ready.sem, weight_ready.at(1))
                    for t, rows in enumerate(TILE_ROWS):
                        for h in range(4):
                            r = slice(64 * (h % 2), 64 * (h % 2) + 64)
                            mm = nc.tensor.matmul(PS[0:rows, 3 * (h % 2) + t, (h // 2) * P:(h // 2) * P + rows],
                                                  kin[r, h // 2, t * P:t * P + rows],
                                                  qin[r, h // 2, t * P:t * P + rows], start=True, stop=True)
                    mm.then_inc(logit_ready.sem, 1)
                    for n, (t, c) in enumerate(CH):
                        for h in range(4):
                            r = slice(64 * (h % 2), 64 * (h % 2) + 64)
                            e = slice(64 * c, 64 * c + 64)
                            mm = nc.tensor.matmul(PS[r, 6 + c, t * 256 + (h // 2) * P:t * 256 + (h // 2 + 1) * P],
                                                  kdec[e, t, 64 * h:64 * h + 64], vb[e, t, h * P:(h + 1) * P],
                                                  start=True, stop=True)
                    mm.then_inc(out_ready.sem, 1)
                    pe.wait_ge(seq_ready.sem, seq_ready.at(1))
                    pe.wait_ge(state_in.sem, state_in.at(32))
                    for half in range(2):
                        for a in range(2):
                            for j in range(4):
                                c = P * (2 * half + a)
                                mm = nc.tensor.matmul(PS[32 * j:32 * j + 32, 4, c:c + P], QB[:, a, 4 * half + j, :],
                                                      S0[:, 4 * half + j, a, :], start=True, stop=True)
                    mm.then_inc(turned.sem, 1)
                    for h in range(4):
                        r = slice(64 * (h % 2), 64 * (h % 2) + 64)
                        for t, rows in enumerate(TILE_ROWS):
                            mm = nc.tensor.matmul(PS[:, h, t * P:t * P + rows], vb[:, t, h * P:(h + 1) * P],
                                                  att[:, t, h, 0:rows], start=(t == 0), stop=False,
                                                  skip_group_check=True)
                        for n in range(1, 4):
                            mm = nc.tensor.matmul(PS[:, h, 64 * n:64 * n + 64], S[r, n, h // 2, :],
                                                  qin[r, h // 2, 64 * n:64 * n + 64], start=False, stop=(n == 3),
                                                  skip_group_check=True)
                        mm.then_inc(out_ready.sem, 1)
                        if h == 0:
                            pe.wait_ge(turned_read.sem, turned_read.at(1))
                            for c in range(4):
                                mm = nc.tensor.transpose(PS[:, 4, c * P:(c + 1) * P], old_rows[:, c * P:(c + 1) * P],
                                                         ident[:])
                            mm.then_inc(turned.sem, 1)
                    pe.wait_ge(turned_read.sem, turned_read.at(2))
                    pe.wait_ge(expanded.sem, expanded.at(1))
                    for a in range(2):
                        for hh in range(2):
                            for half in range(2):
                                h = 2 * a + hh
                                mm = nc.tensor.matmul(PS[64 * hh:64 * hh + 64, 4 + 2 * a + half, :],
                                                      kdec[0:64, 2, 64 * h:64 * h + 64],
                                                      vx[:, h, 4 * half:4 * half + 4, :], start=True, stop=True)
                    mm.then_inc(out_ready.sem, 1)
                    pe.wait_ge(squared.sem, squared.at(5))
                    for h in range(4):
                        mm = nc.tensor.matmul(PS[:, h, 0:NT], ones[:], sq[:, h, :], start=True, stop=True)
                    mm.then_inc(summed.sem, 1)

                @block.scalar
                def _(act):
                    step = Chain(act, act_step)
                    act.wait_ge(scaled.sem, scaled.at(1))
                    step(nc.scalar.activation(x[:], x[:], ACT.Exp, scale=-1.0))
                    nc.scalar.activation(x[:], x[:], ACT.Ln, bias=1.0).then_inc(logged.sem, 1)
                    act.wait_ge(tail_ready.sem, tail_ready.at(1))
                    nc.scalar.activation(EB[:], PS[:, 0:2, 0:NT], ACT.Exp)
                    nc.scalar.activation(EN[:], PS[:, 0:2, 0:NT], ACT.Exp, scale=-1.0)
                    nc.scalar.activation(ED[:, 0:2, :].rearrange("p t n -> p (t n)"), PS[:, 2, :], ACT.Exp)
                    nc.scalar.activation(ED[0:64, 2, :], PS[0:64, 3, 0:256], ACT.Exp)
                    nc.scalar.activation(EL[:].rearrange("p a n -> p (a n)"), PS[:, 4, 0:24], ACT.Exp)\
                        .then_inc(exponent.sem, 1)
                    nc.scalar.activation(rT[:], rT[:], ACT.Silu).then_inc(squared.sem, 1)
                    for h in range(4):
                        act.wait_ge(out_read.sem, out_read.at(h + 1))
                        nc.scalar.activation(sq[:, h, :], OT[:, 4 + h, :], ACT.Square).then_inc(squared.sem, 1)
                    act.wait_ge(summed.sem, summed.at(1))
                    nc.scalar.activation(rs[:], PS[:, 0:4, 0:NT], ACT.Ln, scale=1.0 / P, bias=eps[:, 0:1])\
                        .then_inc(variance.sem, 1)
                    act.wait_ge(variance.sem, variance.at(1))
                    nc.scalar.activation(rs[:], rs[:], ACT.Exp, scale=-0.5).then_inc(deviation.sem, 1)
                    act_step.count = step.n

                @block.vector
                def _(dve):
                    step = Chain(dve, dve_step)
                    dve.wait_ge(logit_ready.sem, logit_ready.at(1))
                    dve.wait_ge(loads.sem, loads.at(32))
                    for t, rows in enumerate(TILE_ROWS):
                        last = nc.vector.tensor_tensor(x[0:rows, t, :], PS[0:rows, t, 0:256], ba2[0:rows, :], ALU.add)
                    step(nc.vector.memset(x[64:128, 2, :], 0.0))
                    step(nc.vector.tensor_scalar(soft[:], x[:], -1.0, 0.0, ALU.mult, ALU.max))
                    nc.vector.scalar_tensor_tensor(out=x[:], in0=x[:], scalar=-1.0, in1=x[:], op0=ALU.mult, op1=ALU.max).then_inc(scaled.sem, 1)
                    dve.wait_ge(pool_step.sem, pool_step.at(BUILT))
                    step(nc.vector.tensor_scalar(neg_upto[:], upto[:], INV, None, ALU.mult))
                    step(nc.vector.tensor_tensor(neg_after[:], same[:], upto[:], ALU.subtract))
                    step(nc.vector.tensor_scalar(neg_after[:], neg_after[:], INV, None, ALU.mult))
                    dve.wait_ge(logged.sem, logged.at(1))
                    nc.vector.tensor_tensor(soft[:], soft[:], x[:], ALU.add).then_inc(keep_ready.sem, 1)
                    dve.wait_ge(exponent.sem, exponent.at(1))
                    nc.vector.scalar_tensor_tensor(out=qin[:], in0=qkT[:, 0:2, :], scalar=SCALE, in1=EB[:],
                                                   op0=ALU.mult, op1=ALU.mult)
                    nc.vector.tensor_tensor(kin[:], qkT[:, 2:4, :], EN[:], ALU.mult)
                    dve.wait_ge(out_ready.sem, out_ready.at(1))
                    nc.vector.tensor_tensor(kdec[:, 0:2, :], PS[:, 5:7, 0:256], ED[:, 0:2, :], ALU.mult)
                    nc.vector.tensor_tensor(kdec[0:64, 2, :], PS[0:64, 7, 0:256], ED[0:64, 2, :], ALU.mult)\
                        .then_inc(weight_ready.sem, 1)
                    dve.wait_ge(keep_ready.sem, keep_ready.at(1))
                    step(nc.vector.memset(QB, 0.0))
                    for hh in range(2):
                        r = slice(64 * hh, 64 * hh + 64)
                        last = nc.vector.tensor_copy(QB[r, :, :, 8 * hh:8 * hh + 8],
                                                     qin[r, :, NPR:NT].rearrange("p a (b q) -> p a b q", q=LS))
                    step(last)
                    dve.wait_ge(logit_ready.sem, logit_ready.at(2))
                    for t, rows in enumerate(TILE_ROWS):
                        for hh in range(2):
                            a = PS[0:rows, 3 * hh + t, 0:256].rearrange("p (a c) -> p a c", a=2)[:, :, 0:rows]
                            m = rep(upto[0:rows, kinds[t], 0:rows], 1, 2)
                            to = att[0:rows, t, :, 0:rows].rearrange("p (a g) c -> p a g c", g=2)[:, :, hh, :]
                            nc.vector.tensor_tensor(to, a, m, ALU.mult)
                    nc.vector.memset(att[64:128, 2, :, :], 0.0)
                    nc.vector.memset(vb[64:128, 2, :], 0.0)
                    dve.wait_ge(out_ready.sem, out_ready.at(2))
                    for n in range(4):
                        t, c = CH[n]
                        new = PS[:, 6 + c, t * 256:t * 256 + 256].rearrange("p (a v) -> p a v", a=2)
                        if n == 0:
                            step(nc.vector.tensor_copy(S[:, 1, :, :], new))
                            continue
                        for a in range(2):
                            last = nc.vector.scalar_tensor_tensor(out=S[:, n + 1, a, :], in0=S[:, n, a, :],
                                                                  scalar=EL[:, a, n:n + 1], in1=new[:, a, :],
                                                                  op0=ALU.mult, op1=ALU.add)
                        if n < 3:
                            step(last)
                        else:
                            last.then_inc(seq_ready.sem, 1)
                    dve.wait_ge(turned.sem, turned.at(1))
                    nc.vector.tensor_copy(old_rows, PS[:, 4, :]).then_inc(turned_read.sem, 1)
                    for h in range(4):
                        v = vb[0:64, 2, h * P:(h + 1) * P]
                        m = in_seq[:]
                        m = bass.AP(m.tensor, m.offset, [list(a) for a in m.ap] + [[0, P]])
                        last = nc.vector.tensor_tensor(vx[:, h, :, :], rep(v, 1, NB), m, ALU.mult)
                    last.then_inc(expanded.sem, 1)
                    dve.wait_ge(turned.sem, turned.at(2))
                    nc.vector.tensor_copy(old, PS[:, 4, :]).then_inc(turned_read.sem, 1)
                    dve.wait_ge(turned_read.sem, turned_read.at(2))
                    for h in range(4):
                        dve.wait_ge(out_ready.sem, out_ready.at(3 + h))
                        nc.vector.tensor_copy(OT[:, 4 + h, 0:NPR], PS[:, h, 0:NPR])
                        src = old[:, P * (h // 2) + 8 * (h % 2):P * (h // 2) + 8 * (h % 2) + 1]
                        src = bass.AP(src.tensor, src.offset, [list(src.ap[0]), [2 * P, 2], [32, 4], [1, LS]])
                        nc.vector.tensor_tensor(
                            OT[:, 4 + h, NPR:NT].rearrange("p (e j q) -> p e j q", e=2, j=4),
                            PS[:, h, NPR:NT].rearrange("p (e j q) -> p e j q", e=2, j=4), src, ALU.add)\
                            .then_inc(out_read.sem, 1)
                    dve.wait_ge(out_ready.sem, out_ready.at(7))
                    dve.wait_ge(state_in.sem, state_in.at(32))
                    for a in range(2):
                        e = EL[:, a, 4:12]
                        e = bass.AP(e.tensor, e.offset, [list(q) for q in e.ap] + [[0, P]])
                        step(nc.vector.tensor_tensor(so[:, :, a, :], S0[:, :, a, :], e, ALU.mult))
                        for half in range(2):
                            v = so[:, 4 * half:4 * half + 4, a, :]
                            src = PS[:, 4 + 2 * a + half, :].rearrange("p (b v) -> p b v", b=4)
                            step(nc.vector.tensor_tensor(v, v, src, ALU.add))
                    dve.wait_ge(deviation.sem, deviation.at(1))
                    step(nc.vector.tensor_tensor(rs[:], rs[:], OT[:, 4:8, :], ALU.mult))
                    nc.vector.scalar_tensor_tensor(out=OT[:, 4:8, :], in0=rs[:], scalar=og[:, 0:1], in1=rT[:],
                                                   op0=ALU.mult, op1=ALU.mult).then_inc(centred.sem, 1)
                    dve_step.count = step.n

                @block.sync
                def _(sp):
                    sp.dma_start(wa2[:], io["w_a2"]).then_inc(loads.sem, 16)
                    sp.dma_start(ba2[:], bass.AP(io["b_a2"].tensor, 0, [[0, P], [1, 256]])).then_inc(loads.sem, 16)
                    sp.dma_start(og[:], io["onorm_g"]).then_inc(state_in.sem, 16)
                    sp.dma_start(S0[:], io["gla_s"]).then_inc(state_in.sem, 16)
                    sp.wait_ge(centred.sem, centred.at(1))
                    store(sp, io["o_pgla"], S[:, 4, :, :])
                    store(sp, io["o_sgla"], so[:])
            loads.close(32)
            state_in.close(32)
            pool_step.close(pool_step.count)
            turned.close(2)
            turned_read.close(2)
            expanded.close(1)
            act_step.close(act_step.count)
            dve_step.close(dve_step.count)
            logit_ready.close(2)
            keep_ready.close(1)
            tail_ready.close(1)
            weight_ready.close(1)
            out_ready.close(7)
            out_read.close(4)
            scaled.close(1)
            logged.close(1)
            exponent.close(1)
            seq_ready.close(1)
            squared.close(5)
            for s in (summed, variance, deviation, centred):
                s.close(1)
            stored.close(32)

        centre_ready = signal("centre_ready")
        turned = signal("turned")
        turned_read = signal("turned_read")
        table_in = signal("table_in")
        first_values_in = signal("first_values_in")
        mlp_in = signal("mlp_in")
        chosen = signal("chosen")

        def odd_stage(n0):
            stage = ExitStack()
            with stage:
                def tile(name, shape):
                    return sb(name, shape, F32, stage)

                Q2 = tile("Q2", [P, 8, NT])
                kskw = tile("kskw", [P, 4, NT])
                vsvw = tile("vsvw", [P, 3, 512])
                kcvc = tile("kcvc", [P, 4, NT])
                GT = tile("GT", [P, 3, 48])
                GS = tile("GS", [P, NB, 3])
                Bs = tile("Bs", [P, PAST + LS])
                Bw = tile("Bw", [P, WIN + LS])
                qkg = tile("qkg", [P, 4])
                w_gt = tile("w_gt", [P, KT, 48])
                pages = sb("c_pages", [1, NB * NPG], I32, stage)
                bias_tables(Bs, ((pages, "pages"), (w_gt, "w_gt"), (qkg, "qk_g")))
                n1 = project_stage(1, n0, [(True, Q2[:, 0:4, :]), (True, Q2[:, 4:8, :]), (True, kcvc[:]),
                                           (True, kskw[:]), (False, vsvw)], w_gt, 48, GT, True)
                OT = tile("OT1", [P, KT, NT])
                KC = tile("KC", [P, 2, NB * 64 + 16])
                VC = tile("VC", [64, NB + 1, 256])
                with ExitStack() as early:
                    mlp = {"w1": sb("w1", [P, 2, 2, 8, P], F32, early), "w2": sb("w2", [P, 2, 64], F32, early),
                           "b1": sb("b1", [P, 2], F32, early), "b2k": sb("b2k", [P, 1], F32, early),
                           "b2v": sb("b2v", [64, 64], F32, early)}
                    C = [sb(f"C{i}", [P, 2 * NPG, 4, 8, 8], F32, early) for i in range(2)]

                    def load_first(sp):
                        for name in ("w1", "w2", "b1", "b2k"):
                            sp.dma_start(mlp[name][:], io["cmp_" + name]).then_inc(mlp_in.sem, 16)
                        sp.dma_start(mlp["b2v"][:], bass.AP(io["cmp_b2v"].tensor, 0, [[0, 64], [1, 64]]))\
                            .then_inc(mlp_in.sem, 16)
                        load_pair(sp, C, pages, 0, 0, 0)

                    def load_first_pool(pool):
                        load_pair(pool, C, pages, 0, 0, 1)
                    qk_norms(Q2, kskw, kcvc, vsvw, GT, GS, Bs, Bw, qkg, OT, load_first, load_first_pool)
                    compress(kcvc, KC, VC, GS, qkg, mlp, C, pages, OT)
                KS = [tile("KS0", [P, NPG, 2, P])]
                KW = [tile("KW0", [P, 2, WIN])]

                def load_first_keys(sp):
                    for p in range(NPG):
                        page = sp.value_load(pages[0:1, p:p + 1], min_val=0, max_val=NPOOL - 1)
                        sp.dma_start(KS[0][:, p, :, :].rearrange("p a n -> p (a n)"),
                                     io["slc_kT"][bass.ds(page, 1), :, :].rearrange("a p n -> p (a n)"))\
                            .then_inc(page_in[0].sem, 16)
                    sp.dma_start(KW[0][:].rearrange("p t n -> p (t n)"),
                                 io["win_kT"][0:1, :, :].rearrange("a p n -> p (a n)")).then_inc(page_in[0].sem, 16)
                sparse_prompt(Q2, kskw, vsvw, GT, KC, VC, OT, load_first_keys)
                sparse_sample(Q2, kskw, vsvw, GS, Bs, Bw, KC, VC, OT, KS, KW, pages)
                return out_stage(1, n1, OT)

        def bias_tables(Bs, small):
            BANKS = 5
            with ExitStack() as stage:
                rel = sb("rel", [33, 16], F32, stage)
                relb = sb("relb", [33, 16, P], F32, stage)
                rel8 = sb("rel8", [33, 16, 8], F32, stage)
                one_hot = sb("one_hot", [33, NDIST], F32, stage)
                F = sb("F", [P, NDIST], F32, stage)
                FP = sb("FP", [P, 16, NDIST_P], F32, stage)
                block = stage.enter_context(nc.Block(no_gpsimd_drain=True))

                @block.sync
                def _(sp):
                    sp.dma_start(rel[0:32, :], io["rel_table"]).then_inc(table_in.sem, 16)
                    sp.dma_start(one_hot[:], io["one_hot"]).then_inc(table_in.sem, 16)
                    for dst, name in small:
                        sp.dma_start(dst[:], io[name]).then_inc(table_in.sem, 16)
                    sp.wait_ge(act_step.sem, act_step.at(1))
                    sp.dma_start(io["bias_rows"], F[:]).then_inc(loads.sem, 16)
                    sp.wait_ge(loads.sem, loads.at(16))
                    f = io["bias_rows"].tensor
                    for h in range(16):
                        sp.dma_start(Bs[8 * h:8 * h + 8, :],
                                     bass.AP(f, 8 * h * NDIST + DIST_HI - PAST, [[NDIST - 1, 8], [1, PAST + LS]]))\
                            .then_inc(loads.sem, 16)
                    for h in range(0, 16, 4):
                        sp.wait_ge(act_step.sem, act_step.at(h + 5))
                        sp.dma_start(io["bias_prompt"][:, h:h + 4, :], FP[:, h:h + 4, :]).then_inc(loads.sem, 16)
                    sp.wait_ge(loads.sem, loads.at(21 * 16))

                @block.gpsimd
                def _(pool):
                    pool.memset(rel[32:33, :], NEG).then_inc(pool_step.sem, 1)

                @block.vector
                def _(dve):
                    dve.wait_ge(table_in.sem, table_in.at(80))
                    dve.wait_ge(pool_step.sem, pool_step.at(1))
                    r = rel[:]
                    r = bass.AP(r.tensor, r.offset, [list(x) for x in r.ap] + [[0, P]])
                    nc.vector.tensor_copy(relb[:], r).then_inc(dve_step.sem, 1)
                    r = bass.AP(r.tensor, r.offset, [list(x) for x in rel[:].ap] + [[0, 8]])
                    nc.vector.tensor_copy(rel8[:], r).then_inc(dve_step.sem, 1)

                @block.tensor
                def _(pe):
                    pe.wait_ge(dve_step.sem, dve_step.at(2))
                    for c in range(0, NDIST, 512):
                        n = min(512, NDIST - c)
                        mm = nc.tensor.matmul(PS[:, c // 512, 0:n], rel8[:].rearrange("p h q -> p (h q)"), one_hot[:, c:c + n],
                                              start=True, stop=True)
                    mm.then_inc(turned.sem, 1)
                    for h in range(16):
                        if h >= BANKS:
                            pe.wait_ge(act_step.sem, act_step.at(h - BANKS + 2))
                        nc.tensor.matmul(PS[:, 3 + h % BANKS, 0:NDIST_P], relb[:, h, :],
                                         one_hot[:, DIST_HI - 255:DIST_HI - 255 + NDIST_P], start=True, stop=True)\
                            .then_inc(turned.sem, 1)

                @block.scalar
                def _(act):
                    act.wait_ge(turned.sem, turned.at(1))
                    nc.scalar.activation(F[:], PS[:, 0:3, :].rearrange("p a n -> p (a n)")[:, 0:NDIST], ACT.Copy)\
                        .then_inc(act_step.sem, 1)
                    for h in range(16):
                        act.wait_ge(turned.sem, turned.at(h + 2))
                        nc.scalar.activation(FP[:, h, :], PS[:, 3 + h % BANKS, 0:NDIST_P], ACT.Copy)\
                            .then_inc(act_step.sem, 1)
            table_in.close(80)
            loads.close(21 * 16)
            pool_step.close(1)
            dve_step.close(2)
            turned.close(17)
            act_step.close(17)

        def qk_norms(Q2, kskw, kcvc, vsvw, GT, GS, Bs, Bw, qkg, OT, load_first, load_first_pool):
            with ExitStack() as stage:
                sel8 = sb("sel8", [8, P], F32, stage)
                low8 = sb("low8", [8, 8], F32, stage)
                sq = OT[:, 0:4, :]
                block = stage.enter_context(nc.Block(no_gpsimd_drain=True))

                @block.sync
                def _(sp):
                    store(sp, io["o_kcvc"], kcvc[:])
                    store(sp, io["o_vsvw"][0:NPR, :].rearrange("(t p) n -> p t n", p=P), vsvw[:, 0:2, :])
                    store(sp, io["o_vsvw"][NPR:NT, :], vsvw[0:64, 2, :])
                    sp.dma_start(io["new_rows"][1], vsvw[0:64, 2, :]).then_inc(loads.sem, 16)
                    sp.wait_ge(act_step.sem, act_step.at(1))
                    sp.dma_start(io["gate_rows"].rearrange("b l h c -> (b l) (h c)"), GT[0:64, 2, :])\
                        .then_inc(loads.sem, 16)
                    sp.wait_ge(loads.sem, loads.at(32))
                    sp.wait_ge(centred.sem, centred.at(1))
                    store(sp, io["o_kskw"], kskw[:])
                    load_first(sp)

                @block.gpsimd
                def _(pool):
                    load_first_pool(pool)
                    step = Chain(pool, pool_step)
                    step(pool.memset(sel8[:], 0.0))
                    step(pool.affine_select(out=sel8[:], in_=sel8[:], compare_op=ALU.not_equal, fill=1.0, base=0,
                                            pattern=[[0, 16], [1, 8]], channel_multiplier=-1))
                    pool_step.count = step.n

                @block.tensor
                def _(pe):
                    pe.wait_ge(squared.sem, squared.at(1))
                    for m in range(4):
                        mm = nc.tensor.matmul(PS[:, m, 0:NT], halves[:], sq[:, m, :], start=True, stop=True)
                    mm.then_inc(summed.sem, 1)
                    pe.wait_ge(squared.sem, squared.at(2))
                    for m in range(4):
                        mm = nc.tensor.matmul(PS[:, 4 + m, 0:NT], halves[:], H[:, m, :], start=True, stop=True)
                    mm.then_inc(summed.sem, 1)
                    pe.wait_ge(variance.sem, variance.at(1))
                    for m in range(4):
                        mm = nc.tensor.matmul(PS[:, m, 0:NT], halves[:], H[:, 4 + m, :], start=True, stop=True)
                    mm.then_inc(summed.sem, 1)
                    pe.wait_ge(pool_step.sem, pool_step.at(2))
                    pe.wait_ge(variance.sem, variance.at(2))
                    pe.wait_ge(dve_step.sem, dve_step.at(1))
                    mm = nc.tensor.matmul(PS[:, 7, 0:8], sel8[:], low8[:], start=True, stop=True)
                    mm.then_inc(out_ready.sem, 1)

                @block.scalar
                def _(act):
                    nc.scalar.activation(sq, kskw[:], ACT.Square).then_inc(squared.sem, 1)
                    nc.scalar.activation(H[:], Q2[:], ACT.Square).then_inc(squared.sem, 1)
                    nc.scalar.activation(GT[:, 0:2, :], GT[:, 0:2, :], ACT.Sigmoid)
                    nc.scalar.activation(GT[0:64, 2, :], GT[0:64, 2, :], ACT.Sigmoid).then_inc(act_step.sem, 1)
                    for n, (to, bank) in enumerate(((sq, 0), (H[:, 0:4, :], 4), (H[:, 4:8, :], 0))):
                        act.wait_ge(summed.sem, summed.at(n + 1))
                        nc.scalar.activation(to, PS[:, bank:bank + 4, 0:NT], ACT.Ln, scale=1.0 / 64,
                                             bias=eps[:, 0:1]).then_inc(variance.sem, 1)
                        if n == 0:
                            act.wait_ge(variance.sem, variance.at(1))
                            nc.scalar.activation(sq, sq, ACT.Exp, scale=-0.5).then_inc(deviation.sem, 1)
                    act.wait_ge(variance.sem, variance.at(3))
                    for n in range(2):
                        nc.scalar.activation(H[:, 4 * n:4 * n + 4, :], H[:, 4 * n:4 * n + 4, :], ACT.Exp,
                                             scale=-0.5).then_inc(deviation.sem, 1)

                @block.vector
                def _(dve):
                    step = Chain(dve, dve_step)
                    step(nc.vector.tensor_scalar(low8[:], strict[0:8, 0:8], -1.0, -NEG, ALU.add, ALU.mult))
                    step(nc.vector.tensor_scalar(qkg[:, 0:1], qkg[:, 0:1], SCALE, None, ALU.mult))
                    dve.wait_ge(deviation.sem, deviation.at(1))
                    for m in range(2):
                        last = nc.vector.scalar_tensor_tensor(out=kskw[:, 2 * m:2 * m + 2, :], in0=sq[:, 2 * m:2 * m + 2, :],
                                                              scalar=qkg[:, 2 + m:3 + m], in1=kskw[:, 2 * m:2 * m + 2, :],
                                                              op0=ALU.mult, op1=ALU.mult)
                    last.then_inc(centred.sem, 1)
                    for n in range(2):
                        dve.wait_ge(deviation.sem, deviation.at(n + 2))
                        part = slice(4 * n, 4 * n + 4)
                        nc.vector.scalar_tensor_tensor(out=Q2[:, part, :], in0=H[:, part, :], scalar=qkg[:, 0:1],
                                                       in1=Q2[:, part, :], op0=ALU.mult, op1=ALU.mult)
                    step(nc.vector.tensor_copy(Bw[:], Bs[:, PAST - WIN:PAST + LS]))
                    dve.wait_ge(out_ready.sem, out_ready.at(1))
                    nc.vector.tensor_tensor(Bw[:, 0:8], Bw[:, 0:8], PS[:, 7, 0:8], ALU.add)
                    dve_step.count = step.n
            loads.close(32)
            stored.close(16 * 4)
            pool_step.close(pool_step.count)
            dve_step.close(dve_step.count)
            act_step.close(1)
            out_ready.close(1)
            squared.close(2)
            summed.close(3)
            variance.close(3)
            deviation.close(3)
            centred.close(1)

        def load_pair(eng, C, pages, g, i, s, used=None):
            for p in range(NPG * s, NPG * s + NPG):
                at = g * (2 * NPG) + p
                cell = pages[0:1, at:at + 1] if isinstance(at, int) else pages[0:1, bass.ds(at, 1)]
                page = eng.value_load(cell, min_val=0, max_val=NPOOL - 1)
                src = io["cmp_k"] if i == 0 else io["cmp_v"]
                if p == NPG * s and used is not None:
                    eng.wait_ge(logit_ready.sem, used)
                eng.dma_start(C[i][:, p, :, :, :].rearrange("p v a s -> p (v a s)"),
                              src[bass.ds(page, 1), :, :].rearrange("a p n -> p (a n)"))\
                    .then_inc((value_in if s else page_in)[i].sem, 16)

        def compress(kcvc, KC, VC, GS, qkg, mlp, C, pages, OT):
            with ExitStack() as stage:
                w1, w2, b1, b2k, b2v = (mlp[name] for name in ("w1", "w2", "b1", "b2k", "b2v"))
                free = H[:].rearrange("p k n -> p (k n)")
                A1 = free[:, 0:2 * 4 * 65].rearrange("p (b v n) -> p b v n", b=2, v=4)
                hid = [free[:, 520 + 512 * i:1032 + 512 * i].rearrange("p (b v n) -> p b v n", b=2, v=4)
                       for i in range(2)]
                free2 = OT[:].rearrange("p k n -> p (k n)")
                PX = free2[:, 0:1024].rearrange("p (i v n) -> p i v n", i=2, v=4)
                rsc = free2[:, 1024:1024 + 2 * 528].rearrange("p (t n) -> p t n", t=2)
                A1p = free[:, 1544:1544 + 4 * 17].rearrange("p (v n) -> p v n", v=4)
                hidp = free[:, 1624:1624 + 64].rearrange("p (v n) -> p v n", v=4)
                LOADED = 16 * NPG
                PAIRS = NB // 2
                block = stage.enter_context(nc.Block(no_gpsimd_drain=True))

                @block.sync
                def _(sp):
                    load_pair(sp, C, pages, 0, 1, 0)
                    g = io["gate_rows"].tensor
                    for h in range(16):
                        sp.dma_start(GS[8 * h:8 * h + 8, :, :], bass.AP(g, 3 * h, [[48, 8], [8 * 48, NB], [1, 3]]))\
                            .then_inc(loads.sem, 16)
                    with sp.Fori(1, PAIRS) as g:
                        for i in range(2):
                            load_pair(sp, C, pages, g, i, 0, logit_ready.at(i - 1) + 2 * g)
                    sp.wait_ge(loads.sem, loads.at(256))

                @block.gpsimd
                def _(pool):
                    load_pair(pool, C, pages, 0, 1, 1)
                    with pool.Fori(1, PAIRS) as g:
                        for i in range(2):
                            load_pair(pool, C, pages, g, i, 1, logit_ready.at(i - 1) + 2 * g)

                @block.tensor
                def _(pe):
                    pe.wait_ge(mlp_in.sem, mlp_in.at(80))
                    for kvh in range(2):
                        for i in range(2):
                            for t in range(2):
                                for s2 in range(2):
                                    src = kcvc[64 * kvh:64 * kvh + 64, 2 * i + t, 0:NPR]
                                    src = src.rearrange("p (n s) -> p s n", s=2)[:, s2, :]
                                    mm = nc.tensor.matmul(PS[64 * s2:64 * s2 + 64, 4 + 2 * kvh + i, t * P:(t + 1) * P],
                                                          ident[64 * kvh:64 * kvh + 64, 64 * kvh:64 * kvh + 64], src,
                                                          start=True, stop=True)
                    mm.then_inc(turned.sem, 1)
                    pe.wait_ge(turned_read.sem, turned_read.at(1))
                    for i in range(2):
                        for m in range(2):
                            for a in range(8):
                                rhs = PX[:, i, :, :].rearrange("p v (n a) -> p v n a", a=8)[:, :, :, a]
                                mm = nc.tensor.matmul(PS[:, 2 * i + m, 0:64], w1[:, i, m, a, :], rhs,
                                                      start=(a == 0), stop=(a == 7))
                        mm.then_inc(chosen.sem, 1)
                        pe.wait_ge(chosen.sem, chosen.at(4 * i + 4))
                        if i == 0:
                            for v in range(4):
                                mm = nc.tensor.matmul(PS[64 * (v % 2):64 * (v % 2) + 64, 4, (v // 2) * 16:(v // 2) * 16 + 16],
                                                      w2[:, 0, :], hidp[:, v, :], start=True, stop=True)
                        else:
                            for v in range(4):
                                mm = nc.tensor.matmul(PS[0:16, 5, 64 * v:64 * v + 64], hidp[:, v, :], w2[:, 1, :],
                                                      start=True, stop=True)
                        mm.then_inc(turned.sem, 1)
                    pe.wait_ge(turned_read.sem, turned_read.at(3))

                    def one(g, i):
                        for arrived in (page_in[i], value_in[i]):
                            pe.wait_ge(arrived.sem, arrived.at(LOADED) + g * LOADED)
                        pe.wait_ge(weight_ready.sem, weight_ready.at(i - 1) + 2 * g)
                        for m in range(2):
                            for a in range(8):
                                mm = nc.tensor.matmul(PS[:, 2 * i + m, :], w1[:, i, m, a, :], C[i][:, :, :, a, :],
                                                      start=(a == 0), stop=(a == 7))
                        mm.then_inc(logit_ready.sem, 1)

                    def second(g, i):
                        pe.wait_ge(weight_ready.sem, weight_ready.at(i + 1) + 2 * g)
                        pe.wait_ge(out_read.sem, out_read.at(i) + 2 * g)
                        if i == 0:
                            for v in range(4):
                                mm = nc.tensor.matmul(PS[64 * (v % 2):64 * (v % 2) + 64, 4, (v // 2) * P:(v // 2 + 1) * P],
                                                      w2[:, 0, :], hid[0][:, :, v, :], start=True, stop=True)
                        else:
                            for b in range(2):
                                for v in range(4):
                                    mm = nc.tensor.matmul(PS[0:64, 5, 256 * b + 64 * v:256 * b + 64 * v + 64],
                                                          hid[1][:, b, v, :], w2[:, 1, :], start=True, stop=True)
                        mm.then_inc(out_ready.sem, 1)
                    one(0, 0)
                    one(0, 1)
                    second(0, 0)
                    with pe.Fori(1, PAIRS) as g:
                        one(g, 0)
                        second(g - 1, 1)
                        one(g, 1)
                        second(g, 0)
                    second(PAIRS - 1, 1)
                    pe.wait_ge(squared.sem, squared.at(1))
                    for t in range(2):
                        nc.tensor.matmul(PS[:, t, :], halves[:], rsc[:, t, 0:512], start=True, stop=True)
                        mm = nc.tensor.matmul(PS[:, 2 + t, 0:16], halves[:], rsc[:, t, 512:528], start=True, stop=True)
                    mm.then_inc(summed.sem, 1)

                @block.scalar
                def _(act):
                    act.wait_ge(mlp_in.sem, mlp_in.at(80))
                    act.wait_ge(turned.sem, turned.at(1))
                    for i in range(2):
                        for kvh in range(2):
                            to = PX[:, i, :, :].rearrange("p (t k) n -> p t k n", k=2)[:, :, kvh, :]
                            last = nc.scalar.activation(to, PS[:, 4 + 2 * kvh + i, 0:256].rearrange("p (t n) -> p t n", t=2),
                                                        ACT.Copy)
                    last.then_inc(turned_read.sem, 1)
                    for i in range(2):
                        act.wait_ge(chosen.sem, chosen.at(4 * i + 1))
                        nc.scalar.activation(A1p[:, :, 0:16], PS[:, 2 * i + 1, 0:64].rearrange("p (v n) -> p v n", v=4),
                                             ACT.Copy).then_inc(chosen.sem, 1)
                        act.wait_ge(chosen.sem, chosen.at(4 * i + 3))
                        nc.scalar.activation(hidp, hidp, ACT.Gelu_apprx_tanh, bias=b1[:, i:i + 1])\
                            .then_inc(chosen.sem, 1)

                    def one(g, i):
                        act.wait_ge(logit_ready.sem, logit_ready.at(i + 1) + 2 * g)
                        act.wait_ge(keep_ready.sem, keep_ready.at(i) + 2 * g)
                        for b in range(2):
                            to = A1[:, b, :, 0:64].rearrange("p v (g s) -> p g v s", s=8)
                            src = PS[:, 2 * i + 1, 256 * b:256 * b + 256].rearrange("p (g v s) -> p g v s", v=4, s=8)
                            last = nc.scalar.activation(to, src, ACT.Copy)
                        last.then_inc(logged.sem, 1)
                        act.wait_ge(keep_ready.sem, keep_ready.at(i + 1) + 2 * g)
                        nc.scalar.activation(hid[i], hid[i], ACT.Gelu_apprx_tanh, bias=b1[:, i:i + 1])\
                            .then_inc(weight_ready.sem, 1)
                    with act.Fori(0, PAIRS) as g:
                        one(g, 0)
                        one(g, 1)
                    act.wait_ge(out_read.sem, out_read.at(2 * PAIRS))
                    nc.scalar.activation(rsc, KC[:], ACT.Square).then_inc(squared.sem, 1)
                    act.wait_ge(summed.sem, summed.at(1))
                    nc.scalar.activation(rsc[:, :, 0:512], PS[:, 0:2, :], ACT.Ln, scale=1.0 / 64, bias=eps[:, 0:1])
                    nc.scalar.activation(rsc[:, :, 512:528], PS[:, 2:4, 0:16], ACT.Ln, scale=1.0 / 64,
                                         bias=eps[:, 0:1]).then_inc(variance.sem, 1)
                    act.wait_ge(variance.sem, variance.at(1))
                    nc.scalar.activation(rsc, rsc, ACT.Exp, scale=-0.5).then_inc(deviation.sem, 1)

                @block.vector
                def _(dve):
                    step = Chain(dve, dve_step)
                    step(nc.vector.memset(A1[:, :, :, 64:65], 0.0))
                    step(nc.vector.memset(A1p[:, :, 16:17], 0.0))
                    dve.wait_ge(mlp_in.sem, mlp_in.at(80))
                    for i in range(2):
                        dve.wait_ge(chosen.sem, chosen.at(4 * i + 2))
                        nc.vector.tensor_tensor(hidp, A1p[:, :, 1:17],
                                                PS[:, 2 * i, 0:64].rearrange("p (v n) -> p v n", v=4),
                                                ALU.add).then_inc(chosen.sem, 1)
                        dve.wait_ge(turned.sem, turned.at(2 + i))
                        if i == 0:
                            nc.vector.tensor_scalar(KC[:, :, 512:528], PS[:, 4, 0:32].rearrange("p (t n) -> p t n", t=2),
                                                    b2k[:, 0:1], None, ALU.add).then_inc(turned_read.sem, 1)
                        else:
                            nc.vector.tensor_tensor(VC[0:16, NB, :].rearrange("p (v d) -> p v d", v=4),
                                                    PS[0:16, 5, 0:256].rearrange("p (v d) -> p v d", v=4),
                                                    rep(b2v[0:16, :], 1, 4), ALU.add).then_inc(turned_read.sem, 1)

                    def one(g, i):
                        dve.wait_ge(logged.sem, logged.at(i + 1) + 2 * g)
                        dve.wait_ge(out_ready.sem, out_ready.at(i - 1) + 2 * g)
                        for b in range(2):
                            to = hid[i][:, b, :, :].rearrange("p v (g s) -> p g v s", s=8)
                            a0 = PS[:, 2 * i, 256 * b:256 * b + 256].rearrange("p (g v s) -> p g v s", v=4, s=8)
                            a1 = A1[:, b, :, 1:65].rearrange("p v (g s) -> p g v s", s=8)
                            last = nc.vector.tensor_tensor(to, a0, a1, ALU.add)
                        last.then_inc(keep_ready.sem, 1)

                    def second(g, i):
                        dve.wait_ge(out_ready.sem, out_ready.at(i + 1) + 2 * g)
                        if i == 0:
                            nc.vector.tensor_scalar(KC[:, :, bass.ds(g * P, P)],
                                                    PS[:, 4, 0:256].rearrange("p (t n) -> p t n", t=2),
                                                    b2k[:, 0:1], None, ALU.add).then_inc(out_read.sem, 1)
                        else:
                            to = VC[:, bass.ds(2 * g, 2), :].rearrange("p b (v d) -> p b v d", v=4)
                            nc.vector.tensor_tensor(to, PS[0:64, 5, :].rearrange("p (b v d) -> p b v d", b=2, v=4),
                                                    rep(rep(b2v[:], 1, 4), 1, 2), ALU.add).then_inc(out_read.sem, 1)
                    one(0, 0)
                    one(0, 1)
                    second(0, 0)
                    with dve.Fori(1, PAIRS) as g:
                        one(g, 0)
                        second(g - 1, 1)
                        one(g, 1)
                        second(g, 0)
                    second(PAIRS - 1, 1)
                    dve.wait_ge(deviation.sem, deviation.at(1))
                    nc.vector.scalar_tensor_tensor(out=KC[:], in0=rsc, scalar=qkg[:, 1:2], in1=KC[:],
                                                   op0=ALU.mult, op1=ALU.mult)
                    dve_step.count = step.n
            mlp_in.close(80)
            loads.close(256)
            dve_step.close(dve_step.count)
            turned.close(3)
            turned_read.close(3)
            chosen.close(8)
            for s in (logit_ready, keep_ready, logged, weight_ready, out_ready, out_read):
                s.close(2 * PAIRS)
            for s in page_in + value_in:
                s.close(LOADED * PAIRS)
            for s in (squared, summed, variance, deviation):
                s.close(1)

        def sparse_prompt(Q2, kskw, vsvw, GT, KC, VC, OT, load_first_keys):
            BATCHES = [(t, v) for t in range(2) for v in range(4)]
            with ExitStack() as stage:
                def tile(name, shape):
                    return sb(name, shape, F32, stage)
                B1 = tile("B1", [P, 16, 256])
                zs = [tile(f"zs{i}", [P, 8, 256]) for i in range(2)]
                zc = [tile(f"zc{i}", [P, 4, 16]) for i in range(2)]
                mx = tile("mx", [P, 2, 12])
                sm = tile("sm", [P, 2, 12])
                pT = H[:].rearrange("p k n -> p (k n)").rearrange("p (s g q) -> p s g q", s=5, g=4)
                block = stage.enter_context(nc.Block(no_gpsimd_drain=True))

                def shape(t):
                    return P * (t + 1), 7 if t == 0 else 15

                def rounds(t):
                    out = [(2 * br + kt, 4 * br, kt * P) for br in range(2) for kt in range(t + 1)]
                    return out + [(4, None, 0)]
                first_round = []
                for t, v in BATCHES:
                    first_round.append(sum(len(rounds(t2)) for t2, _ in BATCHES[:len(first_round)]))

                @block.sync
                def _(sp):
                    f = io["bias_prompt"].tensor
                    for h, n, sig in ((0, 4, loads), (4, 12, table_in)):
                        sp.dma_start(B1[:, h:h + n, :], bass.AP(f, 127 + h * NDIST_P,
                                                                [[16 * NDIST_P - 1, P], [NDIST_P, n], [1, 256]]))\
                            .then_inc(sig.sem, 16)
                    load_first_keys(sp)
                    store(sp, io["o_wink"], io["win_k"][:, LS:WIN, :])
                    store(sp, io["o_winv"], io["win_v"][:, LS:WIN, :])

                @block.tensor
                def _(pe):
                    def scores(n):
                        t, v = BATCHES[n]
                        nk, ncmp = shape(t)
                        r = slice(64 * (v % 2), 64 * (v % 2) + 64)
                        if n:
                            pe.wait_ge(scaled.sem, scaled.at(n))
                        for g in range(4):
                            q = Q2[r, 4 * (v // 2) + g, t * P:(t + 1) * P]
                            for br in range(2):
                                nc.tensor.matmul(PS[:, 2 * br + g // 2, (g % 2) * 256:(g % 2) * 256 + nk], q,
                                                 kskw[r, 2 * br + v // 2, 0:nk], start=True, stop=True)
                            mm = nc.tensor.matmul(PS[:, 4, 16 * g:16 * g + ncmp], q, KC[r, v // 2, 512:512 + ncmp],
                                                  start=True, stop=True)
                        mm.then_inc(logit_ready.sem, 1)

                    def turn(n):
                        t, v = BATCHES[n]
                        _, ncmp = shape(t)
                        pe.wait_ge(weight_ready.sem, weight_ready.at(n + 1))
                        for k, (slot, row, k0) in enumerate(rounds(t)):
                            at = first_round[n] + k
                            if at >= 2:
                                pe.wait_ge(turned_read.sem, turned_read.at(at - 1))
                            for g in range(4):
                                if row is None:
                                    mm = nc.tensor.transpose(PS[0:ncmp, 5 + at % 2, g * P:(g + 1) * P],
                                                             zc[n % 2][:, g, 0:ncmp], ident[:])
                                else:
                                    mm = nc.tensor.transpose(PS[:, 5 + at % 2, g * P:(g + 1) * P],
                                                             zs[n % 2][:, row + g, k0:k0 + P], ident[:])
                            mm.then_inc(turned.sem, 1)

                    def values(n):
                        t, v = BATCHES[n]
                        _, ncmp = shape(t)
                        last = first_round[n] + len(rounds(t))
                        pe.wait_ge(turned_read.sem, turned_read.at(last))
                        if n:
                            pe.wait_ge(out_read.sem, out_read.at(n))
                        r = slice(64 * (v % 2), 64 * (v % 2) + 64)
                        for g in range(4):
                            to = PS[r, 7, g * P:(g + 1) * P]
                            for br in range(2):
                                for kt in range(t + 1):
                                    nc.tensor.matmul(to, vsvw[:, kt, 256 * br + 64 * v:256 * br + 64 * v + 64],
                                                     pT[:, 2 * br + kt, g, :], start=(br == 0 and kt == 0), stop=False,
                                                     skip_group_check=True)
                            mm = nc.tensor.matmul(to, VC[0:ncmp, NB, 64 * v:64 * v + 64], pT[0:ncmp, 4, g, :],
                                                  start=False, stop=True, skip_group_check=True)
                        mm.then_inc(out_ready.sem, 1)
                    scores(0)
                    for n in range(len(BATCHES)):
                        if n + 1 < len(BATCHES):
                            scores(n + 1)
                        turn(n)
                        values(n)

                @block.scalar
                def _(act):
                    def exps(n):
                        nk, ncmp = shape(BATCHES[n][0])
                        act.wait_ge(centre_ready.sem, centre_ready.at(n + 1))
                        for j in range(12):
                            z = zs[n % 2][:, j, 0:nk] if j < 8 else zc[n % 2][:, j - 8, 0:ncmp]
                            last = nc.scalar.activation(z, z, ACT.Exp, bias=mx[:, n % 2, j:j + 1],
                                                        accum_out=sm[:, n % 2, j:j + 1])
                        last.then_inc(exponent.sem, 1)

                    def copies(n):
                        t, _ = BATCHES[n]
                        _, ncmp = shape(t)
                        if n:
                            act.wait_ge(out_ready.sem, out_ready.at(n))
                        for k, (slot, row, k0) in enumerate(rounds(t)):
                            at = first_round[n] + k
                            act.wait_ge(turned.sem, turned.at(at + 1))
                            rows = P if row is not None else ncmp
                            nc.scalar.activation(pT[0:rows, slot, :, :].rearrange("p g q -> p (g q)"),
                                                 PS[0:rows, 5 + at % 2, :], ACT.Copy).then_inc(turned_read.sem, 1)
                    exps(0)
                    for n in range(len(BATCHES)):
                        copies(n)
                        if n + 1 < len(BATCHES):
                            exps(n + 1)

                @block.vector
                def _(dve):
                    step = Chain(dve, dve_step)
                    dve.wait_ge(loads.sem, loads.at(16))

                    def last_dim(ap, n):
                        return bass.AP(ap.tensor, ap.offset, [list(x) for x in ap.ap] + [[0, n]])

                    def centre(n):
                        t, v = BATCHES[n]
                        nk, ncmp = shape(t)
                        z, c, m = zs[n % 2], zc[n % 2], mx[:, n % 2, :]
                        bias = B1[:, 4 * v:4 * v + 4, 0:nk] if t else B1[:, 4 * v:4 * v + 4, P:2 * P]
                        k0 = 31 if t else P + 31
                        bias_c = B1[:, 4 * v:4 * v + 4, k0:k0 + 16 * (ncmp - 1) + 1:16]
                        dve.wait_ge(logit_ready.sem, logit_ready.at(n + 1))
                        if n >= 2:
                            dve.wait_ge(turned.sem, turned.at(first_round[n - 1]))
                        zp = PS[:, 0:4, :].rearrange("p a (h k) -> p (a h) k", h=2)[:, :, 0:nk]
                        nc.vector.tensor_tensor(z[:, :, 0:nk].rearrange("p (b g) k -> p b g k", b=2),
                                                zp.rearrange("p (b g) k -> p b g k", b=2), rep(bias, 1, 2), ALU.add)
                        nc.vector.tensor_tensor(c[:, :, 0:ncmp],
                                                PS[:, 4, 0:64].rearrange("p (g k) -> p g k", g=4)[:, :, 0:ncmp],
                                                bias_c, ALU.add).then_inc(scaled.sem, 1)
                        dve.wait_ge(scaled.sem, scaled.at(n + 1))
                        nc.vector.tensor_reduce(m[:, 0:8], z[:, :, 0:nk], AX.X, ALU.max, negate=True)
                        step(nc.vector.tensor_reduce(m[:, 8:12], c[:, :, 0:ncmp], AX.X, ALU.max, negate=True))
                        nc.vector.tensor_scalar(m, m, -NEG / 10, None, ALU.min).then_inc(centre_ready.sem, 1)

                    def weights(n):
                        t, v = BATCHES[n]
                        nk, ncmp = shape(t)
                        z, c, s = zs[n % 2], zc[n % 2], sm[:, n % 2, :]
                        dve.wait_ge(exponent.sem, exponent.at(n + 1))
                        step(nc.vector.tensor_scalar(s, s, 1e-30, None, ALU.max))
                        step(nc.vector.reciprocal(s, s))
                        gate = GT[:, t, 12 * v:12 * v + 12].rearrange("p (g b) -> p b g", b=3)
                        nc.vector.tensor_tensor(s[:, 0:8].rearrange("p (b g) -> p b g", b=2),
                                                s[:, 0:8].rearrange("p (b g) -> p b g", b=2), gate[:, 1:3, :], ALU.mult)
                        step(nc.vector.tensor_tensor(s[:, 8:12], s[:, 8:12], gate[:, 0, :], ALU.mult))
                        nc.vector.tensor_tensor(z[:, :, 0:nk], z[:, :, 0:nk], last_dim(s[:, 0:8], nk), ALU.mult)
                        nc.vector.tensor_tensor(c[:, :, 0:ncmp], c[:, :, 0:ncmp], last_dim(s[:, 8:12], ncmp),
                                                ALU.mult).then_inc(weight_ready.sem, 1)

                    def outs(n):
                        t, v = BATCHES[n]
                        r = slice(64 * (v % 2), 64 * (v % 2) + 64)
                        dve.wait_ge(out_ready.sem, out_ready.at(n + 1))
                        nc.vector.tensor_copy(OT[r, 4 * (v // 2):4 * (v // 2) + 4, t * P:(t + 1) * P],
                                              PS[r, 7, :].rearrange("p (g q) -> p g q", g=4)).then_inc(out_read.sem, 1)
                    centre(0)
                    for n in range(len(BATCHES)):
                        weights(n)
                        if n:
                            outs(n - 1)
                        if n == 0:
                            dve.wait_ge(table_in.sem, table_in.at(16))
                        if n + 1 < len(BATCHES):
                            centre(n + 1)
                    outs(len(BATCHES) - 1)
                    dve_step.count = step.n
            table_in.close(16)
            stored.close(32)
            loads.close(16)
            dve_step.close(dve_step.count)
            for s in (logit_ready, scaled, centre_ready, exponent, weight_ready, out_ready, out_read):
                s.close(len(BATCHES))
            n = sum(len(rounds(t)) for t, _ in BATCHES)
            turned.close(n)
            turned_read.close(n)

        def sparse_sample(Q2, kskw, vsvw, GS, Bs, Bw, KC, VC, OT, KS, KW, pages):
            NC = PAST // 16 - 1
            NS, NW = PAST + LS, WIN + LS
            LOADED = 16 * (NPG + 1)
            HALF = NPG // 2
            LOADED_V = 16 * (NPG - HALF + 2)
            with ExitStack() as stage:
                def tile(name, shape):
                    return sb(name, shape, F32, stage)
                KS = KS + [tile("KS1", [P, NPG, 2, P])]
                KW = KW + [tile("KW1", [P, 2, WIN])]
                VS = tile("VS", [P, NPG, 256])
                VW = tile("VW", [P, 4, 256])
                VN = vsvw[0:LS, 0, :]
                QB = tile("QB2", [P, 2, P])
                pT = tile("pT2", [P, 15, P])
                free = H[:].rearrange("p k n -> p (k n)")
                work = [free[:, 0:NS + NW + NC], tile("z1", [P, NS + NW + NC])[:]]
                zs = [w[:, 0:NS] for w in work]
                zw = [w[:, NS:NS + NW] for w in work]
                zc = [w[:, NS + NW:NS + NW + NC] for w in work]
                pc = free[:, 1640:1640 + NC]
                hit = free[:, 1710:1724]
                drop = free[:, 1730:1746]
                block_no = free[:, 1750:1766]
                stats = [free[:, 1770 + 10 * i:1780 + 10 * i] for i in range(2)]
                same_q = free[:, 1920:1920 + P]
                VCs = free[0:64, 2048:2304]
                out_rows = free[:, 2304:2304 + P]
                zsp = PS[:, 0:3, :].rearrange("p a n -> p (a n)")[:, 0:NS]
                zwp = PS[:, 3:5, :].rearrange("p a n -> p (a n)")[:, 0:NW]
                zcp = PS[:, 2, 256:256 + NC]
                block = stage.enter_context(nc.Block(no_gpsimd_drain=True))
                BUILT = 12

                def load(eng, b, what, sig, used=None):
                    i = sig[1]
                    src = io["slc_kT"] if what == "keys" else io["slc_v"]
                    span = {"keys": range(NPG), "first values": range(HALF), "values": range(HALF, NPG)}[what]
                    for p in span:
                        at = b * NPG + p
                        cell = pages[0:1, at:at + 1] if isinstance(at, int) else pages[0:1, bass.ds(at, 1)]
                        page = eng.value_load(cell, min_val=0, max_val=NPOOL - 1)
                        if p == span[0] and used is not None:
                            eng.wait_ge(*used)
                        dst = KS[i][:, p, :, :].rearrange("p a n -> p (a n)") if what == "keys" else VS[:, p, :]
                        eng.dma_start(dst, src[bass.ds(page, 1), :, :].rearrange("a p n -> p (a n)"))\
                            .then_inc(sig[0].sem, 16)
                    one = slice(b, b + 1) if isinstance(b, int) else bass.ds(b, 1)
                    new = slice(LS * b, LS * b + LS) if isinstance(b, int) else bass.ds(b * LS, LS)
                    if what == "keys":
                        eng.dma_start(KW[i][:].rearrange("p t n -> p (t n)"),
                                      io["win_kT"][one, :, :].rearrange("a p n -> p (a n)")).then_inc(sig[0].sem, 16)
                    elif what == "values":
                        eng.dma_start(VW[:], io["win_v"][one, :, :].rearrange("a (c p) n -> p (a c) n", p=P))\
                            .then_inc(sig[0].sem, 16)
                        eng.dma_start(VN, io["new_rows"][1, new, :]).then_inc(sig[0].sem, 16)

                @block.sync
                def _(sp):
                    load(sp, 1, "keys", (page_in[1], 1))
                    load(sp, 0, "first values", (first_values_in, 0))
                    with sp.Fori(1, NB // 2) as g:
                        for i in range(2):
                            load(sp, 2 * g + i, "keys", (page_in[i], i), (logit_ready.sem, logit_ready.at(i - 1) + 2 * g))
                            load(sp, 2 * g + (i - 1), "first values", (first_values_in, 0),
                                 (out_ready.sem, out_ready.at(i - 1) + 2 * g))
                    load(sp, NB - 1, "first values", (first_values_in, 0), (out_ready.sem, out_ready.at(NB - 1)))

                @block.gpsimd
                def _(pool):
                    step = Chain(pool, pool_step)

                    def pick(t, op, base, pattern, mult, fill=0.0):
                        step(pool.affine_select(out=t, in_=t, compare_op=op, fill=fill, base=base, pattern=pattern,
                                                channel_multiplier=mult))
                    step(pool.memset(QB[:], 0.0))
                    step(pool.memset(same_q, 0.0))
                    for d in range(-3, 4):
                        pick(same_q, ALU.not_equal, -8 * d, [[-1, P]], 1, 1.0)
                    v = same_q.rearrange("p (c i) -> p c i", i=32)
                    pick(v, ALU.is_ge, 0, [[-32, 4], [0, 32]], 1)
                    pick(v, ALU.is_ge, 31, [[32, 4], [0, 32]], -1)
                    step(pool.iota(block_no, pattern=[[1, 16]], base=0, channel_multiplier=0,
                                   allow_small_or_imprecise_dtypes=True))
                    assert step.n == BUILT
                    pool_step.count = step.n
                    pool.wait_ge(stored.sem, stored.at(0))
                    load(pool, 0, "values", (value_in[0], 0))
                    with pool.Fori(1, NB) as b:
                        load(pool, b, "values", (value_in[0], 0), (out_ready.sem, out_ready.at(0) + b))

                def pipeline(eng, scores, values, step=None, per=0):
                    scores(0, 0)
                    with eng.Fori(0, NB // 2 - 1) as g:
                        if step is not None:
                            step.loop(g, per)
                        for i in range(2):
                            b = 2 * g + i
                            scores(b + 1, 1 - i)
                            values(b, i)
                        if step is not None:
                            step.done(NB // 2 - 1)
                    scores(NB - 1, 1)
                    values(NB - 2, 0)
                    values(NB - 1, 1)

                @block.tensor
                def _(pe):
                    def scores(b, i):
                        pe.wait_ge(page_in[i].sem, page_in[i].at(LOADED - i * (LOADED // 2)) + b * (LOADED // 2))
                        pe.wait_ge(seq_ready.sem, seq_ready.at(1) + b)
                        for t in range(2):
                            mm = nc.tensor.matmul(zcp, QB[:, t, :], KC[:, t, bass.ds(b * 64, NC)] if not
                                                  isinstance(b, int) else KC[:, t, 64 * b:64 * b + NC],
                                                  start=(t == 0), stop=(t == 1))
                        mm.then_inc(chosen.sem, 1)
                        new = bass.ds(b * LS + NPR, LS) if not isinstance(b, int) else \
                            slice(LS * b + NPR, LS * b + NPR + LS)
                        for bank, keys in ((0, KS[i][:, 0:4]), (1, KS[i][:, 4:8]), (3, None)):
                            for kv in range(4):
                                r = slice(32 * kv, 32 * kv + 32)
                                k = KW[i][:, kv // 2, :] if keys is None else keys[:, :, kv // 2, :]
                                nc.tensor.matmul(PS[r, bank, :], QB[:, kv // 2, r], k, start=True, stop=True)
                        for t in range(2):
                            nc.tensor.matmul(PS[:, 4, 0:LS], QB[:, t, :], kskw[:, 2 + t, new],
                                             start=(t == 0), stop=(t == 1))
                        pe.wait_ge(scaled.sem, scaled.at(1) + 2 * b)
                        for t in range(2):
                            mm = nc.tensor.matmul(PS[:, 2, 0:LS], QB[:, t, :], kskw[:, t, new],
                                                  start=(t == 0), stop=(t == 1))
                        mm.then_inc(logit_ready.sem, 1)
                        pe.wait_ge(keep_ready.sem, keep_ready.at(1) + b)
                        nc.tensor.matmul(PS[:, 5, 0:NC], same_q, pc, start=True, stop=True).then_inc(chosen.sem, 1)

                    def values(b, i):
                        pe.wait_ge(weight_ready.sem, weight_ready.at(1) + b)
                        pe.wait_ge(out_read.sem, out_read.at(0) + 2 * b)
                        rounds = [[(P, P * k, zs[i][:, (4 * n + k) * P:(4 * n + k + 1) * P]) for k in range(4)]
                                  for n in range(2)]
                        rounds.append([(P, P * k, zw[i][:, k * P:(k + 1) * P]) for k in range(4)])
                        rounds.append([(LS, 0, zs[i][:, PAST:NS]), (LS, P, zw[i][:, WIN:NW]), (NC, 2 * P, zc[i])])
                        for n, items in enumerate(rounds):
                            if n >= 2:
                                pe.wait_ge(turned_read.sem, turned_read.at(n - 1) + 4 * b)
                            for rows, c, src in items:
                                mm = nc.tensor.transpose(PS[0:rows, 6 + n % 2, c:c + P], src, ident[:])
                            mm.then_inc(turned.sem, 1)
                        pe.wait_ge(turned_read.sem, turned_read.at(4) + 4 * b)
                        pe.wait_ge(value_in[0].sem, value_in[0].at(LOADED_V) + b * LOADED_V)
                        pe.wait_ge(first_values_in.sem, first_values_in.at(16 * HALF) + b * (16 * HALF))
                        pe.wait_ge(scaled.sem, scaled.at(4) + 2 * b if not isinstance(b, int) else
                                   scaled.at(min(4 + 2 * b, 2 * NB)))
                        parts = [(VS[:, k, :], k, P) for k in range(NPG)] + [(VW[:, k, :], 8 + k, P) for k in range(4)]
                        parts += [(VN[:, 0:256], 12, LS), (VN[:, 256:512], 13, LS), (VCs[0:NC, :], 14, NC)]
                        for n, (v, k, rows) in enumerate(parts):
                            for kv in range(4):
                                r = slice(32 * kv, 32 * kv + 32)
                                mm = nc.tensor.matmul(PS[r, 4, 256:320], pT[0:rows, k, r], v[:, 64 * kv:64 * kv + 64],
                                                      start=(n == 0), stop=(n == len(parts) - 1))
                        mm.then_inc(out_ready.sem, 1)
                        pe.wait_ge(tail_ready.sem, tail_ready.at(1) + b)
                        nc.tensor.transpose(PS[:, 6, 0:P], out_rows, ident[:]).then_inc(summed.sem, 1)

                    pe.wait_ge(pool_step.sem, pool_step.at(BUILT))
                    pipeline(pe, scores, values)

                @block.scalar
                def _(act):
                    def scores(b, i):
                        at = bass.ds(b * LS + NPR, LS) if not isinstance(b, int) else \
                            slice(LS * b + NPR, LS * b + NPR + LS)
                        act.wait_ge(logit_ready.sem, logit_ready.at(0) + b)
                        for kvh in range(2):
                            r = slice(64 * kvh, 64 * kvh + 64)
                            for t in range(2):
                                c = 32 * (2 * t + kvh)
                                last = nc.scalar.activation(QB[r, t, c:c + 32].rearrange("p (g q) -> p g q", g=4),
                                                            Q2[r, 4 * t:4 * t + 4, at], ACT.Copy)
                        last.then_inc(seq_ready.sem, 1)
                        st = stats[i]
                        act.wait_ge(centre_ready.sem, centre_ready.at(1) + 2 * b)
                        nc.scalar.activation(zc[i], zc[i], ACT.Exp, bias=st[:, 0:1], accum_out=st[:, 1:2])\
                            .then_inc(exponent.sem, 1)

                    def exps(b, i):
                        st = stats[i]
                        act.wait_ge(centre_ready.sem, centre_ready.at(2) + 2 * b)
                        nc.scalar.activation(zw[i], zw[i], ACT.Exp, bias=st[:, 4:5], accum_out=st[:, 7:8])
                        nc.scalar.activation(zs[i], zs[i], ACT.Exp, bias=st[:, 3:4], accum_out=st[:, 6:7])\
                            .then_inc(exponent.sem, 1)

                    def copies(b, i):
                        act.wait_ge(out_ready.sem, out_ready.at(0) + b)
                        one = bass.ds(b, 1) if not isinstance(b, int) else slice(b, b + 1)
                        nc.scalar.activation(VCs, VC[:, one, :].rearrange("p a n -> p (a n)"), ACT.Copy)
                        for n in range(3):
                            act.wait_ge(turned.sem, turned.at(n + 1) + 4 * b)
                            nc.scalar.activation(pT[:, 4 * n:4 * n + 4, :].rearrange("p k r -> p (k r)"),
                                                 PS[:, 6 + n % 2, :], ACT.Copy).then_inc(turned_read.sem, 1)
                        act.wait_ge(turned.sem, turned.at(4) + 4 * b)
                        nc.scalar.activation(pT[0:LS, 12:14, :].rearrange("p k r -> p (k r)"), PS[0:LS, 7, 0:2 * P],
                                             ACT.Copy)
                        nc.scalar.activation(pT[0:NC, 14, :], PS[0:NC, 7, 2 * P:3 * P], ACT.Copy)\
                            .then_inc(turned_read.sem, 1)

                    def first(b, i):
                        scores(b, i)
                        if isinstance(b, int) and b == 0:
                            exps(b, i)

                    def values(b, i):
                        copies(b, i)
                        if not isinstance(b, int) or b + 1 < NB:
                            exps(b + 1, 1 - i)
                    act.wait_ge(pool_step.sem, pool_step.at(BUILT))
                    pipeline(act, first, values)

                @block.vector
                def _(dve):
                    step = Chain(dve, dve_step)

                    def weights(b, i):
                        st = stats[i]
                        gate = gates(b)
                        dve.wait_ge(exponent.sem, exponent.at(2) + 2 * b)
                        step(nc.vector.reciprocal(st[:, 6:8], st[:, 6:8]))
                        step(nc.vector.tensor_tensor(st[:, 6:8], st[:, 6:8], gate[:, 1:3], ALU.mult))
                        nc.vector.tensor_scalar(zw[i], zw[i], st[:, 7:8], None, ALU.mult)
                        nc.vector.tensor_scalar(zs[i], zs[i], st[:, 6:7], None, ALU.mult).then_inc(weight_ready.sem, 1)

                    def gates(b):
                        one = bass.ds(b, 1) if not isinstance(b, int) else slice(b, b + 1)
                        return GS[:, one, :].rearrange("p a c -> p (a c)")

                    def scores(b, i):
                        st = stats[i]
                        dve.wait_ge(chosen.sem, chosen.at(1) + 2 * b)
                        nc.vector.tensor_tensor(zc[i], zcp, Bs[:, 31:31 + 16 * (NC - 1) + 1:16], ALU.add)\
                            .then_inc(scaled.sem, 1)
                        dve.wait_ge(scaled.sem, scaled.at(1) + 2 * b)
                        nc.vector.tensor_reduce(st[:, 0:1], zc[i], AX.X, ALU.max, negate=True)\
                            .then_inc(centre_ready.sem, 1)
                        if not isinstance(b, int) or b > 0:
                            weights(b - 1, 1 - i)
                        dve.wait_ge(exponent.sem, exponent.at(1) + 2 * b)
                        step(nc.vector.reciprocal(st[:, 2:3], st[:, 1:2]))
                        nc.vector.tensor_scalar(pc, zc[i], st[:, 2:3], None, ALU.mult).then_inc(keep_ready.sem, 1)
                        dve.wait_ge(keep_ready.sem, keep_ready.at(1) + b)
                        step(nc.vector.tensor_scalar(zc[i], pc, gates(b)[:, 0:1], None, ALU.mult))
                        dve.wait_ge(logit_ready.sem, logit_ready.at(1) + b)
                        nc.vector.tensor_tensor(zw[i], zwp, Bw[:], ALU.add)
                        nc.vector.tensor_tensor(zs[i], zsp, Bs[:], ALU.add).then_inc(scaled.sem, 1)
                        dve.wait_ge(chosen.sem, chosen.at(2) + 2 * b)
                        w = PS[:, 5, 3:4]
                        w = bass.AP(w.tensor, w.offset, [list(w.ap[0]), [4, 14], [1, 5]])
                        step(nc.vector.tensor_reduce(drop[:, 0:14], w, AX.X, ALU.add))
                        step(nc.vector.tensor_reduce(st[:, 8:9], drop[:, 0:14], AX.X, ALU.min))
                        step(nc.vector.scalar_tensor_tensor(out=hit, in0=drop[:, 0:14], scalar=st[:, 8:9],
                                                            in1=block_no[:, 1:15], op0=ALU.is_le, op1=ALU.mult))
                        step(nc.vector.tensor_reduce(st[:, 9:10], hit, AX.X, ALU.max))
                        step(nc.vector.tensor_scalar(drop, block_no, st[:, 9:10], NEG, ALU.is_equal, ALU.mult))
                        dve.wait_ge(scaled.sem, scaled.at(2) + 2 * b)
                        d = bass.AP(drop.tensor, drop.offset, [list(x) for x in drop.ap] + [[0, 64]])
                        v = zs[i][:, 0:PAST].rearrange("p (j k) -> p j k", j=16)
                        step(nc.vector.tensor_tensor(v, v, d, ALU.add))
                        nc.vector.tensor_reduce(st[:, 4:5], zw[i], AX.X, ALU.max, negate=True)
                        nc.vector.tensor_reduce(st[:, 3:4], zs[i], AX.X, ALU.max, negate=True)\
                            .then_inc(centre_ready.sem, 1)

                    def values(b, i):
                        if isinstance(b, int) and b == NB - 1:
                            weights(b, i)
                        dve.wait_ge(out_ready.sem, out_ready.at(1) + b)
                        nc.vector.tensor_copy(out_rows.rearrange("p (k d) -> p k d", k=2),
                                              rep(PS[:, 4, 256:320], 1, 2)).then_inc(tail_ready.sem, 1)
                        dve.wait_ge(summed.sem, summed.at(1) + b)
                        at = bass.ds(b * LS + NPR, LS) if not isinstance(b, int) else \
                            slice(LS * b + NPR, LS * b + NPR + LS)
                        for kvh in range(2):
                            r = slice(64 * kvh, 64 * kvh + 64)
                            src = PS[r, 6, 0:P].rearrange("p (t k g q) -> p t k g q", t=2, k=2, g=4)[:, :, kvh, :, :]
                            to = OT[r, :, at].rearrange("p (t g) q -> p t g q", t=2)
                            nc.vector.tensor_copy(to, src).then_inc(out_read.sem, 1)
                    dve.wait_ge(pool_step.sem, pool_step.at(BUILT))
                    pipeline(dve, scores, values, step, 20)
                    dve_step.count = step.n
            pool_step.close(pool_step.count)
            dve_step.close(dve_step.count)
            for s in (logit_ready, weight_ready, out_ready, seq_ready, keep_ready, tail_ready, summed):
                s.close(NB)
            for s in (scaled, centre_ready, exponent, out_read, chosen):
                s.close(2 * NB)
            turned.close(4 * NB)
            turned_read.close(4 * NB)
            for s in page_in:
                s.close(LOADED * (NB // 2))
            value_in[0].close(LOADED_V * NB)
            first_values_in.close(16 * HALF * NB)
        n = 0
        n = first_ada_stage(n)
        n = ffn_stage(0, 0, n, 0, ADA_FIRST, ADA_SLOTS - ADA_FIRST)
        n = even_stage(n)
        n = ffn_stage(0, 1, n, 1, 0, ADA_SLOTS)
        n = ffn_stage(1, 0, n)
        n = odd_stage(n)
        n = ffn_stage(1, 1, n)
        assert n == NSLOT

        with nc.Block() as block:
            @block.sync
            def _(sp):
                sp.dma_start(io["yT"], X[:]).then_inc(stored.sem, 16)
                sp.wait_ge(stored.sem, stored.at(16))


def bucket_one_hot():
    dist = DIST_HI - np.arange(NDIST)
    d = np.maximum(dist, 0)
    ratio = np.log(np.maximum(d, 16).astype(np.float32) / np.float32(16)) / np.float32(math.log(1024 / 16))
    bucket = np.where(d < 16, d, np.minimum(16 + (ratio * np.float32(16)).astype(np.int32), 31))
    bucket = np.where(dist < 0, 32, bucket)
    return (np.arange(33)[:, None] == bucket[None, :]).astype(np.float32)


def slots_of(w):
    n = w.shape[1] // 512
    return w.reshape(KT, P, n, 512).transpose(2, 1, 0, 3).reshape(n, P, SLOT)


def weight_slots(i):
    out = []

    def ffn(l, f, ada=None):
        w = i["ffn_w_in"][l, f].reshape(D, 2, DFF // 256, 256).transpose(0, 2, 1, 3).reshape(D, 2 * DFF)
        w_in = slots_of(w)
        w = np.zeros((OUT_GROUPS * D, D), np.float32)
        w[:DFF] = i["ffn_w_out"][l, f]
        w = w.reshape(OUT_GROUPS, D, D)
        w = np.stack([slots_of(w[g]) for g in range(OUT_GROUPS)], axis=1)
        w_out = w.reshape(OUT_SLOTS, P, SLOT)
        before, body, rounds, after = ffn_plan(0 if ada is None else len(ada))
        per_h = sum(kind == "h" for kind, _ in body)
        order = before + [(kind, k + r * (per_h if kind == "h" else 2)) for r in range(rounds)
                          for kind, k in body] + after
        at = {"h": w_in, "o": w_out, "a": ada}
        out.append(np.stack([at[kind][k] for kind, k in order]))

    ada = [slots_of(i["ada_w"][l]) for l in range(2)]
    out.append(ada[0][:ADA_FIRST])
    ffn(0, 0, ada[0][ADA_FIRST:])
    w = i["even_w_in"][0]
    out.append(slots_of(w[:, :3072]))
    out.append(slots_of(i["even_w_out"][0]))
    ffn(0, 1, ada[1])
    ffn(1, 0)
    w = i["odd_w_in"][0]
    q = w[:, :1024].reshape(D, 2, 2, 4, 64).transpose(0, 1, 3, 2, 4).reshape(D, 1024)
    kc, vc, ks, vs, kw, vw = [w[:, 1024 + 256 * n:1280 + 256 * n] for n in range(6)]
    out.append(slots_of(np.concatenate([q, kc, vc, ks, kw, vs, vw], axis=1)))
    wo = i["odd_w_out"][0].reshape(2, 2, 4, 64, D).transpose(0, 2, 1, 3, 4).reshape(D, D)
    out.append(slots_of(wo))
    ffn(1, 1)
    return np.concatenate(out, axis=0)


def lay_out(i):
    def feat(a):
        a = a.reshape(a.shape[:-1] + (KT, P))
        return np.moveaxis(a, -1, 0)

    x = np.concatenate([i["x_prompt"].reshape(NPR, D), i["x_sample"].reshape(NB * LS, D)])
    c = np.concatenate([i["c_prompt"], i["c_sample"]])
    a = {}
    a["xT"] = feat(x).transpose(0, 2, 1)
    a["cT"] = feat(c).transpose(0, 2, 1)
    a["norm_gT"] = feat(i["norm_g"])
    a["ada_bT"] = feat(i["ada_b"].reshape(2, 9, D)).reshape(P, 2, 9 * KT)
    a["w_slots"] = weight_slots(i)
    a["w_a1"] = i["even_w_in"][0][:, 3072:].reshape(KT, P, 16).transpose(1, 0, 2)
    a["w_a2"] = i["gla_w_a2"][0]
    a["b_a2"] = i["gla_b_a2"]
    a["onorm_g"] = i["gla_onorm_g"].reshape(P, 1)
    a["w_gt"] = i["odd_w_in"][0][:, 2560:].reshape(KT, P, 48).transpose(1, 0, 2)
    a["pages"] = i["page_table"].reshape(1, NB * NPG)
    a["sb_kT"] = i["cache_sb_k"][0].reshape(NPOOL, PAGE, 4, P).transpose(0, 3, 2, 1).reshape(NPOOL, P, 4 * PAGE)
    a["sb_v"] = i["cache_sb_v"][0].reshape(NPOOL, PAGE, 512)
    a["gla_s"] = i["state_gla"][0].reshape(NB, 2, P, P).transpose(2, 0, 1, 3)
    a["slc_kT"] = i["cache_slc_k"][0].reshape(NPOOL, PAGE, 2, P).transpose(0, 3, 2, 1).reshape(NPOOL, P, 2 * PAGE)
    a["slc_v"] = i["cache_slc_v"][0].reshape(NPOOL, PAGE, 256)
    for n in "kv":
        t = i["cache_cmp_" + n][0].reshape(NPOOL, 8, 8, 2, 4, 64)
        a["cmp_" + n] = t.transpose(0, 3, 5, 4, 2, 1).reshape(NPOOL, P, 256)
    a["win_kT"] = i["cache_win_k"][0].reshape(NB, WIN, 2, P).transpose(0, 3, 2, 1).reshape(NB, P, 2 * WIN)
    a["win_k"] = i["cache_win_k"][0].reshape(NB, WIN, 256)
    a["win_v"] = i["cache_win_v"][0].reshape(NB, WIN, 256)
    g = i["nsa_qk_g"][0].T
    a["qk_g"] = np.concatenate([g, g])
    w1 = i["cmp_w1"][0].reshape(2, 2, 8, P, P)
    a["cmp_w1"] = w1.transpose(3, 0, 1, 2, 4)
    a["cmp_b1"] = i["cmp_b1"][0].T
    a["cmp_w2"] = i["cmp_w2"][0].transpose(1, 0, 2)
    b2 = i["cmp_b2"][0]
    a["cmp_b2k"] = np.concatenate([b2[0], b2[0]]).reshape(P, 1)
    a["cmp_b2v"] = b2[1:2]
    a["rel_table"] = i["rel_table"]
    a["one_hot"] = bucket_one_hot()
    return {k: np.ascontiguousarray(v) for k, v in a.items()}


OUTS = {
    "yT": (P, KT, NT), "o_sbk": (P, 4, NT), "o_sbv": (NT, 512), "o_pgla": (P, 2, P), "o_sgla": (P, NB, 2, P),
    "o_kcvc": (P, 4, NT), "o_kskw": (P, 4, NT), "o_vsvw": (NT, 512),
    "o_wink": (NB, WIN - LS, 256), "o_winv": (NB, WIN - LS, 256),
}


def kernel(**inputs):
    import concourse.bacc as _bacc
    from concourse.bass_utils import run_bass_kernel_spmd as _run

    arrays = lay_out({k: np.asarray(v) for k, v in inputs.items()})
    nc = _bacc.Bacc("TRN2", target_bir_lowering=False, num_devices=1)
    io = {}
    for name, a in arrays.items():
        io[name] = nc.dram_tensor(name, a.shape, mybir.dt.from_np(a.dtype), kind="ExternalInput").ap()
    for name, shape in OUTS.items():
        io[name] = nc.dram_tensor(name, shape, F32, kind="ExternalOutput").ap()
    io["bias_rows"] = nc.dram_tensor("bias_rows", (P, NDIST), F32, kind="Internal").ap()
    io["bias_prompt"] = nc.dram_tensor("bias_prompt", (P, 16, NDIST_P), F32, kind="Internal").ap()
    io["gate_rows"] = nc.dram_tensor("gate_rows", (NB, LS, 16, 3), F32, kind="Internal").ap()
    io["new_rows"] = nc.dram_tensor("new_rows", (2, NB * LS, 512), F32, kind="Internal").ap()
    build(nc, io)
    o = _run(nc, [arrays], core_ids=[0]).results[0]

    def rows(t, heads):
        t = t.transpose(2, 1, 0).reshape(NT, heads, 64)
        return t[:NPR].reshape(1, 1, NPR, heads, 64), t[NPR:].reshape(1, NB, LS, heads, 64)

    def natural(t, heads):
        t = t.reshape(NT, heads, 64)
        return t[:NPR].reshape(1, 1, NPR, heads, 64), t[NPR:].reshape(1, NB, LS, heads, 64)

    y = o["yT"].transpose(2, 1, 0).reshape(NT, D)
    p_sbk, s_sbk = rows(o["o_sbk"], 8)
    p_sbv, s_sbv = natural(o["o_sbv"], 8)
    p_gla = o["o_pgla"].transpose(1, 0, 2).reshape(1, 1, 4, 64, P)
    s_gla = o["o_sgla"].transpose(1, 2, 0, 3).reshape(1, NB, 4, 64, P)
    p_kc, s_kc = rows(o["o_kcvc"][:, 0:2], 4)
    p_vc, s_vc = rows(o["o_kcvc"][:, 2:4], 4)
    p_ks, s_ks = rows(o["o_kskw"][:, 0:2], 4)
    p_kw, s_kw = rows(o["o_kskw"][:, 2:4], 4)
    p_vs, s_vs = natural(o["o_vsvw"][:, 0:256], 4)
    p_vw, s_vw = natural(o["o_vsvw"][:, 256:512], 4)

    def window(old, new):
        return np.concatenate([old.reshape(1, NB, WIN - LS, 4, 64), new], axis=2)

    return (y[:NPR].reshape(1, NPR, D), y[NPR:].reshape(NB, LS, D), p_sbk, p_sbv, p_gla, p_kc, p_vc, p_ks, p_vs,
            p_kw, p_vw, s_sbk, s_sbv, s_gla, s_kc, s_vc, s_ks, s_vs, window(o["o_wink"], s_kw),
            window(o["o_winv"], s_vw))
```
